# Optimizing a Trainium2 kernel written in Bass

```python
import math
import jax, jax.numpy as jnp
from jax import lax
import numpy as np
import jax
import jax.numpy as jnp

D_MODEL = 1024
BATCH = 1
SEQ = 256
DEPTH = 2

N_MIXERS = 4
ALPHA = (2 * DEPTH) ** 0.25
BETA = (8 * DEPTH) ** -0.25
LN_EPS = 1e-5

ML_HEADS = 4
ML_DV = D_MODEL // ML_HEADS
ML_DK = ML_DV // 2
ML_CHUNK = 64
ML_IN = 2 * ML_HEADS * ML_DK + 2 * D_MODEL + 4 * ML_HEADS

GLA_HEADS = 4
GLA_DK = D_MODEL // 2 // GLA_HEADS
GLA_DV = D_MODEL // GLA_HEADS
GLA_RANK = 16
GLA_TAU = 16.0
GLA_CHUNK = 32
GLA_IN = 2 * GLA_HEADS * GLA_DK + 2 * D_MODEL + 2 * GLA_RANK

LRU_WIDTH = D_MODEL
LRU_BLOCKS = 4
LRU_BW = LRU_WIDTH // LRU_BLOCKS
CONV_WIDTH = 4
LRU_C = 8.0
LRU_IN = 2 * LRU_WIDTH

MLA_HEADS = 8
MLA_NOPE = 128
MLA_ROPE = 64
MLA_DV = 128
MLA_Q_RANK = 384
MLA_KV_RANK = 256
MLA_IN = MLA_Q_RANK + MLA_KV_RANK + MLA_ROPE
ROPE_THETA = 10000.0
Q_BLOCK = 128

N_EXPERTS = 16
EXPERT_FF = 1024
CAPACITY_FACTOR = 2

N_MLSTM = (DEPTH - 0 + N_MIXERS - 1) // N_MIXERS
N_GLA = (DEPTH - 1 + N_MIXERS - 1) // N_MIXERS
N_LRU = (DEPTH - 2 + N_MIXERS - 1) // N_MIXERS
N_MLA = (DEPTH - 3 + N_MIXERS - 1) // N_MIXERS


def layer_norm(x, g, b):
    xf = x.astype(jnp.float32)
    mu = jnp.mean(xf, axis=-1, keepdims=True)
    var = jnp.mean(jnp.square(xf - mu), axis=-1, keepdims=True)
    return ((xf - mu) * lax.rsqrt(var + LN_EPS) * g + b).astype(x.dtype)

def rms_norm(x, g):
    xf = x.astype(jnp.float32)
    return (xf * lax.rsqrt(jnp.mean(jnp.square(xf), axis=-1, keepdims=True) + LN_EPS) * g).astype(x.dtype)

def head_norm(h, g):
    hf = h.astype(jnp.float32)
    mu = jnp.mean(hf, axis=-1, keepdims=True)
    var = jnp.mean(jnp.square(hf - mu), axis=-1, keepdims=True)
    hn = (hf - mu) * lax.rsqrt(var + LN_EPS)
    return hn.reshape(h.shape[0], h.shape[1], -1) * g.astype(jnp.float32)

def to_chunks(t, L):
    B, S = t.shape[0], t.shape[1]
    t = t.reshape((B, S // L, L) + t.shape[2:])
    return jnp.moveaxis(t, (1, 2), (0, 3))

def from_chunks(t):
    t = jnp.moveaxis(t, (0, 3), (1, 2))
    return t.reshape((t.shape[0], t.shape[1] * t.shape[2]) + t.shape[3:])

def flip_seq(t):
    return jnp.flip(t, axis=1)

def mlstm_chunked(q, k, v, ig, fg):
    B, S, H, DK = q.shape
    DV = v.shape[-1]
    L = ML_CHUNK
    mask = jnp.tril(jnp.ones((L, L), dtype=bool))

    def step(carry, inp):
        C, n, m = carry
        qb, kb, vb, ib, fb = inp
        b = jnp.cumsum(jax.nn.log_sigmoid(fb), axis=-1)
        g = b[..., -1]
        logD = jnp.where(mask, b[..., :, None] - b[..., None, :] + ib[..., None, :], -jnp.inf)
        inter = b + m[..., None]
        m_t = jnp.maximum(inter, jnp.max(logD, axis=-1))
        s = jnp.einsum('bhtd,bhsd->bhts', qb, kb) * jnp.exp(logD - m_t[..., None])
        w_inter = jnp.exp(inter - m_t)
        num = jnp.einsum('bhts,bhsv->bhtv', s, vb) + w_inter[..., None] * jnp.einsum('bhtd,bhdv->bhtv', qb, C)
        den = jnp.sum(s, axis=-1) + w_inter * jnp.einsum('bhtd,bhd->bht', qb, n)
        h = num / jnp.maximum(jnp.abs(den), jnp.exp(-m_t))[..., None]
        lw = g[..., None] - b + ib
        m_new = jnp.maximum(g + m, jnp.max(lw, axis=-1))
        ws = jnp.exp(lw - m_new[..., None])
        wc = jnp.exp(g + m - m_new)
        kw = kb * ws[..., None]
        C = wc[..., None, None] * C + jnp.einsum('bhsd,bhsv->bhdv', kw, vb)
        n = wc[..., None] * n + jnp.sum(kw, axis=-2)
        return (C, n, m_new), h

    init = (jnp.zeros((B, H, DK, DV), jnp.float32), jnp.zeros((B, H, DK), jnp.float32),
            jnp.zeros((B, H), jnp.float32))
    xs = (to_chunks(q, L), to_chunks(k, L), to_chunks(v, L), to_chunks(ig, L), to_chunks(fg, L))
    _, h = lax.scan(step, init, xs)
    return from_chunks(h)

def mlstm_mixer(x, w_in, gate_b, norm_g, w_out):
    B, S, _ = x.shape
    f32 = jnp.float32
    qk = ML_HEADS * ML_DK
    z = x @ w_in
    q, k, v, o, gates = jnp.split(z, [qk, 2 * qk, 2 * qk + D_MODEL, 2 * qk + 2 * D_MODEL], axis=-1)
    q = q.reshape(B, S, ML_HEADS, ML_DK).astype(f32) * (ML_DK ** -0.5)
    k = k.reshape(B, S, ML_HEADS, ML_DK).astype(f32)
    v = v.reshape(B, S, ML_HEADS, ML_DV).astype(f32)
    gates = gates.reshape(B, S, 2, 2, ML_HEADS).astype(f32) + gate_b.astype(f32)
    h_fwd = mlstm_chunked(q, k, v, gates[:, :, 0, 0], gates[:, :, 0, 1])
    h_bwd = flip_seq(mlstm_chunked(flip_seq(q), flip_seq(k), flip_seq(v),
                                   flip_seq(gates[:, :, 1, 0]), flip_seq(gates[:, :, 1, 1])))
    h = head_norm(h_fwd + h_bwd, norm_g).astype(x.dtype)
    return (jax.nn.sigmoid(o) * h) @ w_out

def gla_chunked(q, k, v, loga):
    B, S, H, DK = q.shape
    DV = v.shape[-1]
    L = GLA_CHUNK
    mask = jnp.tril(jnp.ones((L, L), dtype=bool))[:, :, None]

    def step(state, inp):
        qb, kb, vb, ab = inp
        b = jnp.cumsum(ab, axis=-2)
        dec = jnp.exp(jnp.where(mask, b[:, :, :, None, :] - b[:, :, None, :, :], -jnp.inf))
        A = jnp.einsum('bhtd,bhtsd,bhsd->bhts', qb, dec, kb)
        o = jnp.einsum('bhts,bhsv->bhtv', A, vb) + jnp.einsum('bhtd,bhdv->bhtv', qb * jnp.exp(b), state)
        g = b[:, :, -1, :]
        state = jnp.exp(g)[..., None] * state + jnp.einsum('bhsd,bhsv->bhdv', kb * jnp.exp(g[:, :, None, :] - b), vb)
        return state, o

    init = jnp.zeros((B, H, DK, DV), jnp.float32)
    xs = (to_chunks(q, L), to_chunks(k, L), to_chunks(v, L), to_chunks(loga, L))
    _, o = lax.scan(step, init, xs)
    return from_chunks(o)

def gla_mixer(x, w_in, gate_w, gate_b, norm_g, w_out):
    B, S, _ = x.shape
    f32 = jnp.float32
    qk = GLA_HEADS * GLA_DK
    z = x @ w_in
    q, k, v, r, glr = jnp.split(z, [qk, 2 * qk, 2 * qk + D_MODEL, 2 * qk + 2 * D_MODEL], axis=-1)
    q = q.reshape(B, S, GLA_HEADS, GLA_DK).astype(f32) * (GLA_DK ** -0.5)
    k = k.reshape(B, S, GLA_HEADS, GLA_DK).astype(f32)
    v = v.reshape(B, S, GLA_HEADS, GLA_DV).astype(f32)
    glr = glr.reshape(B, S, 2, GLA_RANK).astype(f32)
    loga = jax.nn.log_sigmoid(jnp.einsum('bsgr,grk->bsgk', glr, gate_w.astype(f32)) + gate_b.astype(f32)) / GLA_TAU
    loga = loga.reshape(B, S, 2, GLA_HEADS, GLA_DK)
    o_fwd = gla_chunked(q, k, v, loga[:, :, 0])
    o_bwd = flip_seq(gla_chunked(flip_seq(q), flip_seq(k), flip_seq(v), flip_seq(loga[:, :, 1])))
    o = head_norm(o_fwd + o_bwd, norm_g).astype(x.dtype)
    return (jax.nn.silu(r) * o) @ w_out

def rglru_direction(u, wa, ba, wx, bx, lam):
    B, S, W = u.shape
    ub = u.reshape(B, S, LRU_BLOCKS, LRU_BW)
    r = jax.nn.sigmoid(jnp.einsum('bsni,nij->bsnj', ub, wa).reshape(B, S, W) + ba)
    i = jax.nn.sigmoid(jnp.einsum('bsni,nij->bsnj', ub, wx).reshape(B, S, W) + bx)
    log_a = LRU_C * r * jax.nn.log_sigmoid(lam)
    a = jnp.exp(log_a)
    gated = jnp.sqrt(-jnp.expm1(2.0 * log_a)) * (i * u)

    def step(h, inp):
        a_t, g_t = inp
        h = a_t * h + g_t
        return h, h

    _, hs = lax.scan(step, jnp.zeros((B, W), jnp.float32), (jnp.swapaxes(a, 0, 1), jnp.swapaxes(gated, 0, 1)))
    return jnp.swapaxes(hs, 0, 1)

def rglru_mixer(x, w_in, conv_w, conv_b, gate_a_w, gate_a_b, gate_x_w, gate_x_b, lam, w_out):
    f32 = jnp.float32
    z = x @ w_in
    gate_branch, u = jnp.split(z, [LRU_WIDTH], axis=-1)
    u = lax.conv_general_dilated(u, conv_w[:, None, :].astype(u.dtype), window_strides=(1,),
                                 padding=[(CONV_WIDTH // 2, CONV_WIDTH - 1 - CONV_WIDTH // 2)],
                                 dimension_numbers=('NWC', 'WIO', 'NWC'),
                                 feature_group_count=LRU_WIDTH) + conv_b
    u = u.astype(f32)
    h_fwd = rglru_direction(u, gate_a_w[0].astype(f32), gate_a_b[0].astype(f32), gate_x_w[0].astype(f32),
                            gate_x_b[0].astype(f32), lam[0].astype(f32))
    h_bwd = flip_seq(rglru_direction(flip_seq(u), gate_a_w[1].astype(f32), gate_a_b[1].astype(f32),
                                     gate_x_w[1].astype(f32), gate_x_b[1].astype(f32), lam[1].astype(f32)))
    h = (h_fwd + h_bwd).astype(x.dtype)
    return (jax.nn.gelu(gate_branch) * h) @ w_out

def apply_rope(t, cos, sin):
    half = t.shape[-1] // 2
    t1, t2 = t[..., :half], t[..., half:]
    return jnp.concatenate([t1 * cos - t2 * sin, t2 * cos + t1 * sin], axis=-1)

def mla_mixer(x, positions, w_in, q_norm_g, kv_norm_g, w_uq, w_ukv, w_out):
    B, S, _ = x.shape
    f32 = jnp.float32
    z = x @ w_in
    cq, ckv, k_rope = jnp.split(z, [MLA_Q_RANK, MLA_Q_RANK + MLA_KV_RANK], axis=-1)
    q = (rms_norm(cq, q_norm_g) @ w_uq).reshape(B, S, MLA_HEADS, MLA_NOPE + MLA_ROPE)
    kv = (rms_norm(ckv, kv_norm_g) @ w_ukv).reshape(B, S, MLA_HEADS, MLA_NOPE + MLA_DV)
    q_nope, q_rope = jnp.split(q, [MLA_NOPE], axis=-1)
    k_nope, v = jnp.split(kv, [MLA_NOPE], axis=-1)
    half = MLA_ROPE // 2
    freq = ROPE_THETA ** (-jnp.arange(half, dtype=f32) / half)
    ang = positions.astype(f32)[..., None] * freq
    cos = jnp.cos(ang).astype(x.dtype)
    sin = jnp.sin(ang).astype(x.dtype)
    q_rope = apply_rope(q_rope, cos[:, :, None, :], sin[:, :, None, :])
    k_rope = apply_rope(k_rope, cos, sin)
    scale = (MLA_NOPE + MLA_ROPE) ** -0.5
    nq = S // Q_BLOCK
    qn_blocks = jnp.moveaxis(q_nope.reshape(B, nq, Q_BLOCK, MLA_HEADS, MLA_NOPE), 1, 0)
    qr_blocks = jnp.moveaxis(q_rope.reshape(B, nq, Q_BLOCK, MLA_HEADS, MLA_ROPE), 1, 0)

    def attend(blk):
        qn, qr = blk
        s = (jnp.einsum('bqhd,bkhd->bhqk', qn, k_nope) + jnp.einsum('bqhd,bkd->bhqk', qr, k_rope)).astype(f32) * scale
        p = jax.nn.softmax(s, axis=-1).astype(v.dtype)
        return jnp.einsum('bhqk,bkhv->bqhv', p, v)

    out = lax.map(attend, (qn_blocks, qr_blocks))
    out = jnp.moveaxis(out, 0, 1).reshape(B, S, MLA_HEADS * MLA_DV)
    return out @ w_out

def ec_moe(x, w_router, w_gate, w_up, w_down):
    B, N, _ = x.shape
    cap = CAPACITY_FACTOR * N // N_EXPERTS
    aff = jax.nn.softmax(jnp.einsum('bnd,de->bne', x, w_router).astype(jnp.float32), axis=-1)
    gates, idx = lax.top_k(jnp.swapaxes(aff, 1, 2), cap)
    bidx = jnp.arange(B)[:, None, None]
    xin = x[bidx, idx]
    h = jax.nn.silu(jnp.einsum('becd,edf->becf', xin, w_gate)) * jnp.einsum('becd,edf->becf', xin, w_up)
    out = jnp.einsum('becf,efd->becd', h, w_down) * gates[..., None].astype(x.dtype)
    return jnp.zeros_like(x).at[bidx, idx].add(out.astype(x.dtype))

def first_inputs(seed: int = 0) -> dict:
    key = jax.random.key(seed)
    keys = iter(jax.random.split(key, 64))
    f32 = jnp.float32

    def nrm(shape, scale):
        return jax.random.normal(next(keys), shape, f32) * scale

    def gain(shape):
        return 1.0 + nrm(shape, 0.02)

    D = D_MODEL
    x = jax.random.normal(next(keys), (BATCH, SEQ, D), f32)
    positions = (jnp.arange(SEQ, dtype=jnp.int32)[None, :]
                 + jax.random.randint(next(keys), (BATCH, 1), 0, SEQ, dtype=jnp.int32))
    mlstm_w_in = nrm((N_MLSTM, D, ML_IN), D ** -0.5)
    ig_b = nrm((N_MLSTM, 2, 1, ML_HEADS), 0.1)
    fg_b = 3.0 + 3.0 * jax.random.uniform(next(keys), (N_MLSTM, 2, 1, ML_HEADS), f32)
    mlstm_gate_b = jnp.concatenate([ig_b, fg_b], axis=2)
    mlstm_norm_g = gain((N_MLSTM, D))
    mlstm_w_out = nrm((N_MLSTM, D, D), BETA * D ** -0.5)
    gla_w_in = nrm((N_GLA, D, GLA_IN), D ** -0.5)
    gla_gate_w = nrm((N_GLA, 2, GLA_RANK, GLA_HEADS * GLA_DK), GLA_RANK ** -0.5)
    gla_gate_b = nrm((N_GLA, 2, GLA_HEADS * GLA_DK), 0.1)
    gla_norm_g = gain((N_GLA, D))
    gla_w_out = nrm((N_GLA, D, D), BETA * D ** -0.5)
    lru_w_in = nrm((N_LRU, D, LRU_IN), D ** -0.5)
    lru_conv_w = nrm((N_LRU, CONV_WIDTH, LRU_WIDTH), CONV_WIDTH ** -0.5)
    lru_conv_b = nrm((N_LRU, LRU_WIDTH), 0.02)
    lru_gate_a_w = nrm((N_LRU, 2, LRU_BLOCKS, LRU_BW, LRU_BW), LRU_BW ** -0.5)
    lru_gate_a_b = nrm((N_LRU, 2, LRU_WIDTH), 0.1)
    lru_gate_x_w = nrm((N_LRU, 2, LRU_BLOCKS, LRU_BW, LRU_BW), LRU_BW ** -0.5)
    lru_gate_x_b = nrm((N_LRU, 2, LRU_WIDTH), 0.1)
    a0 = jax.random.uniform(next(keys), (N_LRU, 2, LRU_WIDTH), f32, minval=0.9, maxval=0.999)
    s0 = a0 ** (1.0 / LRU_C)
    lru_lambda = jnp.log(s0) - jnp.log1p(-s0)
    lru_w_out = nrm((N_LRU, LRU_WIDTH, D), BETA * LRU_WIDTH ** -0.5)
    mla_w_in = nrm((N_MLA, D, MLA_IN), D ** -0.5)
    mla_q_norm_g = gain((N_MLA, MLA_Q_RANK))
    mla_kv_norm_g = gain((N_MLA, MLA_KV_RANK))
    mla_w_uq = nrm((N_MLA, MLA_Q_RANK, MLA_HEADS * (MLA_NOPE + MLA_ROPE)), MLA_Q_RANK ** -0.5)
    mla_w_ukv = nrm((N_MLA, MLA_KV_RANK, MLA_HEADS * (MLA_NOPE + MLA_DV)), MLA_KV_RANK ** -0.5)
    mla_w_out = nrm((N_MLA, MLA_HEADS * MLA_DV, D), BETA * (MLA_HEADS * MLA_DV) ** -0.5)
    moe_router = nrm((DEPTH, D, N_EXPERTS), D ** -0.5)
    moe_w_gate = nrm((DEPTH, N_EXPERTS, D, EXPERT_FF), D ** -0.5)
    moe_w_up = nrm((DEPTH, N_EXPERTS, D, EXPERT_FF), D ** -0.5)
    moe_w_down = nrm((DEPTH, N_EXPERTS, EXPERT_FF, D), BETA * EXPERT_FF ** -0.5)
    ln_g = gain((DEPTH, 2, D))
    ln_b = nrm((DEPTH, 2, D), 0.02)
    return {
        'x': x, 'positions': positions,
        'mlstm_w_in': mlstm_w_in, 'mlstm_gate_b': mlstm_gate_b, 'mlstm_norm_g': mlstm_norm_g, 'mlstm_w_out': mlstm_w_out,
        'gla_w_in': gla_w_in, 'gla_gate_w': gla_gate_w, 'gla_gate_b': gla_gate_b, 'gla_norm_g': gla_norm_g, 'gla_w_out': gla_w_out,
        'lru_w_in': lru_w_in, 'lru_conv_w': lru_conv_w, 'lru_conv_b': lru_conv_b,
        'lru_gate_a_w': lru_gate_a_w, 'lru_gate_a_b': lru_gate_a_b, 'lru_gate_x_w': lru_gate_x_w, 'lru_gate_x_b': lru_gate_x_b,
        'lru_lambda': lru_lambda, 'lru_w_out': lru_w_out,
        'mla_w_in': mla_w_in, 'mla_q_norm_g': mla_q_norm_g, 'mla_kv_norm_g': mla_kv_norm_g,
        'mla_w_uq': mla_w_uq, 'mla_w_ukv': mla_w_ukv, 'mla_w_out': mla_w_out,
        'moe_router': moe_router, 'moe_w_gate': moe_w_gate, 'moe_w_up': moe_w_up, 'moe_w_down': moe_w_down,
        'ln_g': ln_g, 'ln_b': ln_b,
    }

def first_block(x, positions,
              mlstm_w_in, mlstm_gate_b, mlstm_norm_g, mlstm_w_out,
              gla_w_in, gla_gate_w, gla_gate_b, gla_norm_g, gla_w_out,
              lru_w_in, lru_conv_w, lru_conv_b, lru_gate_a_w, lru_gate_a_b, lru_gate_x_w, lru_gate_x_b,
              lru_lambda, lru_w_out,
              mla_w_in, mla_q_norm_g, mla_kv_norm_g, mla_w_uq, mla_w_ukv, mla_w_out,
              moe_router, moe_w_gate, moe_w_up, moe_w_down,
              ln_g, ln_b):
    for i in range(DEPTH):
        m = i % N_MIXERS
        j = i // N_MIXERS
        if m == 0:
            h = mlstm_mixer(x, mlstm_w_in[j], mlstm_gate_b[j], mlstm_norm_g[j], mlstm_w_out[j])
        elif m == 1:
            h = gla_mixer(x, gla_w_in[j], gla_gate_w[j], gla_gate_b[j], gla_norm_g[j], gla_w_out[j])
        elif m == 2:
            h = rglru_mixer(x, lru_w_in[j], lru_conv_w[j], lru_conv_b[j], lru_gate_a_w[j], lru_gate_a_b[j],
                            lru_gate_x_w[j], lru_gate_x_b[j], lru_lambda[j], lru_w_out[j])
        else:
            h = mla_mixer(x, positions, mla_w_in[j], mla_q_norm_g[j], mla_kv_norm_g[j],
                          mla_w_uq[j], mla_w_ukv[j], mla_w_out[j])
        x = layer_norm(ALPHA * x + h, ln_g[i, 0], ln_b[i, 0])
        y = ec_moe(x, moe_router[i], moe_w_gate[i], moe_w_up[i], moe_w_down[i])
        x = layer_norm(ALPHA * x + y, ln_g[i, 1], ln_b[i, 1])
    return x


HEAD_DIM = 64
NORM_EPS = 1e-6
NEG_INF = -1e30
FORCE_SELECT = 1e9

NSA_HEADS = 8
NSA_KV_GROUPS = 2
NSA_HEADS_PER_GROUP = NSA_HEADS // NSA_KV_GROUPS
NSA_CMP_LEN = 32
NSA_CMP_STRIDE = 16
NSA_SEL_LEN = 64
NSA_SEL_TOPK = 16
NSA_WINDOW = 512
NSA_BRANCHES = 3

MOBA_HEADS = 8
MOBA_BLOCK = 256
MOBA_TOPK = 3

MEM_LEN = 256
MEM_HEADS = 4

RET_HEADS = 4
RET_QK_DIM = D_MODEL // RET_HEADS
RET_V_DIM = 2 * D_MODEL // RET_HEADS
RET_CHUNK = 128

NSA_Q_W = NSA_HEADS * HEAD_DIM
NSA_KV_W = NSA_KV_GROUPS * HEAD_DIM
MOBA_W = MOBA_HEADS * HEAD_DIM
MEM_W = MEM_HEADS * HEAD_DIM
RET_QK_W = RET_HEADS * RET_QK_DIM
RET_V_W = RET_HEADS * RET_V_DIM

EVEN_SPLITS = (NSA_Q_W, NSA_KV_W, NSA_KV_W, NSA_KV_W, NSA_KV_W, NSA_KV_W, NSA_KV_W,
               NSA_BRANCHES * NSA_HEADS, NSA_Q_W,
               MOBA_W, MOBA_W, MOBA_W, MOBA_W,
               MEM_W, MEM_W)
ODD_SPLITS = (RET_QK_W, RET_QK_W, RET_V_W, RET_V_W, MEM_W, MEM_W)
EVEN_IN_W = sum(EVEN_SPLITS)
EVEN_OUT_W = NSA_Q_W + MOBA_W + MEM_W
ODD_IN_W = sum(ODD_SPLITS)
ODD_OUT_W = RET_V_W + MEM_W


def _split(h, sizes):
    cuts = np.cumsum(np.array(sizes))[:-1].tolist()
    return jnp.split(h, cuts, axis=-1)

def rms_norm_2(x, g):
    xf = x.astype(jnp.float32)
    y = xf * lax.rsqrt(jnp.mean(xf * xf, axis=-1, keepdims=True) + NORM_EPS)
    return (y * g.astype(jnp.float32)).astype(x.dtype)

def rotary_tables(positions, inv_freq):
    ang = positions.astype(jnp.float32)[..., None] * inv_freq
    return jnp.cos(ang), jnp.sin(ang)

def apply_rotary(x, cos, sin):
    x1, x2 = jnp.split(x, 2, axis=-1)
    c = cos[:, :, None, :].astype(x.dtype)
    s = sin[:, :, None, :].astype(x.dtype)
    return jnp.concatenate([x1 * c - x2 * s, x1 * s + x2 * c], axis=-1)

def masked_softmax(s, mask):
    s = jnp.where(mask, s.astype(jnp.float32), NEG_INF)
    m = jnp.max(s, axis=-1, keepdims=True)
    p = jnp.where(mask, jnp.exp(s - m), 0.0)
    return p / jnp.maximum(jnp.sum(p, axis=-1, keepdims=True), 1e-30)

def nsa_compress(a, pe, w1, w2):
    T = a.shape[1]
    n_cmp = (T - NSA_CMP_LEN) // NSA_CMP_STRIDE + 1
    idx = np.arange(n_cmp)[:, None] * NSA_CMP_STRIDE + np.arange(NSA_CMP_LEN)[None, :]
    blocks = a[:, idx] + pe[None, None, :, None, :].astype(a.dtype)
    hid = jax.nn.silu(jnp.einsum('bnlgd,lde->bnge', blocks, w1))
    return jnp.einsum('bnge,ef->bngf', hid, w2)

def nsa_attention(q, kc, vc, ks, vs, kw, vw, gates):
    Bsz, T = q.shape[0], q.shape[1]
    G, I, D = NSA_KV_GROUPS, NSA_HEADS_PER_GROUP, HEAD_DIM
    n_cmp = kc.shape[1]
    n_sel = T // NSA_SEL_LEN
    k_sel = min(NSA_SEL_TOPK, n_sel)
    scale = HEAD_DIM ** -0.5
    cmp_start = jnp.arange(n_cmp) * NSA_CMP_STRIDE
    cmp_end = cmp_start + NSA_CMP_LEN - 1
    sel_start = jnp.arange(n_sel) * NSA_SEL_LEN
    overlap = ((cmp_start[:, None] < sel_start[None, :] + NSA_SEL_LEN) &
               (cmp_start[:, None] + NSA_CMP_LEN > sel_start[None, :])).astype(jnp.float32)
    ks_blk = ks.reshape(Bsz, n_sel, NSA_SEL_LEN, G, D).transpose(0, 3, 1, 2, 4)
    vs_blk = vs.reshape(Bsz, n_sel, NSA_SEL_LEN, G, D).transpose(0, 3, 1, 2, 4)
    kw_pad = jnp.pad(kw, ((0, 0), (NSA_WINDOW, 0), (0, 0), (0, 0)))
    vw_pad = jnp.pad(vw, ((0, 0), (NSA_WINDOW, 0), (0, 0), (0, 0)))
    b_idx = jnp.arange(Bsz)[:, None, None, None]
    g_idx = jnp.arange(G)[None, :, None, None]
    sel_blocks = jnp.arange(n_sel)

    def block(bi):
        t0 = bi * Q_BLOCK
        t = t0 + jnp.arange(Q_BLOCK)
        qb = lax.dynamic_slice_in_dim(q, t0, Q_BLOCK, axis=1).reshape(Bsz, Q_BLOCK, G, I, D)
        gb = lax.dynamic_slice_in_dim(gates, t0, Q_BLOCK, axis=1).reshape(Bsz, Q_BLOCK, NSA_BRANCHES, G, I)
        s_c = jnp.einsum('bqgid,bngd->bgiqn', qb, kc) * scale
        p_c = masked_softmax(s_c, cmp_end[None, :] <= t[:, None])
        o_c = jnp.einsum('bgiqn,bngd->bqgid', p_c.astype(vc.dtype), vc)
        imp = jnp.einsum('bgiqn,ns->bgqs', p_c, overlap)
        cur = t // NSA_SEL_LEN
        forced = ((sel_blocks[None, :] == 0) | (sel_blocks[None, :] == cur[:, None]) |
                  (sel_blocks[None, :] == cur[:, None] - 1))
        imp = jnp.where(forced, FORCE_SELECT, imp)
        imp = jnp.where(sel_blocks[None, :] <= cur[:, None], imp, NEG_INF)
        _, sel = lax.top_k(imp, k_sel)
        k_g = ks_blk[b_idx, g_idx, sel]
        v_g = vs_blk[b_idx, g_idx, sel]
        kpos = sel[..., None] * NSA_SEL_LEN + jnp.arange(NSA_SEL_LEN)
        mask_s = (kpos <= t[None, None, :, None, None]).reshape(Bsz, G, 1, Q_BLOCK, k_sel * NSA_SEL_LEN)
        s_s = jnp.einsum('bqgid,bgqkld->bgiqkl', qb, k_g).reshape(Bsz, G, I, Q_BLOCK, k_sel * NSA_SEL_LEN) * scale
        p_s = masked_softmax(s_s, mask_s).reshape(Bsz, G, I, Q_BLOCK, k_sel, NSA_SEL_LEN)
        o_s = jnp.einsum('bgiqkl,bgqkld->bqgid', p_s.astype(v_g.dtype), v_g)
        kwb = lax.dynamic_slice_in_dim(kw_pad, t0, Q_BLOCK + NSA_WINDOW, axis=1)
        vwb = lax.dynamic_slice_in_dim(vw_pad, t0, Q_BLOCK + NSA_WINDOW, axis=1)
        wpos = t0 - NSA_WINDOW + jnp.arange(Q_BLOCK + NSA_WINDOW)
        mask_w = ((wpos[None, :] <= t[:, None]) & (wpos[None, :] > t[:, None] - NSA_WINDOW) &
                  (wpos[None, :] >= 0))
        s_w = jnp.einsum('bqgid,bjgd->bgiqj', qb, kwb) * scale
        p_w = masked_softmax(s_w, mask_w)
        o_w = jnp.einsum('bgiqj,bjgd->bqgid', p_w.astype(vwb.dtype), vwb)
        o = (gb[:, :, 0, :, :, None] * o_c + gb[:, :, 1, :, :, None] * o_s +
             gb[:, :, 2, :, :, None] * o_w)
        return o.reshape(Bsz, Q_BLOCK, NSA_Q_W)

    out = lax.map(block, jnp.arange(T // Q_BLOCK))
    return out.transpose(1, 0, 2, 3).reshape(Bsz, T, NSA_Q_W)

def moba_attention(q, k, v):
    Bsz, T, H, D = q.shape
    n_blk = -(-T // MOBA_BLOCK)
    pad = n_blk * MOBA_BLOCK - T
    k_pad = jnp.pad(k, ((0, 0), (0, pad), (0, 0), (0, 0)))
    v_pad = jnp.pad(v, ((0, 0), (0, pad), (0, 0), (0, 0)))
    k_blk = k_pad.reshape(Bsz, n_blk, MOBA_BLOCK, H, D)
    k_mean = jnp.mean(k_blk.astype(jnp.float32), axis=2).astype(k.dtype)
    k_blk = k_blk.transpose(0, 3, 1, 2, 4)
    v_blk = v_pad.reshape(Bsz, n_blk, MOBA_BLOCK, H, D).transpose(0, 3, 1, 2, 4)
    top = max(1, min(MOBA_TOPK, n_blk - 1))
    scale = HEAD_DIM ** -0.5
    b_idx = jnp.arange(Bsz)[:, None, None, None]
    h_idx = jnp.arange(H)[None, :, None, None]
    blocks = jnp.arange(n_blk)

    def block(bi):
        t0 = bi * Q_BLOCK
        t = t0 + jnp.arange(Q_BLOCK)
        cur = t0 // MOBA_BLOCK
        qb = lax.dynamic_slice_in_dim(q, t0, Q_BLOCK, axis=1)
        gate = jnp.einsum('bqhd,bnhd->bhqn', qb, k_mean).astype(jnp.float32)
        gate = jnp.where(blocks < cur, gate, NEG_INF)
        _, sel = lax.top_k(gate, top)
        k_g = k_blk[b_idx, h_idx, sel]
        v_g = v_blk[b_idx, h_idx, sel]
        s_sel = jnp.einsum('bqhd,bhqksd->bhqks', qb, k_g).reshape(Bsz, H, Q_BLOCK, top * MOBA_BLOCK)
        m_sel = jnp.broadcast_to((sel < cur)[..., None],
                                 (Bsz, H, Q_BLOCK, top, MOBA_BLOCK)).reshape(Bsz, H, Q_BLOCK, top * MOBA_BLOCK)
        k_own = lax.dynamic_slice_in_dim(k_pad, cur * MOBA_BLOCK, MOBA_BLOCK, axis=1)
        v_own = lax.dynamic_slice_in_dim(v_pad, cur * MOBA_BLOCK, MOBA_BLOCK, axis=1)
        s_own = jnp.einsum('bqhd,bshd->bhqs', qb, k_own)
        own_pos = cur * MOBA_BLOCK + jnp.arange(MOBA_BLOCK)
        m_own = jnp.broadcast_to(own_pos[None, :] <= t[:, None], (Bsz, H, Q_BLOCK, MOBA_BLOCK))
        p = masked_softmax(jnp.concatenate([s_sel, s_own], axis=-1) * scale,
                           jnp.concatenate([m_sel, m_own], axis=-1)).astype(v.dtype)
        p_sel = p[..., :top * MOBA_BLOCK].reshape(Bsz, H, Q_BLOCK, top, MOBA_BLOCK)
        p_own = p[..., top * MOBA_BLOCK:]
        o = (jnp.einsum('bhqks,bhqksd->bqhd', p_sel, v_g) +
             jnp.einsum('bhqs,bshd->bqhd', p_own, v_own))
        return o.reshape(Bsz, Q_BLOCK, H * D)

    out = lax.map(block, jnp.arange(T // Q_BLOCK))
    return out.transpose(1, 0, 2, 3).reshape(Bsz, T, H * D)

def memory_attention(q, mem_n, w_mem_kv):
    Bsz, T = q.shape[0], q.shape[1]
    k, v = jnp.split(mem_n @ w_mem_kv, 2, axis=-1)
    k = k.reshape(Bsz, -1, MEM_HEADS, HEAD_DIM)
    v = v.reshape(Bsz, -1, MEM_HEADS, HEAD_DIM)
    s = jnp.einsum('bthd,bmhd->bhtm', q, k).astype(jnp.float32) * (HEAD_DIM ** -0.5)
    p = jax.nn.softmax(s, axis=-1).astype(v.dtype)
    return jnp.einsum('bhtm,bmhd->bthd', p, v).reshape(Bsz, T, MEM_W)

def retention(q, k, v):
    Bsz, T, H, _ = q.shape
    C = RET_CHUNK
    NC = T // C
    log_g = jnp.log(1.0 - 2.0 ** (-5.0 - jnp.arange(H, dtype=jnp.float32)))
    i = jnp.arange(C, dtype=jnp.float32)
    diff = i[:, None] - i[None, :]
    decay = jnp.where(diff >= 0, jnp.exp(jnp.maximum(diff, 0.0)[None] * log_g[:, None, None]), 0.0)
    q_decay = jnp.exp((i + 1.0)[None, :] * log_g[:, None])
    k_decay = jnp.exp((C - 1.0 - i)[None, :] * log_g[:, None])
    chunk_decay = jnp.exp(C * log_g)

    def to_chunks(a):
        return a.astype(jnp.float32).reshape(Bsz, NC, C, H, -1).transpose(1, 0, 3, 2, 4)

    def step(state, inp):
        qc, kc, vc = inp
        inner = jnp.einsum('bhid,bhjd->bhij', qc, kc) * decay
        o = (jnp.einsum('bhij,bhjv->bhiv', inner, vc) +
             jnp.einsum('bhid,bhdv->bhiv', qc, state) * q_decay[None, :, :, None])
        state = (state * chunk_decay[None, :, None, None] +
                 jnp.einsum('bhjd,bhjv->bhdv', kc * k_decay[None, :, :, None], vc))
        return state, o

    state0 = jnp.zeros((Bsz, H, q.shape[-1], v.shape[-1]), jnp.float32)
    _, o = lax.scan(step, state0, (to_chunks(q), to_chunks(k), to_chunks(v)))
    return o.transpose(1, 0, 3, 2, 4).reshape(Bsz, T, H, v.shape[-1])

def head_group_norm(o):
    mu = jnp.mean(o, axis=-1, keepdims=True)
    var = jnp.mean(jnp.square(o - mu), axis=-1, keepdims=True)
    return (o - mu) * lax.rsqrt(var + NORM_EPS)

def even_layer(x, mem_n, cos, sin, norm_g, w_in, gate_b, pe_k, w1_k, w2_k, pe_v, w1_v, w2_v, w_mem_kv, w_out):
    Bsz, T, _ = x.shape
    h = rms_norm_2(x, norm_g)
    (nq, nkc, nvc, nks, nvs, nkw, nvw, ng, nz, mq, mk, mv, mz, eq, ez) = _split(h @ w_in, EVEN_SPLITS)

    def heads(a):
        return a.reshape(Bsz, T, -1, HEAD_DIM)

    def rot(a):
        return apply_rotary(heads(a), cos, sin)

    kc = nsa_compress(rot(nkc), pe_k, w1_k, w2_k)
    vc = nsa_compress(heads(nvc), pe_v, w1_v, w2_v)
    gates = jax.nn.sigmoid(ng + gate_b).reshape(Bsz, T, NSA_BRANCHES, NSA_HEADS)
    a_out = nsa_attention(rot(nq), kc, vc, rot(nks), heads(nvs), rot(nkw), heads(nvw), gates)
    b_out = moba_attention(rot(mq), rot(mk), heads(mv))
    m_out = memory_attention(heads(eq), mem_n, w_mem_kv)
    y = jnp.concatenate([a_out * jax.nn.silu(nz), b_out * jax.nn.silu(mz),
                         m_out * jax.nn.silu(ez)], axis=-1) @ w_out
    return x + y

def odd_layer(x, mem_n, rcos, rsin, norm_g, w_in, w_mem_kv, w_out):
    Bsz, T, _ = x.shape
    h = rms_norm_2(x, norm_g)
    rq, rk, rv, rz, eq, ez = _split(h @ w_in, ODD_SPLITS)
    q = apply_rotary(rq.reshape(Bsz, T, RET_HEADS, RET_QK_DIM), rcos, rsin)
    k = apply_rotary(rk.reshape(Bsz, T, RET_HEADS, RET_QK_DIM), rcos, rsin) * (RET_QK_DIM ** -0.5)
    v = rv.reshape(Bsz, T, RET_HEADS, RET_V_DIM)
    r_out = head_group_norm(retention(q, k, v)).reshape(Bsz, T, RET_V_W).astype(x.dtype)
    m_out = memory_attention(eq.reshape(Bsz, T, MEM_HEADS, HEAD_DIM), mem_n, w_mem_kv)
    y = jnp.concatenate([r_out * jax.nn.silu(rz), m_out * jax.nn.silu(ez)], axis=-1) @ w_out
    return x + y

def second_inputs(seed: int = 0) -> dict:
    key = jax.random.key(seed)
    ks = jax.random.split(key, 24)

    def nrm(k, shape, scale):
        return jax.random.normal(k, shape, jnp.float32) * scale

    def gain(k):
        return 1.0 + nrm(k, (D_MODEL,), 0.02)

    x = nrm(ks[0], (BATCH, SEQ, D_MODEL), 1.0)
    mem = nrm(ks[1], (BATCH, MEM_LEN, D_MODEL), 1.0)
    positions = jnp.broadcast_to(jnp.arange(SEQ, dtype=jnp.int32)[None, :], (BATCH, SEQ))
    cmp_in = NSA_CMP_LEN * HEAD_DIM
    return {
        'x': x,
        'mem': mem,
        'positions': positions,
        'l0_norm_g': gain(ks[2]),
        'l0_w_in': nrm(ks[3], (D_MODEL, EVEN_IN_W), D_MODEL ** -0.5),
        'l0_nsa_gate_b': nrm(ks[4], (NSA_BRANCHES * NSA_HEADS,), 0.1),
        'l0_cmp_pe_k': nrm(ks[5], (NSA_CMP_LEN, HEAD_DIM), 0.1),
        'l0_cmp_w1_k': nrm(ks[6], (NSA_CMP_LEN, HEAD_DIM, HEAD_DIM), cmp_in ** -0.5),
        'l0_cmp_w2_k': nrm(ks[7], (HEAD_DIM, HEAD_DIM), HEAD_DIM ** -0.5),
        'l0_cmp_pe_v': nrm(ks[8], (NSA_CMP_LEN, HEAD_DIM), 0.1),
        'l0_cmp_w1_v': nrm(ks[9], (NSA_CMP_LEN, HEAD_DIM, HEAD_DIM), cmp_in ** -0.5),
        'l0_cmp_w2_v': nrm(ks[10], (HEAD_DIM, HEAD_DIM), HEAD_DIM ** -0.5),
        'l0_w_mem_kv': nrm(ks[11], (D_MODEL, 2 * MEM_W), D_MODEL ** -0.5),
        'l0_w_out': nrm(ks[12], (EVEN_OUT_W, D_MODEL), EVEN_OUT_W ** -0.5),
        'l1_norm_g': gain(ks[13]),
        'l1_w_in': nrm(ks[14], (D_MODEL, ODD_IN_W), D_MODEL ** -0.5),
        'l1_w_mem_kv': nrm(ks[15], (D_MODEL, 2 * MEM_W), D_MODEL ** -0.5),
        'l1_w_out': nrm(ks[16], (ODD_OUT_W, D_MODEL), ODD_OUT_W ** -0.5),
        'mem_norm_g': gain(ks[17]),
        'final_norm_g': gain(ks[18]),
    }

def second_block(x, mem, positions, l0_norm_g, l0_w_in, l0_nsa_gate_b, l0_cmp_pe_k, l0_cmp_w1_k, l0_cmp_w2_k,
              l0_cmp_pe_v, l0_cmp_w1_v, l0_cmp_w2_v, l0_w_mem_kv, l0_w_out,
              l1_norm_g, l1_w_in, l1_w_mem_kv, l1_w_out, mem_norm_g, final_norm_g):
    attn_inv = 1.0 / (ROPE_THETA ** (jnp.arange(0, HEAD_DIM, 2, dtype=jnp.float32) / HEAD_DIM))
    ret_inv = 1.0 / (ROPE_THETA ** jnp.linspace(0.0, 1.0, RET_QK_DIM // 2, dtype=jnp.float32))
    cos, sin = rotary_tables(positions, attn_inv)
    rcos, rsin = rotary_tables(positions, ret_inv)
    mem_n = rms_norm_2(mem, mem_norm_g)
    layer_params = (
        (l0_norm_g, l0_w_in, l0_nsa_gate_b, l0_cmp_pe_k, l0_cmp_w1_k, l0_cmp_w2_k,
         l0_cmp_pe_v, l0_cmp_w1_v, l0_cmp_w2_v, l0_w_mem_kv, l0_w_out),
        (l1_norm_g, l1_w_in, l1_w_mem_kv, l1_w_out),
    )
    for layer in range(DEPTH):
        if layer % 2 == 0:
            x = even_layer(x, mem_n, cos, sin, *layer_params[layer])
        else:
            x = odd_layer(x, mem_n, rcos, rsin, *layer_params[layer])
    return rms_norm_2(x, final_norm_g)


N_EVEN = (DEPTH + 1) // 2
N_ODD = DEPTH // 2

D_FF = 2816
FFN_RES = 0.5

POOL_WINDOWS = (2, 4, 8, 16)
N_POOL_GROUPS = 4
POOL_WIDTH = D_MODEL // 2
POOL_GROUP = POOL_WIDTH // N_POOL_GROUPS

CONV_WIDTH_3 = D_MODEL // 2
CONV_KERNEL = 31

AB_IN = POOL_WIDTH + 2 * CONV_WIDTH_3
AB_OUT = POOL_WIDTH + CONV_WIDTH_3

N_HEADS = 16
ATTN_WIDTH = N_HEADS * HEAD_DIM
N_IDX_HEADS = 8
IDX_DIM = 64
TOPK_MAX = 256
C_SPLITS = (ATTN_WIDTH, ATTN_WIDTH, ATTN_WIDTH, N_IDX_HEADS * IDX_DIM, IDX_DIM, N_IDX_HEADS)
C_IN = sum(C_SPLITS)

REL_BUCKETS = 32
REL_MAX_DIST = 128


def _offsets(sizes):
    out, acc = [], 0
    for s in sizes[:-1]:
        acc += s
        out.append(acc)
    return out

def rms_norm_3(x, g):
    xf = x.astype(jnp.float32)
    y = xf * lax.rsqrt(jnp.mean(xf * xf, axis=-1, keepdims=True) + NORM_EPS)
    return (y * g.astype(jnp.float32)).astype(x.dtype)

def swiglu(h, w_gate, w_up, w_down):
    return (jax.nn.silu(h @ w_gate) * (h @ w_up)) @ w_down

def pool_mixer(u, pool_w, pool_scale):
    B, S, _ = u.shape
    uf = u.astype(jnp.float32).reshape(B, S, N_POOL_GROUPS, POOL_GROUP)
    c0 = jnp.concatenate([jnp.zeros((B, 1, N_POOL_GROUPS, POOL_GROUP), jnp.float32),
                          jnp.cumsum(uf, axis=1)], axis=1)
    t = jnp.arange(S, dtype=jnp.int32)[:, None]
    win = jnp.array(POOL_WINDOWS, dtype=jnp.int32)[None, :]
    lo = jnp.maximum(t + 1 - win, 0)
    g_idx = jnp.arange(N_POOL_GROUPS, dtype=jnp.int32)[None, :]
    lo_sum = c0[:, lo, g_idx, :]
    count = (t + 1 - lo).astype(jnp.float32)
    mean = (c0[:, 1:] - lo_sum) / count[None, :, :, None]
    y = jnp.einsum('bsgc,gcd->bsgd', mean - uf, pool_w.astype(jnp.float32))
    y = y * pool_scale.astype(jnp.float32).reshape(N_POOL_GROUPS, POOL_GROUP)
    return y.reshape(B, S, POOL_WIDTH).astype(u.dtype)

def conv_module(a, gate, conv_w, conv_b, ln_g, ln_b):
    z = a * jax.nn.sigmoid(gate)
    z = lax.conv_general_dilated(
        z, conv_w[:, None, :].astype(z.dtype), window_strides=(1,),
        padding=[(CONV_KERNEL - 1, 0)], dimension_numbers=('NWC', 'WIO', 'NWC'),
        feature_group_count=CONV_WIDTH_3) + conv_b
    zf = z.astype(jnp.float32)
    mu = jnp.mean(zf, axis=-1, keepdims=True)
    var = jnp.mean(jnp.square(zf - mu), axis=-1, keepdims=True)
    zf = (zf - mu) * lax.rsqrt(var + NORM_EPS) * ln_g.astype(jnp.float32) + ln_b.astype(jnp.float32)
    return jax.nn.silu(zf).astype(a.dtype)

def t5_bucket(dist):
    max_exact = REL_BUCKETS // 2
    d = jnp.maximum(dist, max_exact).astype(jnp.float32)
    large = max_exact + (jnp.log(d / max_exact) / math.log(REL_MAX_DIST / max_exact)
                         * (REL_BUCKETS - max_exact)).astype(jnp.int32)
    large = jnp.minimum(large, REL_BUCKETS - 1)
    return jnp.where(dist < max_exact, dist, large)

def dsa_attention(q, k, v, qi, ki, wi, rel_bias):
    S = q.shape[1]
    top_k = min(TOPK_MAX, S // 4)
    nb = S // Q_BLOCK
    pos = jnp.arange(S, dtype=jnp.int32)
    idx_scale = (N_IDX_HEADS * IDX_DIM) ** -0.5
    attn_scale = HEAD_DIM ** -0.5

    def one_seq(args):
        qb, kb, vb, qib, kib, wib = args
        kib32 = kib.astype(jnp.float32)

        def one_block(bargs):
            q_t, qi_t, wi_t, t = bargs
            rel = jax.nn.relu(jnp.einsum('thd,sd->ths', qi_t.astype(jnp.float32), kib32))
            score = jnp.einsum('ths,th->ts', rel, wi_t.astype(jnp.float32)) * idx_scale
            score = jnp.where(pos[None, :] <= t[:, None], score, -jnp.inf)
            _, sel = lax.top_k(score, top_k)
            k_sel = kb[sel]
            v_sel = vb[sel]
            logits = jnp.einsum('thd,tkhd->thk', q_t, k_sel).astype(jnp.float32) * attn_scale
            bias = rel_bias[t5_bucket(t[:, None] - sel)]
            logits = logits + jnp.transpose(bias, (0, 2, 1)).astype(jnp.float32)
            logits = jnp.where((sel <= t[:, None])[:, None, :], logits, -jnp.inf)
            p = jax.nn.softmax(logits, axis=-1).astype(v_sel.dtype)
            return jnp.einsum('thk,tkhd->thd', p, v_sel)

        blocks = (qb.reshape(nb, Q_BLOCK, N_HEADS, HEAD_DIM),
                  qib.reshape(nb, Q_BLOCK, N_IDX_HEADS, IDX_DIM),
                  wib.reshape(nb, Q_BLOCK, N_IDX_HEADS),
                  pos.reshape(nb, Q_BLOCK))
        out = lax.map(one_block, blocks)
        return out.reshape(S, ATTN_WIDTH)

    return lax.map(one_seq, (q, k, v, qi, ki, wi))

def third_inputs(seed: int = 0) -> dict:
    key = jax.random.key(seed)
    ks = jax.random.split(key, 24)
    f32 = jnp.float32

    def w(k, shape, fan_in):
        return jax.random.normal(k, shape, f32) * (fan_in ** -0.5)

    def gain(k, shape):
        return 1.0 + 0.02 * jax.random.normal(k, shape, f32)

    def small(k, shape):
        return 0.01 * jax.random.normal(k, shape, f32)

    return {
        'x': jax.random.normal(ks[0], (BATCH, SEQ, D_MODEL), f32),
        'ffn1_norm': gain(ks[1], (DEPTH, D_MODEL)),
        'ffn1_w_gate': w(ks[2], (DEPTH, D_MODEL, D_FF), D_MODEL),
        'ffn1_w_up': w(ks[3], (DEPTH, D_MODEL, D_FF), D_MODEL),
        'ffn1_w_down': w(ks[4], (DEPTH, D_FF, D_MODEL), D_FF),
        'mix_norm': gain(ks[5], (DEPTH, D_MODEL)),
        'ffn2_norm': gain(ks[6], (DEPTH, D_MODEL)),
        'ffn2_w_gate': w(ks[7], (DEPTH, D_MODEL, D_FF), D_MODEL),
        'ffn2_w_up': w(ks[8], (DEPTH, D_MODEL, D_FF), D_MODEL),
        'ffn2_w_down': w(ks[9], (DEPTH, D_FF, D_MODEL), D_FF),
        'ab_w_in': w(ks[10], (N_EVEN, D_MODEL, AB_IN), D_MODEL),
        'pool_w': w(ks[11], (N_EVEN, N_POOL_GROUPS, POOL_GROUP, POOL_GROUP), POOL_GROUP),
        'pool_scale': gain(ks[12], (N_EVEN, POOL_WIDTH)),
        'conv_w': w(ks[13], (N_EVEN, CONV_KERNEL, CONV_WIDTH_3), CONV_KERNEL),
        'conv_b': small(ks[14], (N_EVEN, CONV_WIDTH_3)),
        'conv_ln_g': gain(ks[15], (N_EVEN, CONV_WIDTH_3)),
        'conv_ln_b': small(ks[16], (N_EVEN, CONV_WIDTH_3)),
        'ab_w_out': w(ks[17], (N_EVEN, AB_OUT, D_MODEL), AB_OUT),
        'c_w_in': w(ks[18], (N_ODD, D_MODEL, C_IN), D_MODEL),
        'c_w_out': w(ks[19], (N_ODD, ATTN_WIDTH, D_MODEL), ATTN_WIDTH),
        'rel_bias': 0.1 * jax.random.normal(ks[20], (REL_BUCKETS, N_HEADS), f32),
        'final_norm': gain(ks[21], (D_MODEL,)),
    }

def third_block(x, ffn1_norm, ffn1_w_gate, ffn1_w_up, ffn1_w_down, mix_norm, ffn2_norm,
              ffn2_w_gate, ffn2_w_up, ffn2_w_down, ab_w_in, pool_w, pool_scale, conv_w,
              conv_b, conv_ln_g, conv_ln_b, ab_w_out, c_w_in, c_w_out, rel_bias, final_norm):
    B, S, _ = x.shape
    ab_cuts = _offsets((POOL_WIDTH, CONV_WIDTH_3, CONV_WIDTH_3))
    c_cuts = _offsets(C_SPLITS)
    for layer in range(DEPTH):
        h = rms_norm_3(x, ffn1_norm[layer])
        x = x + FFN_RES * swiglu(h, ffn1_w_gate[layer], ffn1_w_up[layer], ffn1_w_down[layer])
        h = rms_norm_3(x, mix_norm[layer])
        i = layer // 2
        if layer % 2 == 0:
            proj = h @ ab_w_in[i]
            u_pool, u_val, u_gate = jnp.split(proj, ab_cuts, axis=-1)
            y_pool = pool_mixer(u_pool, pool_w[i], pool_scale[i])
            y_conv = conv_module(u_val, u_gate, conv_w[i], conv_b[i], conv_ln_g[i], conv_ln_b[i])
            y = jnp.concatenate([y_pool, y_conv], axis=-1) @ ab_w_out[i]
        else:
            proj = h @ c_w_in[i]
            q, k, v, qi, ki, wi = jnp.split(proj, c_cuts, axis=-1)
            attn = dsa_attention(q.reshape(B, S, N_HEADS, HEAD_DIM),
                                 k.reshape(B, S, N_HEADS, HEAD_DIM),
                                 v.reshape(B, S, N_HEADS, HEAD_DIM),
                                 qi.reshape(B, S, N_IDX_HEADS, IDX_DIM), ki, wi, rel_bias)
            y = attn @ c_w_out[i]
        x = x + y
        h = rms_norm_3(x, ffn2_norm[layer])
        x = x + FFN_RES * swiglu(h, ffn2_w_gate[layer], ffn2_w_up[layer], ffn2_w_down[layer])
    return rms_norm_3(x, final_norm)


_first_inputs = third_inputs


def third_inputs(seed=0):
    import zlib

    import numpy as np

    out = dict(_first_inputs(seed))
    spreads = {}
    factors = {'ffn1_norm': 2.961,
     'ffn2_norm': 11.707,
     'pool_scale': 38.357,
     'conv_b': 3.816,
     'conv_ln_g': 47.054,
     'conv_ln_b': 90.109,
     'rel_bias': 18.649,
     'final_norm': 20.714}
    for name, (base, spread) in spreads.items():
        noise = np.random.default_rng([zlib.crc32(name.encode()), seed]).standard_normal(out[name].shape)
        drawn = base * np.exp(spread * noise) if base else spread * noise
        out[name] = __import__('jax').numpy.asarray(drawn.astype(out[name].dtype))
    for name, factor in factors.items():
        out[name] = (out[name] * factor).astype(out[name].dtype)
    return out


def setup_inputs(seed=0):
    out = dict(first_inputs(seed))
    for name, value in second_inputs(seed + 1).items():
        if name != "x":
            out[name + "_2"] = value
    for name, value in third_inputs(seed + 2).items():
        if name != "x":
            out[name + "_3"] = value
    return out


def reference(
    x, positions, mlstm_w_in, mlstm_gate_b, mlstm_norm_g, mlstm_w_out, gla_w_in, gla_gate_w,
    gla_gate_b, gla_norm_g, gla_w_out, lru_w_in, lru_conv_w, lru_conv_b, lru_gate_a_w,
    lru_gate_a_b, lru_gate_x_w, lru_gate_x_b, lru_lambda, lru_w_out, mla_w_in, mla_q_norm_g,
    mla_kv_norm_g, mla_w_uq, mla_w_ukv, mla_w_out, moe_router, moe_w_gate, moe_w_up, moe_w_down,
    ln_g, ln_b, mem_2, positions_2, l0_norm_g_2, l0_w_in_2, l0_nsa_gate_b_2, l0_cmp_pe_k_2,
    l0_cmp_w1_k_2, l0_cmp_w2_k_2, l0_cmp_pe_v_2, l0_cmp_w1_v_2, l0_cmp_w2_v_2, l0_w_mem_kv_2,
    l0_w_out_2, l1_norm_g_2, l1_w_in_2, l1_w_mem_kv_2, l1_w_out_2, mem_norm_g_2, final_norm_g_2,
    ffn1_norm_3, ffn1_w_gate_3, ffn1_w_up_3, ffn1_w_down_3, mix_norm_3, ffn2_norm_3,
    ffn2_w_gate_3, ffn2_w_up_3, ffn2_w_down_3, ab_w_in_3, pool_w_3, pool_scale_3, conv_w_3,
    conv_b_3, conv_ln_g_3, conv_ln_b_3, ab_w_out_3, c_w_in_3, c_w_out_3, rel_bias_3,
    final_norm_3,
):
    x = first_block(
        x, positions, mlstm_w_in, mlstm_gate_b, mlstm_norm_g, mlstm_w_out, gla_w_in, gla_gate_w,
        gla_gate_b, gla_norm_g, gla_w_out, lru_w_in, lru_conv_w, lru_conv_b, lru_gate_a_w,
        lru_gate_a_b, lru_gate_x_w, lru_gate_x_b, lru_lambda, lru_w_out, mla_w_in, mla_q_norm_g,
        mla_kv_norm_g, mla_w_uq, mla_w_ukv, mla_w_out, moe_router, moe_w_gate, moe_w_up,
        moe_w_down, ln_g, ln_b,
    )
    x = second_block(
        x, mem_2, positions_2, l0_norm_g_2, l0_w_in_2, l0_nsa_gate_b_2, l0_cmp_pe_k_2,
        l0_cmp_w1_k_2, l0_cmp_w2_k_2, l0_cmp_pe_v_2, l0_cmp_w1_v_2, l0_cmp_w2_v_2,
        l0_w_mem_kv_2, l0_w_out_2, l1_norm_g_2, l1_w_in_2, l1_w_mem_kv_2, l1_w_out_2,
        mem_norm_g_2, final_norm_g_2,
    )
    return third_block(
        x, ffn1_norm_3, ffn1_w_gate_3, ffn1_w_up_3, ffn1_w_down_3, mix_norm_3, ffn2_norm_3,
        ffn2_w_gate_3, ffn2_w_up_3, ffn2_w_down_3, ab_w_in_3, pool_w_3, pool_scale_3, conv_w_3,
        conv_b_3, conv_ln_g_3, conv_ln_b_3, ab_w_out_3, c_w_in_3, c_w_out_3, rel_bias_3,
        final_norm_3,
    )


_drawn_inputs = setup_inputs


def setup_inputs(seed=0):
    import zlib

    import numpy as np

    out = dict(_drawn_inputs(seed))
    spreads = {}
    factors = {'mlstm_norm_g': 3.41,
     'gla_norm_g': 3.893,
     'l0_norm_g_2': 4.005,
     'l0_nsa_gate_b_2': 5.298,
     'l0_cmp_pe_k_2': 8.0,
     'mem_norm_g_2': 8.0,
     'pool_scale_3': 2.822,
     'c_w_in_3': 5.794,
     'c_w_out_3': 5.714,
     'rel_bias_3': 8.0,
     'final_norm_3': 2.789}
    for name, (base, spread) in spreads.items():
        noise = np.random.default_rng([zlib.crc32(name.encode()), seed]).standard_normal(out[name].shape)
        drawn = base * np.exp(spread * noise) if base else spread * noise
        out[name] = jnp.asarray(drawn.astype(out[name].dtype))
    for name, factor in factors.items():
        out[name] = (out[name] * factor).astype(out[name].dtype)
    return out
```

```python
import math
from contextlib import ExitStack, contextmanager

import numpy as np
import concourse.bass as bass
from concourse import mybir

F32 = mybir.dt.float32
I32 = mybir.dt.int32
ALU = mybir.AluOpType
ACT = mybir.ActivationFunctionType
AX = mybir.AxisListType.X

P = 128
T = 256
TT = T // P
D = 1024
DC = D // P
BANK = 512
SLOTS = 6
SLOT = 4096
NEG = -1e30
DEPTH = 2
ALPHA = (2 * DEPTH) ** 0.25
SET = 30

ML_HEADS, ML_DK, ML_DV = 4, 128, 256
GLA_RANK, GLA_TAU = 16, 16.0
E, CAP, FF = 16, 2 * T // 16, 1024
QUADS = E * CAP // P
EQ = P // CAP
HD = 64
NCMP = (T - 32) // 16 + 1
RET_HEADS, RET_QK, RET_V = 4, 256, 512
D_FF = 2816
FFC = D_FF // P
CONV_K = 31
TOPK = T // 4

ARENA = 6656 * TT
WORK = 6400


def const_layout():
    at, cols = {}, 0
    for name, n in (("ident", P), ("ones", P), ("keep_fwd", P), ("keep_bwd", P), ("neg_fwd", 2 * T), ("neg_bwd", 2 * T),
                    ("neg_causal", 2 * T), ("neg_cmp", 2 * NCMP), ("row_cmp", 2), ("ret_inv", P), ("attn_inv", 32),
                    ("decay", RET_HEADS * 2 * P), ("slot_no", CAP), ("pool_count", 4 * 16), ("dist_bucket", T)):
        at[name] = (cols, n)
        cols += n
    return at, cols


def const_table():
    at, cols = const_layout()
    out = np.zeros((P, cols), np.float32)

    def put(name, value):
        value = np.asarray(value, np.float32)
        a, n = at[name]
        out[:value.shape[0], a:a + n] = value.reshape(value.shape[0], n)

    p = np.arange(P)
    t = np.arange(T)
    put("ident", np.eye(P))
    put("ones", np.ones((P, P)))
    put("keep_fwd", p[:, None] <= p[None, :])
    put("keep_bwd", p[:, None] >= p[None, :])
    s = p[:, None, None] + P * np.arange(TT)[None, :, None]
    put("neg_fwd", np.where(s <= t, 0.0, NEG))
    put("neg_bwd", np.where(s >= t, 0.0, NEG))
    put("neg_causal", np.where(t[None, None, :] <= s, 0.0, NEG))
    end = np.arange(NCMP) * 16 + 31
    put("neg_cmp", np.where(end[None, None, :] <= s, 0.0, NEG))
    put("row_cmp", s[:, :, 0] >= end[0])
    f = np.float32
    put("ret_inv", np.tile(f(1.0) / (f(10000.0) ** np.linspace(0.0, 1.0, P).astype(f)), (P, 1)))
    put("attn_inv", np.tile(f(1.0) / (f(10000.0) ** (np.arange(0, HD, 2, dtype=f) / f(HD))), (P, 1)))
    lg = np.log(1.0 - 2.0 ** (-5.0 - np.arange(RET_HEADS)))
    diff = p[None, :] - p[:, None]
    put("decay", np.stack([np.stack([np.where(diff >= 0, np.exp(np.maximum(diff, 0) * g), 0.0),
                                     np.exp((diff + P) * g)]) for g in lg]).transpose(2, 0, 1, 3))
    put("slot_no", np.tile(np.arange(CAP) + 1.0, (P, 1)))
    tt = np.arange(16)
    put("pool_count", np.tile(np.stack([1.0 / np.minimum(tt + 1, w) for w in (2, 4, 8, 16)]).reshape(1, -1), (P, 1)))
    dist = T - 1 - t
    d = np.maximum(dist, 16).astype(f)
    large = 16 + (np.log(d / f(16)) / f(math.log(128 / 16)) * f(16)).astype(np.int32)
    bucket = np.where(dist < 16, dist, np.minimum(large, 31))
    put("dist_bucket", np.arange(32)[:, None] == bucket[None, :])
    return out


class Machine:

    def __init__(self, nc, ctx, consts):
        self.nc = nc
        self.ctx = ctx
        self.consts = consts
        self.layout, cols = const_layout()
        self.cst = self.sbuf("constants", [P, cols])
        self.ring = self.sbuf("weight_ring", [P, SLOTS, SLOT])
        self.arena = self.sbuf("arena", [P, ARENA])
        self.x = self.sbuf("x", [P, TT, D])
        self.xT = self.sbuf("xT", [P, DC, T])
        self.work = self.sbuf("work", [P, WORK])
        self.small = self.sbuf("small", [P, 640])
        self.small_i = self.sbuf("small_integers", [P, 2], I32)
        self.keep = self.work[:, 4864:5376]
        self.ps = ctx.enter_context(nc.psum_tensor("accumulators", [P, 8, BANK], F32))
        self.sets = [[ctx.enter_context(nc.semaphore(f"set{k}_{i}")) for i in range(SET)] for k in range(2)]
        self.turn = 0
        self.slot_loaded = [ctx.enter_context(nc.semaphore(f"slot{i}_loaded")) for i in range(SLOTS)]
        self.unit_used = ctx.enter_context(nc.semaphore("unit_used"))
        self.loads = [0] * SLOTS
        self.last_unit = [0] * SLOTS
        self.units = 0
        self.queue = []
        self.bias_stored = ctx.enter_context(nc.semaphore("bias_stored"))

    def sbuf(self, name, shape, dt=F32):
        return self.ctx.enter_context(self.nc.sbuf_tensor(name, shape, dt))

    def const(self, name, shape=None, rows=P):
        a, n = self.layout[name]
        v = self.cst[0:rows, a:a + n]
        return v

    @contextmanager
    def stage(self, *names):
        mine, other = self.sets[self.turn], self.sets[1 - self.turn]
        self.turn = 1 - self.turn
        assert len(names) <= SET
        with self.nc.Block() as block:
            @block.gpsimd
            def _(pool):
                pool.sem_clear(range(other[0].num, other[-1].num + 1))

            yield block, {n: mine[i] for i, n in enumerate(names)}


class Stream:

    def __init__(self, m, units, full, depth, first, group, parts):
        self.m, self.n, self.depth, self.group, self.parts = m, units, depth, group, parts
        self.groups = full // group if full // group >= 2 else 0
        self.base = m.units
        m.units += units
        self.slots = [(first + r) % SLOTS for r in range(depth)]
        self.load_base = [m.loads[s] for s in self.slots]
        self.free_at = [m.last_unit[s] for s in self.slots]
        self.inc = 16 * len(parts(0, 0, m.ring[:, 0, :]))
        for u in range(units):
            s = self.slots[u % depth]
            m.loads[s] += self.inc
            m.last_unit[s] = self.base + u + 1
        m.queue.append(self)

    def slot(self, j):
        return self.m.ring[:, self.slots[j % self.depth], :]

    def load(self, sp, g, j):
        for dst, src in self.parts(g, j, self.slot(j)):
            sp.dma_start(dst, src).then_inc(self.m.slot_loaded[self.slots[j % self.depth]], 16)

    def prefetch(self, sp):
        for j in range(min(self.depth, self.n)):
            if self.free_at[j]:
                sp.wait_ge(self.m.unit_used, self.free_at[j])
            self.load(sp, 0, j)

    def load_rest(self, sp):
        def one(g, j):
            sp.wait_ge(self.m.unit_used, self.base + 1 + g * self.group + (j - self.depth))
            self.load(sp, g, j)

        first = min(self.group, self.n) if self.groups else 0
        for j in range(self.depth, first):
            one(0, j)
        if self.groups:
            with sp.Fori(1, self.groups) as g:
                for j in range(self.group):
                    one(g, j)
        for u in range(max(self.depth, self.groups * self.group), self.n):
            one(u // self.group, u % self.group)

    def each(self, eng, body):
        if self.groups:
            with eng.Fori(0, self.groups) as g:
                for j in range(self.group):
                    body(g, j)
        for u in range(self.groups * self.group, self.n):
            body(u // self.group, u % self.group)

    def wait_loaded(self, eng, g, j):
        turn = g * (self.group // self.depth) + (j // self.depth + 1)
        eng.wait_ge(self.m.slot_loaded[self.slots[j % self.depth]], self.load_base[j % self.depth] + self.inc * turn)

    def wait_used(self, eng, g, j):
        eng.wait_ge(self.m.unit_used, self.base + 1 + g * self.group + j)

    def next(self):
        q = self.m.queue
        i = q.index(self)
        return q[i + 1] if i + 1 < len(q) else None


def columns_stream(m, w, n, first):
    wv = w.rearrange("(c p) n -> p c n", p=P)

    def parts(g, j, slot):
        u = g * 3 + j
        width = min(BANK, n - u * BANK) if isinstance(u, int) else BANK
        dst = slot.rearrange("p (c n) -> p c n", c=DC)[:, :, 0:width]
        return [(dst, wv[:, :, bass.ds(u * BANK, width)])]

    return Stream(m, -(-n // BANK), n // BANK, 3, first, 3, parts)


def rows_stream(m, w, rows, first):
    wv = w.rearrange("(c p) n -> p c n", p=P)
    chunks = rows // P

    def parts(g, j, slot):
        a = 4 * (g * 3 + j)
        k = min(4, chunks - a)
        return [(slot[:, 0:k * D].rearrange("p (c n) -> p c n", c=k), wv[:, a:a + k, :])]

    return Stream(m, -(-chunks // 4), 0, 3, first, 3, parts)


def expert_stream(m, wg, wu, wd, first):
    ws = [w.rearrange("(q e) (c p) n -> q c p e n", e=EQ, p=P) for w in (wg, wu, wd)]

    def parts(g, j, slot):
        return [(slot.rearrange("p (e n) -> p e n", e=EQ), ws[j // DC][g, j % DC])]

    return Stream(m, QUADS * 3 * DC, QUADS * 3 * DC, SLOTS, first, 3 * DC, parts)


def ffn_stream(m, wg, wu, first):
    gv, uv = (w.rearrange("(c p) n -> p c n", p=P) for w in (wg, wu))

    def parts(g, j, slot):
        s = slot.rearrange("p (w c n) -> p w c n", w=2, c=DC)
        at = bass.ds((g * 3 + j) * T, T)
        return [(s[:, 0], gv[:, :, at]), (s[:, 1], uv[:, :, at])]

    return Stream(m, D_FF // T, D_FF // T, 3, first, 3, parts)


def chain(eng, sem, start=0):
    done = [start]

    def link(ins):
        done[0] += 1
        ins.then_inc(sem, 1)
        eng.wait_ge(sem, done[0])

    return link


def bview(ap, axis, n):
    u = ap.unsqueeze(axis)
    shape = list(u.shape)
    shape[axis] = n
    return u.to_broadcast(shape)



def transposed(m, n, src, dst, gain=None):
    ident = m.const("ident")
    with m.stage("turned", "vector_moved", "scalar_moved") as (block, s):
        def half(c):
            return m.ps[:, (c % 16) // 2, (c % 2) * T:(c % 2) * T + T]

        @block.tensor
        def _(pe):
            for c in range(n):
                if c >= 16 and c % 2 == 0:
                    pe.wait_ge(s["vector_moved"] if c % 4 == 0 else s["scalar_moved"], ((c - 16) // 4 + 1) * 2)
                for t in range(TT):
                    last = pe.transpose(half(c)[:, t * P:(t + 1) * P], src(c, t), ident)
                last.then_inc(s["turned"], 1)

        @block.vector
        def _(dve):
            for c in [c for c in range(n) if c % 4 < 2]:
                dve.wait_ge(s["turned"], min(c // 2 * 2 + 2, n))
                if gain is None:
                    dve.tensor_copy(dst(c), half(c)).then_inc(s["vector_moved"], 1)
                else:
                    dve.tensor_scalar(dst(c), half(c), gain(c), None, ALU.mult).then_inc(s["vector_moved"], 1)

        @block.scalar
        def _(act):
            for c in [c for c in range(n) if c % 4 >= 2]:
                act.wait_ge(s["turned"], min(c // 2 * 2 + 2, n))
                if gain is None:
                    act.copy(dst(c), half(c)).then_inc(s["scalar_moved"], 1)
                else:
                    act.activation(dst(c), half(c), ACT.Copy, scale=gain(c)).then_inc(s["scalar_moved"], 1)


def project(m, stream, n, lhs, z):
    def width(g, j):
        return min(BANK, n - (g * 3 + j) * BANK) if isinstance(g, int) else BANK

    with m.stage("scalar_freed", "vector_freed") as (block, s):
        @block.sync
        def _(sp):
            stream.load_rest(sp)
            if stream.next():
                stream.next().prefetch(sp)

        @block.tensor
        def _(pe):
            def unit(g, j):
                stream.wait_loaded(pe, g, j)
                pe.wait_ge(s["scalar_freed"], g * 3 + j + 1)
                pe.wait_ge(s["vector_freed"], g * 3 + j + 1)
                w = stream.slot(j).rearrange("p (c n) -> p c n", c=DC)
                for t in range(TT):
                    for c in range(DC):
                        last = pe.matmul(m.ps[:, 2 * j + t, 0:width(g, j)], lhs(c, t), w[:, c, 0:width(g, j)],
                                         start=(c == 0), stop=(c == DC - 1))
                last.then_inc(m.unit_used, 1)

            stream.each(pe, unit)

        @block.scalar
        def _(act):
            act.sem_inc(s["scalar_freed"], 3)

            def unit(g, j):
                stream.wait_used(act, g, j)
                act.copy(z[:, 0, bass.ds((g * 3 + j) * BANK, width(g, j))],
                         m.ps[:, 2 * j, 0:width(g, j)]).then_inc(s["scalar_freed"], 1)

            stream.each(act, unit)

        @block.vector
        def _(dve):
            dve.sem_inc(s["vector_freed"], 3)

            def unit(g, j):
                stream.wait_used(dve, g, j)
                dve.tensor_copy(z[:, 1, bass.ds((g * 3 + j) * BANK, width(g, j))],
                                m.ps[:, 2 * j + 1, 0:width(g, j)]).then_inc(s["vector_freed"], 1)

            stream.each(dve, unit)


def project_out(m, stream, chunks, lhs, keep, add):
    with m.stage("residual") as (block, s):
        @block.sync
        def _(sp):
            stream.load_rest(sp)
            if stream.next():
                stream.next().prefetch(sp)

        @block.tensor
        def _(pe):
            for u in range(stream.n):
                stream.wait_loaded(pe, u // 3, u % 3)
                w = stream.slot(u % 3).rearrange("p (c n) -> p c n", c=4)
                for c in range(4 * u, min(4 * u + 4, chunks)):
                    for t in range(TT):
                        for h in range(2):
                            last = pe.matmul(m.ps[:, 2 * t + h, :], lhs(c, t), w[:, c - 4 * u, h * BANK:(h + 1) * BANK],
                                             start=(c == 0), stop=(c == chunks - 1))
                last.then_inc(m.unit_used, 1)

        @block.vector
        def _(dve):
            acc = m.ps[:, 0:4, :].rearrange("p (t h) n -> p t (h n)", t=TT)
            link = chain(dve, s["residual"])
            if keep != 1.0:
                link(dve.tensor_scalar(m.x[:, :, :], m.x[:, :, :], keep, None, ALU.mult))
            stream.wait_used(dve, 0, stream.n - 1)
            link(dve.scalar_tensor_tensor(m.x[:, :, :], acc, add, m.x[:, :, :], ALU.mult, ALU.add))


def layer_normed(m, g, b, eps=1e-5):
    gb = m.work[:, 0:2 * D].rearrange("p (k n) -> p k n", k=2)
    stats = m.small[:, 0:24].rearrange("p (t h k) -> p t h k", t=TT, h=2)
    mv = m.small[:, 24:28].rearrange("p (t k) -> p t k", t=TT)
    rstd = m.small[:, 28:30]
    with m.stage("vec_loaded", "var_ready", "std_ready", "steps") as (block, s):
        @block.sync
        def _(sp):
            sp.dma_start(gb[:, 0, :], g.partition_broadcast(P)).then_inc(s["vec_loaded"], 16)
            sp.dma_start(gb[:, 1, :], b.partition_broadcast(P)).then_inc(s["vec_loaded"], 16)

        @block.vector
        def _(dve):
            link = chain(dve, s["steps"])
            for t in range(TT):
                for h in range(2):
                    dve.bn_stats(stats[:, t, h, :], m.x[:, t, h * BANK:(h + 1) * BANK]).then_inc(s["steps"], 1)
            dve.wait_ge(s["steps"], 4)
            link = chain(dve, s["steps"], 4)
            for t in range(TT):
                link(dve.bn_aggr(mv[:, t, :], stats[:, t, :, :]))
            dve.tensor_scalar(rstd, mv[:, :, 1], eps, None, ALU.add).then_inc(s["var_ready"], 1)
            dve.wait_ge(s["std_ready"], 1)
            link(dve.reciprocal(rstd, rstd))
            for t in range(TT):
                link(dve.tensor_scalar(m.x[:, t, :], m.x[:, t, :], mv[:, t, 0:1], rstd[:, t:t + 1], ALU.subtract, ALU.mult))
            dve.wait_ge(s["vec_loaded"], 32)
            link(dve.tensor_tensor(m.x[:, :, :], m.x[:, :, :], bview(gb[:, 0, :], 1, TT), ALU.mult))
            link(dve.tensor_tensor(m.x[:, :, :], m.x[:, :, :], bview(gb[:, 1, :], 1, TT), ALU.add))

        @block.scalar
        def _(act):
            act.wait_ge(s["var_ready"], 1)
            act.activation(rstd, rstd, ACT.Sqrt).then_inc(s["std_ready"], 1)


def turn_x(m):
    transposed(m, DC, lambda c, t: m.x[:, t, c * P:(c + 1) * P], lambda c: m.xT[:, c, :])


def lhs_x(m):
    return lambda c, t: m.xT[:, c, t * P:(t + 1) * P]


def head_normed(dve, link, eps_added, std_ready, o, out, stats, mv, rstd, eps):
    link(dve.bn_stats(stats, o))
    link(dve.bn_aggr(mv, stats))
    dve.tensor_scalar(rstd, mv[:, 1:2], eps, None, ALU.add).then_inc(eps_added[0], 1)
    eps_added[1] += 1
    dve.wait_ge(std_ready, eps_added[1])
    link(dve.reciprocal(rstd, rstd))
    link(dve.tensor_scalar(out, o, mv[:, 0:1], rstd, ALU.subtract, ALU.mult))



def mlstm(m, in_stream, out_stream, gate_b, norm_g):
    NIN = 2 * ML_HEADS * ML_DK + 2 * D + 4 * ML_HEADS
    z = m.arena[:, 0:2 * NIN].rearrange("p (t n) -> p t n", t=TT)
    H = ML_HEADS
    project(m, in_stream, NIN, lhs_x(m), z)
    G = z[:, :, 3 * D:3 * D + 16]
    w = m.work
    gb = w[:, 0:16]
    tmp = w[:, 16:16 + 32].rearrange("p (k t n) -> p k t n", k=2, t=TT)
    rows = w[0:H, 128:128 + 4 * T].rearrange("p (d k t) -> p d k t", d=2, k=2)
    A = w[0:H, 1152:1152 + 2 * T].rearrange("p (d t) -> p d t", d=2)
    M = w[0:H, 1664:1664 + 2 * T].rearrange("p (d t) -> p d t", d=2)
    B = w[0:H, 2176:2176 + 2 * T].rearrange("p (d t) -> p d t", d=2)
    EM = w[0:H, 2688:2688 + 2 * T].rearrange("p (d t) -> p d t", d=2)
    cols = m.small[:, 0:32].rearrange("p (k d t h) -> p k d t h", k=2, d=2, t=TT)
    ident = m.const("ident")
    ones = m.const("ones")
    rps = m.ps[0:H, 0:2, :].rearrange("p b n -> p (b n)").rearrange("p (d k t) -> p d k t", d=2, k=2)
    with m.stage("bias_loaded", "gates_ready", "exp_in", "exp_out", "steps", "turned", "rows_ready", "back_turned",
                 "m_ready", "em_ready") as (block, s):
        @block.sync
        def _(sp):
            sp.dma_start(gb, gate_b.rearrange("a b h -> (a b h)").partition_broadcast(P)).then_inc(s["bias_loaded"], 16)

        @block.vector
        def _(dve):
            link = chain(dve, s["steps"])
            dve.wait_ge(s["bias_loaded"], 16)
            link(dve.tensor_tensor(G, G, bview(gb, 1, TT), ALU.add))
            Gf = G.rearrange("p t (d k h) -> p t d k h", d=2, k=2)[:, :, :, 1, :]
            lo, ab = (tmp[:, k].rearrange("p t (d h) -> p t d h", d=2) for k in range(2))
            for t in range(TT):
                link(dve.tensor_scalar(lo[:, t], Gf[:, t], 0.0, None, ALU.min))
                link(dve.scalar_tensor_tensor(ab[:, t], lo[:, t], 2.0, Gf[:, t], ALU.mult, ALU.subtract))
            dve.sem_inc(s["exp_in"], 1)
            dve.wait_ge(s["exp_out"], 2)
            for t in range(TT):
                link(dve.tensor_tensor(Gf[:, t], lo[:, t], ab[:, t], ALU.subtract))
            dve.sem_inc(s["gates_ready"], 1)
            dve.wait_ge(s["turned"], 1)
            link(dve.tensor_copy(rows, rps))
            for d in range(2):
                way = slice(None) if d == 0 else slice(None, None, -1)
                link(dve.tensor_tensor_scan(B[:, d, way], ones[0:H, 0:1].to_broadcast([H, T]), rows[:, d, 1, way], 0.0,
                                            ALU.mult, ALU.add))
                link(dve.tensor_tensor(A[:, d, :], rows[:, d, 0, :], B[:, d, :], ALU.subtract))
                link(dve.tensor_tensor_scan(M[:, d, way], ones[0:H, 0:1].to_broadcast([H, T]), A[:, d, way], 0.0,
                                            ALU.mult, ALU.max))
                link(dve.tensor_tensor(B[:, d, :], B[:, d, :], M[:, d, :], ALU.add))
            dve.sem_inc(s["m_ready"], 1)
            dve.wait_ge(s["back_turned"], 1)
            link(dve.tensor_copy(cols, m.ps[:, 2, 0:32].rearrange("p (k d t h) -> p k d t h", k=2, d=2, t=TT)))

        @block.scalar
        def _(act):
            act.wait_ge(s["exp_in"], 1)
            ab = tmp[:, 1]
            act.activation(ab, ab, ACT.Exp).then_inc(s["exp_out"], 1)
            act.wait_ge(s["exp_out"], 1)
            act.activation(ab, ab, ACT.Ln, bias=m.const("ones")[:, 0:1]).then_inc(s["exp_out"], 1)
            act.wait_ge(s["m_ready"], 1)
            act.activation(EM, B, ACT.Exp, scale=-1.0).then_inc(s["em_ready"], 1)

        @block.tensor
        def _(pe):
            pe.wait_ge(s["gates_ready"], 1)
            for d in range(2):
                for k in range(2):
                    for t in range(TT):
                        a = 8 * d + 4 * k
                        last = pe.transpose(rps[:, d, k, t * P:(t + 1) * P], G[:, t, a:a + H], ident)
            last.then_inc(s["turned"], 1)
            pe.wait_ge(s["em_ready"], 1)
            for k, src in enumerate((A, EM)):
                for d in range(2):
                    for t in range(TT):
                        a = ((k * 2 + d) * 2 + t) * H
                        last = pe.transpose(m.ps[:, 2, a:a + H], src[:, d, t * P:(t + 1) * P], ident[0:H, 0:H])
            last.then_inc(s["back_turned"], 1)

    h_acc = w[:, 3200:3200 + 2 * ML_DV].rearrange("p (t n) -> p t n", t=TT)
    qk = w[:, 128:128 + 512].rearrange("p (k t n) -> p k t n", k=2, t=TT)
    qkT = w[:, 640:640 + 512].rearrange("p (k t) -> p k t", k=2)
    Wt = w[:, 3712:3712 + 2 * 512].rearrange("p (d k t) -> p d k t", d=2, k=2)
    Wf = [w[:, 4736:4736 + 1024].rearrange("p (d n) -> p d n", d=2)]
    hcol = m.small[:, 32:64].rearrange("p (k d t o) -> p k d t o", k=2, d=2, t=TT)[:, :, :, :, 0:1]
    den = m.small[:, 64:72]
    Mh = w[0:H, 5760:5760 + 512].rearrange("p (d t) -> p d t", d=2)
    stats, mv, rstd = m.small[:, 80:92], m.small[:, 92:96], m.small[:, 96:98]
    with m.nc.Fori(0, H) as h:
        with m.stage("staged", "turned", "moved", "m_staged", "scores", "m_spread", "steps", "exp_in", "exp_out",
                     "weights_ready", "sums_ready", "eps_added", "std_ready") as (block, s):
            @block.vector
            def _(dve):
                link = chain(dve, s["steps"])
                dve.tensor_scalar(qk[:, 0], z[:, :, bass.ds(h * ML_DK, ML_DK)], ML_DK ** -0.5, None, ALU.mult).then_inc(s["staged"], 1)
                dve.tensor_copy(qk[:, 1], z[:, :, bass.ds(h * ML_DK + H * ML_DK, ML_DK)]).then_inc(s["staged"], 1)
                for d in range(2):
                    dve.tensor_scalar(Mh[:, d, :], M[:, d, :], ident[0:H, bass.ds(h, 1)], None, ALU.mult).then_inc(s["m_staged"], 1)
                for k in range(2):
                    for d in range(2):
                        link(dve.tensor_copy(hcol[:, k, d, :, 0], cols[:, k, d, :, bass.ds(h, 1)].rearrange("p t o -> p (t o)")))
                dve.wait_ge(s["turned"], 1)
                dve.tensor_copy(qkT, m.ps[:, 0, :].rearrange("p (k t) -> p k t", k=2)).then_inc(s["moved"], 1)
                dve.wait_ge(s["m_spread"], 1)
                for d in range(2):
                    neg = m.const("neg_fwd" if d == 0 else "neg_bwd").rearrange("p (k t) -> p k t", k=2)
                    dve.scalar_tensor_tensor(Wt[:, d], bview(m.ps[:, 2 + d, 0:T], 1, 2), -1.0, neg,
                                             ALU.mult, ALU.add).then_inc(s["exp_in"], 1)
                dve.wait_ge(s["exp_out"], 4)
                dve.wait_ge(s["scores"], 1)
                for d in range(2):
                    dve.tensor_tensor(Wf[0][:, d, :], Wt[:, d].rearrange("p k t -> p (k t)"),
                                      m.ps[:, 1, :], ALU.mult).then_inc(s["weights_ready"], 1)
                for d in range(2):
                    for t in range(TT):
                        o = m.ps[:, 4 + 2 * d + t, :]
                        dc = den[:, 2 * d + t:2 * d + t + 1]
                        dve.wait_ge(s["sums_ready"], 2 * d + t + 1)
                        link(dve.tensor_scalar(dc, o[:, ML_DV:ML_DV + 1], -1.0, None, ALU.mult))
                        link(dve.tensor_tensor(dc, dc, o[:, ML_DV:ML_DV + 1], ALU.max))
                        link(dve.tensor_tensor(dc, dc, hcol[:, 1, d, t, :], ALU.max))
                        link(dve.reciprocal(dc, dc))
                        if d == 0:
                            link(dve.tensor_scalar(h_acc[:, t, :], o[:, 0:ML_DV], dc, None, ALU.mult))
                        else:
                            link(dve.scalar_tensor_tensor(h_acc[:, t, :], o[:, 0:ML_DV], dc, h_acc[:, t, :], ALU.mult, ALU.add))
                added = [s["eps_added"], 0]
                for t in range(TT):
                    head_normed(dve, link, added, s["std_ready"], h_acc[:, t, :],
                                z[:, t, bass.ds(h * ML_DV + 2 * H * ML_DK, ML_DV)], stats[:, 6 * t:6 * t + 6], mv[:, 2 * t:2 * t + 2],
                                rstd[:, t:t + 1], 1e-5)

            @block.tensor
            def _(pe):
                pe.wait_ge(s["staged"], 2)
                for k in range(2):
                    for t in range(TT):
                        last = pe.transpose(m.ps[:, 0, k * T + t * P:k * T + (t + 1) * P], qk[:, k, t, :], ident)
                last.then_inc(s["turned"], 1)
                pe.wait_ge(s["m_staged"], 2)
                for d in range(2):
                    last = pe.matmul(m.ps[:, 2 + d, 0:T], ones[0:H, :], Mh[:, d, :], start=True, stop=True)
                last.then_inc(s["m_spread"], 1)
                pe.wait_ge(s["moved"], 1)
                for k in range(2):
                    last = pe.matmul(m.ps[:, 1, k * T:(k + 1) * T], qkT[:, 1, k * P:(k + 1) * P], qkT[:, 0, :], start=True, stop=True)
                last.then_inc(s["scores"], 1)
                for d in range(2):
                    pe.wait_ge(s["weights_ready"], d + 1)
                    for t in range(TT):
                        srcs = [k for k in range(2) if (k <= t if d == 0 else k >= t)]
                        o = m.ps[:, 4 + 2 * d + t, :]
                        for i, k in enumerate(srcs):
                            pe.matmul(o[:, 0:ML_DV], Wf[0][:, d, k * T + t * P:k * T + (t + 1) * P],
                                      z[:, k, bass.ds(h * ML_DV + 2 * H * ML_DK, ML_DV)], start=(i == 0), stop=(i == len(srcs) - 1))
                        for i, k in enumerate(srcs):
                            last = pe.matmul(o[:, ML_DV:ML_DV + 1], Wf[0][:, d, k * T + t * P:k * T + (t + 1) * P],
                                             ones[:, 0:1], start=(i == 0), stop=(i == len(srcs) - 1))
                        last.then_inc(s["sums_ready"], 1)

            @block.scalar
            def _(act):
                for d in range(2):
                    act.wait_ge(s["exp_in"], d + 1)
                    act.wait_ge(s["steps"], 4)
                    for k in range(2):
                        act.activation(Wt[:, d, k, :], Wt[:, d, k, :], ACT.Exp, bias=hcol[:, 0, d, k, :]).then_inc(s["exp_out"], 1)
                for t in range(TT):
                    act.wait_ge(s["eps_added"], t + 1)
                    act.activation(rstd[:, t:t + 1], rstd[:, t:t + 1], ACT.Sqrt).then_inc(s["std_ready"], 1)
        with m.stage() as (block, s):
            pass
    v0 = 2 * H * ML_DK
    gated(m, z, [(v0, v0 + D, D)], ACT.Sigmoid)
    mixed_out(m, out_stream, z, [v0 + c * P for c in range(DC)], ALPHA, 1.0, norm_g)


def gated(m, z, parts, func):
    with m.stage("gate_ready", "steps", "freed") as (block, s):
        @block.scalar
        def _(act):
            for i, (a, b, n) in enumerate(parts):
                act.activation(z[:, :, b:b + n], z[:, :, b:b + n], func).then_inc(s["gate_ready"], 1)

        @block.vector
        def _(dve):
            for i, (a, b, n) in enumerate(parts):
                dve.wait_ge(s["gate_ready"], i + 1)
                dve.tensor_tensor(z[:, :, a:a + n], z[:, :, a:a + n], z[:, :, b:b + n], ALU.mult).then_inc(s["steps"], 1)


def mixed_out(m, stream, z, chunks, keep, add, norm_g=None):
    n = len(chunks)
    zT = m.work[:, 0:n * T].rearrange("p (c t) -> p c t", c=n)
    gain = None
    if norm_g is not None:
        gcol = m.small[:, 600:600 + n]
        load_columns(m, gcol, norm_g)
        gain = lambda c: gcol[:, c:c + 1]
    transposed(m, n, lambda c, t: z[:, t, chunks[c]:chunks[c] + P], lambda c: zT[:, c, :], gain)
    project_out(m, stream, n, lambda c, t: zT[:, c, t * P:(t + 1) * P], keep, add)


def load_columns(m, dst, vec):
    with m.stage("columns_loaded") as (block, s):
        @block.sync
        def _(sp):
            with m.nc.allow_non_contiguous_dma("a vector of one value a partition"):
                sp.dma_start(dst, vec.rearrange("(c p) -> p c", p=P)).then_inc(s["columns_loaded"], 16)
            sp.wait_ge(s["columns_loaded"], 16)


def moe(m, stream, router):
    ar = m.arena
    xin = ar[:, 0:4096].rearrange("p (c n) -> p c n", c=DC)
    outs = ar[:, 4096:8192].rearrange("p (q n) -> p q n", q=QUADS)
    scatter = ar[:, 8192:9216].rearrange("p (q t) -> p q t", q=QUADS)
    sel = ar[:, 9216:10240].rearrange("p (t e j) -> p t e j", t=TT, e=E)
    selg = ar[:, 10240:11264].rearrange("p (t e j) -> p t e j", t=TT, e=E)
    hid = ar[:, 11264:12288]
    w = m.work
    rt = w[:, 0:DC * E].rearrange("p (c e) -> p c e", c=DC)
    aff = w[:, 128:128 + 2 * E].rearrange("p (t e) -> p t e", t=TT)
    pos = w[:, 160:160 + 2 * E].rearrange("p (t e) -> p t e", t=TT)
    rmax, rsum = m.small[:, 0:2], m.small[:, 2:4]
    affT = w[0:E, 256:512]
    left = w[0:E, 512:768]
    took = w[0:E, 768:1024]
    count = w[0:E, 1024:1280]
    top = m.small[0:E, 16:24]
    ident, ones = m.const("ident"), m.const("ones")
    slot_no = m.const("slot_no")
    with m.stage("router_loaded", "logits", "max_ready", "exp_ready", "steps", "aff_ready", "aff_turned", "pos_ready",
                 "pos_turned", "sel_ready", "gathered", "scat_turned", "vector_moved", "scalar_moved") as (block, s):
        @block.sync
        def _(sp):
            sp.dma_start(rt, router.rearrange("(c p) e -> p c e", p=P)).then_inc(s["router_loaded"], 16)

        @block.tensor
        def _(pe):
            pe.wait_ge(s["router_loaded"], 16)
            for t in range(TT):
                for c in range(DC):
                    last = pe.matmul(m.ps[:, 0, t * E:(t + 1) * E], m.xT[:, c, t * P:(t + 1) * P], rt[:, c, :],
                                     start=(c == 0), stop=(c == DC - 1))
            last.then_inc(s["logits"], 1)
            pe.wait_ge(s["aff_ready"], 1)
            for t in range(TT):
                last = pe.transpose(m.ps[0:E, 1, t * P:(t + 1) * P], aff[:, t, :], ident)
            last.then_inc(s["aff_turned"], 1)
            pe.wait_ge(s["pos_ready"], 1)
            for t in range(TT):
                last = pe.transpose(m.ps[:, 0, t * E:(t + 1) * E], took[:, t * P:(t + 1) * P], ident[0:E, 0:E])
            last.then_inc(s["pos_turned"], 1)
            pe.wait_ge(s["sel_ready"], 1)
            for c in range(DC):
                if c >= 6:
                    pe.wait_ge(s["vector_moved"] if c % 2 == 0 else s["scalar_moved"], (c - 6) // 2 + 1)
                for t in range(TT):
                    last = pe.matmul(m.ps[:, 2 + c % 6, :], m.x[:, t, c * P:(c + 1) * P],
                                     sel[:, t].rearrange("p e j -> p (e j)"), start=(t == 0), stop=(t == TT - 1))
                last.then_inc(s["gathered"], 1)
            pe.wait_ge(s["sel_ready"], 2)
            for q in range(QUADS):
                for t in range(TT):
                    last = pe.transpose(m.ps[:, q // 2, (q % 2) * T + t * P:(q % 2) * T + (t + 1) * P],
                                        selg[:, t].rearrange("p e j -> p (e j)")[:, q * P:(q + 1) * P], ident)
            last.then_inc(s["scat_turned"], 1)

        @block.vector
        def _(dve):
            link = chain(dve, s["steps"])
            dve.wait_ge(s["logits"], 1)
            lg = m.ps[:, 0, 0:2 * E].rearrange("p (t e) -> p t e", t=TT)
            link(dve.tensor_reduce(rmax, lg, AX, ALU.max))
            dve.tensor_tensor(aff, lg, bview(rmax, 2, E), ALU.subtract).then_inc(s["max_ready"], 1)
            dve.wait_ge(s["exp_ready"], 1)
            link(dve.tensor_reduce(rsum, aff, AX, ALU.add))
            link(dve.reciprocal(rsum, rsum))
            dve.tensor_tensor(aff, aff, bview(rsum, 2, E), ALU.mult).then_inc(s["aff_ready"], 1)
            dve.wait_ge(s["aff_turned"], 1)
            link(dve.tensor_copy(left, m.ps[0:E, 1, 0:T]))
            for _ in range(CAP // 8):
                link(dve.max(top, left))
                link(dve.match_replace(left, top, left, -1.0))
            link(dve.tensor_scalar(took, left, -1.0, None, ALU.is_equal))
            link(dve.tensor_tensor_scan(count, ones[0:E, 0:1].to_broadcast([E, T]), took, 0.0, ALU.mult, ALU.add))
            dve.tensor_tensor(took, took, count, ALU.mult).then_inc(s["pos_ready"], 1)
            dve.wait_ge(s["pos_turned"], 1)
            link(dve.tensor_copy(pos, m.ps[:, 0, 0:2 * E].rearrange("p (t e) -> p t e", t=TT)))
            for t in range(TT):
                link(dve.tensor_tensor(sel[:, t], bview(slot_no, 1, E), bview(pos[:, t, :], 2, CAP), ALU.is_equal))
            dve.sem_inc(s["sel_ready"], 1)
            for t in range(TT):
                link(dve.tensor_tensor(selg[:, t], sel[:, t], bview(aff[:, t, :], 2, CAP), ALU.mult))
            dve.sem_inc(s["sel_ready"], 1)
            for c in range(0, DC, 2):
                dve.wait_ge(s["gathered"], c + 1)
                dve.tensor_copy(xin[:, c, :], m.ps[:, 2 + c % 6, :]).then_inc(s["vector_moved"], 1)
            dve.wait_ge(s["scat_turned"], 1)
            dve.tensor_copy(scatter.rearrange("p q t -> p (q t)"),
                            m.ps[:, 0:2, :].rearrange("p b n -> p (b n)")).then_inc(s["vector_moved"], 1)
            link(dve.tensor_scalar(m.x[:, :, :], m.x[:, :, :], ALPHA, None, ALU.mult))

        @block.scalar
        def _(act):
            act.wait_ge(s["max_ready"], 1)
            act.activation(aff, aff, ACT.Exp).then_inc(s["exp_ready"], 1)
            for c in range(1, DC, 2):
                act.wait_ge(s["gathered"], c + 1)
                act.copy(xin[:, c, :], m.ps[:, 2 + c % 6, :]).then_inc(s["scalar_moved"], 1)

    xq = w[:, 1280:1280 + D].rearrange("p (c n) -> p c n", c=DC)
    hT = w[:, 2304:2304 + D].rearrange("p (c n) -> p c n", c=DC)
    sg = w[:, 3328:3328 + D]
    gate = m.ps[:, 0:2, :].rearrange("p b n -> p (b n)")
    up = m.ps[:, 2:4, :].rearrange("p b n -> p (b n)")
    down = m.ps[:, 4:6, :].rearrange("p b n -> p (b n)")
    turn = m.ps[:, 6:8, :].rearrange("p b n -> p (b n)")
    GATE, UP, DOWN = DC - 1, 2 * DC - 1, 3 * DC - 1
    with m.stage("tokens_staged", "gate_done", "hidden_ready", "hidden_turned", "hT_ready", "answer_moved",
                 "steps") as (block, s):
        @block.sync
        def _(sp):
            stream.load_rest(sp)
            if stream.next():
                stream.next().prefetch(sp)

        @block.tensor
        def _(pe):
            def unit(g, j):
                if j == 0:
                    pe.wait_ge(s["tokens_staged"], g + 1)
                if j == 2 * DC:
                    pe.wait_ge(s["hidden_ready"], g + 1)
                    for c in range(DC):
                        last = pe.transpose(turn[:, c * P:(c + 1) * P], hid[:, c * P:(c + 1) * P], ident)
                    last.then_inc(s["hidden_turned"], 1)
                    pe.wait_ge(s["hT_ready"], g + 1)
                stream.wait_loaded(pe, g, j)
                w4 = stream.slot(j).rearrange("p (e n) -> p e n", e=EQ)
                acc = (gate, up, down)[j // DC]
                lhs = xq if j < 2 * DC else hT
                c = j % DC
                for half in range(2):
                    for e in range(EQ):
                        last = pe.matmul(acc[e * CAP:(e + 1) * CAP, half * BANK:(half + 1) * BANK],
                                         lhs[:, c, e * CAP:(e + 1) * CAP], w4[:, e, half * BANK:(half + 1) * BANK],
                                         start=(c == 0), stop=(c == DC - 1), tile_position=(0, e * CAP))
                last.then_inc(m.unit_used, 1)

            stream.each(pe, unit)

        @block.scalar
        def _(act):
            with act.Fori(0, QUADS) as g:
                stream.wait_used(act, g, GATE)
                act.activation(sg, gate, ACT.Silu).then_inc(s["gate_done"], 1)
                stream.wait_used(act, g, DOWN)
                act.copy(outs[:, bass.ds(g, 1), :].rearrange("p o n -> p (o n)"), down).then_inc(s["answer_moved"], 1)

        @block.vector
        def _(dve):
            with dve.Fori(0, QUADS) as g:
                dve.tensor_copy(xq, xin[:, :, bass.ds(g * P, P)]).then_inc(s["tokens_staged"], 1)
                stream.wait_used(dve, g, UP)
                dve.wait_ge(s["gate_done"], g + 1)
                dve.tensor_tensor(hid, sg, up, ALU.mult).then_inc(s["hidden_ready"], 1)
                dve.wait_ge(s["hidden_turned"], g + 1)
                dve.tensor_copy(hT.rearrange("p c n -> p (c n)"), turn).then_inc(s["hT_ready"], 1)
                dve.wait_ge(s["answer_moved"], g + 1)

    with m.stage("summed", "steps") as (block, s):
        @block.tensor
        def _(pe):
            for t in range(TT):
                for half in range(2):
                    for q in range(QUADS):
                        last = pe.matmul(m.ps[:, 2 * t + half, :], scatter[:, q, t * P:(t + 1) * P],
                                         outs[:, q, half * BANK:(half + 1) * BANK], start=(q == 0), stop=(q == QUADS - 1))
                last.then_inc(s["summed"], 1)

        @block.vector
        def _(dve):
            for t in range(TT):
                dve.wait_ge(s["summed"], t + 1)
                dve.tensor_tensor(m.x[:, t, :], m.ps[:, 2 * t:2 * t + 2, :].rearrange("p h n -> p (h n)"),
                                  m.x[:, t, :], ALU.add).then_inc(s["steps"], 1)



def gla(m, in_stream, out_stream, gate_w, gate_b, norm_g):
    H, DK, DV = 4, P, 2 * P
    NIN = 2 * H * DK + 2 * D + 2 * GLA_RANK
    z = m.arena[:, 0:2 * NIN].rearrange("p (t n) -> p t n", t=TT)
    project(m, in_stream, NIN, lhs_x(m), z)
    w = m.work
    gbc = m.small[:, 0:2 * H]
    load_columns(m, gbc, gate_b.rearrange("d n -> (d n)"))
    gw = w[0:GLA_RANK, 0:2 * H * DK].rearrange("p (d n) -> p d n", d=2)
    lowT = w[0:GLA_RANK, 1024:1024 + 2 * T].rearrange("p (d t) -> p d t", d=2)
    ident = m.const("ident")
    with m.stage("turned", "steps", "gate_w_loaded") as (block, s):
        @block.sync
        def _(sp):
            sp.dma_start(gw, gate_w.rearrange("d r n -> r d n")).then_inc(s["gate_w_loaded"], 16)
            sp.wait_ge(s["gate_w_loaded"], 16)

        @block.tensor
        def _(pe):
            for d in range(2):
                for t in range(TT):
                    a = NIN - 2 * GLA_RANK + d * GLA_RANK
                    last = pe.transpose(m.ps[0:GLA_RANK, 0, d * T + t * P:d * T + (t + 1) * P], z[:, t, a:a + GLA_RANK], ident)
            last.then_inc(s["turned"], 1)

        @block.vector
        def _(dve):
            dve.wait_ge(s["turned"], 1)
            dve.tensor_copy(lowT, m.ps[0:GLA_RANK, 0, :].rearrange("p (d t) -> p d t", d=2)).then_inc(s["steps"], 1)

    qk = w[:, 1536:2048].rearrange("p (k t n) -> p k t n", k=2, t=TT)
    qkT = w[:, 2048:2560].rearrange("p (k t) -> p k t", k=2)
    gwh = w[0:GLA_RANK, 2560:2816].rearrange("p (d n) -> p d n", d=2)
    bh = m.small[:, 10:12]
    lo = w[:, 2816:3328].rearrange("p (d t) -> p d t", d=2)
    ab = w[:, 3328:3840].rearrange("p (d t) -> p d t", d=2)
    B = w[:, 3840:4352].rearrange("p (d t) -> p d t", d=2)
    QE = w[:, 4352:5120].rearrange("p (d i t) -> p d i t", d=2, i=3)
    KE = w[:, 5120:5888].rearrange("p (d i t) -> p d i t", d=2, i=3)
    Wf = w[:, 2816:3584].rearrange("p (d i t) -> p d i t", d=2, i=3)
    neg = m.small[:, 12:18].rearrange("p (d i) -> p d i", d=2)
    stats, mv, rstd = m.small[:, 80:92], m.small[:, 92:96], m.small[:, 96:98]
    ones = m.const("ones")
    v0 = 2 * H * DK
    centre = [[P // 2, P + P // 2, P - 1], [P // 2, P + P // 2, P]]
    q_tile = [[0, 1, 1], [0, 1, 0]]
    k_tile = [[0, 1, 0], [0, 1, 1]]
    with m.nc.Fori(0, H) as h:
        with m.stage("staged", "turned", "moved", "gates_staged", "gates_made", "steps", "exp_in", "ln_out",
                     "sums_ready", "decays_out", "products_ready", "scores", "weights_ready", "out_ready", "eps_added",
                     "std_ready") as (block, s):
            @block.vector
            def _(dve):
                link = chain(dve, s["steps"])
                dve.tensor_scalar(qk[:, 0], z[:, :, bass.ds(h * DK, DK)], DK ** -0.5, None, ALU.mult).then_inc(s["staged"], 1)
                dve.tensor_copy(qk[:, 1], z[:, :, bass.ds(h * DK + H * DK, DK)]).then_inc(s["staged"], 1)
                dve.tensor_copy(gwh, gw[:, :, bass.ds(h * DK, DK)]).then_inc(s["gates_staged"], 1)
                link(dve.tensor_copy(bh, gbc.rearrange("p (d h) -> p d h", d=2)[:, :, bass.ds(h, 1)].rearrange("p d o -> p (d o)")))
                dve.wait_ge(s["turned"], 1)
                dve.tensor_copy(qkT, m.ps[:, 0, :].rearrange("p (k t) -> p k t", k=2)).then_inc(s["moved"], 1)
                dve.wait_ge(s["gates_made"], 1)
                for d in range(2):
                    y = m.ps[:, 1, d * T:(d + 1) * T]
                    link(dve.tensor_scalar(lo[:, d], y, bh[:, d:d + 1], 0.0, ALU.add, ALU.min))
                    link(dve.tensor_scalar(ab[:, d], y, bh[:, d:d + 1], None, ALU.add))
                link(dve.scalar_tensor_tensor(ab, lo, 2.0, ab, ALU.mult, ALU.subtract))
                dve.sem_inc(s["exp_in"], 1)
                dve.wait_ge(s["ln_out"], 2)
                link(dve.tensor_tensor(lo, lo, ab, ALU.subtract))
                link(dve.tensor_scalar(lo, lo, 1.0 / GLA_TAU, None, ALU.mult))
                for d in range(2):
                    way = slice(None) if d == 0 else slice(None, None, -1)
                    link(dve.tensor_tensor_scan(B[:, d, way], ones[:, 0:1].to_broadcast([P, T]), lo[:, d, way], 0.0,
                                                ALU.mult, ALU.add))
                for d in range(2):
                    for i in range(3):
                        c = centre[d][i]
                        link(dve.tensor_scalar(neg[:, d, i:i + 1], B[:, d, c:c + 1], -1.0, None, ALU.mult))
                dve.sem_inc(s["sums_ready"], 1)
                dve.wait_ge(s["decays_out"], 12)
                dve.wait_ge(s["moved"], 1)
                for d in range(2):
                    for X, k, tiles in ((QE, 0, q_tile[d]), (KE, 1, k_tile[d])):
                        dve.tensor_tensor(X[:, d, 0:2, :], X[:, d, 0:2, :], qkT[:, k, :].rearrange("p (i t) -> p i t", i=2),
                                          ALU.mult).then_inc(s["products_ready"], 1)
                        c = tiles[2]
                        dve.tensor_tensor(X[:, d, 2, :], X[:, d, 2, :], qkT[:, k, c * P:(c + 1) * P],
                                          ALU.mult).then_inc(s["products_ready"], 1)
                dve.wait_ge(s["scores"], 1)
                for d in range(2):
                    keep = m.const("keep_fwd" if d == 0 else "keep_bwd")
                    sc = m.ps[:, 2 + d, 0:3 * P].rearrange("p (i t) -> p i t", i=3)
                    link(dve.tensor_tensor(Wf[:, d, 0:2, :], sc[:, 0:2, :], bview(keep, 1, 2), ALU.mult))
                    link(dve.tensor_copy(Wf[:, d, 2, :], sc[:, 2, :]))
                dve.tensor_tensor(Wf[:, 0, 0:2, :], Wf[:, 0, 0:2, :], Wf[:, 1, 0:2, :], ALU.add).then_inc(s["weights_ready"], 1)
                added = [s["eps_added"], 0]
                dve.wait_ge(s["out_ready"], 2)
                for t in range(TT):
                    head_normed(dve, link, added, s["std_ready"], m.ps[:, 4 + t, 0:DV], z[:, t, bass.ds(h * DV + v0, DV)],
                                stats[:, 6 * t:6 * t + 6], mv[:, 2 * t:2 * t + 2], rstd[:, t:t + 1], 1e-5)

            @block.tensor
            def _(pe):
                pe.wait_ge(s["staged"], 2)
                for k in range(2):
                    for t in range(TT):
                        last = pe.transpose(m.ps[:, 0, k * T + t * P:k * T + (t + 1) * P], qk[:, k, t, :], ident)
                last.then_inc(s["turned"], 1)
                pe.wait_ge(s["gates_staged"], 1)
                for d in range(2):
                    last = pe.matmul(m.ps[:, 1, d * T:(d + 1) * T], gwh[:, d, :], lowT[:, d, :], start=True, stop=True)
                last.then_inc(s["gates_made"], 1)
                pe.wait_ge(s["products_ready"], 8)
                for d in range(2):
                    for i in range(3):
                        last = pe.matmul(m.ps[:, 2 + d, i * P:(i + 1) * P], KE[:, d, i, :], QE[:, d, i, :], start=True, stop=True)
                last.then_inc(s["scores"], 1)
                pe.wait_ge(s["weights_ready"], 1)
                v = z[:, :, bass.ds(h * DV + v0, DV)]
                for t, d in ((0, 1), (1, 0)):
                    pe.matmul(m.ps[:, 4 + t, 0:DV], Wf[:, 0, t, :], v[:, t, :], start=True, stop=False)
                    pe.matmul(m.ps[:, 4 + t, 0:DV], Wf[:, d, 2, :], v[:, 1 - t, :], start=False, stop=True).then_inc(s["out_ready"], 1)

            @block.scalar
            def _(act):
                act.wait_ge(s["exp_in"], 1)
                act.activation(ab, ab, ACT.Exp).then_inc(s["ln_out"], 1)
                act.wait_ge(s["ln_out"], 1)
                act.activation(ab, ab, ACT.Ln, bias=ones[:, 0:1]).then_inc(s["ln_out"], 1)
                act.wait_ge(s["sums_ready"], 1)
                for d in range(2):
                    for i in range(3):
                        c, qt, kt = centre[d][i], q_tile[d][i], k_tile[d][i]
                        act.activation(QE[:, d, i, :], B[:, d, qt * P:(qt + 1) * P], ACT.Exp,
                                       bias=neg[:, d, i:i + 1]).then_inc(s["decays_out"], 1)
                        act.activation(KE[:, d, i, :], B[:, d, kt * P:(kt + 1) * P], ACT.Exp, scale=-1.0,
                                       bias=B[:, d, c:c + 1]).then_inc(s["decays_out"], 1)
                for t in range(TT):
                    act.wait_ge(s["eps_added"], t + 1)
                    act.activation(rstd[:, t:t + 1], rstd[:, t:t + 1], ACT.Sqrt).then_inc(s["std_ready"], 1)
        with m.stage() as (block, s):
            pass
    gated(m, z, [(v0, v0 + D, D)], ACT.Silu)
    mixed_out(m, out_stream, z, [v0 + c * P for c in range(DC)], ALPHA, 1.0, norm_g)



def rms_scaled(m, src, dst, eps):
    square = m.work[:, 2 * D:3 * D]
    ss = m.small[:, 0:2]
    with m.stage("squares", "mean_ready", "std_ready", "steps") as (block, s):
        @block.scalar
        def _(act):
            for t in range(TT):
                act.activation(square, src[:, t, :], ACT.Square, accum_out=ss[:, t:t + 1]).then_inc(s["squares"], 1)
                act.wait_ge(s["squares"], t + 1)
            act.wait_ge(s["mean_ready"], 1)
            act.activation(ss, ss, ACT.Sqrt).then_inc(s["std_ready"], 1)

        @block.vector
        def _(dve):
            link = chain(dve, s["steps"])
            dve.wait_ge(s["squares"], TT)
            dve.tensor_scalar(ss, ss, 1.0 / D, eps, ALU.mult, ALU.add).then_inc(s["mean_ready"], 1)
            dve.wait_ge(s["std_ready"], 1)
            link(dve.reciprocal(ss, ss))
            for t in range(TT):
                link(dve.tensor_scalar(dst[:, t, :], src[:, t, :], ss[:, t:t + 1], None, ALU.mult))


def rms_turned(m, src, gain, eps=1e-6):
    gcol = m.small[:, 600:600 + DC]
    scaled = m.work[:, 0:2 * D].rearrange("p (t n) -> p t n", t=TT)
    load_columns(m, gcol, gain)
    rms_scaled(m, src, scaled, eps)
    transposed(m, DC, lambda c, t: scaled[:, t, c * P:(c + 1) * P], lambda c: m.xT[:, c, :], lambda c: gcol[:, c:c + 1])


def rms_normed(m, gain, eps=1e-6):
    rms_scaled(m, m.x, m.x, eps)
    g = m.work[:, 0:D]
    with m.stage("gain_loaded", "steps") as (block, s):
        @block.sync
        def _(sp):
            sp.dma_start(g, gain.partition_broadcast(P)).then_inc(s["gain_loaded"], 16)

        @block.vector
        def _(dve):
            dve.wait_ge(s["gain_loaded"], 16)
            dve.tensor_tensor(m.x[:, :, :], m.x[:, :, :], bview(g, 1, TT), ALU.mult).then_inc(s["steps"], 1)


TURN = 6.28125
TURN_LOW = float(np.float32(2 * math.pi - TURN))
TURN_LAST = 2 * math.pi - TURN - TURN_LOW
ROUND = 1.5 * 2.0 ** 23
HALF_TURN = 3.1415925


def rotary_tables(m, positions, tables):
    pos_i = m.small_i[:, 0:2]
    pos = m.small[:, 0:2]
    with m.stage("positions_loaded", "angles_ready", "steps", "made") as (block, s):
        @block.sync
        def _(sp):
            with m.nc.allow_non_contiguous_dma("one position a partition"):
                sp.dma_start(pos_i, positions[0].rearrange("(t p) -> p t", p=P)).then_inc(s["positions_loaded"], 16)

        @block.vector
        def _(dve):
            link = chain(dve, s["steps"])
            dve.wait_ge(s["positions_loaded"], 16)
            link(dve.tensor_copy(pos, pos_i))
            for cos, sin, freq, n in tables:
                k = m.work[:, 0:2 * n].rearrange("p (t n) -> p t n", t=TT)
                for t in range(TT):
                    link(dve.tensor_scalar(sin[:, t], freq, pos[:, t:t + 1], None, ALU.mult))
                link(dve.tensor_scalar(k, sin, 1.0 / (2 * math.pi), None, ALU.mult))
                link(dve.tensor_scalar(k, k, ROUND, None, ALU.add))
                link(dve.tensor_scalar(k, k, -ROUND, None, ALU.add))
                for part in (TURN, TURN_LOW, TURN_LAST):
                    link(dve.scalar_tensor_tensor(sin, k, -part, sin, ALU.mult, ALU.add))
                link(dve.tensor_scalar(cos, sin, math.pi / 2, None, ALU.add))
                link(dve.tensor_scalar(k, cos, math.pi, -2 * math.pi, ALU.is_gt, ALU.mult))
                link(dve.tensor_tensor(cos, cos, k, ALU.add))
                for x in (cos, sin):
                    link(dve.tensor_scalar(x, x, -HALF_TURN, HALF_TURN, ALU.max, ALU.min))
            dve.sem_inc(s["angles_ready"], 1)

        @block.scalar
        def _(act):
            act.wait_ge(s["angles_ready"], 1)
            for cos, sin, freq, n in tables:
                act.activation(cos, cos, ACT.Sin).then_inc(s["made"], 1)
                act.activation(sin, sin, ACT.Sin).then_inc(s["made"], 1)


def rotated(m, z, regions, cos, sin, half, tmp):
    with m.stage("steps") as (block, s):
        @block.vector
        def _(dve):
            link = chain(dve, s["steps"])
            for col, n in regions:
                for t in range(TT):
                    zz = z[:, t, col:col + n * 2 * half].rearrange("p (h k j) -> p h k j", k=2, j=half)
                    a, b = zz[:, :, 0, :], zz[:, :, 1, :]
                    c, sn = bview(cos[:, t], 1, n), bview(sin[:, t], 1, n)
                    ta = tmp[:, 0:n * half].rearrange("p (h j) -> p h j", h=n)
                    tb = tmp[:, n * half:2 * n * half].rearrange("p (h j) -> p h j", h=n)
                    link(dve.tensor_tensor(ta, a, sn, ALU.mult))
                    link(dve.tensor_tensor(tb, b, sn, ALU.mult))
                    link(dve.tensor_tensor(a, a, c, ALU.mult))
                    link(dve.tensor_tensor(b, b, c, ALU.mult))
                    link(dve.tensor_tensor(a, a, tb, ALU.subtract))
                    link(dve.tensor_tensor(b, b, ta, ALU.add))


def attention(m, iters, z, kv, q_at, k_at, v_at, scale, neg=None, bias=None, cmp=None, base=0):
    w = m.work
    qn = 1 if cmp else 2
    qs = w[:, base:base + 256].rearrange("p (t n) -> p t n", t=TT)
    ks = w[:, base + 256:base + 512].rearrange("p (b t n) -> p b t n", b=2, t=TT)
    qT = w[0:HD, base + 512:base + 1024].rearrange("p (b t) -> p b t", b=2)
    kT = w[0:HD, base + 1024:base + 1536].rearrange("p (b t) -> p b t", b=2)
    L = w[:, base + 1536:base + 2560].rearrange("p (b t s) -> p b t s", b=2, t=TT)
    PT = w[:, base + 2560:base + 3584].rearrange("p (b s t) -> p b s t", b=2, s=2)
    bm = w[:, base + 3584:base + 4608].rearrange("p (b t s) -> p b t s", b=2, t=TT)
    Lc = w[:, base + 3584:base + 3584 + 2 * NCMP].rearrange("p (t s) -> p t s", t=TT)
    PTc = w[0:NCMP, base + 3648:base + 3648 + T]
    mx = m.small[:, 0:6]
    sm = m.small[:, 6:12]
    fac = m.small[:, 12:18].rearrange("p (b t) -> p b t", b=3)
    ident = m.const("ident")
    with m.nc.Fori(0, iters) as i:
        with m.stage("staged", "turned", "moved", "bias_loaded", "steps") as (block, s):
            @block.sync
            def _(sp):
                if bias is not None:
                    for b in range(2):
                        for t in range(TT):
                            sp.dma_start(bm[:, b, t, :], bias(i, b, t)).then_inc(s["bias_loaded"], 16)

            @block.vector
            def _(dve):
                dve.tensor_copy(qs[:, :, 0:qn * HD], z[:, :, bass.ds(q_at(i), qn * HD)]).then_inc(s["staged"], 1)
                for b in range(2):
                    dve.tensor_copy(ks[:, b], kv[:, :, bass.ds(k_at(i, b), HD)]).then_inc(s["staged"], 1)
                dve.wait_ge(s["turned"], 1)
                dve.tensor_copy(qT[:, 0:qn], m.ps[0:HD, 0, 0:qn * T].rearrange("p (b t) -> p b t", b=qn)).then_inc(s["moved"], 1)
                if bias is not None:
                    dve.wait_ge(s["bias_loaded"], 64)
                    dve.tensor_tensor(bm, bm, bview(neg, 1, 2), ALU.add).then_inc(s["steps"], 1)

            @block.tensor
            def _(pe):
                pe.wait_ge(s["staged"], 3)
                for b in range(qn):
                    for t in range(TT):
                        last = pe.transpose(m.ps[0:HD, 0, b * T + t * P:b * T + (t + 1) * P], qs[:, t, b * HD:(b + 1) * HD], ident)
                last.then_inc(s["turned"], 1)
                for b in range(2):
                    for t in range(TT):
                        last = pe.transpose(m.ps[0:HD, 1, b * T + t * P:b * T + (t + 1) * P], ks[:, b, t, :], ident)
                last.then_inc(s["turned"], 1)

            @block.scalar
            def _(act):
                act.wait_ge(s["turned"], 2)
                act.copy(kT, m.ps[0:HD, 1, :].rearrange("p (b t) -> p b t", b=2)).then_inc(s["moved"], 1)

        with m.stage("scores", "cmp_scores", "max_ready", "exp_out", "turned", "vector_moved", "scalar_moved",
                     "sums_ready", "steps") as (block, s):
            @block.tensor
            def _(pe):
                for b in range(2):
                    for t in range(TT):
                        last = pe.matmul(m.ps[:, b, t * T:(t + 1) * T], qT[:, b % qn, t * P:(t + 1) * P], kT[:, b, :],
                                         start=True, stop=True)
                last.then_inc(s["scores"], 1)
                if cmp:
                    for t in range(TT):
                        last = pe.matmul(m.ps[:, 5, t * NCMP:(t + 1) * NCMP], qT[:, 0, t * P:(t + 1) * P],
                                         cmp["keys"](i), start=True, stop=True)
                    last.then_inc(s["cmp_scores"], 1)
                for b in range(2):
                    pe.wait_ge(s["exp_out"], 2 * b + 2)
                    for k in range(2):
                        for t in range(TT):
                            last = pe.transpose(m.ps[:, 2 + b, k * T + t * P:k * T + (t + 1) * P],
                                                L[:, b, t, k * P:(k + 1) * P], ident)
                    last.then_inc(s["turned"], 1)
                if cmp:
                    pe.wait_ge(s["exp_out"], 6)
                    for t in range(TT):
                        last = pe.transpose(m.ps[0:NCMP, 6, t * P:(t + 1) * P], Lc[:, t, :], ident)
                    last.then_inc(s["turned"], 1)
                pe.wait_ge(s["vector_moved"], 1)
                pe.wait_ge(s["scalar_moved"], 1)
                for b in range(2):
                    for t in range(TT):
                        for k in range(2):
                            last = pe.matmul(m.ps[:, 4, (b * 2 + t) * HD:(b * 2 + t + 1) * HD], PT[:, b, k, t * P:(t + 1) * P],
                                             kv[:, k, bass.ds(v_at(i, b), HD)], start=(k == 0), stop=(k == 1))
                if cmp:
                    pe.wait_ge(s["vector_moved"], 2)
                    for t in range(TT):
                        last = pe.matmul(m.ps[:, 4, (4 + t) * HD:(5 + t) * HD], PTc[:, t * P:(t + 1) * P],
                                         cmp["values"](i), start=True, stop=True)
                last.then_inc(s["sums_ready"], 1)

            @block.vector
            def _(dve):
                link = chain(dve, s["steps"])
                dve.wait_ge(s["scores"], 1)
                sc = m.ps[:, 0:2, :].rearrange("p b (t s) -> p b t s", t=TT)
                if bias is not None:
                    link(dve.scalar_tensor_tensor(L, sc, scale, bm, ALU.mult, ALU.add))
                elif neg is not None:
                    for b in range(2):
                        link(dve.scalar_tensor_tensor(L[:, b], sc[:, b], scale, neg, ALU.mult, ALU.add))
                else:
                    link(dve.tensor_scalar(L, sc, scale, None, ALU.mult))
                link(dve.tensor_reduce(mx[:, 0:4], L.rearrange("p b t s -> p (b t) s"), AX, ALU.max))
                if cmp:
                    dve.wait_ge(s["cmp_scores"], 1)
                    link(dve.scalar_tensor_tensor(Lc, m.ps[:, 5, 0:2 * NCMP].rearrange("p (t s) -> p t s", t=TT), scale,
                                                  m.const("neg_cmp").rearrange("p (t s) -> p t s", t=TT), ALU.mult, ALU.add))
                    link(dve.tensor_reduce(mx[:, 4:6], Lc, AX, ALU.max))
                n = 6 if cmp else 4
                dve.tensor_scalar(mx[:, 0:n], mx[:, 0:n], -1.0, None, ALU.mult).then_inc(s["max_ready"], 1)
                dve.wait_ge(s["turned"], 1)
                dve.tensor_copy(PT[:, 0].rearrange("p s t -> p (s t)"), m.ps[:, 2, :]).then_inc(s["vector_moved"], 1)
                if cmp:
                    dve.wait_ge(s["turned"], 3)
                    dve.tensor_copy(PTc, m.ps[0:NCMP, 6, 0:T]).then_inc(s["vector_moved"], 1)
                dve.wait_ge(s["exp_out"], n)
                link(dve.reciprocal(sm[:, 0:n], sm[:, 0:n]))
                if cmp:
                    link(dve.tensor_tensor(sm[:, 4:6], sm[:, 4:6], m.const("row_cmp"), ALU.mult))
                    for b, branch in enumerate((1, 2, 0)):
                        link(dve.tensor_tensor(fac[:, b, :], sm[:, 2 * b:2 * b + 2], cmp["gate"](i, branch), ALU.mult))
                dve.wait_ge(s["sums_ready"], 1)
                for t in range(TT):
                    if cmp:
                        o = z[:, t, bass.ds(q_at(i), HD)]
                        for b in range(3):
                            part = m.ps[:, 4, (b * 2 + t) * HD:(b * 2 + t + 1) * HD]
                            if b == 0:
                                link(dve.tensor_scalar(o, part, fac[:, b, t:t + 1], None, ALU.mult))
                            else:
                                link(dve.scalar_tensor_tensor(o, part, fac[:, b, t:t + 1], o, ALU.mult, ALU.add))
                    else:
                        for b in range(2):
                            link(dve.tensor_scalar(z[:, t, bass.ds(q_at(i) + b * HD, HD)],
                                                   m.ps[:, 4, (b * 2 + t) * HD:(b * 2 + t + 1) * HD],
                                                   sm[:, 2 * b + t:2 * b + t + 1], None, ALU.mult))

            @block.scalar
            def _(act):
                act.wait_ge(s["max_ready"], 1)
                for b in range(2):
                    for t in range(TT):
                        j = 2 * b + t
                        act.activation(L[:, b, t, :], L[:, b, t, :], ACT.Exp, bias=mx[:, j:j + 1],
                                       accum_out=sm[:, j:j + 1]).then_inc(s["exp_out"], 1)
                if cmp:
                    for t in range(TT):
                        act.activation(Lc[:, t, :], Lc[:, t, :], ACT.Exp, bias=mx[:, 4 + t:5 + t],
                                       accum_out=sm[:, 4 + t:5 + t]).then_inc(s["exp_out"], 1)
                act.wait_ge(s["turned"], 2)
                act.copy(PT[:, 1].rearrange("p s t -> p (s t)"), m.ps[:, 3, :]).then_inc(s["scalar_moved"], 1)


def memory_attention(m, z, q0, kvm):
    attention(m, 2, z, kvm, lambda i: i * (2 * HD) + q0, lambda i, b: i * (2 * HD) + b * HD,
              lambda i, b: i * (2 * HD) + (b + 4) * HD, HD ** -0.5)


def compressed(m, z, a, keys, values, aT, blk):
    w = m.work
    w1 = w[0:HD, 0:4096].rearrange("p (k l e) -> p k l e", k=2, l=32)
    w2 = m.small[0:HD, 400:528].rearrange("p (k e) -> p k e", k=2)
    pe_rows = m.small[0:32, 528:592].rearrange("p (o d) -> p o d", o=1)
    pe2_rows = w[0:32, 4096:4160]
    peT = w[0:HD, 4160:4224].rearrange("p (k l) -> p k l", k=2)
    hid = m.small[0:HD, 288:348].rearrange("p (k n) -> p k n", k=2)
    ident = m.const("ident")
    with m.stage("weights_loaded", "turned", "moved", "blocks_ready", "hidden", "silu_out", "made", "steps") as (block, s):
        @block.sync
        def _(sp):
            for k, kind in enumerate(("k", "v")):
                sp.dma_start(w1[:, k], a[f"l0_cmp_w1_{kind}_2"].rearrange("l d e -> d l e")).then_inc(s["weights_loaded"], 16)
                sp.dma_start(w2[:, k], a[f"l0_cmp_w2_{kind}_2"]).then_inc(s["weights_loaded"], 16)
            sp.dma_start(pe_rows[:, 0, :], a["l0_cmp_pe_k_2"]).then_inc(s["weights_loaded"], 16)
            sp.dma_start(pe2_rows, a["l0_cmp_pe_v_2"]).then_inc(s["weights_loaded"], 16)

        @block.tensor
        def _(pe):
            pe.wait_ge(s["weights_loaded"], 96)
            for k in range(2):
                for g in range(2):
                    for t in range(TT):
                        c = 512 + k * 128 + g * HD
                        last = pe.transpose(m.ps[0:HD, k, g * T + t * P:g * T + (t + 1) * P], z[:, t, c:c + HD], ident)
                last.then_inc(s["turned"], 1)
            for k, rows in enumerate((pe_rows[:, 0, :], pe2_rows)):
                last = pe.transpose(m.ps[0:HD, 2, k * 32:(k + 1) * 32], rows, ident[0:32, 0:32])
            last.then_inc(s["turned"], 1)
            for k in range(2):
                pe.wait_ge(s["blocks_ready"], k + 1)
                for l in range(32):
                    last = pe.matmul(m.ps[0:HD, 3 + k, 0:2 * NCMP], w1[:, k, l, :], blk[:, k, l], start=(l == 0), stop=(l == 31))
                last.then_inc(s["hidden"], 1)
            pe.wait_ge(s["silu_out"], 2)
            pe.matmul(m.ps[0:HD, 5, 0:2 * NCMP], w2[:, 0, :], hid[:, 0, :], start=True, stop=True).then_inc(s["made"], 1)
            for g in range(2):
                last = pe.matmul(m.ps[0:NCMP, 6, g * HD:(g + 1) * HD], hid[:, 1, g * NCMP:(g + 1) * NCMP], w2[:, 1, :],
                                 start=True, stop=True)
            last.then_inc(s["made"], 1)

        @block.vector
        def _(dve):
            link = chain(dve, s["steps"])
            dve.wait_ge(s["turned"], 3)
            for k in range(2):
                link(dve.tensor_copy(aT[:, k], m.ps[0:HD, k, :].rearrange("p (g t) -> p g t", g=2)))
            link(dve.tensor_copy(peT, m.ps[0:HD, 2, 0:64].rearrange("p (k l) -> p k l", k=2)))
            for k in range(2):
                for l in range(32):
                    last = dve.tensor_scalar(blk[:, k, l].rearrange("p (g n) -> p g n", g=2), aT[:, k, :, l:l + 16 * NCMP - 15:16],
                                             peT[:, k, l:l + 1], None, ALU.add)
                last.then_inc(s["blocks_ready"], 1)
            dve.wait_ge(s["made"], 2)
            link(dve.tensor_copy(keys, m.ps[0:HD, 5, 0:2 * NCMP]))
            link(dve.tensor_copy(values, m.ps[0:NCMP, 6, 0:2 * HD]))

        @block.scalar
        def _(act):
            for k in range(2):
                act.wait_ge(s["hidden"], k + 1)
                act.activation(hid[:, k, :], m.ps[0:HD, 3 + k, 0:2 * NCMP], ACT.Silu).then_inc(s["silu_out"], 1)


def even_layer(m, in_stream, out_stream, a, kvm, cos, sin):
    NIN = 4376
    ar = m.arena
    z = ar[:, 0:2 * NIN].rearrange("p (t n) -> p t n", t=TT)
    project(m, in_stream, NIN, lhs_x(m), z)
    rotated(m, z, [(0, 10), (768, 2), (1024, 2), (1816, 16)], cos, sin, HD // 2, m.work[:, 0:1024])
    keys = m.small[0:HD, 128:158]
    values = m.small[0:NCMP, 160:288]
    aT = ar[0:HD, 10672:11696].rearrange("p (k g t) -> p k g t", k=2, g=2)
    blk = ar[0:HD, 8752:10672].rearrange("p (k l n) -> p k l n", k=2, l=32)
    compressed(m, z, a, keys, values, aT, blk)
    gates = z[:, :, 1280:1304]
    gb = m.small[:, 0:24]
    with m.stage("bias_loaded", "added", "gates_ready") as (block, s):
        @block.sync
        def _(sp):
            sp.dma_start(gb, a["l0_nsa_gate_b_2"].partition_broadcast(P)).then_inc(s["bias_loaded"], 16)

        @block.vector
        def _(dve):
            dve.wait_ge(s["bias_loaded"], 16)
            dve.tensor_tensor(gates, gates, bview(gb, 1, TT), ALU.add).then_inc(s["added"], 1)

        @block.scalar
        def _(act):
            act.wait_ge(s["added"], 1)
            act.activation(gates, gates, ACT.Sigmoid).then_inc(s["gates_ready"], 1)

    neg = m.const("neg_causal").rearrange("p (t s) -> p t s", t=TT)
    for g in range(2):
        cmp = dict(
            keys=lambda i: keys[:, g * NCMP:(g + 1) * NCMP],
            values=lambda i: values[:, g * HD:(g + 1) * HD],
            gate=lambda i, branch: z[:, :, bass.ds(i + (1280 + branch * 8 + g * 4), 1)].rearrange("p t o -> p (t o)"))
        attention(m, 4, z, z, lambda i: i * HD + g * 4 * HD, lambda i, b: 768 + b * 256 + g * HD,
                  lambda i, b: 896 + b * 256 + g * HD, HD ** -0.5, neg=neg, cmp=cmp)
    attention(m, 4, z, z, lambda i: i * (2 * HD) + 1816, lambda i, b: i * (2 * HD) + (2328 + b * HD),
              lambda i, b: i * (2 * HD) + (2840 + b * HD), HD ** -0.5, neg=neg)
    memory_attention(m, z, 3864, kvm)
    gated(m, z, [(0, 1304, 512), (1816, 3352, 512), (3864, 4120, 256)], ACT.Silu)
    mixed_out(m, out_stream, z, [c * P for c in range(4)] + [1816 + c * P for c in range(4)] + [3864, 3992], 1.0, 1.0)


def odd_layer(m, in_stream, out_stream, kvm, cos, sin):
    H, QK, V = RET_HEADS, RET_QK, RET_V
    NIN = 6656
    z = m.arena[:, 0:2 * NIN].rearrange("p (t n) -> p t n", t=TT)
    project(m, in_stream, NIN, lhs_x(m), z)
    rotated(m, z, [(0, 4), (1024, 4)], cos, sin, QK // 2, m.work[:, 0:1024])
    memory_attention(m, z, 6144, kvm)
    w = m.work
    qk = w[:, 0:1024].rearrange("p (k t n) -> p k t n", k=2, t=TT)
    qkT = w[:, 1024:2048].rearrange("p (k c t) -> p k c t", k=2, c=2)
    W = w[:, 2048:2560].rearrange("p (k t) -> p k t", k=2)
    dec = m.const("decay").rearrange("p (h n) -> p h n", h=H)
    decay = w[:, 2560:2816].rearrange("p (i t) -> p i t", i=2)
    stats, mv, rstd = m.small[:, 80:92], m.small[:, 92:96], m.small[:, 96:98]
    ident = m.const("ident")
    v0 = 2 * H * QK
    with m.nc.Fori(0, H) as h:
        with m.stage("staged", "turned", "q_moved", "k_moved", "scores", "weights_ready", "out_ready", "steps",
                     "eps_added", "std_ready") as (block, s):
            @block.vector
            def _(dve):
                link = chain(dve, s["steps"])
                dve.tensor_copy(qk[:, 0], z[:, :, bass.ds(h * QK, QK)]).then_inc(s["staged"], 1)
                dve.tensor_scalar(qk[:, 1], z[:, :, bass.ds(h * QK + H * QK, QK)], QK ** -0.5, None, ALU.mult).then_inc(s["staged"], 1)
                link(dve.tensor_copy(decay.rearrange("p i t -> p (i t)"), dec[:, bass.ds(h, 1), :].rearrange("p o n -> p (o n)")))
                dve.wait_ge(s["turned"], 1)
                dve.tensor_copy(qkT[:, 0].rearrange("p c t -> p (c t)"), m.ps[:, 0, :]).then_inc(s["q_moved"], 1)
                dve.wait_ge(s["scores"], 1)
                sc = m.ps[:, 2, :].rearrange("p (k t) -> p k t", k=2)
                for k in range(2):
                    link(dve.tensor_tensor(W[:, k, k * P:(k + 1) * P], sc[:, k, k * P:(k + 1) * P], decay[:, 0, :], ALU.mult))
                dve.tensor_tensor(W[:, 0, P:T], sc[:, 0, P:T], decay[:, 1, :], ALU.mult).then_inc(s["weights_ready"], 1)
                dve.wait_ge(s["out_ready"], 2)
                added = [s["eps_added"], 0]
                for t in range(TT):
                    head_normed(dve, link, added, s["std_ready"], m.ps[:, 4 + t, :], z[:, t, bass.ds(h * V + v0, V)],
                                stats[:, 6 * t:6 * t + 6], mv[:, 2 * t:2 * t + 2], rstd[:, t:t + 1], 1e-6)

            @block.tensor
            def _(pe):
                pe.wait_ge(s["staged"], 2)
                for k in range(2):
                    for c in range(2):
                        for t in range(TT):
                            last = pe.transpose(m.ps[:, k, c * T + t * P:c * T + (t + 1) * P], qk[:, k, t, c * P:(c + 1) * P], ident)
                    last.then_inc(s["turned"], 1)
                pe.wait_ge(s["q_moved"], 1)
                pe.wait_ge(s["k_moved"], 1)
                for k in range(2):
                    for c in range(2):
                        last = pe.matmul(m.ps[:, 2, k * T:(k + 1) * T], qkT[:, 1, c, k * P:(k + 1) * P], qkT[:, 0, c, :],
                                         start=(c == 0), stop=(c == 1))
                last.then_inc(s["scores"], 1)
                pe.wait_ge(s["weights_ready"], 1)
                v = z[:, :, bass.ds(h * V + v0, V)]
                for t in range(TT):
                    for k in range(t + 1):
                        last = pe.matmul(m.ps[:, 4 + t, :], W[:, k, t * P:(t + 1) * P], v[:, k, :], start=(k == 0), stop=(k == t))
                    last.then_inc(s["out_ready"], 1)

            @block.scalar
            def _(act):
                act.wait_ge(s["turned"], 2)
                act.copy(qkT[:, 1].rearrange("p c t -> p (c t)"), m.ps[:, 1, :]).then_inc(s["k_moved"], 1)
                for t in range(TT):
                    act.wait_ge(s["eps_added"], t + 1)
                    act.activation(rstd[:, t:t + 1], rstd[:, t:t + 1], ACT.Sqrt).then_inc(s["std_ready"], 1)
        with m.stage() as (block, s):
            pass
    gated(m, z, [(v0, 4096, 2048), (6144, 6400, 256)], ACT.Silu)
    mixed_out(m, out_stream, z, [v0 + c * P for c in range(16)] + [6144, 6272], 1.0, 1.0)


def second_block(m, q, a):
    kvm0 = m.arena[:, 12288:13312].rearrange("p (t n) -> p t n", t=TT)
    kvm1 = m.work[:, 5376:6400].rearrange("p (t n) -> p t n", t=TT)
    acos, asin = (m.arena[:, 12160 + 64 * i:12224 + 64 * i].rearrange("p (t n) -> p t n", t=TT) for i in range(2))
    rcos, rsin = (m.keep[:, 256 * i:256 * i + 256].rearrange("p (t n) -> p t n", t=TT) for i in range(2))
    rotary_tables(m, a["positions_2"], [(acos, asin, m.const("attn_inv"), HD // 2), (rcos, rsin, m.const("ret_inv"), P)])
    mem = m.arena[:, 0:2 * D].rearrange("p (t n) -> p t n", t=TT)
    with m.stage("memory_loaded") as (block, s):
        @block.sync
        def _(sp):
            sp.dma_start(mem, a["mem_2"][0].rearrange("(t p) n -> p t n", p=P)).then_inc(s["memory_loaded"], 16)
            sp.wait_ge(s["memory_loaded"], 16)
    rms_turned(m, mem, a["mem_norm_g_2"])
    project(m, next(q), 2 * 4 * HD, lhs_x(m), kvm0)
    project(m, next(q), 2 * 4 * HD, lhs_x(m), kvm1)
    rms_turned(m, m.x, a["l0_norm_g_2"])
    even_layer(m, next(q), next(q), a, kvm0, acos, asin)
    rms_turned(m, m.x, a["l1_norm_g_2"])
    odd_layer(m, next(q), next(q), kvm1, rcos, rsin)
    rms_normed(m, a["final_norm_g_2"])



def ffn(m, gu_stream, down_stream, norm):
    rms_turned(m, m.x, norm)
    hT = m.arena[:, 0:FFC * T].rearrange("p (c t) -> p c t", c=FFC)
    sg = m.work[:, 0:3 * BANK].rearrange("p (j n) -> p j n", j=3)
    with m.stage("gate_freed", "up_freed") as (block, s):
        @block.sync
        def _(sp):
            gu_stream.load_rest(sp)
            gu_stream.next().prefetch(sp)

        @block.tensor
        def _(pe):
            def unit(g, j):
                gu_stream.wait_loaded(pe, g, j)
                pe.wait_ge(s["gate_freed"], g * 3 + j + 1)
                pe.wait_ge(s["up_freed"], g * 3 + j + 1)
                w = gu_stream.slot(j).rearrange("p (w c n) -> p w c n", w=2, c=DC)
                for k in range(2):
                    for f in range(2):
                        for c in range(DC):
                            last = pe.matmul(m.ps[:, 2 * j + k, f * T:(f + 1) * T], w[:, k, c, f * P:(f + 1) * P],
                                             m.xT[:, c, :], start=(c == 0), stop=(c == DC - 1))
                last.then_inc(m.unit_used, 1)

            gu_stream.each(pe, unit)

        @block.scalar
        def _(act):
            act.sem_inc(s["gate_freed"], 3)

            def unit(g, j):
                gu_stream.wait_used(act, g, j)
                act.wait_ge(s["up_freed"], g * 3 + j + 1)
                act.activation(sg[:, j, :], m.ps[:, 2 * j, :], ACT.Silu).then_inc(s["gate_freed"], 1)

            gu_stream.each(act, unit)

        @block.vector
        def _(dve):
            dve.sem_inc(s["up_freed"], 3)

            def unit(g, j):
                gu_stream.wait_used(dve, g, j)
                dve.wait_ge(s["gate_freed"], g * 3 + j + 4)
                dve.tensor_tensor(hT[:, bass.ds((g * 3 + j) * 2, 2), :], sg[:, j, :].rearrange("p (f t) -> p f t", f=2),
                                  m.ps[:, 2 * j + 1, :].rearrange("p (f t) -> p f t", f=2), ALU.mult).then_inc(s["up_freed"], 1)

            gu_stream.each(dve, unit)
    project_out(m, down_stream, FFC, lambda c, t: hT[:, c, t * P:(t + 1) * P], 1.0, 0.5)


def pool_conv(m, in_stream, out_stream, a):
    NIN = 3 * BANK
    C = 4
    ar, w = m.arena, m.work
    z = ar[:, 0:2 * NIN].rearrange("p (t n) -> p t n", t=TT)
    project(m, in_stream, NIN, lhs_x(m), z)
    uT = ar[:, 3072:6144].rearrange("p (c t) -> p c t", c=12)
    transposed(m, 12, lambda c, t: z[:, t, c * P:(c + 1) * P], lambda c: uT[:, c, :])
    yT = ar[:, 6144:8192].rearrange("p (c t) -> p c t", c=DC)
    dm = ar[:, 8192:9216].rearrange("p (c t) -> p c t", c=C)
    pw = ar[:, 9216:9728].rearrange("p (c d) -> p c d", c=C)
    PAD = CONV_K - 1
    zp = ar[:, 9728:9728 + C * (T + PAD)].rearrange("p (c t) -> p c t", c=C)
    acc = ar[:, 10880:11904].rearrange("p (c t) -> p c t", c=C)
    tn = ar[:, 0:1024].rearrange("p (t n) -> p t n", t=TT)
    cw_rows = ar[0:CONV_K, 1024:1536]
    cw = m.small[:, 100:100 + C * 32].rearrange("p (c k) -> p c k", c=C)
    scale, cb, lg, lb = (m.small[:, 300 + 4 * i:304 + 4 * i] for i in range(4))
    load_columns(m, scale, a["pool_scale_3"][0])
    load_columns(m, cb, a["conv_b_3"][0])
    load_columns(m, lg, a["conv_ln_g_3"][0])
    load_columns(m, lb, a["conv_ln_b_3"][0])
    OFF = 16
    lv = [w[:, k * C * (T + OFF):(k + 1) * C * (T + OFF)].rearrange("p (c t) -> p c t", c=C) for k in range(5)]
    stats, mv, rstd = m.small[:, 80:92], m.small[:, 92:96], m.small[:, 96:98]
    ident = m.const("ident")
    first = m.const("pool_count").rearrange("p (g t) -> p g t", g=C)
    with m.stage("weights_loaded", "cw_turned", "means_ready", "pooled", "sig_out", "conv_done", "acc_turned", "eps_added",
                 "std_ready", "normed", "back_turned", "pool_out", "conv_out", "steps", "taps", "zeroed") as (block, s):
        @block.sync
        def _(sp):
            sp.dma_start(pw, a["pool_w_3"][0].rearrange("g c d -> c g d")).then_inc(s["weights_loaded"], 16)
            sp.dma_start(cw_rows, a["conv_w_3"][0]).then_inc(s["weights_loaded"], 16)

        @block.gpsimd
        def _(pool):
            pool.memset(zp[:, :, 0:PAD], 0.0).then_inc(s["zeroed"], 1)
            for k in range(5):
                pool.memset(lv[k][:, :, 0:OFF], 0.0).then_inc(s["zeroed"], 1)

        @block.vector
        def _(dve):
            link = chain(dve, s["steps"])
            dve.wait_ge(s["zeroed"], 6)
            dve.wait_ge(s["cw_turned"], 1)
            link(dve.tensor_copy(cw[:, :, 0:CONV_K], m.ps[:, 0, 0:C * 32].rearrange("p (c k) -> p c k", c=C)[:, :, 0:CONV_K]))
            link(dve.tensor_copy(lv[0][:, :, OFF:], uT[:, 0:C, :]))
            for k in range(4):
                src, dst = lv[k][:, k if k else 0:, :], lv[k + 1][:, k if k else 0:, :]
                sh = 1 << k
                link(dve.tensor_tensor(dst[:, :, OFF:], src[:, :, OFF:], src[:, :, OFF - sh:OFF - sh + T], ALU.add))
            for g in range(C):
                sums = lv[g + 1][:, g, OFF:]
                link(dve.tensor_tensor(dm[:, g, 0:16], sums[:, 0:16], first[:, g, :], ALU.mult))
                link(dve.tensor_scalar(dm[:, g, 16:], sums[:, 16:], 1.0 / (2 << g), None, ALU.mult))
            dve.tensor_tensor(dm, dm, uT[:, 0:C, :], ALU.subtract).then_inc(s["means_ready"], 1)
            dve.wait_ge(s["sig_out"], 1)
            link(dve.tensor_tensor(zp[:, :, PAD:], uT[:, C:2 * C, :], uT[:, 2 * C:3 * C, :], ALU.mult))
            for k in range(CONV_K):
                for c in range(C):
                    if k == 0:
                        dve.tensor_scalar(acc[:, c, :], zp[:, c, 0:T], cw[:, c, 0:1], cb[:, c:c + 1], ALU.mult,
                                          ALU.add).then_inc(s["taps"], 1)
                    else:
                        dve.wait_ge(s["taps"], (k - 1) * C + c + 1)
                        dve.scalar_tensor_tensor(acc[:, c, :], zp[:, c, k:k + T], cw[:, c, k:k + 1], acc[:, c, :],
                                                 ALU.mult, ALU.add).then_inc(s["taps"], 1)
            added = [s["eps_added"], 0]
            dve.wait_ge(s["acc_turned"], 1)
            for t in range(TT):
                head_normed(dve, link, added, s["std_ready"], m.ps[:, 4 + t, :], tn[:, t, :], stats[:, 6 * t:6 * t + 6],
                            mv[:, 2 * t:2 * t + 2], rstd[:, t:t + 1], 1e-6)
            dve.sem_inc(s["normed"], 1)
            dve.wait_ge(s["pooled"], 1)
            for g in range(C):
                dve.tensor_scalar(yT[:, g, :], m.ps[:, g // 2, (g % 2) * T:(g % 2 + 1) * T], scale[:, g:g + 1], None,
                                  ALU.mult).then_inc(s["pool_out"], 1)

        @block.tensor
        def _(pe):
            pe.wait_ge(s["weights_loaded"], 32)
            for c in range(C):
                last = pe.transpose(m.ps[:, 0, c * 32:c * 32 + CONV_K], cw_rows[:, c * P:(c + 1) * P], ident[0:CONV_K, 0:CONV_K])
            last.then_inc(s["cw_turned"], 1)
            pe.wait_ge(s["means_ready"], 1)
            for g in range(C):
                last = pe.matmul(m.ps[:, g // 2, (g % 2) * T:(g % 2 + 1) * T], pw[:, g, :], dm[:, g, :], start=True, stop=True)
            last.then_inc(s["pooled"], 1)
            pe.wait_ge(s["taps"], CONV_K * C)
            for t in range(TT):
                for c in range(C):
                    last = pe.transpose(m.ps[:, 4 + t, c * P:(c + 1) * P], acc[:, c, t * P:(t + 1) * P], ident)
            last.then_inc(s["acc_turned"], 1)
            pe.wait_ge(s["normed"], 1)
            for c in range(C):
                for t in range(TT):
                    last = pe.transpose(m.ps[:, 6 + c // 2, (c % 2) * T + t * P:(c % 2) * T + (t + 1) * P],
                                        tn[:, t, c * P:(c + 1) * P], ident)
            last.then_inc(s["back_turned"], 1)

        @block.scalar
        def _(act):
            act.activation(uT[:, 2 * C:3 * C, :], uT[:, 2 * C:3 * C, :], ACT.Sigmoid).then_inc(s["sig_out"], 1)
            for t in range(TT):
                act.wait_ge(s["eps_added"], t + 1)
                act.activation(rstd[:, t:t + 1], rstd[:, t:t + 1], ACT.Sqrt).then_inc(s["std_ready"], 1)
            act.wait_ge(s["back_turned"], 1)
            for c in range(C):
                act.activation(yT[:, C + c, :], m.ps[:, 6 + c // 2, (c % 2) * T:(c % 2 + 1) * T], ACT.Silu,
                               bias=lb[:, c:c + 1], scale=lg[:, c:c + 1]).then_inc(s["conv_out"], 1)
    project_out(m, out_stream, DC, lambda c, t: yT[:, c, t * P:(t + 1) * P], 1.0, 1.0)


HEADS = 16
IDX_HEADS, IDX_DIM = 8, 64


def expand_bias(m, a, rows, tiles):
    rb = m.small[0:32, 0:HEADS]
    line = m.work[0:HEADS, 0:2 * T]
    with m.stage("loaded", "spread", "ready", "stored", "zeroed") as (block, s):
        @block.sync
        def _(sp):
            sp.dma_start(rb, a["rel_bias_3"]).then_inc(s["loaded"], 16)
            sp.wait_ge(s["ready"], 1)
            sp.dma_start(rows, line).then_inc(s["stored"], 16)
            sp.wait_ge(s["stored"], 16)
            for t in range(TT):
                src = bass.AP(rows.tensor, T - 1 - t * P, [[2 * T, HEADS], [-1, P], [1, T]])
                sp.dma_start(tiles[:, t], src).then_inc(m.bias_stored, 16)

        @block.tensor
        def _(pe):
            pe.wait_ge(s["loaded"], 16)
            pe.matmul(m.ps[0:HEADS, 0, 0:T], rb, m.const("dist_bucket")[0:32, :], start=True, stop=True).then_inc(s["spread"], 1)

        @block.vector
        def _(dve):
            dve.memset(line[:, T:], 0.0).then_inc(s["zeroed"], 1)
            dve.wait_ge(s["spread"], 1)
            dve.wait_ge(s["zeroed"], 1)
            dve.tensor_copy(line[:, 0:T], m.ps[0:HEADS, 0, 0:T]).then_inc(s["ready"], 1)


def selected_attention(m, in_stream, out_stream, tiles):
    NIN = 3 * D + IDX_HEADS * IDX_DIM + IDX_DIM + IDX_HEADS
    ar, w = m.arena, m.work
    z = ar[:, 0:2 * NIN].rearrange("p (t n) -> p t n", t=TT)
    project(m, in_stream, NIN, lhs_x(m), z)
    qi0, ki0, wi0 = 3 * D, 3 * D + IDX_HEADS * IDX_DIM, 3 * D + IDX_HEADS * IDX_DIM + IDX_DIM
    score = ar[:, 7312:7824].rearrange("p (t s) -> p t s", t=TT)
    neg = ar[:, 7824:8336].rearrange("p (t s) -> p t s", t=TT)
    kiT = ar[0:IDX_DIM, 8336:8592]
    causal = m.const("neg_causal").rearrange("p (t s) -> p t s", t=TT)
    ident = m.const("ident")
    with m.stage("turned", "steps") as (block, s):
        @block.tensor
        def _(pe):
            for t in range(TT):
                last = pe.transpose(m.ps[0:IDX_DIM, 0, t * P:(t + 1) * P], z[:, t, ki0:ki0 + IDX_DIM], ident)
            last.then_inc(s["turned"], 1)

        @block.vector
        def _(dve):
            dve.memset(score, 0.0).then_inc(s["steps"], 1)
            dve.wait_ge(s["turned"], 1)
            dve.tensor_copy(kiT, m.ps[0:IDX_DIM, 0, 0:T]).then_inc(s["steps"], 1)

    qs = w[:, 0:256].rearrange("p (t n) -> p t n", t=TT)
    qT = w[0:IDX_DIM, 256:768].rearrange("p (b t) -> p b t", b=2)
    R = w[:, 768:1792].rearrange("p (b t s) -> p b t s", b=2, t=TT)
    wi = m.small[:, 0:4].rearrange("p (t b) -> p t b", t=TT)
    with m.nc.Fori(0, IDX_HEADS // 2) as i:
        with m.stage("staged", "turned", "moved", "scores", "relu_out", "steps") as (block, s):
            @block.vector
            def _(dve):
                link = chain(dve, s["steps"])
                dve.tensor_copy(qs, z[:, :, bass.ds(i * (2 * IDX_DIM) + qi0, 2 * IDX_DIM)]).then_inc(s["staged"], 1)
                link(dve.tensor_copy(wi, z[:, :, bass.ds(i * 2 + wi0, 2)]))
                dve.wait_ge(s["turned"], 1)
                dve.tensor_copy(qT, m.ps[0:IDX_DIM, 0, :].rearrange("p (b t) -> p b t", b=2)).then_inc(s["moved"], 1)
                for b in range(2):
                    dve.wait_ge(s["relu_out"], b + 1)
                    for t in range(TT):
                        link(dve.scalar_tensor_tensor(score[:, t, :], R[:, b, t, :], wi[:, t, b:b + 1], score[:, t, :],
                                                      ALU.mult, ALU.add))

            @block.tensor
            def _(pe):
                pe.wait_ge(s["staged"], 1)
                for b in range(2):
                    for t in range(TT):
                        last = pe.transpose(m.ps[0:IDX_DIM, 0, b * T + t * P:b * T + (t + 1) * P],
                                            qs[:, t, b * IDX_DIM:(b + 1) * IDX_DIM], ident)
                last.then_inc(s["turned"], 1)
                pe.wait_ge(s["moved"], 1)
                for b in range(2):
                    for t in range(TT):
                        last = pe.matmul(m.ps[:, 1 + b, t * T:(t + 1) * T], qT[:, b, t * P:(t + 1) * P], kiT, start=True, stop=True)
                    last.then_inc(s["scores"], 1)

            @block.scalar
            def _(act):
                for b in range(2):
                    act.wait_ge(s["scores"], b + 1)
                    act.activation(R[:, b].rearrange("p t s -> p (t s)"), m.ps[:, 1 + b, :], ACT.Relu).then_inc(s["relu_out"], 1)
        with m.stage() as (block, s):
            pass

    top = m.small[:, 8:24].rearrange("p (t k) -> p t k", t=TT)
    STRUCK = -3e38
    with m.stage("steps") as (block, s):
        @block.vector
        def _(dve):
            link = chain(dve, s["steps"])
            link(dve.tensor_scalar(score, score, (IDX_HEADS * IDX_DIM) ** -0.5, None, ALU.mult))
            link(dve.tensor_tensor(score, score, causal, ALU.add))
            for _ in range(TOPK // 8):
                for t in range(TT):
                    link(dve.max(top[:, t, :], score[:, t, :]))
                    link(dve.match_replace(score[:, t, :], top[:, t, :], score[:, t, :], STRUCK))
            link(dve.tensor_scalar(neg, score, STRUCK / 2, NEG, ALU.is_gt, ALU.mult))
            link(dve.tensor_tensor(neg, neg, causal, ALU.add))

        @block.sync
        def _(sp):
            sp.wait_ge(m.bias_stored, 32)
    attention(m, HEADS // 2, z, z, lambda i: i * (2 * HD), lambda i, b: i * (2 * HD) + (D + b * HD),
              lambda i, b: i * (2 * HD) + (2 * D + b * HD), HD ** -0.5, neg=neg,
              bias=lambda i, b, t: tiles[bass.ds(i * 2 + b, 1), t].rearrange("o p s -> (o p) s"))
    mixed_out(m, out_stream, z, [c * P for c in range(DC)], 1.0, 1.0)


def third_block(m, q, a, rows, tiles):
    expand_bias(m, a, rows, tiles)
    for layer in range(DEPTH):
        ffn(m, next(q), next(q), a["ffn1_norm_3"][layer])
        rms_turned(m, m.x, a["mix_norm_3"][layer])
        if layer == 0:
            pool_conv(m, next(q), next(q), a)
        else:
            selected_attention(m, next(q), next(q), tiles)
        ffn(m, next(q), next(q), a["ffn2_norm_3"][layer])
    rms_normed(m, a["final_norm_3"])


USED = ["x", "mlstm_w_in", "mlstm_gate_b", "mlstm_norm_g", "mlstm_w_out", "gla_w_in", "gla_gate_w", "gla_gate_b",
        "gla_norm_g", "gla_w_out", "moe_router", "moe_w_gate", "moe_w_up", "moe_w_down", "ln_g", "ln_b",
        "mem_2", "positions_2", "l0_norm_g_2", "l0_w_in_2", "l0_nsa_gate_b_2", "l0_cmp_pe_k_2", "l0_cmp_w1_k_2",
        "l0_cmp_w2_k_2", "l0_cmp_pe_v_2", "l0_cmp_w1_v_2", "l0_cmp_w2_v_2", "l0_w_mem_kv_2", "l0_w_out_2", "l1_norm_g_2",
        "l1_w_in_2", "l1_w_mem_kv_2", "l1_w_out_2", "mem_norm_g_2", "final_norm_g_2",
        "ffn1_norm_3", "ffn1_w_gate_3", "ffn1_w_up_3", "ffn1_w_down_3", "mix_norm_3", "ffn2_norm_3", "ffn2_w_gate_3",
        "ffn2_w_up_3", "ffn2_w_down_3", "ab_w_in_3", "pool_w_3", "pool_scale_3", "conv_w_3", "conv_b_3", "conv_ln_g_3",
        "conv_ln_b_3", "ab_w_out_3", "c_w_in_3", "c_w_out_3", "rel_bias_3", "final_norm_3"]


def streams(m, a):
    columns_stream(m, a["mlstm_w_in"][0], 3088, 0)
    rows_stream(m, a["mlstm_w_out"][0], D, 3)
    expert_stream(m, a["moe_w_gate"][0], a["moe_w_up"][0], a["moe_w_down"][0], 0)
    columns_stream(m, a["gla_w_in"][0], 3104, 0)
    rows_stream(m, a["gla_w_out"][0], D, 3)
    expert_stream(m, a["moe_w_gate"][1], a["moe_w_up"][1], a["moe_w_down"][1], 0)
    columns_stream(m, a["l0_w_mem_kv_2"], 512, 0)
    columns_stream(m, a["l1_w_mem_kv_2"], 512, 3)
    columns_stream(m, a["l0_w_in_2"], 4376, 0)
    rows_stream(m, a["l0_w_out_2"], 1280, 3)
    columns_stream(m, a["l1_w_in_2"], 6656, 0)
    rows_stream(m, a["l1_w_out_2"], 2304, 3)
    for layer, (w_in, n, w_out) in enumerate((("ab_w_in_3", 1536, "ab_w_out_3"), ("c_w_in_3", 3656, "c_w_out_3"))):
        ffn_stream(m, a["ffn1_w_gate_3"][layer], a["ffn1_w_up_3"][layer], 0)
        rows_stream(m, a["ffn1_w_down_3"][layer], D_FF, 3)
        columns_stream(m, a[w_in][0], n, 0)
        rows_stream(m, a[w_out][0], D, 3)
        ffn_stream(m, a["ffn2_w_gate_3"][layer], a["ffn2_w_up_3"][layer], 0)
        rows_stream(m, a["ffn2_w_down_3"][layer], D_FF, 3)


def layers(m, a, rows, tiles):
    q = iter(m.queue)
    turn_x(m)
    mlstm(m, next(q), next(q), a["mlstm_gate_b"][0], a["mlstm_norm_g"][0])
    layer_normed(m, a["ln_g"][0, 0], a["ln_b"][0, 0])
    turn_x(m)
    moe(m, next(q), a["moe_router"][0])
    layer_normed(m, a["ln_g"][0, 1], a["ln_b"][0, 1])
    turn_x(m)
    gla(m, next(q), next(q), a["gla_gate_w"][0], a["gla_gate_b"][0], a["gla_norm_g"][0])
    layer_normed(m, a["ln_g"][1, 0], a["ln_b"][1, 0])
    turn_x(m)
    moe(m, next(q), a["moe_router"][1])
    layer_normed(m, a["ln_g"][1, 1], a["ln_b"][1, 1])
    second_block(m, q, a)
    third_block(m, q, a, rows, tiles)


def program(nc, a, consts, out, rows, tiles):
    with ExitStack() as ctx:
        m = Machine(nc, ctx, consts)
        streams(m, a)
        with m.stage("inputs_loaded") as (block, s):
            @block.sync
            def _(sp):
                sp.dma_start(m.x[:, :, :], a["x"][0].rearrange("(t p) n -> p t n", p=P)).then_inc(s["inputs_loaded"], 16)
                sp.dma_start(m.cst[:, :], consts).then_inc(s["inputs_loaded"], 16)
                m.queue[0].prefetch(sp)
                sp.wait_ge(s["inputs_loaded"], 32)
        layers(m, a, rows, tiles)
        with m.stage("stored") as (block, s):
            @block.sync
            def _(sp):
                sp.dma_start(out[0].rearrange("(t p) n -> p t n", p=P), m.x[:, :, :]).then_inc(s["stored"], 16)
                sp.wait_ge(s["stored"], 16)



def kernel(**inputs):
    import numpy as _np
    import concourse.bacc as _bacc
    from concourse import mybir as _mybir
    from concourse.bass_utils import run_bass_kernel_spmd as _run

    nc = _bacc.Bacc("TRN2", target_bir_lowering=False, num_devices=1)
    arrays, aps = {}, {}
    for name in USED:
        a = _np.ascontiguousarray(inputs[name])
        arrays[f"in_{name}"] = a
        aps[name] = nc.dram_tensor(f"in_{name}", a.shape, _mybir.dt.from_np(a.dtype), kind="ExternalInput").ap()
    table = const_table()
    arrays["constants_dram"] = table
    consts = nc.dram_tensor("constants_dram", table.shape, F32, kind="ExternalInput").ap()
    out = nc.dram_tensor("out_dram", (1, T, D), F32, kind="ExternalOutput").ap()
    rows = nc.dram_tensor("bias_rows", (HEADS, 2 * T), F32, kind="Internal").ap()
    tiles = nc.dram_tensor("bias_tiles", (HEADS, TT, P, T), F32, kind="Internal").ap()
    program(nc, aps, consts, out, rows, tiles)
    r = _run(nc, [arrays], core_ids=[0])
    return r.results[0]["out_dram"]
```

```python
import math
from contextlib import ExitStack, contextmanager

import numpy as np
import concourse.bass as bass
from concourse import mybir

F32 = mybir.dt.float32
F32R = mybir.dt.float32r
I32 = mybir.dt.int32
ALU = mybir.AluOpType
ACT = mybir.ActivationFunctionType
AX = mybir.AxisListType.X

P = 128
T = 256
TT = T // P
D = 1024
DC = D // P
BANK = 512
SLOTS = 6
SLOT = 4096
NEG = -1e30
DEPTH = 2
ALPHA = (2 * DEPTH) ** 0.25
SET = 30

ML_HEADS, ML_DK, ML_DV = 4, 128, 256
GLA_RANK, GLA_TAU = 16, 16.0
E, CAP, FF = 16, 2 * T // 16, 1024
QUADS = E * CAP // P
EQ = P // CAP
HD = 64
NCMP = (T - 32) // 16 + 1
RET_HEADS, RET_QK, RET_V = 4, 256, 512
D_FF = 2816
FFC = D_FF // P
CONV_K = 31
TOPK = T // 4

ARENA = 6656 * TT
WORK = 6144


def const_layout():
    at, cols = {}, 0
    for name, n in (("ident", P), ("ones", P), ("keep_fwd", P), ("keep_bwd", P), ("neg_fwd", 2 * T), ("neg_bwd", 2 * T),
                    ("neg_causal", 2 * T), ("neg_cmp", 2 * NCMP), ("row_cmp", 2), ("ret_inv", P), ("attn_inv", 32),
                    ("slot_no", CAP), ("pool_count", 4 * 16),
                    ("decay", RET_HEADS * 2 * P), ("dist_bucket", T)):
        at[name] = (cols, n)
        cols += n
    return at, cols


def const_table():
    at, cols = const_layout()
    out = np.zeros((P, cols), np.float32)

    def put(name, value):
        value = np.asarray(value, np.float32)
        a, n = at[name]
        out[:value.shape[0], a:a + n] = value.reshape(value.shape[0], n)

    p = np.arange(P)
    t = np.arange(T)
    put("ident", np.eye(P))
    put("ones", np.ones((P, P)))
    put("keep_fwd", p[:, None] <= p[None, :])
    put("keep_bwd", p[:, None] >= p[None, :])
    s = p[:, None, None] + P * np.arange(TT)[None, :, None]
    put("neg_fwd", np.where(s <= t, 0.0, NEG))
    put("neg_bwd", np.where(s >= t, 0.0, NEG))
    put("neg_causal", np.where(t[None, None, :] <= s, 0.0, NEG))
    end = np.arange(NCMP) * 16 + 31
    put("neg_cmp", np.where(end[None, None, :] <= s, 0.0, NEG))
    put("row_cmp", s[:, :, 0] >= end[0])
    f = np.float32
    put("ret_inv", np.tile(f(1.0) / (f(10000.0) ** np.linspace(0.0, 1.0, P).astype(f)), (P, 1)))
    put("attn_inv", np.tile(f(1.0) / (f(10000.0) ** (np.arange(0, HD, 2, dtype=f) / f(HD))), (P, 1)))
    lg = np.log(1.0 - 2.0 ** (-5.0 - np.arange(RET_HEADS)))
    diff = p[None, :] - p[:, None]
    put("decay", np.stack([np.stack([np.where(diff >= 0, np.exp(np.maximum(diff, 0) * g), 0.0),
                                     np.exp((diff + P) * g)]) for g in lg]).transpose(2, 0, 1, 3))
    put("slot_no", np.tile(np.arange(CAP) + 1.0, (P, 1)))
    tt = np.arange(16)
    put("pool_count", np.tile(np.stack([1.0 / np.minimum(tt + 1, w) for w in (2, 4, 8, 16)]).reshape(1, -1), (P, 1)))
    dist = T - 1 - t
    d = np.maximum(dist, 16).astype(f)
    large = 16 + (np.log(d / f(16)) / f(math.log(128 / 16)) * f(16)).astype(np.int32)
    bucket = np.where(dist < 16, dist, np.minimum(large, 31))
    put("dist_bucket", np.arange(32)[:, None] == bucket[None, :])
    return out


class Machine:

    def __init__(self, nc, ctx, consts):
        self.nc = nc
        self.ctx = ctx
        self.consts = consts
        self.layout, cols = const_layout()
        cols = self.layout["decay"][0]
        plan = [("weight_ring", SLOTS * SLOT), ("arena", ARENA), ("work", WORK), ("xT", 2 * DC * T), ("x", TT * D),
                ("constants", cols), ("small", 640), ("small_integers", 2)]
        total = sum(-(-n // 8) * 8 for _, n in plan)
        self.slab = ctx.enter_context(nc.sbuf_tensor("slab", [P, total], F32))
        at, self.at = nc.sbuf_base - 4 * total, {}
        for name, n in plan:
            self.at[name] = at
            at += 4 * (-(-n // 8) * 8)
        self.ring = self.place("weight_ring", [P, SLOTS, SLOT])
        self.halves = self.place("weight_halves", [P, 2, 2, SLOT // 2], F32R, self.at["weight_ring"] + 4 * 4 * SLOT)
        self.arena = self.place("arena", [P, ARENA])
        self.arena_r = self.place("arena_halves", [P, ARENA], F32R, self.at["arena"])
        self.work = self.place("work", [P, WORK])
        self.work_r = self.place("work_halves", [P, WORK], F32R, self.at["work"])
        self.xT = self.place("xT", [P, DC, T])
        self.xT_r = self.place("xT_halves", [P, 2, DC, T], F32R, self.at["xT"])
        self.x = self.place("x", [P, TT, D])
        self.cst = self.place("constants", [P, cols])
        self.small = self.place("small", [P, 640])
        self.small_i = self.place("small_integers", [P, 2], I32)
        self.keep = self.work[:, 4608:5120]
        self.ps = ctx.enter_context(nc.psum_tensor("accumulators", [P, 8, BANK], F32))
        self.sets = [[ctx.enter_context(nc.semaphore(f"set{k}_{i}")) for i in range(SET)] for k in range(2)]
        self.turn = 0
        self.stages = 0
        self.slot_loaded = [ctx.enter_context(nc.semaphore(f"slot{i}_loaded")) for i in range(SLOTS)]
        self.unit_used = ctx.enter_context(nc.semaphore("unit_used"))
        self.loads = [0] * SLOTS
        self.last_unit = [0] * SLOTS
        self.units = 0
        self.queue = []
        self.bias_stored = ctx.enter_context(nc.semaphore("bias_stored"))
        self.norm_rows = self.work[:, 4096:6144].rearrange("p (k n) -> p k n", k=2)
        self.norm_loaded = ctx.enter_context(nc.semaphore("norm_loaded"))
        self.norms = 0
        self.router = self.small[:, 228:228 + DC * E].rearrange("p (c e) -> p c e", c=DC)
        self.router_loaded = ctx.enter_context(nc.semaphore("router_loaded"))
        self.routers = 0
        self.columns_loaded = ctx.enter_context(nc.semaphore("columns_loaded"))
        self.columns, self.column_end = {}, 480

    def place(self, name, shape, dt=F32, offset=None):
        return self.nc.alloc_sbuf_tensor_at(name, shape, dt, offset=self.at[name] if offset is None else offset)

    def const(self, name, shape=None, rows=P):
        a, n = self.layout[name]
        v = self.cst[0:rows, a:a + n]
        return v

    def load_columns(self, eng, name, vec):
        n = vec.shape[0] // P
        a = self.column_end
        self.column_end += n
        assert self.column_end <= 640
        self.columns[name] = self.small[:, a:a + n]
        with self.nc.allow_non_contiguous_dma("one value a partition"):
            eng.dma_start(self.columns[name], vec.rearrange("(c p) -> p c", p=P)).then_inc(self.columns_loaded, 16)

    def load_norm(self, sp, norm):
        if norm is not None:
            for k in range(2):
                sp.dma_start(self.norm_rows[:, k, :], norm[k].partition_broadcast(P)).then_inc(self.norm_loaded, 16)
            self.norms += 1
            if len(norm) > 2:
                sp.dma_start(self.router, norm[2].rearrange("(c p) e -> p c e", p=P)).then_inc(self.router_loaded, 16)
                self.routers += 1

    @contextmanager
    def stage(self, title, *names):
        mine, other = self.sets[self.turn], self.sets[1 - self.turn]
        self.turn = 1 - self.turn
        assert len(names) <= SET
        self.stages += 1
        with self.nc.Block(f"{title}_s{self.stages}", no_gpsimd_drain=True) as block:
            @block.gpsimd
            def _(pool):
                pool.sem_clear(range(other[0].num, other[-1].num + 1))

            yield block, {n: mine[i] for i, n in enumerate(names)}


class Stream:

    def __init__(self, m, units, full, depth, first, group, parts, split=False):
        self.m, self.n, self.depth, self.group, self.parts = m, units, depth, group, parts
        self.groups = full // group if full // group >= 2 else 0
        self.base = m.units
        m.units += units
        self.slots = [(first + r) % SLOTS for r in range(depth)]
        self.load_base = [m.loads[s] for s in self.slots]
        self.free_at = [m.last_unit[s] for s in self.slots]
        self.inc = 16 * len(parts(0, 0, m.ring[:, 0, :]))
        for u in range(units):
            s = self.slots[u % depth]
            m.loads[s] += self.inc
            m.last_unit[s] = self.base + u + 1
        if split:
            m.last_unit[4] = m.last_unit[5] = self.base + units
        m.queue.append(self)

    def slot(self, j):
        return self.m.ring[:, self.slots[j % self.depth], :]

    def load(self, sp, g, j):
        for dst, src in self.parts(g, j, self.slot(j)):
            sp.dma_start(dst, src).then_inc(self.m.slot_loaded[self.slots[j % self.depth]], 16)

    def prefetch(self, sp):
        for j in range(min(self.depth, self.n)):
            if self.free_at[j] > 0:
                sp.wait_ge(self.m.unit_used, self.free_at[j])
            self.load(sp, 0, j)

    def load_rest(self, sp):
        def one(g, j):
            sp.wait_ge(self.m.unit_used, self.base + 1 + g * self.group + (j - self.depth))
            self.load(sp, g, j)

        first = min(self.group, self.n) if self.groups else 0
        for j in range(self.depth, first):
            one(0, j)
        if self.groups:
            with sp.Fori(1, self.groups) as g:
                for j in range(self.group):
                    one(g, j)
        for u in range(max(self.depth, self.groups * self.group), self.n):
            one(u // self.group, u % self.group)

    def each(self, eng, body, peel=False):
        first = 1 if peel and self.groups else 0
        for j in range(self.group * first):
            body(0, j)
        if self.groups:
            with eng.Fori(first, self.groups) as g:
                for j in range(self.group):
                    body(g, j)
        for u in range(self.groups * self.group, self.n):
            body(u // self.group, u % self.group)

    def wait_loaded(self, eng, g, j):
        turn = g * (self.group // self.depth) + (j // self.depth + 1)
        eng.wait_ge(self.m.slot_loaded[self.slots[j % self.depth]], self.load_base[j % self.depth] + self.inc * turn)

    def wait_used(self, eng, g, j):
        eng.wait_ge(self.m.unit_used, self.base + 1 + g * self.group + j)

    def next(self):
        q = self.m.queue
        i = q.index(self)
        return q[i + 1] if i + 1 < len(q) else None


def columns_stream(m, w, n, first):
    wv = w.rearrange("(c p) n -> p c n", p=P)

    def parts(g, j, slot):
        u = g * 2 + j
        width = min(BANK, n - u * BANK) if isinstance(u, int) else BANK
        dst = slot.rearrange("p (c n) -> p c n", c=DC)[:, :, 0:width]
        return [(dst, wv[:, :, bass.ds(u * BANK, width)])]

    return Stream(m, -(-n // BANK), n // BANK, 2, first, 2, parts, True)


def rows_stream(m, w, rows, first, split=True):
    wv = w.rearrange("(c p) n -> p c n", p=P)
    chunks = rows // P

    def parts(g, j, slot):
        a = 4 * (g * 2 + j)
        k = min(4, chunks - a)
        return [(slot[:, 0:k * D].rearrange("p (c n) -> p c n", c=k), wv[:, a:a + k, :])]

    return Stream(m, -(-chunks // 4), 0, 2, first, 2, parts, split)


def expert_stream(m, wg, wu, wd, first):
    ws = [w.rearrange("(q e) (c p) n -> q c p e n", e=EQ, p=P) for w in (wg, wu, wd)]

    def parts(g, j, slot):
        return [(slot.rearrange("p (e n) -> p e n", e=EQ), ws[j // DC][g, j % DC])]

    return Stream(m, QUADS * 3 * DC, QUADS * 3 * DC, SLOTS, first, 3 * DC, parts)


def ffn_stream(m, wg, wu, first):
    gv, uv = (w.rearrange("(c p) n -> p c n", p=P) for w in (wg, wu))

    def parts(g, j, slot):
        s = slot.rearrange("p (w c n) -> p w c n", w=2, c=DC)
        at = bass.ds((g * 2 + j) * T, T)
        return [(s[:, 0], gv[:, :, at]), (s[:, 1], uv[:, :, at])]

    return Stream(m, D_FF // T, D_FF // T, 2, first, 2, parts, True)


PASSES = ((0, 0), (0, 1), (1, 0))


def high_part(m, stream, act, s, g, j, k, words=SLOT // 2):
    if k == 0:
        stream.wait_loaded(act, g, j)
    u = g * stream.group + j
    if not (isinstance(u, int) and u == 0):
        act.wait_ge(s["halves_used"], u * 2 + (k - 1))
    act.copy(m.halves[:, k, 0, 0:words], stream.slot(j)[:, k * (SLOT // 2):k * (SLOT // 2) + words]).then_inc(s["high_ready"], 1)


def low_part(m, stream, dve, s, g, j, k, last=True, words=SLOT // 2):
    u = g * stream.group + j
    dve.wait_ge(s["high_ready"], u * 2 + k + 1)
    ins = dve.tensor_tensor(m.halves[:, k, 1, 0:words], stream.slot(j)[:, k * (SLOT // 2):k * (SLOT // 2) + words],
                            m.halves[:, k, 0, 0:words].bitcast(F32), ALU.subtract)
    ins.then_inc(s["low_ready"], 1)
    if k == 1 or last:
        dve.wait_ge(s["low_ready"], u * 2 + k + 1)
        dve.sem_inc(m.unit_used, 1)


def chain(eng, sem, start=0):
    done = [start]

    def link(ins):
        done[0] += 1
        ins.then_inc(sem, 1)
        eng.wait_ge(sem, done[0])

    return link


def bview(ap, axis, n):
    u = ap.unsqueeze(axis)
    shape = list(u.shape)
    shape[axis] = n
    return u.to_broadcast(shape)



def transposed(m, n, src, dst, gain=None, low=None):
    ident = m.const("ident")
    with m.stage("transposed", "turned", "vector_moved", "scalar_moved") as (block, s):
        def half(c):
            return m.ps[:, (c % 16) // 2, (c % 2) * T:(c % 2) * T + T]

        @block.tensor
        def _(pe):
            for c in range(n):
                if c >= 16 and c % 2 == 0:
                    if low is not None:
                        pe.wait_ge(s["vector_moved"], c - 14)
                    else:
                        pe.wait_ge(s["vector_moved"] if c % 4 == 0 else s["scalar_moved"], ((c - 16) // 4 + 1) * 2)
                for t in range(TT):
                    last = pe.transpose(half(c)[:, t * P:(t + 1) * P], src(c, t), ident)
                last.then_inc(s["turned"], 1)

        @block.vector
        def _(dve):
            for c in range(n):
                if low is not None:
                    dve.wait_ge(s["scalar_moved"], min(c // 2 * 2 + 2, n))
                    high = dst(c).bitcast(F32)
                    if gain is None:
                        dve.tensor_tensor(low(c), half(c), high, ALU.subtract).then_inc(s["vector_moved"], 1)
                    else:
                        dve.scalar_tensor_tensor(low(c), half(c), gain(c), high, ALU.mult, ALU.subtract).then_inc(s["vector_moved"], 1)
                elif c % 4 < 2:
                    dve.wait_ge(s["turned"], min(c // 2 * 2 + 2, n))
                    if gain is None:
                        dve.tensor_copy(dst(c), half(c)).then_inc(s["vector_moved"], 1)
                    else:
                        dve.tensor_scalar(dst(c), half(c), gain(c), None, ALU.mult).then_inc(s["vector_moved"], 1)

        @block.scalar
        def _(act):
            for c in [c for c in range(n) if low is not None or c % 4 >= 2]:
                act.wait_ge(s["turned"], min(c // 2 * 2 + 2, n))
                if gain is None:
                    act.copy(dst(c), half(c)).then_inc(s["scalar_moved"], 1)
                else:
                    act.activation(dst(c), half(c), ACT.Copy, scale=gain(c)).then_inc(s["scalar_moved"], 1)


def project(m, stream, n, lhs, z):
    def width(g, j):
        return min(BANK, n - (g * 2 + j) * BANK) if isinstance(g, int) else BANK

    def back(g, j):
        return (g, j - 1) if j else (g - 1, 1)

    with m.stage("project", "high_ready", "low_ready", "halves_used", "scalar_freed", "vector_freed") as (block, s):
        @block.sync
        def _(sp):
            stream.load_rest(sp)
            follow(m, stream, sp, s)

        @block.tensor
        def _(pe):
            def unit(g, j):
                pe.wait_ge(s["scalar_freed"], g * 2 + j + 1)
                pe.wait_ge(s["vector_freed"], g * 2 + j + 1)
                for k in range(2):
                    pe.wait_ge(s["low_ready"], (g * 2 + j) * 2 + k + 1)
                    for t in range(TT):
                        for c in range(DC // 2):
                            for i, (xp, wp) in enumerate(PASSES):
                                w = m.halves[:, k, wp, :].rearrange("p (c n) -> p c n", c=DC // 2)
                                last = pe.matmul(m.ps[:, 2 * j + t, 0:width(g, j)], lhs(xp, k * (DC // 2) + c, t),
                                                 w[:, c, 0:width(g, j)], start=(k == 0 and c == 0 and i == 0),
                                                 stop=(k == 1 and c == DC // 2 - 1 and i == 2))
                    last.then_inc(s["halves_used"], 1)

            stream.each(pe, unit)

        @block.scalar
        def _(act):
            act.sem_inc(s["scalar_freed"], 2)

            def move(g, j):
                act.wait_ge(s["halves_used"], (g * 2 + j) * 2 + 2)
                act.copy(z[:, 0, bass.ds((g * 2 + j) * BANK, width(g, j))],
                         m.ps[:, 2 * j, 0:width(g, j)]).then_inc(s["scalar_freed"], 1)

            def unit(g, j):
                for k in range(2):
                    high_part(m, stream, act, s, g, j, k)
                if not (isinstance(g, int) and g == 0 and j == 0):
                    move(*back(g, j))

            stream.each(act, unit, peel=True)
            move((stream.n - 1) // 2, (stream.n - 1) % 2)

        @block.vector
        def _(dve):
            dve.sem_inc(s["vector_freed"], 2)

            def move(g, j):
                dve.wait_ge(s["halves_used"], (g * 2 + j) * 2 + 2)
                dve.tensor_copy(z[:, 1, bass.ds((g * 2 + j) * BANK, width(g, j))],
                                m.ps[:, 2 * j + 1, 0:width(g, j)]).then_inc(s["vector_freed"], 1)

            def unit(g, j):
                for k in range(2):
                    low_part(m, stream, dve, s, g, j, k, last=False)
                if not (isinstance(g, int) and g == 0 and j == 0):
                    move(*back(g, j))

            stream.each(dve, unit, peel=True)
            move((stream.n - 1) // 2, (stream.n - 1) % 2)


def follow(m, stream, sp, s, halves=None):
    nxt = stream.next()
    if nxt:
        if nxt.depth > 2:
            sp.wait_ge(s["halves_used"], halves if halves else 2 * stream.n)
        nxt.prefetch(sp)


def project_out(m, stream, chunks, lhs, keep, add, split=True, norm=None):
    total = chunks // 2
    with m.stage("project_out", "high_ready", "low_ready", "halves_used", "residual", "done") as (block, s):
        @block.sync
        def _(sp):
            stream.load_rest(sp)
            m.load_norm(sp, norm)
            follow(m, stream, sp, s, total)

        @block.tensor
        def _(pe):
            if split:
                for u in range(total):
                    pe.wait_ge(s["low_ready"], u + 1)
                    for c in range(2):
                        for t in range(TT):
                            for h in range(2):
                                for i, (xp, wp) in enumerate(PASSES):
                                    w = m.halves[:, u % 2, wp, :].rearrange("p (c n) -> p c n", c=2)
                                    last = pe.matmul(m.ps[:, 2 * t + h, :], lhs(xp, 2 * u + c, t),
                                                     w[:, c, h * BANK:(h + 1) * BANK], start=(u == 0 and c == 0 and i == 0),
                                                     stop=(u == total - 1 and c == 1 and i == 2))
                    last.then_inc(s["halves_used"], 1)
            else:
                for u in range(stream.n):
                    stream.wait_loaded(pe, u // 2, u % 2)
                    w = stream.slot(u % 2).rearrange("p (c n) -> p c n", c=4)
                    for c in range(4 * u, min(4 * u + 4, chunks)):
                        for t in range(TT):
                            for h in range(2):
                                last = pe.matmul(m.ps[:, 2 * t + h, :], lhs(c, t), w[:, c - 4 * u, h * BANK:(h + 1) * BANK],
                                                 start=(c == 0), stop=(c == chunks - 1))
                    last.then_inc(m.unit_used, 1)

        @block.scalar
        def _(act):
            if split:
                for u in range(total):
                    high_part(m, stream, act, s, u // 4, u // 2 % 2, u % 2)

        @block.vector
        def _(dve):
            acc = m.ps[:, 0:4, :].rearrange("p (t h) n -> p t (h n)", t=TT)
            link = chain(dve, s["residual"])
            if keep != 1.0:
                link(dve.tensor_scalar(m.x[:, :, :], m.x[:, :, :], keep, None, ALU.mult))
            if split:
                for u in range(total):
                    low_part(m, stream, dve, s, u // 4, u // 2 % 2, u % 2, last=(u == total - 1))
                dve.wait_ge(s["halves_used"], total)
            else:
                stream.wait_used(dve, 0, stream.n - 1)
            link(dve.scalar_tensor_tensor(m.x[:, :, :], acc, add, m.x[:, :, :], ALU.mult, ALU.add))


def layer_normed(m, eps=1e-5):
    gb = m.norm_rows
    stats = m.small[:, 0:24].rearrange("p (t h k) -> p t h k", t=TT, h=2)
    mv = m.small[:, 24:28].rearrange("p (t k) -> p t k", t=TT)
    rstd = m.small[:, 28:30]
    with m.stage("layer_normed_0", "var_ready", "std_ready", "steps") as (block, s):
        @block.vector
        def _(dve):
            link = chain(dve, s["steps"])
            for t in range(TT):
                for h in range(2):
                    dve.bn_stats(stats[:, t, h, :], m.x[:, t, h * BANK:(h + 1) * BANK]).then_inc(s["steps"], 1)
            dve.wait_ge(s["steps"], 4)
            link = chain(dve, s["steps"], 4)
            for t in range(TT):
                link(dve.bn_aggr(mv[:, t, :], stats[:, t, :, :]))
            dve.tensor_scalar(rstd, mv[:, :, 1], eps, None, ALU.add).then_inc(s["var_ready"], 1)
            dve.wait_ge(s["std_ready"], 1)
            link(dve.reciprocal(rstd, rstd))
            for t in range(TT):
                link(dve.tensor_scalar(m.x[:, t, :], m.x[:, t, :], mv[:, t, 0:1], rstd[:, t:t + 1], ALU.subtract, ALU.mult))
            dve.wait_ge(m.norm_loaded, 32 * m.norms)
            link(dve.tensor_tensor(m.x[:, :, :], m.x[:, :, :], bview(gb[:, 0, :], 1, TT), ALU.mult))
            link(dve.tensor_tensor(m.x[:, :, :], m.x[:, :, :], bview(gb[:, 1, :], 1, TT), ALU.add))

        @block.scalar
        def _(act):
            act.wait_ge(s["var_ready"], 1)
            act.activation(rstd, rstd, ACT.Sqrt).then_inc(s["std_ready"], 1)


def turn_x(m, split=True):
    if split:
        transposed(m, DC, lambda c, t: m.x[:, t, c * P:(c + 1) * P], lambda c: m.xT_r[:, 0, c, :], None,
                   lambda c: m.xT_r[:, 1, c, :])
    else:
        transposed(m, DC, lambda c, t: m.x[:, t, c * P:(c + 1) * P], lambda c: m.xT[:, c, :])


def lhs_x(m):
    return lambda part, c, t: m.xT_r[:, part, c, t * P:(t + 1) * P]


def head_normed(dve, link, eps_added, std_ready, o, out, stats, mv, rstd, eps):
    link(dve.bn_stats(stats, o))
    link(dve.bn_aggr(mv, stats))
    dve.tensor_scalar(rstd, mv[:, 1:2], eps, None, ALU.add).then_inc(eps_added[0], 1)
    eps_added[1] += 1
    dve.wait_ge(std_ready, eps_added[1])
    link(dve.reciprocal(rstd, rstd))
    link(dve.tensor_scalar(out, o, mv[:, 0:1], rstd, ALU.subtract, ALU.mult))



def mlstm(m, in_stream, out_stream, gate_b, norm):
    NIN = 2 * ML_HEADS * ML_DK + 2 * D + 4 * ML_HEADS
    z = m.arena[:, 0:2 * NIN].rearrange("p (t n) -> p t n", t=TT)
    H = ML_HEADS
    project(m, in_stream, NIN, lhs_x(m), z)
    G = z[:, :, 3 * D:3 * D + 16]
    w = m.work
    gb = w[:, 0:16]
    tmp = w[:, 16:16 + 32].rearrange("p (k t n) -> p k t n", k=2, t=TT)
    rows = w[0:H, 128:128 + 4 * T].rearrange("p (d k t) -> p d k t", d=2, k=2)
    A = w[0:H, 1152:1152 + 2 * T].rearrange("p (d t) -> p d t", d=2)
    M = w[0:H, 1664:1664 + 2 * T].rearrange("p (d t) -> p d t", d=2)
    B = w[0:H, 2176:2176 + 2 * T].rearrange("p (d t) -> p d t", d=2)
    EM = w[0:H, 2688:2688 + 2 * T].rearrange("p (d t) -> p d t", d=2)
    cols = m.small[:, 0:32].rearrange("p (k d t h) -> p k d t h", k=2, d=2, t=TT)
    ident = m.const("ident")
    ones = m.const("ones")
    rps = m.ps[0:H, 0:2, :].rearrange("p b n -> p (b n)").rearrange("p (d k t) -> p d k t", d=2, k=2)
    with m.stage("mlstm_0", "bias_loaded", "gates_ready", "exp_in", "exp_out", "steps", "turned", "rows_ready", "back_turned",
                 "m_ready", "em_ready") as (block, s):
        @block.sync
        def _(sp):
            sp.dma_start(gb, gate_b.rearrange("a b h -> (a b h)").partition_broadcast(P)).then_inc(s["bias_loaded"], 16)
            sp.wait_ge(m.columns_loaded, 16 * len(m.columns))

        @block.vector
        def _(dve):
            link = chain(dve, s["steps"])
            dve.wait_ge(s["bias_loaded"], 16)
            link(dve.tensor_tensor(G, G, bview(gb, 1, TT), ALU.add))
            Gf = G.rearrange("p t (d k h) -> p t d k h", d=2, k=2)[:, :, :, 1, :]
            lo, ab = (tmp[:, k].rearrange("p t (d h) -> p t d h", d=2) for k in range(2))
            for t in range(TT):
                link(dve.tensor_scalar(lo[:, t], Gf[:, t], 0.0, None, ALU.min))
                link(dve.scalar_tensor_tensor(ab[:, t], lo[:, t], 2.0, Gf[:, t], ALU.mult, ALU.subtract))
            dve.sem_inc(s["exp_in"], 1)
            dve.wait_ge(s["exp_out"], 2)
            for t in range(TT):
                link(dve.tensor_tensor(Gf[:, t], lo[:, t], ab[:, t], ALU.subtract))
            dve.sem_inc(s["gates_ready"], 1)
            dve.wait_ge(s["turned"], 1)
            link(dve.tensor_copy(rows, rps))
            for d in range(2):
                way = slice(None) if d == 0 else slice(None, None, -1)
                link(dve.tensor_tensor_scan(B[:, d, way], ones[0:H, 0:1].to_broadcast([H, T]), rows[:, d, 1, way], 0.0,
                                            ALU.mult, ALU.add))
                link(dve.tensor_tensor(A[:, d, :], rows[:, d, 0, :], B[:, d, :], ALU.subtract))
                link(dve.tensor_tensor_scan(M[:, d, way], ones[0:H, 0:1].to_broadcast([H, T]), A[:, d, way], 0.0,
                                            ALU.mult, ALU.max))
                link(dve.tensor_tensor(B[:, d, :], B[:, d, :], M[:, d, :], ALU.add))
            dve.sem_inc(s["m_ready"], 1)
            dve.wait_ge(s["back_turned"], 1)
            link(dve.tensor_copy(cols, m.ps[:, 2, 0:32].rearrange("p (k d t h) -> p k d t h", k=2, d=2, t=TT)))

        @block.scalar
        def _(act):
            act.wait_ge(s["exp_in"], 1)
            ab = tmp[:, 1]
            act.activation(ab, ab, ACT.Exp).then_inc(s["exp_out"], 1)
            act.wait_ge(s["exp_out"], 1)
            act.activation(ab, ab, ACT.Ln, bias=m.const("ones")[:, 0:1]).then_inc(s["exp_out"], 1)
            act.wait_ge(s["m_ready"], 1)
            act.activation(EM, B, ACT.Exp, scale=-1.0).then_inc(s["em_ready"], 1)

        @block.tensor
        def _(pe):
            pe.wait_ge(s["gates_ready"], 1)
            for d in range(2):
                for k in range(2):
                    for t in range(TT):
                        a = 8 * d + 4 * k
                        last = pe.transpose(rps[:, d, k, t * P:(t + 1) * P], G[:, t, a:a + H], ident)
            last.then_inc(s["turned"], 1)
            pe.wait_ge(s["em_ready"], 1)
            for k, src in enumerate((A, EM)):
                for d in range(2):
                    for t in range(TT):
                        a = ((k * 2 + d) * 2 + t) * H
                        last = pe.transpose(m.ps[:, 2, a:a + H], src[:, d, t * P:(t + 1) * P], ident[0:H, 0:H])
            last.then_inc(s["back_turned"], 1)

    h_acc = w[:, 3200:3200 + 2 * ML_DV].rearrange("p (t n) -> p t n", t=TT)
    qk = w[:, 128:128 + 512].rearrange("p (k t n) -> p k t n", k=2, t=TT)
    qkT = w[:, 640:640 + 512].rearrange("p (k t) -> p k t", k=2)
    Wt = w[:, 3712:3712 + 2 * 512].rearrange("p (d k t) -> p d k t", d=2, k=2)
    Wf = [w[:, 4736:4736 + 1024].rearrange("p (d n) -> p d n", d=2)]
    hcol = m.small[:, 32:64].rearrange("p (k d t o) -> p k d t o", k=2, d=2, t=TT)[:, :, :, :, 0:1]
    den = m.small[:, 64:72]
    Mh = A
    stats, mv, rstd = m.small[:, 80:92], m.small[:, 92:96], m.small[:, 96:98]
    with m.nc.Fori(0, H) as h:
        with m.stage("mlstm_1", "staged", "turned", "moved", "m_staged", "scores", "m_spread", "steps", "exp_in", "exp_out",
                     "weights_ready", "sums_ready", "eps_added", "std_ready") as (block, s):
            @block.vector
            def _(dve):
                link = chain(dve, s["steps"])
                dve.tensor_scalar(qk[:, 0], z[:, :, bass.ds(h * ML_DK, ML_DK)], ML_DK ** -0.5, None, ALU.mult).then_inc(s["staged"], 1)
                dve.tensor_copy(qk[:, 1], z[:, :, bass.ds(h * ML_DK + H * ML_DK, ML_DK)]).then_inc(s["staged"], 1)
                for d in range(2):
                    dve.tensor_scalar(Mh[:, d, :], M[:, d, :], ident[0:H, bass.ds(h, 1)], None, ALU.mult).then_inc(s["m_staged"], 1)
                for k in range(2):
                    for d in range(2):
                        link(dve.tensor_copy(hcol[:, k, d, :, 0], cols[:, k, d, :, bass.ds(h, 1)].rearrange("p t o -> p (t o)")))
                dve.wait_ge(s["turned"], 1)
                dve.tensor_copy(qkT, m.ps[:, 0, :].rearrange("p (k t) -> p k t", k=2)).then_inc(s["moved"], 1)
                dve.wait_ge(s["m_spread"], 1)
                for d in range(2):
                    neg = m.const("neg_fwd" if d == 0 else "neg_bwd").rearrange("p (k t) -> p k t", k=2)
                    dve.scalar_tensor_tensor(Wt[:, d], bview(m.ps[:, 2 + d, 0:T], 1, 2), -1.0, neg,
                                             ALU.mult, ALU.add).then_inc(s["exp_in"], 1)
                dve.wait_ge(s["exp_out"], 4)
                dve.wait_ge(s["scores"], 1)
                for d in range(2):
                    dve.tensor_tensor(Wf[0][:, d, :], Wt[:, d].rearrange("p k t -> p (k t)"),
                                      m.ps[:, 1, :], ALU.mult).then_inc(s["weights_ready"], 1)
                for d in range(2):
                    for t in range(TT):
                        o = m.ps[:, 4 + 2 * d + t, :]
                        dc = den[:, 2 * d + t:2 * d + t + 1]
                        dve.wait_ge(s["sums_ready"], 2 * d + t + 1)
                        link(dve.tensor_scalar(dc, o[:, ML_DV:ML_DV + 1], -1.0, None, ALU.mult))
                        link(dve.tensor_tensor(dc, dc, o[:, ML_DV:ML_DV + 1], ALU.max))
                        link(dve.tensor_tensor(dc, dc, hcol[:, 1, d, t, :], ALU.max))
                        link(dve.reciprocal(dc, dc))
                        if d == 0:
                            link(dve.tensor_scalar(h_acc[:, t, :], o[:, 0:ML_DV], dc, None, ALU.mult))
                        else:
                            link(dve.scalar_tensor_tensor(h_acc[:, t, :], o[:, 0:ML_DV], dc, h_acc[:, t, :], ALU.mult, ALU.add))
                added = [s["eps_added"], 0]
                for t in range(TT):
                    head_normed(dve, link, added, s["std_ready"], h_acc[:, t, :],
                                z[:, t, bass.ds(h * ML_DV + 2 * H * ML_DK, ML_DV)], stats[:, 6 * t:6 * t + 6], mv[:, 2 * t:2 * t + 2],
                                rstd[:, t:t + 1], 1e-5)

            @block.tensor
            def _(pe):
                pe.wait_ge(s["staged"], 2)
                for k in range(2):
                    for t in range(TT):
                        last = pe.transpose(m.ps[:, 0, k * T + t * P:k * T + (t + 1) * P], qk[:, k, t, :], ident)
                last.then_inc(s["turned"], 1)
                pe.wait_ge(s["m_staged"], 2)
                for d in range(2):
                    last = pe.matmul(m.ps[:, 2 + d, 0:T], ones[0:H, :], Mh[:, d, :], start=True, stop=True)
                last.then_inc(s["m_spread"], 1)
                pe.wait_ge(s["moved"], 1)
                for k in range(2):
                    last = pe.matmul(m.ps[:, 1, k * T:(k + 1) * T], qkT[:, 1, k * P:(k + 1) * P], qkT[:, 0, :], start=True, stop=True)
                last.then_inc(s["scores"], 1)
                for d in range(2):
                    pe.wait_ge(s["weights_ready"], d + 1)
                    for t in range(TT):
                        srcs = [k for k in range(2) if (k <= t if d == 0 else k >= t)]
                        o = m.ps[:, 4 + 2 * d + t, :]
                        for i, k in enumerate(srcs):
                            pe.matmul(o[:, 0:ML_DV], Wf[0][:, d, k * T + t * P:k * T + (t + 1) * P],
                                      z[:, k, bass.ds(h * ML_DV + 2 * H * ML_DK, ML_DV)], start=(i == 0), stop=(i == len(srcs) - 1))
                        for i, k in enumerate(srcs):
                            last = pe.matmul(o[:, ML_DV:ML_DV + 1], Wf[0][:, d, k * T + t * P:k * T + (t + 1) * P],
                                             ones[:, 0:1], start=(i == 0), stop=(i == len(srcs) - 1))
                        last.then_inc(s["sums_ready"], 1)

            @block.scalar
            def _(act):
                for d in range(2):
                    act.wait_ge(s["exp_in"], d + 1)
                    act.wait_ge(s["steps"], 4)
                    for k in range(2):
                        act.activation(Wt[:, d, k, :], Wt[:, d, k, :], ACT.Exp, bias=hcol[:, 0, d, k, :]).then_inc(s["exp_out"], 1)
                for t in range(TT):
                    act.wait_ge(s["eps_added"], t + 1)
                    act.activation(rstd[:, t:t + 1], rstd[:, t:t + 1], ACT.Sqrt).then_inc(s["std_ready"], 1)
        with m.stage("mlstm_2") as (block, s):
            pass
    v0 = 2 * H * ML_DK
    gated(m, z, [(v0, v0 + D, D)], ACT.Sigmoid)
    mixed_out(m, out_stream, z, [v0 + c * P for c in range(DC)], ALPHA, 1.0, "mlstm_norm_g", norm=norm)


def gated(m, z, parts, func):
    with m.stage("gated_0", "gate_ready", "steps", "freed") as (block, s):
        @block.scalar
        def _(act):
            for i, (a, b, n) in enumerate(parts):
                act.activation(z[:, :, b:b + n], z[:, :, b:b + n], func).then_inc(s["gate_ready"], 1)

        @block.vector
        def _(dve):
            for i, (a, b, n) in enumerate(parts):
                dve.wait_ge(s["gate_ready"], i + 1)
                dve.tensor_tensor(z[:, :, a:a + n], z[:, :, a:a + n], z[:, :, b:b + n], ALU.mult).then_inc(s["steps"], 1)


def mixed_out(m, stream, z, chunks, keep, add, gains=None, split=True, norm=None):
    n = len(chunks)
    gain = None
    if gains is not None:
        gain = lambda c: m.columns[gains][:, c:c + 1]
    src = lambda c, t: z[:, t, chunks[c]:chunks[c] + P]
    if split:
        zT = m.work_r[:, 0:2 * n * T].rearrange("p (k c t) -> p k c t", k=2, c=n)
        transposed(m, n, src, lambda c: zT[:, 0, c, :], gain, lambda c: zT[:, 1, c, :])
        project_out(m, stream, n, lambda part, c, t: zT[:, part, c, t * P:(t + 1) * P], keep, add, norm=norm)
    else:
        zT = m.work[:, 0:n * T].rearrange("p (c t) -> p c t", c=n)
        transposed(m, n, src, lambda c: zT[:, c, :], gain)
        project_out(m, stream, n, lambda c, t: zT[:, c, t * P:(t + 1) * P], keep, add, False)




def moe(m, stream, norm):
    ar = m.arena
    xin = ar[:, 0:4096].rearrange("p (c n) -> p c n", c=DC)
    outs = ar[:, 4096:8192].rearrange("p (q n) -> p q n", q=QUADS)
    scatter = ar[:, 8192:9216].rearrange("p (q t) -> p q t", q=QUADS)
    sel = ar[:, 9216:10240].rearrange("p (t e j) -> p t e j", t=TT, e=E)
    selg = ar[:, 10240:11264].rearrange("p (t e j) -> p t e j", t=TT, e=E)
    hid = ar[:, 11264:12288]
    w = m.work
    rt = m.router
    aff = w[:, 128:128 + 2 * E].rearrange("p (t e) -> p t e", t=TT)
    pos = w[:, 160:160 + 2 * E].rearrange("p (t e) -> p t e", t=TT)
    rmax, rsum = m.small[:, 0:2], m.small[:, 2:4]
    affT = w[0:E, 256:512]
    left = w[0:E, 512:768]
    took = w[0:E, 768:1024]
    count = w[0:E, 1024:1280]
    top = m.small[0:E, 16:24]
    ident, ones = m.const("ident"), m.const("ones")
    slot_no = m.const("slot_no")
    with m.stage("moe_0", "logits", "max_ready", "exp_ready", "steps", "aff_ready", "aff_turned", "pos_ready",
                 "pos_turned", "sel_ready", "gathered", "scat_turned", "vector_moved", "scalar_moved") as (block, s):
        @block.tensor
        def _(pe):
            pe.wait_ge(m.router_loaded, 16 * m.routers)
            for t in range(TT):
                for c in range(DC):
                    last = pe.matmul(m.ps[:, 0, t * E:(t + 1) * E], m.xT[:, c, t * P:(t + 1) * P], rt[:, c, :],
                                     start=(c == 0), stop=(c == DC - 1))
            last.then_inc(s["logits"], 1)
            pe.wait_ge(s["aff_ready"], 1)
            for t in range(TT):
                last = pe.transpose(m.ps[0:E, 1, t * P:(t + 1) * P], aff[:, t, :], ident)
            last.then_inc(s["aff_turned"], 1)
            pe.wait_ge(s["pos_ready"], 1)
            for t in range(TT):
                last = pe.transpose(m.ps[:, 0, t * E:(t + 1) * E], took[:, t * P:(t + 1) * P], ident[0:E, 0:E])
            last.then_inc(s["pos_turned"], 1)
            pe.wait_ge(s["sel_ready"], 1)
            for c in range(DC):
                if c >= 6:
                    pe.wait_ge(s["vector_moved"] if c % 2 == 0 else s["scalar_moved"], (c - 6) // 2 + 1)
                for t in range(TT):
                    last = pe.matmul(m.ps[:, 2 + c % 6, :], m.x[:, t, c * P:(c + 1) * P],
                                     sel[:, t].rearrange("p e j -> p (e j)"), start=(t == 0), stop=(t == TT - 1))
                last.then_inc(s["gathered"], 1)
            pe.wait_ge(s["sel_ready"], 2)
            for q in range(QUADS):
                for t in range(TT):
                    last = pe.transpose(m.ps[:, q // 2, (q % 2) * T + t * P:(q % 2) * T + (t + 1) * P],
                                        selg[:, t].rearrange("p e j -> p (e j)")[:, q * P:(q + 1) * P], ident)
            last.then_inc(s["scat_turned"], 1)

        @block.vector
        def _(dve):
            link = chain(dve, s["steps"])
            dve.wait_ge(s["logits"], 1)
            lg = m.ps[:, 0, 0:2 * E].rearrange("p (t e) -> p t e", t=TT)
            link(dve.tensor_reduce(rmax, lg, AX, ALU.max))
            dve.tensor_tensor(aff, lg, bview(rmax, 2, E), ALU.subtract).then_inc(s["max_ready"], 1)
            dve.wait_ge(s["exp_ready"], 1)
            link(dve.tensor_reduce(rsum, aff, AX, ALU.add))
            link(dve.reciprocal(rsum, rsum))
            dve.tensor_tensor(aff, aff, bview(rsum, 2, E), ALU.mult).then_inc(s["aff_ready"], 1)
            dve.wait_ge(s["aff_turned"], 1)
            link(dve.tensor_copy(left, m.ps[0:E, 1, 0:T]))
            for _ in range(CAP // 8):
                link(dve.max(top, left))
                link(dve.match_replace(left, top, left, -1.0))
            link(dve.tensor_scalar(took, left, -1.0, None, ALU.is_equal))
            link(dve.tensor_tensor_scan(count, ones[0:E, 0:1].to_broadcast([E, T]), took, 0.0, ALU.mult, ALU.add))
            dve.tensor_tensor(took, took, count, ALU.mult).then_inc(s["pos_ready"], 1)
            dve.wait_ge(s["pos_turned"], 1)
            link(dve.tensor_copy(pos, m.ps[:, 0, 0:2 * E].rearrange("p (t e) -> p t e", t=TT)))
            for t in range(TT):
                link(dve.tensor_tensor(sel[:, t], bview(slot_no, 1, E), bview(pos[:, t, :], 2, CAP), ALU.is_equal))
            dve.sem_inc(s["sel_ready"], 1)
            for t in range(TT):
                link(dve.tensor_tensor(selg[:, t], sel[:, t], bview(aff[:, t, :], 2, CAP), ALU.mult))
            dve.sem_inc(s["sel_ready"], 1)
            for c in range(0, DC, 2):
                dve.wait_ge(s["gathered"], c + 1)
                dve.tensor_copy(xin[:, c, :], m.ps[:, 2 + c % 6, :]).then_inc(s["vector_moved"], 1)
            dve.wait_ge(s["scat_turned"], 1)
            dve.tensor_copy(scatter.rearrange("p q t -> p (q t)"),
                            m.ps[:, 0:2, :].rearrange("p b n -> p (b n)")).then_inc(s["vector_moved"], 1)
            link(dve.tensor_scalar(m.x[:, :, :], m.x[:, :, :], ALPHA, None, ALU.mult))

        @block.scalar
        def _(act):
            act.wait_ge(s["max_ready"], 1)
            act.activation(aff, aff, ACT.Exp).then_inc(s["exp_ready"], 1)
            for c in range(1, DC, 2):
                act.wait_ge(s["gathered"], c + 1)
                act.copy(xin[:, c, :], m.ps[:, 2 + c % 6, :]).then_inc(s["scalar_moved"], 1)

    xq = w[:, 1280:1280 + D].rearrange("p (c n) -> p c n", c=DC)
    hT = w[:, 2304:2304 + D].rearrange("p (c n) -> p c n", c=DC)
    sg = ar[:, 12288:12288 + D]
    gate = m.ps[:, 0:2, :].rearrange("p b n -> p (b n)")
    up = m.ps[:, 2:4, :].rearrange("p b n -> p (b n)")
    down = m.ps[:, 4:6, :].rearrange("p b n -> p (b n)")
    turn = m.ps[:, 6:8, :].rearrange("p b n -> p (b n)")
    GATE, UP, DOWN = DC - 1, 2 * DC - 1, 3 * DC - 1
    with m.stage("moe_1", "tokens_staged", "gate_done", "hidden_ready", "hidden_turned", "hT_ready", "answer_moved",
                 "steps") as (block, s):
        @block.sync
        def _(sp):
            stream.load_rest(sp)
            m.load_norm(sp, norm)
            if stream.next():
                stream.next().prefetch(sp)

        @block.tensor
        def _(pe):
            def unit(g, j):
                if j == 0:
                    pe.wait_ge(s["tokens_staged"], g + 1)
                if j == 2 * DC:
                    pe.wait_ge(s["hidden_ready"], g + 1)
                    for c in range(DC):
                        last = pe.transpose(turn[:, c * P:(c + 1) * P], hid[:, c * P:(c + 1) * P], ident)
                    last.then_inc(s["hidden_turned"], 1)
                    pe.wait_ge(s["hT_ready"], g + 1)
                stream.wait_loaded(pe, g, j)
                w4 = stream.slot(j).rearrange("p (e n) -> p e n", e=EQ)
                acc = (gate, up, down)[j // DC]
                lhs = xq if j < 2 * DC else hT
                c = j % DC
                for half in range(2):
                    for e in range(EQ):
                        last = pe.matmul(acc[e * CAP:(e + 1) * CAP, half * BANK:(half + 1) * BANK],
                                         lhs[:, c, e * CAP:(e + 1) * CAP], w4[:, e, half * BANK:(half + 1) * BANK],
                                         start=(c == 0), stop=(c == DC - 1), tile_position=(0, e * CAP))
                last.then_inc(m.unit_used, 1)

            stream.each(pe, unit)

        @block.scalar
        def _(act):
            with act.Fori(0, QUADS) as g:
                stream.wait_used(act, g, GATE)
                act.activation(sg, gate, ACT.Silu).then_inc(s["gate_done"], 1)
                stream.wait_used(act, g, DOWN)
                act.copy(outs[:, bass.ds(g, 1), :].rearrange("p o n -> p (o n)"), down).then_inc(s["answer_moved"], 1)

        @block.vector
        def _(dve):
            with dve.Fori(0, QUADS) as g:
                dve.tensor_copy(xq, xin[:, :, bass.ds(g * P, P)]).then_inc(s["tokens_staged"], 1)
                stream.wait_used(dve, g, UP)
                dve.wait_ge(s["gate_done"], g + 1)
                dve.tensor_tensor(hid, sg, up, ALU.mult).then_inc(s["hidden_ready"], 1)
                dve.wait_ge(s["hidden_turned"], g + 1)
                dve.tensor_copy(hT.rearrange("p c n -> p (c n)"), turn).then_inc(s["hT_ready"], 1)
                dve.wait_ge(s["answer_moved"], g + 1)

    with m.stage("moe_2", "summed", "steps") as (block, s):
        @block.tensor
        def _(pe):
            for t in range(TT):
                for half in range(2):
                    for q in range(QUADS):
                        last = pe.matmul(m.ps[:, 2 * t + half, :], scatter[:, q, t * P:(t + 1) * P],
                                         outs[:, q, half * BANK:(half + 1) * BANK], start=(q == 0), stop=(q == QUADS - 1))
                last.then_inc(s["summed"], 1)

        @block.vector
        def _(dve):
            for t in range(TT):
                dve.wait_ge(s["summed"], t + 1)
                dve.tensor_tensor(m.x[:, t, :], m.ps[:, 2 * t:2 * t + 2, :].rearrange("p h n -> p (h n)"),
                                  m.x[:, t, :], ALU.add).then_inc(s["steps"], 1)



def gla(m, in_stream, out_stream, gate_w, norm):
    H, DK, DV = 4, P, 2 * P
    NIN = 2 * H * DK + 2 * D + 2 * GLA_RANK
    z = m.arena[:, 0:2 * NIN].rearrange("p (t n) -> p t n", t=TT)
    project(m, in_stream, NIN, lhs_x(m), z)
    w = m.work
    gbc = m.columns["gla_gate_b"]
    gw = w[0:GLA_RANK, 0:2 * H * DK].rearrange("p (d n) -> p d n", d=2)
    lowT = w[0:GLA_RANK, 1024:1024 + 2 * T].rearrange("p (d t) -> p d t", d=2)
    ident = m.const("ident")
    with m.stage("gla_0", "turned", "steps", "gate_w_loaded") as (block, s):
        @block.sync
        def _(sp):
            sp.dma_start(gw, gate_w.rearrange("d r n -> r d n")).then_inc(s["gate_w_loaded"], 16)
            sp.wait_ge(s["gate_w_loaded"], 16)

        @block.tensor
        def _(pe):
            for d in range(2):
                for t in range(TT):
                    a = NIN - 2 * GLA_RANK + d * GLA_RANK
                    last = pe.transpose(m.ps[0:GLA_RANK, 0, d * T + t * P:d * T + (t + 1) * P], z[:, t, a:a + GLA_RANK], ident)
            last.then_inc(s["turned"], 1)

        @block.vector
        def _(dve):
            dve.wait_ge(s["turned"], 1)
            dve.tensor_copy(lowT, m.ps[0:GLA_RANK, 0, :].rearrange("p (d t) -> p d t", d=2)).then_inc(s["steps"], 1)

    qk = w[:, 1536:2048].rearrange("p (k t n) -> p k t n", k=2, t=TT)
    qkT = w[:, 2048:2560].rearrange("p (k t) -> p k t", k=2)
    gwh = w[0:GLA_RANK, 2560:2816].rearrange("p (d n) -> p d n", d=2)
    bh = m.small[:, 10:12]
    lo = w[:, 2816:3328].rearrange("p (d t) -> p d t", d=2)
    ab = w[:, 3328:3840].rearrange("p (d t) -> p d t", d=2)
    B = w[:, 3840:4352].rearrange("p (d t) -> p d t", d=2)
    QE = w[:, 4352:5120].rearrange("p (d i t) -> p d i t", d=2, i=3)
    KE = w[:, 5120:5888].rearrange("p (d i t) -> p d i t", d=2, i=3)
    Wf = w[:, 2816:3584].rearrange("p (d i t) -> p d i t", d=2, i=3)
    neg = m.small[:, 12:18].rearrange("p (d i) -> p d i", d=2)
    stats, mv, rstd = m.small[:, 80:92], m.small[:, 92:96], m.small[:, 96:98]
    ones = m.const("ones")
    v0 = 2 * H * DK
    centre = [[P // 2, P + P // 2, P - 1], [P // 2, P + P // 2, P]]
    q_tile = [[0, 1, 1], [0, 1, 0]]
    k_tile = [[0, 1, 0], [0, 1, 1]]
    with m.nc.Fori(0, H) as h:
        with m.stage("gla_1", "staged", "turned", "moved", "gates_staged", "gates_made", "steps", "exp_in", "ln_out",
                     "sums_ready", "decays_out", "products_ready", "scores", "weights_ready", "out_ready", "eps_added",
                     "std_ready") as (block, s):
            @block.vector
            def _(dve):
                link = chain(dve, s["steps"])
                dve.tensor_scalar(qk[:, 0], z[:, :, bass.ds(h * DK, DK)], DK ** -0.5, None, ALU.mult).then_inc(s["staged"], 1)
                dve.tensor_copy(qk[:, 1], z[:, :, bass.ds(h * DK + H * DK, DK)]).then_inc(s["staged"], 1)
                dve.tensor_copy(gwh, gw[:, :, bass.ds(h * DK, DK)]).then_inc(s["gates_staged"], 1)
                link(dve.tensor_copy(bh, gbc.rearrange("p (d h) -> p d h", d=2)[:, :, bass.ds(h, 1)].rearrange("p d o -> p (d o)")))
                dve.wait_ge(s["turned"], 1)
                dve.tensor_copy(qkT, m.ps[:, 0, :].rearrange("p (k t) -> p k t", k=2)).then_inc(s["moved"], 1)
                dve.wait_ge(s["gates_made"], 1)
                for d in range(2):
                    y = m.ps[:, 1, d * T:(d + 1) * T]
                    link(dve.tensor_scalar(lo[:, d], y, bh[:, d:d + 1], 0.0, ALU.add, ALU.min))
                    link(dve.tensor_scalar(ab[:, d], y, bh[:, d:d + 1], None, ALU.add))
                link(dve.scalar_tensor_tensor(ab, lo, 2.0, ab, ALU.mult, ALU.subtract))
                dve.sem_inc(s["exp_in"], 1)
                dve.wait_ge(s["ln_out"], 2)
                link(dve.tensor_tensor(lo, lo, ab, ALU.subtract))
                link(dve.tensor_scalar(lo, lo, 1.0 / GLA_TAU, None, ALU.mult))
                for d in range(2):
                    way = slice(None) if d == 0 else slice(None, None, -1)
                    link(dve.tensor_tensor_scan(B[:, d, way], ones[:, 0:1].to_broadcast([P, T]), lo[:, d, way], 0.0,
                                                ALU.mult, ALU.add))
                for d in range(2):
                    for i in range(3):
                        c = centre[d][i]
                        link(dve.tensor_scalar(neg[:, d, i:i + 1], B[:, d, c:c + 1], -1.0, None, ALU.mult))
                dve.sem_inc(s["sums_ready"], 1)
                dve.wait_ge(s["decays_out"], 12)
                dve.wait_ge(s["moved"], 1)
                for d in range(2):
                    for X, k, tiles in ((QE, 0, q_tile[d]), (KE, 1, k_tile[d])):
                        dve.tensor_tensor(X[:, d, 0:2, :], X[:, d, 0:2, :], qkT[:, k, :].rearrange("p (i t) -> p i t", i=2),
                                          ALU.mult).then_inc(s["products_ready"], 1)
                        c = tiles[2]
                        dve.tensor_tensor(X[:, d, 2, :], X[:, d, 2, :], qkT[:, k, c * P:(c + 1) * P],
                                          ALU.mult).then_inc(s["products_ready"], 1)
                dve.wait_ge(s["scores"], 1)
                for d in range(2):
                    keep = m.const("keep_fwd" if d == 0 else "keep_bwd")
                    sc = m.ps[:, 2 + d, 0:3 * P].rearrange("p (i t) -> p i t", i=3)
                    link(dve.tensor_tensor(Wf[:, d, 0:2, :], sc[:, 0:2, :], bview(keep, 1, 2), ALU.mult))
                    link(dve.tensor_copy(Wf[:, d, 2, :], sc[:, 2, :]))
                dve.tensor_tensor(Wf[:, 0, 0:2, :], Wf[:, 0, 0:2, :], Wf[:, 1, 0:2, :], ALU.add).then_inc(s["weights_ready"], 1)
                added = [s["eps_added"], 0]
                dve.wait_ge(s["out_ready"], 2)
                for t in range(TT):
                    head_normed(dve, link, added, s["std_ready"], m.ps[:, 4 + t, 0:DV], z[:, t, bass.ds(h * DV + v0, DV)],
                                stats[:, 6 * t:6 * t + 6], mv[:, 2 * t:2 * t + 2], rstd[:, t:t + 1], 1e-5)

            @block.tensor
            def _(pe):
                pe.wait_ge(s["staged"], 2)
                for k in range(2):
                    for t in range(TT):
                        last = pe.transpose(m.ps[:, 0, k * T + t * P:k * T + (t + 1) * P], qk[:, k, t, :], ident)
                last.then_inc(s["turned"], 1)
                pe.wait_ge(s["gates_staged"], 1)
                for d in range(2):
                    last = pe.matmul(m.ps[:, 1, d * T:(d + 1) * T], gwh[:, d, :], lowT[:, d, :], start=True, stop=True)
                last.then_inc(s["gates_made"], 1)
                pe.wait_ge(s["products_ready"], 8)
                for d in range(2):
                    for i in range(3):
                        last = pe.matmul(m.ps[:, 2 + d, i * P:(i + 1) * P], KE[:, d, i, :], QE[:, d, i, :], start=True, stop=True)
                last.then_inc(s["scores"], 1)
                pe.wait_ge(s["weights_ready"], 1)
                v = z[:, :, bass.ds(h * DV + v0, DV)]
                for t, d in ((0, 1), (1, 0)):
                    pe.matmul(m.ps[:, 4 + t, 0:DV], Wf[:, 0, t, :], v[:, t, :], start=True, stop=False)
                    pe.matmul(m.ps[:, 4 + t, 0:DV], Wf[:, d, 2, :], v[:, 1 - t, :], start=False, stop=True).then_inc(s["out_ready"], 1)

            @block.scalar
            def _(act):
                act.wait_ge(s["exp_in"], 1)
                act.activation(ab, ab, ACT.Exp).then_inc(s["ln_out"], 1)
                act.wait_ge(s["ln_out"], 1)
                act.activation(ab, ab, ACT.Ln, bias=ones[:, 0:1]).then_inc(s["ln_out"], 1)
                act.wait_ge(s["sums_ready"], 1)
                for d in range(2):
                    for i in range(3):
                        c, qt, kt = centre[d][i], q_tile[d][i], k_tile[d][i]
                        act.activation(QE[:, d, i, :], B[:, d, qt * P:(qt + 1) * P], ACT.Exp,
                                       bias=neg[:, d, i:i + 1]).then_inc(s["decays_out"], 1)
                        act.activation(KE[:, d, i, :], B[:, d, kt * P:(kt + 1) * P], ACT.Exp, scale=-1.0,
                                       bias=B[:, d, c:c + 1]).then_inc(s["decays_out"], 1)
                for t in range(TT):
                    act.wait_ge(s["eps_added"], t + 1)
                    act.activation(rstd[:, t:t + 1], rstd[:, t:t + 1], ACT.Sqrt).then_inc(s["std_ready"], 1)
        with m.stage("gla_2") as (block, s):
            pass
    gated(m, z, [(v0, v0 + D, D)], ACT.Silu)
    mixed_out(m, out_stream, z, [v0 + c * P for c in range(DC)], ALPHA, 1.0, "gla_norm_g", norm=norm)



def rms_scaled(m, src, dst, eps):
    square = m.work[:, 2 * D:3 * D]
    ss = m.small[:, 0:2]
    with m.stage("rms_scaled_0", "squares", "mean_ready", "std_ready", "steps") as (block, s):
        @block.scalar
        def _(act):
            for t in range(TT):
                act.activation(square, src[:, t, :], ACT.Square, accum_out=ss[:, t:t + 1]).then_inc(s["squares"], 1)
                act.wait_ge(s["squares"], t + 1)
            act.wait_ge(s["mean_ready"], 1)
            act.activation(ss, ss, ACT.Sqrt).then_inc(s["std_ready"], 1)

        @block.vector
        def _(dve):
            link = chain(dve, s["steps"])
            dve.wait_ge(s["squares"], TT)
            dve.tensor_scalar(ss, ss, 1.0 / D, eps, ALU.mult, ALU.add).then_inc(s["mean_ready"], 1)
            dve.wait_ge(s["std_ready"], 1)
            link(dve.reciprocal(ss, ss))
            for t in range(TT):
                link(dve.tensor_scalar(dst[:, t, :], src[:, t, :], ss[:, t:t + 1], None, ALU.mult))


def rms_turned(m, src, gain, eps=1e-6):
    gcol = m.columns[gain]
    scaled = m.work[:, 0:2 * D].rearrange("p (t n) -> p t n", t=TT)
    rms_scaled(m, src, scaled, eps)
    transposed(m, DC, lambda c, t: scaled[:, t, c * P:(c + 1) * P], lambda c: m.xT_r[:, 0, c, :], lambda c: gcol[:, c:c + 1],
               lambda c: m.xT_r[:, 1, c, :])


def rms_normed(m, gain, eps=1e-6):
    rms_scaled(m, m.x, m.x, eps)
    g = m.work[:, 0:D]
    with m.stage("rms_normed_0", "gain_loaded", "steps") as (block, s):
        @block.sync
        def _(sp):
            sp.dma_start(g, gain.partition_broadcast(P)).then_inc(s["gain_loaded"], 16)

        @block.vector
        def _(dve):
            dve.wait_ge(s["gain_loaded"], 16)
            dve.tensor_tensor(m.x[:, :, :], m.x[:, :, :], bview(g, 1, TT), ALU.mult).then_inc(s["steps"], 1)


TURN = 6.28125
TURN_LOW = float(np.float32(2 * math.pi - TURN))
TURN_LAST = 2 * math.pi - TURN - TURN_LOW
ROUND = 1.5 * 2.0 ** 23
HALF_TURN = 3.1415925


def rotary_tables(m, positions, tables):
    pos_i = m.small_i[:, 0:2]
    pos = m.small[:, 0:2]
    with m.stage("rotary_tables_0", "positions_loaded", "angles_ready", "steps", "made") as (block, s):
        @block.sync
        def _(sp):
            with m.nc.allow_non_contiguous_dma("one position a partition"):
                sp.dma_start(pos_i, positions[0].rearrange("(t p) -> p t", p=P)).then_inc(s["positions_loaded"], 16)

        @block.vector
        def _(dve):
            link = chain(dve, s["steps"])
            dve.wait_ge(s["positions_loaded"], 16)
            link(dve.tensor_copy(pos, pos_i))
            for cos, sin, freq, n in tables:
                k = m.work[:, 0:2 * n].rearrange("p (t n) -> p t n", t=TT)
                for t in range(TT):
                    link(dve.tensor_scalar(sin[:, t], freq, pos[:, t:t + 1], None, ALU.mult))
                link(dve.tensor_scalar(k, sin, 1.0 / (2 * math.pi), None, ALU.mult))
                link(dve.tensor_scalar(k, k, ROUND, None, ALU.add))
                link(dve.tensor_scalar(k, k, -ROUND, None, ALU.add))
                for part in (TURN, TURN_LOW, TURN_LAST):
                    link(dve.scalar_tensor_tensor(sin, k, -part, sin, ALU.mult, ALU.add))
                link(dve.tensor_scalar(cos, sin, math.pi / 2, None, ALU.add))
                link(dve.tensor_scalar(k, cos, math.pi, -2 * math.pi, ALU.is_gt, ALU.mult))
                link(dve.tensor_tensor(cos, cos, k, ALU.add))
                for x in (cos, sin):
                    link(dve.tensor_scalar(x, x, -HALF_TURN, HALF_TURN, ALU.max, ALU.min))
            dve.sem_inc(s["angles_ready"], 1)

        @block.scalar
        def _(act):
            act.wait_ge(s["angles_ready"], 1)
            for cos, sin, freq, n in tables:
                act.activation(cos, cos, ACT.Sin).then_inc(s["made"], 1)
                act.activation(sin, sin, ACT.Sin).then_inc(s["made"], 1)


def rotated(m, z, regions, cos, sin, half, tmp):
    with m.stage("rotated_0", "steps") as (block, s):
        @block.vector
        def _(dve):
            link = chain(dve, s["steps"])
            for col, n in regions:
                for t in range(TT):
                    zz = z[:, t, col:col + n * 2 * half].rearrange("p (h k j) -> p h k j", k=2, j=half)
                    a, b = zz[:, :, 0, :], zz[:, :, 1, :]
                    c, sn = bview(cos[:, t], 1, n), bview(sin[:, t], 1, n)
                    ta = tmp[:, 0:n * half].rearrange("p (h j) -> p h j", h=n)
                    tb = tmp[:, n * half:2 * n * half].rearrange("p (h j) -> p h j", h=n)
                    link(dve.tensor_tensor(ta, a, sn, ALU.mult))
                    link(dve.tensor_tensor(tb, b, sn, ALU.mult))
                    link(dve.tensor_tensor(a, a, c, ALU.mult))
                    link(dve.tensor_tensor(b, b, c, ALU.mult))
                    link(dve.tensor_tensor(a, a, tb, ALU.subtract))
                    link(dve.tensor_tensor(b, b, ta, ALU.add))


def overlapped(eng, n, first, second):
    first(0, 0)
    if n > 2:
        with eng.Fori(0, (n - 2) // 2) as g:
            for r in range(2):
                first(g * 2 + (r + 1), (r + 1) % 2)
                second(g * 2 + r, r)
    first(n - 1, 1)
    second(n - 2, 0)
    second(n - 1, 1)


def ahead(eng, n, body):
    body(0, 0)
    body(1, 1)
    if n > 2:
        with eng.Fori(1, n // 2) as g:
            for r in range(2):
                body(g * 2 + r, r)


def attention(m, n, z, kv, q_at, k_at, v_at, scale, staging, neg=None, bias=None, cmp=None):
    w = m.work
    qn = 1 if cmp else 2
    qs = [staging[:, 512 * p:512 * p + 256].rearrange("p (t n) -> p t n", t=TT) for p in range(2)]
    ks = [staging[:, 512 * p + 256:512 * p + 512].rearrange("p (b t n) -> p b t n", b=2, t=TT) for p in range(2)]
    qT = w[0:HD, 0:512].rearrange("p (b t) -> p b t", b=2)
    kT = w[0:HD, 512:1024].rearrange("p (b t) -> p b t", b=2)
    L = [w[:, 1024 + 1024 * p:2048 + 1024 * p].rearrange("p (b t s) -> p b t s", b=2, t=TT) for p in range(2)]
    PT = w[:, 3072:4096].rearrange("p (b s t) -> p b s t", b=2, s=2)
    mx, sm = ([m.small[:, 24 * p + k:24 * p + k + 6] for p in range(2)] for k in (0, 6))
    fac = [m.small[:, 24 * p + 12:24 * p + 18].rearrange("p (b t) -> p b t", b=3) for p in range(2)]
    ident = m.const("ident")
    K = 6 if cmp else 4
    with m.stage("attention", "staged", "q_turned", "k_turned", "q_moved", "k_moved", "scores", "cmp_scores", "bias0_loaded", "bias1_loaded",
                 "bias_ready", "masked", "first_steps", "max_ready", "exp_out", "p0_turned", "p1_turned", "pc_turned",
                 "p0_moved", "p1_moved", "pc_moved", "second_steps", "sums_ready", "out_done") as (block, s):
        @block.sync
        def _(sp):
            def load(i, p):
                if not (isinstance(i, int) and i < 2):
                    sp.wait_ge(s["masked"], i - 1)
                for b in range(2):
                    sp.dma_start(bias["tiles"][p][:, b], bias["source"](i, b)).then_inc(s["bias0_loaded"] if p == 0 else s["bias1_loaded"], 16)

            if bias:
                ahead(sp, n, load)

        @block.gpsimd
        def _(pool):
            def stage(i, p):
                if not (isinstance(i, int) and i < 2):
                    pool.wait_ge(s["k_turned"], i - 1)
                pool.tensor_copy(qs[p][:, :, 0:qn * HD], z[:, :, bass.ds(q_at(i), qn * HD)]).then_inc(s["staged"], 1)
                for b in range(2):
                    pool.tensor_copy(ks[p][:, b], kv[:, :, bass.ds(k_at(i, b), HD)]).then_inc(s["staged"], 1)
                if bias:
                    pool.wait_ge(s["bias0_loaded"] if p == 0 else s["bias1_loaded"], i * 16 + (32 - 16 * p))
                    pool.tensor_tensor(bias["tiles"][p], bias["tiles"][p], bview(neg, 1, 2), ALU.add).then_inc(s["bias_ready"], 1)

            ahead(pool, n, stage)

        @block.tensor
        def _(pe):
            def turn(i, p):
                for b in range(qn):
                    for t in range(TT):
                        last = pe.transpose(m.ps[0:HD, 0, b * T + t * P:b * T + (t + 1) * P], qs[p][:, t, b * HD:(b + 1) * HD], ident)
                last.then_inc(s["q_turned"], 1)
                for b in range(2):
                    for t in range(TT):
                        last = pe.transpose(m.ps[0:HD, 1, b * T + t * P:b * T + (t + 1) * P], ks[p][:, b, t, :], ident)
                last.then_inc(s["k_turned"], 1)

            def first(i, p):
                later = not (isinstance(i, int) and i == 0)
                pe.wait_ge(s["q_moved"], i + 1)
                pe.wait_ge(s["k_moved"], i + 1)
                more = not (isinstance(i, int) and i == n - 1)
                if more:
                    pe.wait_ge(s["staged"], i * 3 + 6)
                if later:
                    pe.wait_ge(s["masked"], i)
                for b in range(2):
                    for t in range(TT):
                        last = pe.matmul(m.ps[:, 2 + b, t * T:(t + 1) * T], qT[:, b % qn, t * P:(t + 1) * P], kT[:, b, :],
                                         start=True, stop=True)
                last.then_inc(s["scores"], 1)
                if cmp:
                    if later:
                        pe.wait_ge(s["first_steps"], i * 3)
                    for t in range(TT):
                        last = pe.matmul(m.ps[:, 7, t * NCMP:(t + 1) * NCMP], qT[:, 0, t * P:(t + 1) * P],
                                         cmp["keys"], start=True, stop=True)
                    last.then_inc(s["cmp_scores"], 1)
                if more:
                    turn(i + 1, 1 - p)

            def second(i, p):
                for b in range(2):
                    pe.wait_ge(s["exp_out"], i * K + (2 * b + 2))
                    for k in range(2):
                        for t in range(TT):
                            last = pe.transpose(m.ps[:, 4 + b, k * T + t * P:k * T + (t + 1) * P],
                                                L[p][:, b, t, k * P:(k + 1) * P], ident)
                    last.then_inc(s["p0_turned"] if b == 0 else s["p1_turned"], 1)
                if cmp:
                    pe.wait_ge(s["exp_out"], i * K + 6)
                    if not (isinstance(i, int) and i == n - 1):
                        pe.wait_ge(s["first_steps"], i * 3 + 6)
                    for t in range(TT):
                        last = pe.transpose(m.ps[0:NCMP, 7, T + t * P:T + (t + 1) * P], cmp["scores"][p][:, t, :], ident)
                    last.then_inc(s["pc_turned"], 1)
                pe.wait_ge(s["p0_moved"], i + 1)
                pe.wait_ge(s["p1_moved"], i + 1)
                for b in range(2):
                    for t in range(TT):
                        parts = range(2) if neg is None or t else range(1)
                        for k in parts:
                            last = pe.matmul(m.ps[:, 6, (b * 2 + t) * HD:(b * 2 + t + 1) * HD], PT[:, b, k, t * P:(t + 1) * P],
                                             kv[:, k, bass.ds(v_at(i, b), HD)], start=(k == 0), stop=(k == parts[-1]))
                if cmp:
                    pe.wait_ge(s["pc_moved"], i + 1)
                    for t in range(TT):
                        last = pe.matmul(m.ps[:, 6, (4 + t) * HD:(5 + t) * HD], cmp["turned"][:, t * P:(t + 1) * P],
                                         cmp["values"], start=True, stop=True)
                last.then_inc(s["sums_ready"], 1)

            pe.wait_ge(s["staged"], 3)
            turn(0, 0)
            overlapped(pe, n, first, second)

        @block.vector
        def _(dve):
            def first(i, p):
                dve.wait_ge(s["q_turned"], i + 1)
                dve.tensor_copy(qT[:, 0:qn], m.ps[0:HD, 0, 0:qn * T].rearrange("p (b t) -> p b t", b=qn)).then_inc(s["q_moved"], 1)
                dve.wait_ge(s["scores"], i + 1)
                flat = L[p].rearrange("p b t s -> p b (t s)")
                sc = m.ps[:, 2:4, :]
                if bias:
                    dve.wait_ge(s["bias_ready"], i + 1)
                    ins = dve.scalar_tensor_tensor(flat, sc, scale, bias["tiles"][p].rearrange("p b t s -> p b (t s)"), ALU.mult, ALU.add)
                elif neg is not None:
                    ins = dve.scalar_tensor_tensor(flat, sc, scale, bview(neg.rearrange("p t s -> p (t s)"), 1, 2), ALU.mult, ALU.add)
                else:
                    ins = dve.tensor_scalar(flat, sc, scale, None, ALU.mult)
                ins.then_inc(s["masked"], 1)
                dve.wait_ge(s["masked"], i + 1)
                link = chain(dve, s["first_steps"], i * (3 if cmp else 1))
                link(dve.tensor_reduce(mx[p][:, 0:4], L[p].rearrange("p b t s -> p (b t) s"), AX, ALU.max))
                if cmp:
                    dve.wait_ge(s["cmp_scores"], i + 1)
                    link(dve.scalar_tensor_tensor(cmp["scores"][p], m.ps[:, 7, 0:2 * NCMP].rearrange("p (t s) -> p t s", t=TT), scale,
                                                  m.const("neg_cmp").rearrange("p (t s) -> p t s", t=TT), ALU.mult, ALU.add))
                    link(dve.tensor_reduce(mx[p][:, 4:6], cmp["scores"][p], AX, ALU.max))
                dve.tensor_scalar(mx[p][:, 0:K], mx[p][:, 0:K], -1.0, None, ALU.mult).then_inc(s["max_ready"], 1)

            def second(i, p):
                dve.wait_ge(s["p0_turned"], i + 1)
                dve.tensor_copy(PT[:, 0].rearrange("p s t -> p (s t)"), m.ps[:, 4, :]).then_inc(s["p0_moved"], 1)
                if cmp:
                    dve.wait_ge(s["pc_turned"], i + 1)
                    dve.tensor_copy(cmp["turned"], m.ps[0:NCMP, 7, T:2 * T]).then_inc(s["pc_moved"], 1)
                link = chain(dve, s["second_steps"], i * (10 if cmp else 1))
                dve.wait_ge(s["exp_out"], i * K + K)
                link(dve.reciprocal(sm[p][:, 0:K], sm[p][:, 0:K]))
                if cmp:
                    link(dve.tensor_tensor(sm[p][:, 4:6], sm[p][:, 4:6], m.const("row_cmp"), ALU.mult))
                    for b, branch in enumerate((1, 2, 0)):
                        link(dve.tensor_tensor(fac[p][:, b, :], sm[p][:, 2 * b:2 * b + 2], cmp["gate"](i, branch), ALU.mult))
                dve.wait_ge(s["sums_ready"], i + 1)
                for t in range(TT):
                    if cmp:
                        o = z[:, t, bass.ds(q_at(i), HD)]
                        for b in range(3):
                            part = m.ps[:, 6, (b * 2 + t) * HD:(b * 2 + t + 1) * HD]
                            if b == 0:
                                ins = dve.tensor_scalar(o, part, fac[p][:, b, t:t + 1], None, ALU.mult)
                            else:
                                ins = dve.scalar_tensor_tensor(o, part, fac[p][:, b, t:t + 1], o, ALU.mult, ALU.add)
                            if t == 0 or b < 2:
                                link(ins)
                    else:
                        for b in range(2):
                            ins = dve.tensor_scalar(z[:, t, bass.ds(q_at(i) + b * HD, HD)],
                                                    m.ps[:, 6, (b * 2 + t) * HD:(b * 2 + t + 1) * HD],
                                                    sm[p][:, 2 * b + t:2 * b + t + 1], None, ALU.mult)
                ins.then_inc(s["out_done"], 1)

            overlapped(dve, n, first, second)

        @block.scalar
        def _(act):
            def first(i, p):
                act.wait_ge(s["k_turned"], i + 1)
                act.copy(kT, m.ps[0:HD, 1, :].rearrange("p (b t) -> p b t", b=2)).then_inc(s["k_moved"], 1)
                act.wait_ge(s["max_ready"], i + 1)
                for b in range(2):
                    for t in range(TT):
                        j = 2 * b + t
                        act.activation(L[p][:, b, t, :], L[p][:, b, t, :], ACT.Exp, bias=mx[p][:, j:j + 1],
                                       accum_out=sm[p][:, j:j + 1]).then_inc(s["exp_out"], 1)
                if cmp:
                    for t in range(TT):
                        act.activation(cmp["scores"][p][:, t, :], cmp["scores"][p][:, t, :], ACT.Exp, bias=mx[p][:, 4 + t:5 + t],
                                       accum_out=sm[p][:, 4 + t:5 + t]).then_inc(s["exp_out"], 1)

            def second(i, p):
                act.wait_ge(s["p1_turned"], i + 1)
                act.copy(PT[:, 1].rearrange("p s t -> p (s t)"), m.ps[:, 5, :]).then_inc(s["p1_moved"], 1)

            overlapped(act, n, first, second)


def memory_attention(m, z, q0, kvm, staging):
    attention(m, 2, z, kvm, lambda i: i * (2 * HD) + q0, lambda i, b: i * (2 * HD) + b * HD,
              lambda i, b: i * (2 * HD) + (b + 4) * HD, HD ** -0.5, staging)


def compressed(m, z, a, keys, values, aT, blk):
    w = m.work
    w1 = w[0:HD, 0:4096].rearrange("p (k l e) -> p k l e", k=2, l=32)
    w2 = w[0:HD, 4224:4352].rearrange("p (k e) -> p k e", k=2)
    pe_rows = w[0:32, 4352:4416].rearrange("p (o d) -> p o d", o=1)
    pe2_rows = w[0:32, 4096:4160]
    peT = w[0:HD, 4160:4224].rearrange("p (k l) -> p k l", k=2)
    hid = m.small[0:HD, 288:348].rearrange("p (k n) -> p k n", k=2)
    ident = m.const("ident")
    with m.stage("compressed_0", "weights_loaded", "turned", "moved", "blocks_ready", "hidden", "silu_out", "made", "steps") as (block, s):
        @block.sync
        def _(sp):
            for k, kind in enumerate(("k", "v")):
                sp.dma_start(w1[:, k], a[f"l0_cmp_w1_{kind}_2"].rearrange("l d e -> d l e")).then_inc(s["weights_loaded"], 16)
                sp.dma_start(w2[:, k], a[f"l0_cmp_w2_{kind}_2"]).then_inc(s["weights_loaded"], 16)
            sp.dma_start(pe_rows[:, 0, :], a["l0_cmp_pe_k_2"]).then_inc(s["weights_loaded"], 16)
            sp.dma_start(pe2_rows, a["l0_cmp_pe_v_2"]).then_inc(s["weights_loaded"], 16)

        @block.tensor
        def _(pe):
            pe.wait_ge(s["weights_loaded"], 96)
            for k in range(2):
                for g in range(2):
                    for t in range(TT):
                        c = 512 + k * 128 + g * HD
                        last = pe.transpose(m.ps[0:HD, k, g * T + t * P:g * T + (t + 1) * P], z[:, t, c:c + HD], ident)
                last.then_inc(s["turned"], 1)
            for k, rows in enumerate((pe_rows[:, 0, :], pe2_rows)):
                last = pe.transpose(m.ps[0:HD, 2, k * 32:(k + 1) * 32], rows, ident[0:32, 0:32])
            last.then_inc(s["turned"], 1)
            for k in range(2):
                pe.wait_ge(s["blocks_ready"], k + 1)
                for l in range(32):
                    last = pe.matmul(m.ps[0:HD, 3 + k, 0:2 * NCMP], w1[:, k, l, :], blk[:, k, l], start=(l == 0), stop=(l == 31))
                last.then_inc(s["hidden"], 1)
            pe.wait_ge(s["silu_out"], 2)
            pe.matmul(m.ps[0:HD, 5, 0:2 * NCMP], w2[:, 0, :], hid[:, 0, :], start=True, stop=True).then_inc(s["made"], 1)
            for g in range(2):
                last = pe.matmul(m.ps[0:NCMP, 6, g * HD:(g + 1) * HD], hid[:, 1, g * NCMP:(g + 1) * NCMP], w2[:, 1, :],
                                 start=True, stop=True)
            last.then_inc(s["made"], 1)

        @block.vector
        def _(dve):
            link = chain(dve, s["steps"])
            dve.wait_ge(s["turned"], 3)
            for k in range(2):
                link(dve.tensor_copy(aT[:, k], m.ps[0:HD, k, :].rearrange("p (g t) -> p g t", g=2)))
            link(dve.tensor_copy(peT, m.ps[0:HD, 2, 0:64].rearrange("p (k l) -> p k l", k=2)))
            for k in range(2):
                for l in range(32):
                    last = dve.tensor_scalar(blk[:, k, l].rearrange("p (g n) -> p g n", g=2), aT[:, k, :, l:l + 16 * NCMP - 15:16],
                                             peT[:, k, l:l + 1], None, ALU.add)
                last.then_inc(s["blocks_ready"], 1)
            dve.wait_ge(s["made"], 2)
            link(dve.tensor_copy(keys, m.ps[0:HD, 5, 0:2 * NCMP]))
            link(dve.tensor_copy(values, m.ps[0:NCMP, 6, 0:2 * HD]))

        @block.scalar
        def _(act):
            for k in range(2):
                act.wait_ge(s["hidden"], k + 1)
                act.activation(hid[:, k, :], m.ps[0:HD, 3 + k, 0:2 * NCMP], ACT.Silu).then_inc(s["silu_out"], 1)


def even_layer(m, in_stream, out_stream, a, kvm, cos, sin):
    NIN = 4376
    ar = m.arena
    z = ar[:, 0:2 * NIN].rearrange("p (t n) -> p t n", t=TT)
    project(m, in_stream, NIN, lhs_x(m), z)
    rotated(m, z, [(0, 10), (768, 2), (1024, 2), (1816, 16)], cos, sin, HD // 2, m.work[:, 0:1024])
    keys = m.small[0:HD, 128:158]
    values = m.small[0:NCMP, 160:288]
    aT = ar[0:HD, 10672:11696].rearrange("p (k g t) -> p k g t", k=2, g=2)
    blk = ar[0:HD, 8752:10672].rearrange("p (k l n) -> p k l n", k=2, l=32)
    compressed(m, z, a, keys, values, aT, blk)
    gates = z[:, :, 1280:1304]
    gb = m.small[:, 0:24]
    with m.stage("even_layer_0", "bias_loaded", "added", "gates_ready") as (block, s):
        @block.sync
        def _(sp):
            sp.dma_start(gb, a["l0_nsa_gate_b_2"].partition_broadcast(P)).then_inc(s["bias_loaded"], 16)

        @block.vector
        def _(dve):
            dve.wait_ge(s["bias_loaded"], 16)
            dve.tensor_tensor(gates, gates, bview(gb, 1, TT), ALU.add).then_inc(s["added"], 1)

        @block.scalar
        def _(act):
            act.wait_ge(s["added"], 1)
            act.activation(gates, gates, ACT.Sigmoid).then_inc(s["gates_ready"], 1)

    neg = m.const("neg_causal").rearrange("p (t s) -> p t s", t=TT)
    staging = ar[:, 8752:9776]
    for g in range(2):
        cmp = dict(
            keys=keys[:, g * NCMP:(g + 1) * NCMP],
            values=values[:, g * HD:(g + 1) * HD],
            scores=[ar[:, 9776 + 32 * p:9806 + 32 * p].rearrange("p (t s) -> p t s", t=TT) for p in range(2)],
            turned=ar[0:NCMP, 9840:9840 + T],
            gate=lambda i, branch: z[:, :, bass.ds(i + (1280 + branch * 8 + g * 4), 1)].rearrange("p t o -> p (t o)"))
        attention(m, 4, z, z, lambda i: i * HD + g * 4 * HD, lambda i, b: 768 + b * 256 + g * HD,
                  lambda i, b: 896 + b * 256 + g * HD, HD ** -0.5, staging, neg=neg, cmp=cmp)
    attention(m, 4, z, z, lambda i: i * (2 * HD) + 1816, lambda i, b: i * (2 * HD) + (2328 + b * HD),
              lambda i, b: i * (2 * HD) + (2840 + b * HD), HD ** -0.5, staging, neg=neg)
    memory_attention(m, z, 3864, kvm, staging)
    gated(m, z, [(0, 1304, 512), (1816, 3352, 512), (3864, 4120, 256)], ACT.Silu)
    mixed_out(m, out_stream, z, [c * P for c in range(4)] + [1816 + c * P for c in range(4)] + [3864, 3992], 1.0, 1.0, split=False)


def odd_layer(m, in_stream, out_stream, kvm, cos, sin):
    H, QK, V = RET_HEADS, RET_QK, RET_V
    NIN = 6656
    z = m.arena[:, 0:2 * NIN].rearrange("p (t n) -> p t n", t=TT)
    project(m, in_stream, NIN, lhs_x(m), z)
    rotated(m, z, [(0, 4), (1024, 4)], cos, sin, QK // 2, m.work[:, 0:1024])
    memory_attention(m, z, 6144, kvm, m.work[:, 4096:5120])
    w = m.work
    qk = w[:, 0:1024].rearrange("p (k t n) -> p k t n", k=2, t=TT)
    qkT = w[:, 1024:2048].rearrange("p (k c t) -> p k c t", k=2, c=2)
    W = w[:, 2048:2560].rearrange("p (k t) -> p k t", k=2)
    a0 = m.layout["decay"][0]
    decays = m.consts[:, a0:a0 + H * 2 * P].rearrange("p (h n) -> p h n", h=H)
    decay = w[:, 2560:2816].rearrange("p (i t) -> p i t", i=2)
    stats, mv, rstd = m.small[:, 80:92], m.small[:, 92:96], m.small[:, 96:98]
    ident = m.const("ident")
    v0 = 2 * H * QK
    with m.nc.Fori(0, H) as h:
        with m.stage("odd_layer_0", "decay_loaded", "staged", "turned", "q_moved", "k_moved", "scores", "weights_ready", "out_ready", "steps",
                     "eps_added", "std_ready") as (block, s):
            @block.sync
            def _(sp):
                sp.dma_start(decay.rearrange("p i t -> p (i t)"),
                             decays[:, bass.ds(h, 1), :].rearrange("p o n -> p (o n)")).then_inc(s["decay_loaded"], 16)

            @block.vector
            def _(dve):
                link = chain(dve, s["steps"])
                dve.tensor_copy(qk[:, 0], z[:, :, bass.ds(h * QK, QK)]).then_inc(s["staged"], 1)
                dve.tensor_scalar(qk[:, 1], z[:, :, bass.ds(h * QK + H * QK, QK)], QK ** -0.5, None, ALU.mult).then_inc(s["staged"], 1)
                dve.wait_ge(s["turned"], 1)
                dve.tensor_copy(qkT[:, 0].rearrange("p c t -> p (c t)"), m.ps[:, 0, :]).then_inc(s["q_moved"], 1)
                dve.wait_ge(s["scores"], 1)
                dve.wait_ge(s["decay_loaded"], 16)
                sc = m.ps[:, 2, :].rearrange("p (k t) -> p k t", k=2)
                for k in range(2):
                    link(dve.tensor_tensor(W[:, k, k * P:(k + 1) * P], sc[:, k, k * P:(k + 1) * P], decay[:, 0, :], ALU.mult))
                dve.tensor_tensor(W[:, 0, P:T], sc[:, 0, P:T], decay[:, 1, :], ALU.mult).then_inc(s["weights_ready"], 1)
                dve.wait_ge(s["out_ready"], 2)
                added = [s["eps_added"], 0]
                for t in range(TT):
                    head_normed(dve, link, added, s["std_ready"], m.ps[:, 4 + t, :], z[:, t, bass.ds(h * V + v0, V)],
                                stats[:, 6 * t:6 * t + 6], mv[:, 2 * t:2 * t + 2], rstd[:, t:t + 1], 1e-6)

            @block.tensor
            def _(pe):
                pe.wait_ge(s["staged"], 2)
                for k in range(2):
                    for c in range(2):
                        for t in range(TT):
                            last = pe.transpose(m.ps[:, k, c * T + t * P:c * T + (t + 1) * P], qk[:, k, t, c * P:(c + 1) * P], ident)
                    last.then_inc(s["turned"], 1)
                pe.wait_ge(s["q_moved"], 1)
                pe.wait_ge(s["k_moved"], 1)
                for k in range(2):
                    for c in range(2):
                        last = pe.matmul(m.ps[:, 2, k * T:(k + 1) * T], qkT[:, 1, c, k * P:(k + 1) * P], qkT[:, 0, c, :],
                                         start=(c == 0), stop=(c == 1))
                last.then_inc(s["scores"], 1)
                pe.wait_ge(s["weights_ready"], 1)
                v = z[:, :, bass.ds(h * V + v0, V)]
                for t in range(TT):
                    for k in range(t + 1):
                        last = pe.matmul(m.ps[:, 4 + t, :], W[:, k, t * P:(t + 1) * P], v[:, k, :], start=(k == 0), stop=(k == t))
                    last.then_inc(s["out_ready"], 1)

            @block.scalar
            def _(act):
                act.wait_ge(s["turned"], 2)
                act.copy(qkT[:, 1].rearrange("p c t -> p (c t)"), m.ps[:, 1, :]).then_inc(s["k_moved"], 1)
                for t in range(TT):
                    act.wait_ge(s["eps_added"], t + 1)
                    act.activation(rstd[:, t:t + 1], rstd[:, t:t + 1], ACT.Sqrt).then_inc(s["std_ready"], 1)
        with m.stage("odd_layer_1") as (block, s):
            pass
    gated(m, z, [(v0, 4096, 2048), (6144, 6400, 256)], ACT.Silu)
    mixed_out(m, out_stream, z, [v0 + c * P for c in range(16)] + [6144, 6272], 1.0, 1.0, split=False)


def second_block(m, q, a):
    kvm0 = m.arena[:, 12288:13312].rearrange("p (t n) -> p t n", t=TT)
    kvm1 = m.work[:, 5120:6144].rearrange("p (t n) -> p t n", t=TT)
    acos, asin = (m.arena[:, 12160 + 64 * i:12224 + 64 * i].rearrange("p (t n) -> p t n", t=TT) for i in range(2))
    rcos, rsin = (m.keep[:, 256 * i:256 * i + 256].rearrange("p (t n) -> p t n", t=TT) for i in range(2))
    rotary_tables(m, a["positions_2"], [(acos, asin, m.const("attn_inv"), HD // 2), (rcos, rsin, m.const("ret_inv"), P)])
    mem = m.arena[:, 0:2 * D].rearrange("p (t n) -> p t n", t=TT)
    with m.stage("second_block_0", "memory_loaded") as (block, s):
        @block.sync
        def _(sp):
            sp.dma_start(mem, a["mem_2"][0].rearrange("(t p) n -> p t n", p=P)).then_inc(s["memory_loaded"], 16)
            sp.wait_ge(s["memory_loaded"], 16)
    rms_turned(m, mem, "mem_norm_g")
    project(m, next(q), 2 * 4 * HD, lhs_x(m), kvm0)
    project(m, next(q), 2 * 4 * HD, lhs_x(m), kvm1)
    rms_turned(m, m.x, "l0_norm_g")
    even_layer(m, next(q), next(q), a, kvm0, acos, asin)
    rms_turned(m, m.x, "l1_norm_g")
    odd_layer(m, next(q), next(q), kvm1, rcos, rsin)
    rms_normed(m, a["final_norm_g_2"])



def ffn(m, gu_stream, down_stream, norm):
    rms_turned(m, m.x, norm)
    hT = m.arena_r[:, 0:2 * FFC * T].rearrange("p (k c t) -> p k c t", k=2, c=FFC)
    sg = m.work[:, 0:2 * BANK].rearrange("p (j n) -> p j n", j=2)
    prod = m.work[:, 2 * BANK:3 * BANK].rearrange("p (f t) -> p f t", f=2)
    gs = gu_stream
    with m.stage("ffn", "high_ready", "low_ready", "halves_used", "gate_freed", "up_freed", "steps") as (block, s):
        @block.sync
        def _(sp):
            gs.load_rest(sp)
            follow(m, gs, sp, s)

        @block.tensor
        def _(pe):
            def unit(g, j):
                for k, freed in enumerate((s["gate_freed"], s["up_freed"])):
                    pe.wait_ge(freed, g * 2 + j + 1)
                    pe.wait_ge(s["low_ready"], (g * 2 + j) * 2 + k + 1)
                    for f in range(2):
                        for c in range(DC):
                            for i, (xp, wp) in enumerate(PASSES):
                                w = m.halves[:, k, wp, :].rearrange("p (c n) -> p c n", c=DC)
                                last = pe.matmul(m.ps[:, 2 * j + k, f * T:(f + 1) * T], w[:, c, f * P:(f + 1) * P],
                                                 m.xT_r[:, xp, c, :], start=(c == 0 and i == 0), stop=(c == DC - 1 and i == 2))
                    last.then_inc(s["halves_used"], 1)

            gs.each(pe, unit)

        def back(g, j):
            return (g, j - 1) if j else (g - 1, 1)

        @block.scalar
        def _(act):
            act.sem_inc(s["gate_freed"], 2)

            def silu(g, j):
                act.wait_ge(s["halves_used"], (g * 2 + j) * 2 + 1)
                act.wait_ge(s["up_freed"], g * 2 + j + 1)
                act.activation(sg[:, j, :], m.ps[:, 2 * j, :], ACT.Silu).then_inc(s["gate_freed"], 1)

            def unit(g, j):
                for k in range(2):
                    high_part(m, gs, act, s, g, j, k)
                if not (isinstance(g, int) and g == 0 and j == 0):
                    silu(*back(g, j))

            gs.each(act, unit, peel=True)
            silu((gs.n - 1) // 2, (gs.n - 1) % 2)

        @block.vector
        def _(dve):
            dve.sem_inc(s["up_freed"], 2)

            def hidden(g, j):
                u = g * 2 + j
                link = chain(dve, s["steps"], u * 3)
                dve.wait_ge(s["halves_used"], u * 2 + 2)
                dve.wait_ge(s["gate_freed"], u + 3)
                link(dve.tensor_tensor(prod, sg[:, j, :].rearrange("p (f t) -> p f t", f=2),
                                       m.ps[:, 2 * j + 1, :].rearrange("p (f t) -> p f t", f=2), ALU.mult))
                high = hT[:, 0, bass.ds(u * 2, 2), :]
                link(dve.tensor_copy(high, prod))
                link(dve.tensor_tensor(hT[:, 1, bass.ds(u * 2, 2), :], prod, high.bitcast(F32), ALU.subtract))
                dve.sem_inc(s["up_freed"], 1)

            def unit(g, j):
                for k in range(2):
                    low_part(m, gs, dve, s, g, j, k, last=False)
                if not (isinstance(g, int) and g == 0 and j == 0):
                    hidden(*back(g, j))

            gs.each(dve, unit, peel=True)
            hidden((gs.n - 1) // 2, (gs.n - 1) % 2)
    project_out(m, down_stream, FFC, lambda part, c, t: hT[:, part, c, t * P:(t + 1) * P], 1.0, 0.5)


def pool_conv(m, in_stream, out_stream, a):
    NIN = 3 * BANK
    C = 4
    ar, w = m.arena, m.work
    z = ar[:, 0:2 * NIN].rearrange("p (t n) -> p t n", t=TT)
    project(m, in_stream, NIN, lhs_x(m), z)
    uT = ar[:, 3072:6144].rearrange("p (c t) -> p c t", c=12)
    transposed(m, 12, lambda c, t: z[:, t, c * P:(c + 1) * P], lambda c: uT[:, c, :])
    yT = ar[:, 6144:8192].rearrange("p (c t) -> p c t", c=DC)
    dm = ar[:, 8192:9216].rearrange("p (c t) -> p c t", c=C)
    pw = ar[:, 9216:9728].rearrange("p (c d) -> p c d", c=C)
    PAD = CONV_K - 1
    zp = ar[:, 9728:9728 + C * (T + PAD)].rearrange("p (c t) -> p c t", c=C)
    acc = ar[:, 10880:11904].rearrange("p (c t) -> p c t", c=C)
    tn = ar[:, 0:1024].rearrange("p (t n) -> p t n", t=TT)
    cw_rows = ar[0:CONV_K, 1024:1536]
    cw = m.small[:, 100:100 + C * 32].rearrange("p (c k) -> p c k", c=C)
    scale, cb, lg, lb = (m.columns[k] for k in ("pool_scale", "conv_b", "conv_ln_g", "conv_ln_b"))
    OFF = 16
    lv = [w[:, k * C * (T + OFF):(k + 1) * C * (T + OFF)].rearrange("p (c t) -> p c t", c=C) for k in range(5)]
    stats, mv, rstd = m.small[:, 80:92], m.small[:, 92:96], m.small[:, 96:98]
    ident = m.const("ident")
    first = m.const("pool_count").rearrange("p (g t) -> p g t", g=C)
    with m.stage("pool_conv_0", "weights_loaded", "cw_turned", "means_ready", "pooled", "sig_out", "conv_done", "acc_turned", "eps_added",
                 "std_ready", "normed", "back_turned", "pool_out", "conv_out", "steps", "taps", "zeroed") as (block, s):
        @block.sync
        def _(sp):
            sp.dma_start(pw, a["pool_w_3"][0].rearrange("g c d -> c g d")).then_inc(s["weights_loaded"], 16)
            sp.dma_start(cw_rows, a["conv_w_3"][0]).then_inc(s["weights_loaded"], 16)

        @block.gpsimd
        def _(pool):
            pool.memset(zp[:, :, 0:PAD], 0.0).then_inc(s["zeroed"], 1)
            for k in range(5):
                pool.memset(lv[k][:, :, 0:OFF], 0.0).then_inc(s["zeroed"], 1)

        @block.vector
        def _(dve):
            link = chain(dve, s["steps"])
            dve.wait_ge(s["zeroed"], 6)
            dve.wait_ge(s["cw_turned"], 1)
            link(dve.tensor_copy(cw[:, :, 0:CONV_K], m.ps[:, 0, 0:C * 32].rearrange("p (c k) -> p c k", c=C)[:, :, 0:CONV_K]))
            link(dve.tensor_copy(lv[0][:, :, OFF:], uT[:, 0:C, :]))
            for k in range(4):
                src, dst = lv[k][:, k if k else 0:, :], lv[k + 1][:, k if k else 0:, :]
                sh = 1 << k
                link(dve.tensor_tensor(dst[:, :, OFF:], src[:, :, OFF:], src[:, :, OFF - sh:OFF - sh + T], ALU.add))
            for g in range(C):
                sums = lv[g + 1][:, g, OFF:]
                link(dve.tensor_tensor(dm[:, g, 0:16], sums[:, 0:16], first[:, g, :], ALU.mult))
                link(dve.tensor_scalar(dm[:, g, 16:], sums[:, 16:], 1.0 / (2 << g), None, ALU.mult))
            dve.tensor_tensor(dm, dm, uT[:, 0:C, :], ALU.subtract).then_inc(s["means_ready"], 1)
            dve.wait_ge(s["sig_out"], 1)
            link(dve.tensor_tensor(zp[:, :, PAD:], uT[:, C:2 * C, :], uT[:, 2 * C:3 * C, :], ALU.mult))
            for k in range(CONV_K):
                for c in range(C):
                    if k == 0:
                        dve.tensor_scalar(acc[:, c, :], zp[:, c, 0:T], cw[:, c, 0:1], cb[:, c:c + 1], ALU.mult,
                                          ALU.add).then_inc(s["taps"], 1)
                    else:
                        dve.wait_ge(s["taps"], (k - 1) * C + c + 1)
                        dve.scalar_tensor_tensor(acc[:, c, :], zp[:, c, k:k + T], cw[:, c, k:k + 1], acc[:, c, :],
                                                 ALU.mult, ALU.add).then_inc(s["taps"], 1)
            added = [s["eps_added"], 0]
            dve.wait_ge(s["acc_turned"], 1)
            for t in range(TT):
                head_normed(dve, link, added, s["std_ready"], m.ps[:, 4 + t, :], tn[:, t, :], stats[:, 6 * t:6 * t + 6],
                            mv[:, 2 * t:2 * t + 2], rstd[:, t:t + 1], 1e-6)
            dve.sem_inc(s["normed"], 1)
            dve.wait_ge(s["pooled"], 1)
            for g in range(C):
                dve.tensor_scalar(yT[:, g, :], m.ps[:, g // 2, (g % 2) * T:(g % 2 + 1) * T], scale[:, g:g + 1], None,
                                  ALU.mult).then_inc(s["pool_out"], 1)

        @block.tensor
        def _(pe):
            pe.wait_ge(s["weights_loaded"], 32)
            for c in range(C):
                last = pe.transpose(m.ps[:, 0, c * 32:c * 32 + CONV_K], cw_rows[:, c * P:(c + 1) * P], ident[0:CONV_K, 0:CONV_K])
            last.then_inc(s["cw_turned"], 1)
            pe.wait_ge(s["means_ready"], 1)
            for g in range(C):
                last = pe.matmul(m.ps[:, g // 2, (g % 2) * T:(g % 2 + 1) * T], pw[:, g, :], dm[:, g, :], start=True, stop=True)
            last.then_inc(s["pooled"], 1)
            pe.wait_ge(s["taps"], CONV_K * C)
            for t in range(TT):
                for c in range(C):
                    last = pe.transpose(m.ps[:, 4 + t, c * P:(c + 1) * P], acc[:, c, t * P:(t + 1) * P], ident)
            last.then_inc(s["acc_turned"], 1)
            pe.wait_ge(s["normed"], 1)
            for c in range(C):
                for t in range(TT):
                    last = pe.transpose(m.ps[:, 6 + c // 2, (c % 2) * T + t * P:(c % 2) * T + (t + 1) * P],
                                        tn[:, t, c * P:(c + 1) * P], ident)
            last.then_inc(s["back_turned"], 1)

        @block.scalar
        def _(act):
            act.activation(uT[:, 2 * C:3 * C, :], uT[:, 2 * C:3 * C, :], ACT.Sigmoid).then_inc(s["sig_out"], 1)
            for t in range(TT):
                act.wait_ge(s["eps_added"], t + 1)
                act.activation(rstd[:, t:t + 1], rstd[:, t:t + 1], ACT.Sqrt).then_inc(s["std_ready"], 1)
            act.wait_ge(s["back_turned"], 1)
            for c in range(C):
                act.activation(yT[:, C + c, :], m.ps[:, 6 + c // 2, (c % 2) * T:(c % 2 + 1) * T], ACT.Silu,
                               bias=lb[:, c:c + 1], scale=lg[:, c:c + 1]).then_inc(s["conv_out"], 1)
    yT_r = m.arena_r[:, 0:4096].rearrange("p (k c t) -> p k c t", k=2, c=DC)
    with m.stage("pool_conv_parts", "high_ready", "low_ready") as (block, s):
        @block.scalar
        def _(act):
            for c in range(0, DC, 2):
                act.copy(yT_r[:, 0, c:c + 2, :], yT[:, c:c + 2, :]).then_inc(s["high_ready"], 1)

        @block.vector
        def _(dve):
            for c in range(0, DC, 2):
                dve.wait_ge(s["high_ready"], c // 2 + 1)
                dve.tensor_tensor(yT_r[:, 1, c:c + 2, :], yT[:, c:c + 2, :], yT_r[:, 0, c:c + 2, :].bitcast(F32),
                                  ALU.subtract).then_inc(s["low_ready"], 1)
    project_out(m, out_stream, DC, lambda part, c, t: yT_r[:, part, c, t * P:(t + 1) * P], 1.0, 1.0)


HEADS = 16
IDX_HEADS, IDX_DIM = 8, 64


def expand_bias(m, a, rows, tiles):
    rb = m.small[0:32, 0:HEADS]
    line = m.work[0:HEADS, 0:2 * T]
    bucket = m.work[0:32, 1024:1024 + T]
    with m.stage("expand_bias_0", "loaded", "spread", "ready", "stored", "zeroed") as (block, s):
        @block.sync
        def _(sp):
            a0 = m.layout["dist_bucket"][0]
            sp.dma_start(rb, a["rel_bias_3"]).then_inc(s["loaded"], 16)
            sp.dma_start(bucket, m.consts[0:32, a0:a0 + T]).then_inc(s["loaded"], 16)
            sp.wait_ge(s["ready"], 1)
            sp.dma_start(rows, line).then_inc(s["stored"], 16)
            sp.wait_ge(s["stored"], 16)
            for t in range(TT):
                src = bass.AP(rows.tensor, T - 1 - t * P, [[2 * T, HEADS], [-1, P], [1, T]])
                sp.dma_start(tiles[:, t], src).then_inc(m.bias_stored, 16)

        @block.tensor
        def _(pe):
            pe.wait_ge(s["loaded"], 32)
            pe.matmul(m.ps[0:HEADS, 0, 0:T], rb, bucket, start=True, stop=True).then_inc(s["spread"], 1)

        @block.vector
        def _(dve):
            dve.memset(line[:, T:], 0.0).then_inc(s["zeroed"], 1)
            dve.wait_ge(s["spread"], 1)
            dve.wait_ge(s["zeroed"], 1)
            dve.tensor_copy(line[:, 0:T], m.ps[0:HEADS, 0, 0:T]).then_inc(s["ready"], 1)


def selected_attention(m, in_stream, out_stream, tiles):
    NIN = 3 * D + IDX_HEADS * IDX_DIM + IDX_DIM + IDX_HEADS
    ar, w = m.arena, m.work
    z = ar[:, 0:2 * NIN].rearrange("p (t n) -> p t n", t=TT)
    project(m, in_stream, NIN, lhs_x(m), z)
    qi0, ki0, wi0 = 3 * D, 3 * D + IDX_HEADS * IDX_DIM, 3 * D + IDX_HEADS * IDX_DIM + IDX_DIM
    score = ar[:, 7312:7824].rearrange("p (t s) -> p t s", t=TT)
    neg = ar[:, 7824:8336].rearrange("p (t s) -> p t s", t=TT)
    kiT = ar[0:IDX_DIM, 8336:8592]
    causal = m.const("neg_causal").rearrange("p (t s) -> p t s", t=TT)
    ident = m.const("ident")
    with m.stage("selected_attention_0", "turned", "steps") as (block, s):
        @block.tensor
        def _(pe):
            for t in range(TT):
                last = pe.transpose(m.ps[0:IDX_DIM, 0, t * P:(t + 1) * P], z[:, t, ki0:ki0 + IDX_DIM], ident)
            last.then_inc(s["turned"], 1)

        @block.vector
        def _(dve):
            dve.memset(score, 0.0).then_inc(s["steps"], 1)
            dve.wait_ge(s["turned"], 1)
            dve.tensor_copy(kiT, m.ps[0:IDX_DIM, 0, 0:T]).then_inc(s["steps"], 1)

    qs = w[:, 0:256].rearrange("p (t n) -> p t n", t=TT)
    qT = w[0:IDX_DIM, 256:768].rearrange("p (b t) -> p b t", b=2)
    R = w[:, 768:1792].rearrange("p (b t s) -> p b t s", b=2, t=TT)
    wi = m.small[:, 0:4].rearrange("p (t b) -> p t b", t=TT)
    with m.nc.Fori(0, IDX_HEADS // 2) as i:
        with m.stage("selected_attention_1", "staged", "turned", "moved", "scores", "relu_out", "steps") as (block, s):
            @block.vector
            def _(dve):
                link = chain(dve, s["steps"])
                dve.tensor_copy(qs, z[:, :, bass.ds(i * (2 * IDX_DIM) + qi0, 2 * IDX_DIM)]).then_inc(s["staged"], 1)
                link(dve.tensor_copy(wi, z[:, :, bass.ds(i * 2 + wi0, 2)]))
                dve.wait_ge(s["turned"], 1)
                dve.tensor_copy(qT, m.ps[0:IDX_DIM, 0, :].rearrange("p (b t) -> p b t", b=2)).then_inc(s["moved"], 1)
                for b in range(2):
                    dve.wait_ge(s["relu_out"], b + 1)
                    for t in range(TT):
                        link(dve.scalar_tensor_tensor(score[:, t, :], R[:, b, t, :], wi[:, t, b:b + 1], score[:, t, :],
                                                      ALU.mult, ALU.add))

            @block.tensor
            def _(pe):
                pe.wait_ge(s["staged"], 1)
                for b in range(2):
                    for t in range(TT):
                        last = pe.transpose(m.ps[0:IDX_DIM, 0, b * T + t * P:b * T + (t + 1) * P],
                                            qs[:, t, b * IDX_DIM:(b + 1) * IDX_DIM], ident)
                last.then_inc(s["turned"], 1)
                pe.wait_ge(s["moved"], 1)
                for b in range(2):
                    for t in range(TT):
                        last = pe.matmul(m.ps[:, 1 + b, t * T:(t + 1) * T], qT[:, b, t * P:(t + 1) * P], kiT, start=True, stop=True)
                    last.then_inc(s["scores"], 1)

            @block.scalar
            def _(act):
                for b in range(2):
                    act.wait_ge(s["scores"], b + 1)
                    act.activation(R[:, b].rearrange("p t s -> p (t s)"), m.ps[:, 1 + b, :], ACT.Relu).then_inc(s["relu_out"], 1)
        with m.stage("selected_attention_2") as (block, s):
            pass

    top = m.small[:, 8:24].rearrange("p (t k) -> p t k", t=TT)
    STRUCK = -3e38
    with m.stage("selected_attention_3", "steps") as (block, s):
        @block.vector
        def _(dve):
            link = chain(dve, s["steps"])
            link(dve.tensor_scalar(score, score, (IDX_HEADS * IDX_DIM) ** -0.5, None, ALU.mult))
            link(dve.tensor_tensor(score, score, causal, ALU.add))
            for _ in range(TOPK // 8):
                for t in range(TT):
                    link(dve.max(top[:, t, :], score[:, t, :]))
                    link(dve.match_replace(score[:, t, :], top[:, t, :], score[:, t, :], STRUCK))
            link(dve.tensor_scalar(neg, score, STRUCK / 2, NEG, ALU.is_gt, ALU.mult))
            link(dve.tensor_tensor(neg, neg, causal, ALU.add))

        @block.sync
        def _(sp):
            sp.wait_ge(m.bias_stored, 32)
    bias = dict(tiles=[ar[:, 8592 + 1024 * p:9616 + 1024 * p].rearrange("p (b t s) -> p b t s", b=2, t=TT) for p in range(2)],
                source=lambda i, b: tiles[bass.ds(i * 2 + b, 1)].rearrange("o t p s -> (o p) t s"))
    attention(m, HEADS // 2, z, z, lambda i: i * (2 * HD), lambda i, b: i * (2 * HD) + (D + b * HD),
              lambda i, b: i * (2 * HD) + (2 * D + b * HD), HD ** -0.5, w[:, 4096:5120], neg=neg, bias=bias)
    mixed_out(m, out_stream, z, [c * P for c in range(DC)], 1.0, 1.0)


def third_block(m, q, a, rows, tiles):
    expand_bias(m, a, rows, tiles)
    for layer in range(DEPTH):
        ffn(m, next(q), next(q), f"ffn1_norm_{layer}")
        rms_turned(m, m.x, f"mix_norm_{layer}")
        if layer == 0:
            pool_conv(m, next(q), next(q), a)
        else:
            selected_attention(m, next(q), next(q), tiles)
        ffn(m, next(q), next(q), f"ffn2_norm_{layer}")
    rms_normed(m, a["final_norm_3"])


USED = ["x", "mlstm_w_in", "mlstm_gate_b", "mlstm_norm_g", "mlstm_w_out", "gla_w_in", "gla_gate_w", "gla_gate_b",
        "gla_norm_g", "gla_w_out", "moe_router", "moe_w_gate", "moe_w_up", "moe_w_down", "ln_g", "ln_b",
        "mem_2", "positions_2", "l0_norm_g_2", "l0_w_in_2", "l0_nsa_gate_b_2", "l0_cmp_pe_k_2", "l0_cmp_w1_k_2",
        "l0_cmp_w2_k_2", "l0_cmp_pe_v_2", "l0_cmp_w1_v_2", "l0_cmp_w2_v_2", "l0_w_mem_kv_2", "l0_w_out_2", "l1_norm_g_2",
        "l1_w_in_2", "l1_w_mem_kv_2", "l1_w_out_2", "mem_norm_g_2", "final_norm_g_2",
        "ffn1_norm_3", "ffn1_w_gate_3", "ffn1_w_up_3", "ffn1_w_down_3", "mix_norm_3", "ffn2_norm_3", "ffn2_w_gate_3",
        "ffn2_w_up_3", "ffn2_w_down_3", "ab_w_in_3", "pool_w_3", "pool_scale_3", "conv_w_3", "conv_b_3", "conv_ln_g_3",
        "conv_ln_b_3", "ab_w_out_3", "c_w_in_3", "c_w_out_3", "rel_bias_3", "final_norm_3"]


def columns(a):
    out = [("mlstm_norm_g", a["mlstm_norm_g"][0]), ("gla_gate_b", a["gla_gate_b"][0].rearrange("d n -> (d n)")),
           ("gla_norm_g", a["gla_norm_g"][0]), ("mem_norm_g", a["mem_norm_g_2"]), ("l0_norm_g", a["l0_norm_g_2"]),
           ("l1_norm_g", a["l1_norm_g_2"])]
    out += [(f"{k}_{layer}", a[f"{k}_3"][layer]) for k in ("ffn1_norm", "mix_norm", "ffn2_norm") for layer in range(DEPTH)]
    return out + [(k, a[f"{k}_3"][0]) for k in ("pool_scale", "conv_b", "conv_ln_g", "conv_ln_b")]


def streams(m, a):
    columns_stream(m, a["mlstm_w_in"][0], 3088, 0)
    rows_stream(m, a["mlstm_w_out"][0], D, 2)
    expert_stream(m, a["moe_w_gate"][0], a["moe_w_up"][0], a["moe_w_down"][0], 0)
    columns_stream(m, a["gla_w_in"][0], 3104, 0)
    rows_stream(m, a["gla_w_out"][0], D, 2)
    expert_stream(m, a["moe_w_gate"][1], a["moe_w_up"][1], a["moe_w_down"][1], 0)
    columns_stream(m, a["l0_w_mem_kv_2"], 512, 0)
    columns_stream(m, a["l1_w_mem_kv_2"], 512, 2)
    columns_stream(m, a["l0_w_in_2"], 4376, 0)
    rows_stream(m, a["l0_w_out_2"], 1280, 2, False)
    columns_stream(m, a["l1_w_in_2"], 6656, 0)
    rows_stream(m, a["l1_w_out_2"], 2304, 2, False)
    for layer, (w_in, n, w_out) in enumerate((("ab_w_in_3", 1536, "ab_w_out_3"), ("c_w_in_3", 3656, "c_w_out_3"))):
        ffn_stream(m, a["ffn1_w_gate_3"][layer], a["ffn1_w_up_3"][layer], 0)
        rows_stream(m, a["ffn1_w_down_3"][layer], D_FF, 2)
        columns_stream(m, a[w_in][0], n, 0)
        rows_stream(m, a[w_out][0], D, 2)
        ffn_stream(m, a["ffn2_w_gate_3"][layer], a["ffn2_w_up_3"][layer], 0)
        rows_stream(m, a["ffn2_w_down_3"][layer], D_FF, 2)


def layers(m, a, rows, tiles):
    q = iter(m.queue)
    turn_x(m)
    mlstm(m, next(q), next(q), a["mlstm_gate_b"][0], (a["ln_g"][0, 0], a["ln_b"][0, 0], a["moe_router"][0]))
    layer_normed(m)
    turn_x(m, split=False)
    moe(m, next(q), (a["ln_g"][0, 1], a["ln_b"][0, 1]))
    layer_normed(m)
    turn_x(m)
    gla(m, next(q), next(q), a["gla_gate_w"][0], (a["ln_g"][1, 0], a["ln_b"][1, 0], a["moe_router"][1]))
    layer_normed(m)
    turn_x(m, split=False)
    moe(m, next(q), (a["ln_g"][1, 1], a["ln_b"][1, 1]))
    layer_normed(m)
    second_block(m, q, a)
    third_block(m, q, a, rows, tiles)


def program(nc, a, consts, out, rows, tiles):
    with ExitStack() as ctx:
        m = Machine(nc, ctx, consts)
        streams(m, a)
        with m.stage("program_0", "inputs_loaded") as (block, s):
            @block.scalar
            def _(act):
                for name, vec in columns(a):
                    m.load_columns(act, name, vec)

            @block.sync
            def _(sp):
                sp.dma_start(m.x[:, :, :], a["x"][0].rearrange("(t p) n -> p t n", p=P)).then_inc(s["inputs_loaded"], 16)
                sp.dma_start(m.cst[:, :], consts[:, 0:m.cst.shape[1]]).then_inc(s["inputs_loaded"], 16)
                m.queue[0].prefetch(sp)
                sp.wait_ge(s["inputs_loaded"], 32)
        layers(m, a, rows, tiles)
        with m.stage("program_1", "stored") as (block, s):
            @block.sync
            def _(sp):
                sp.dma_start(out[0].rearrange("(t p) n -> p t n", p=P), m.x[:, :, :]).then_inc(s["stored"], 16)
                sp.wait_ge(s["stored"], 16)



def kernel(**inputs):
    import numpy as _np
    import concourse.bacc as _bacc
    from concourse import mybir as _mybir
    from concourse.bass_utils import run_bass_kernel_spmd as _run

    nc = _bacc.Bacc("TRN2", target_bir_lowering=False, num_devices=1)
    arrays, aps = {}, {}
    for name in USED:
        a = _np.ascontiguousarray(inputs[name])
        arrays[f"in_{name}"] = a
        aps[name] = nc.dram_tensor(f"in_{name}", a.shape, _mybir.dt.from_np(a.dtype), kind="ExternalInput").ap()
    table = const_table()
    arrays["constants_dram"] = table
    consts = nc.dram_tensor("constants_dram", table.shape, F32, kind="ExternalInput").ap()
    out = nc.dram_tensor("out_dram", (1, T, D), F32, kind="ExternalOutput").ap()
    rows = nc.dram_tensor("bias_rows", (HEADS, 2 * T), F32, kind="Internal").ap()
    tiles = nc.dram_tensor("bias_tiles", (HEADS, TT, P, T), F32, kind="Internal").ap()
    program(nc, aps, consts, out, rows, tiles)
    r = _run(nc, [arrays], core_ids=[0])
    return r.results[0]["out_dram"]
```

```python
import math
from contextlib import ExitStack, contextmanager

import numpy as np
import concourse.bass as bass
from concourse import mybir

F32 = mybir.dt.float32
F32R = mybir.dt.float32r
I32 = mybir.dt.int32
ALU = mybir.AluOpType
ACT = mybir.ActivationFunctionType
AX = mybir.AxisListType.X

P = 128
T = 256
TT = T // P
D = 1024
DC = D // P
BANK = 512
SLOTS = 6
SLOT = 4096
NEG = -1e30
DEPTH = 2
ALPHA = (2 * DEPTH) ** 0.25
SET = 30

ML_HEADS, ML_DK, ML_DV = 4, 128, 256
GLA_RANK, GLA_TAU = 16, 16.0
E, CAP, FF = 16, 2 * T // 16, 1024
QUADS = E * CAP // P
EQ = P // CAP
HD = 64
NCMP = (T - 32) // 16 + 1
RET_HEADS, RET_QK, RET_V = 4, 256, 512
D_FF = 2816
FFC = D_FF // P
CONV_K = 31
TOPK = T // 4

ARENA = 6656 * TT
WORK = 6144


def const_layout():
    at, cols = {}, 0
    for name, n in (("ident", P), ("ones", P), ("keep_fwd", P), ("keep_bwd", P), ("neg_fwd", 2 * T), ("neg_bwd", 2 * T),
                    ("neg_causal", 2 * T), ("neg_cmp", 2 * NCMP), ("row_cmp", 2), ("ret_inv", P), ("attn_inv", 32),
                    ("slot_no", CAP), ("pool_count", 4 * 16),
                    ("decay", RET_HEADS * 2 * P), ("dist_bucket", T)):
        at[name] = (cols, n)
        cols += n
    return at, cols


def const_table():
    at, cols = const_layout()
    out = np.zeros((P, cols), np.float32)

    def put(name, value):
        value = np.asarray(value, np.float32)
        a, n = at[name]
        out[:value.shape[0], a:a + n] = value.reshape(value.shape[0], n)

    p = np.arange(P)
    t = np.arange(T)
    put("ident", np.eye(P))
    put("ones", np.ones((P, P)))
    put("keep_fwd", p[:, None] <= p[None, :])
    put("keep_bwd", p[:, None] >= p[None, :])
    s = p[:, None, None] + P * np.arange(TT)[None, :, None]
    put("neg_fwd", np.where(s <= t, 0.0, NEG))
    put("neg_bwd", np.where(s >= t, 0.0, NEG))
    put("neg_causal", np.where(t[None, None, :] <= s, 0.0, NEG))
    end = np.arange(NCMP) * 16 + 31
    put("neg_cmp", np.where(end[None, None, :] <= s, 0.0, NEG))
    put("row_cmp", s[:, :, 0] >= end[0])
    f = np.float32
    put("ret_inv", np.tile(f(1.0) / (f(10000.0) ** np.linspace(0.0, 1.0, P).astype(f)), (P, 1)))
    put("attn_inv", np.tile(f(1.0) / (f(10000.0) ** (np.arange(0, HD, 2, dtype=f) / f(HD))), (P, 1)))
    lg = np.log(1.0 - 2.0 ** (-5.0 - np.arange(RET_HEADS)))
    diff = p[None, :] - p[:, None]
    put("decay", np.stack([np.stack([np.where(diff >= 0, np.exp(np.maximum(diff, 0) * g), 0.0),
                                     np.exp((diff + P) * g)]) for g in lg]).transpose(2, 0, 1, 3))
    put("slot_no", np.tile(np.arange(CAP) + 1.0, (P, 1)))
    tt = np.arange(16)
    put("pool_count", np.tile(np.stack([1.0 / np.minimum(tt + 1, w) for w in (2, 4, 8, 16)]).reshape(1, -1), (P, 1)))
    dist = T - 1 - t
    d = np.maximum(dist, 16).astype(f)
    large = 16 + (np.log(d / f(16)) / f(math.log(128 / 16)) * f(16)).astype(np.int32)
    bucket = np.where(dist < 16, dist, np.minimum(large, 31))
    put("dist_bucket", np.arange(32)[:, None] == bucket[None, :])
    return out


class Machine:

    def __init__(self, nc, ctx, consts):
        self.nc = nc
        self.ctx = ctx
        self.consts = consts
        self.layout, cols = const_layout()
        cols = self.layout["decay"][0]
        plan = [("weight_ring", SLOTS * SLOT), ("arena", ARENA), ("work", WORK), ("xT", 2 * DC * T), ("x", TT * D),
                ("constants", cols), ("small", 640), ("small_integers", 2)]
        total = sum(-(-n // 8) * 8 for _, n in plan)
        self.slab = ctx.enter_context(nc.sbuf_tensor("slab", [P, total], F32))
        at, self.at = nc.sbuf_base - 4 * total, {}
        for name, n in plan:
            self.at[name] = at
            at += 4 * (-(-n // 8) * 8)
        self.ring = self.place("weight_ring", [P, SLOTS, SLOT])
        self.halves = self.place("weight_halves", [P, 2, 2, SLOT // 2], F32R, self.at["weight_ring"] + 4 * 4 * SLOT)
        self.arena = self.place("arena", [P, ARENA])
        self.arena_r = self.place("arena_halves", [P, ARENA], F32R, self.at["arena"])
        self.work = self.place("work", [P, WORK])
        self.work_r = self.place("work_halves", [P, WORK], F32R, self.at["work"])
        self.xT = self.place("xT", [P, DC, T])
        self.xT_r = self.place("xT_halves", [P, 2, DC, T], F32R, self.at["xT"])
        self.x = self.place("x", [P, TT, D])
        self.cst = self.place("constants", [P, cols])
        self.small = self.place("small", [P, 640])
        self.small_i = self.place("small_integers", [P, 2], I32)
        self.keep = self.work[:, 4608:5120]
        self.ps = ctx.enter_context(nc.psum_tensor("accumulators", [P, 8, BANK], F32))
        self.sets = [[ctx.enter_context(nc.semaphore(f"set{k}_{i}")) for i in range(SET)] for k in range(2)]
        self.turn = 0
        self.stages = 0
        self.slot_loaded = [ctx.enter_context(nc.semaphore(f"slot{i}_loaded")) for i in range(SLOTS)]
        self.unit_used = ctx.enter_context(nc.semaphore("unit_used"))
        self.loads = [0] * SLOTS
        self.last_unit = [0] * SLOTS
        self.units = 0
        self.queue = []
        self.bias_stored = ctx.enter_context(nc.semaphore("bias_stored"))
        self.norm_rows = self.work[:, 4096:6144].rearrange("p (k n) -> p k n", k=2)
        self.norm_loaded = ctx.enter_context(nc.semaphore("norm_loaded"))
        self.norms = 0
        self.router = self.small[:, 228:228 + DC * E].rearrange("p (c e) -> p c e", c=DC)
        self.router_loaded = ctx.enter_context(nc.semaphore("router_loaded"))
        self.routers = 0
        self.compressor_loaded = ctx.enter_context(nc.semaphore("compressor_loaded"))
        self.columns_loaded = ctx.enter_context(nc.semaphore("columns_loaded"))
        self.columns, self.column_end = {}, 480

    def place(self, name, shape, dt=F32, offset=None):
        return self.nc.alloc_sbuf_tensor_at(name, shape, dt, offset=self.at[name] if offset is None else offset)

    def const(self, name, shape=None, rows=P):
        a, n = self.layout[name]
        v = self.cst[0:rows, a:a + n]
        return v

    def load_columns(self, eng, name, vec):
        n = vec.shape[0] // P
        a = self.column_end
        self.column_end += n
        assert self.column_end <= 640
        self.columns[name] = self.small[:, a:a + n]
        with self.nc.allow_non_contiguous_dma("one value a partition"):
            eng.dma_start(self.columns[name], vec.rearrange("(c p) -> p c", p=P)).then_inc(self.columns_loaded, 16)

    def load_norm(self, sp, norm):
        if norm is not None:
            for k in range(2):
                sp.dma_start(self.norm_rows[:, k, :], norm[k].partition_broadcast(P)).then_inc(self.norm_loaded, 16)
            self.norms += 1
            if len(norm) > 2:
                sp.dma_start(self.router, norm[2].rearrange("(c p) e -> p c e", p=P)).then_inc(self.router_loaded, 16)
                self.routers += 1

    @contextmanager
    def stage(self, title, *names):
        mine, other = self.sets[self.turn], self.sets[1 - self.turn]
        self.turn = 1 - self.turn
        assert len(names) <= SET
        self.stages += 1
        with self.nc.Block(f"{title}_s{self.stages}", no_gpsimd_drain=True) as block:
            @block.gpsimd
            def _(pool):
                pool.sem_clear(range(other[0].num, other[-1].num + 1))

            yield block, {n: mine[i] for i, n in enumerate(names)}


class Stream:

    def __init__(self, m, units, full, depth, first, group, parts, split=False):
        self.m, self.n, self.depth, self.group, self.parts = m, units, depth, group, parts
        self.groups = full // group if full // group >= 2 else 0
        self.base = m.units
        m.units += units
        self.slots = [(first + r) % SLOTS for r in range(depth)]
        self.load_base = [m.loads[s] for s in self.slots]
        self.free_at = [m.last_unit[s] for s in self.slots]
        self.inc = 16 * len(parts(0, 0, m.ring[:, 0, :]))
        for u in range(units):
            s = self.slots[u % depth]
            m.loads[s] += self.inc
            m.last_unit[s] = self.base + u + 1
        if split:
            m.last_unit[4] = m.last_unit[5] = self.base + units
        m.queue.append(self)

    def slot(self, j):
        return self.m.ring[:, self.slots[j % self.depth], :]

    def load(self, sp, g, j):
        for dst, src in self.parts(g, j, self.slot(j)):
            sp.dma_start(dst, src).then_inc(self.m.slot_loaded[self.slots[j % self.depth]], 16)

    def prefetch(self, sp):
        for j in range(min(self.depth, self.n)):
            if self.free_at[j] > 0:
                sp.wait_ge(self.m.unit_used, self.free_at[j])
            self.load(sp, 0, j)

    def load_rest(self, sp):
        def one(g, j):
            sp.wait_ge(self.m.unit_used, self.base + 1 + g * self.group + (j - self.depth))
            self.load(sp, g, j)

        first = min(self.group, self.n) if self.groups else 0
        for j in range(self.depth, first):
            one(0, j)
        if self.groups:
            with sp.Fori(1, self.groups) as g:
                for j in range(self.group):
                    one(g, j)
        for u in range(max(self.depth, self.groups * self.group), self.n):
            one(u // self.group, u % self.group)

    def each(self, eng, body, peel=False):
        first = 1 if peel and self.groups else 0
        for j in range(self.group * first):
            body(0, j)
        if self.groups:
            with eng.Fori(first, self.groups) as g:
                for j in range(self.group):
                    body(g, j)
        for u in range(self.groups * self.group, self.n):
            body(u // self.group, u % self.group)

    def wait_loaded(self, eng, g, j):
        turn = g * (self.group // self.depth) + (j // self.depth + 1)
        eng.wait_ge(self.m.slot_loaded[self.slots[j % self.depth]], self.load_base[j % self.depth] + self.inc * turn)

    def wait_used(self, eng, g, j):
        eng.wait_ge(self.m.unit_used, self.base + 1 + g * self.group + j)

    def next(self):
        q = self.m.queue
        i = q.index(self)
        return q[i + 1] if i + 1 < len(q) else None


def columns_stream(m, w, n, first):
    wv = w.rearrange("(c p) n -> p c n", p=P)

    def parts(g, j, slot):
        u = g * 2 + j
        width = min(BANK, n - u * BANK) if isinstance(u, int) else BANK
        dst = slot.rearrange("p (c n) -> p c n", c=DC)[:, :, 0:width]
        return [(dst, wv[:, :, bass.ds(u * BANK, width)])]

    return Stream(m, -(-n // BANK), n // BANK, 2, first, 2, parts, True)


def rows_stream(m, w, rows, first):
    wv = w.rearrange("(c p) n -> p c n", p=P)
    chunks = rows // P

    def parts(g, j, slot):
        a = 4 * (g * 2 + j)
        k = min(4, chunks - a)
        return [(slot[:, 0:k * D].rearrange("p (c n) -> p c n", c=k), wv[:, a:a + k, :])]

    return Stream(m, -(-chunks // 4), 0, 2, first, 2, parts, True)


def expert_stream(m, wg, wu, wd, first):
    ws = [w.rearrange("(q e) (c p) n -> q c p e n", e=EQ, p=P) for w in (wg, wu, wd)]

    def parts(g, j, slot):
        return [(slot.rearrange("p (e n) -> p e n", e=EQ), ws[j // DC][g, j % DC])]

    return Stream(m, QUADS * 3 * DC, QUADS * 3 * DC, SLOTS, first, 3 * DC, parts)


def ffn_stream(m, wg, wu, first):
    gv, uv = (w.rearrange("(c p) n -> p c n", p=P) for w in (wg, wu))

    def parts(g, j, slot):
        s = slot.rearrange("p (w c n) -> p w c n", w=2, c=DC)
        at = bass.ds((g * 2 + j) * T, T)
        return [(s[:, 0], gv[:, :, at]), (s[:, 1], uv[:, :, at])]

    return Stream(m, D_FF // T, D_FF // T, 2, first, 2, parts, True)


PASSES = ((0, 0), (0, 1), (1, 0))


def high_part(m, stream, act, s, g, j, k, words=SLOT // 2):
    if k == 0:
        stream.wait_loaded(act, g, j)
    u = g * stream.group + j
    if not (isinstance(u, int) and u == 0):
        act.wait_ge(s["halves_used"], u * 2 + (k - 1))
    act.copy(m.halves[:, k, 0, 0:words], stream.slot(j)[:, k * (SLOT // 2):k * (SLOT // 2) + words]).then_inc(s["high_ready"], 1)


def low_part(m, stream, dve, s, g, j, k, last=True, words=SLOT // 2):
    u = g * stream.group + j
    dve.wait_ge(s["high_ready"], u * 2 + k + 1)
    ins = dve.tensor_tensor(m.halves[:, k, 1, 0:words], stream.slot(j)[:, k * (SLOT // 2):k * (SLOT // 2) + words],
                            m.halves[:, k, 0, 0:words].bitcast(F32), ALU.subtract)
    ins.then_inc(s["low_ready"], 1)
    if k == 1 or last:
        dve.wait_ge(s["low_ready"], u * 2 + k + 1)
        dve.sem_inc(m.unit_used, 1)


def chain(eng, sem, start=0):
    done = [start]

    def link(ins):
        done[0] += 1
        ins.then_inc(sem, 1)
        eng.wait_ge(sem, done[0])

    return link


def bview(ap, axis, n):
    u = ap.unsqueeze(axis)
    shape = list(u.shape)
    shape[axis] = n
    return u.to_broadcast(shape)



def transposed(m, n, src, dst, gain=None, low=None):
    ident = m.const("ident")
    with m.stage("transposed", "turned", "vector_moved", "scalar_moved") as (block, s):
        def half(c):
            return m.ps[:, (c % 16) // 2, (c % 2) * T:(c % 2) * T + T]

        @block.tensor
        def _(pe):
            for c in range(n):
                if c >= 16 and c % 2 == 0:
                    if low is not None:
                        pe.wait_ge(s["vector_moved"], c - 14)
                    else:
                        pe.wait_ge(s["vector_moved"] if c % 4 == 0 else s["scalar_moved"], ((c - 16) // 4 + 1) * 2)
                for t in range(TT):
                    last = pe.transpose(half(c)[:, t * P:(t + 1) * P], src(c, t), ident)
                last.then_inc(s["turned"], 1)

        @block.vector
        def _(dve):
            for c in range(n):
                if low is not None:
                    dve.wait_ge(s["scalar_moved"], min(c // 2 * 2 + 2, n))
                    high = dst(c).bitcast(F32)
                    if gain is None:
                        dve.tensor_tensor(low(c), half(c), high, ALU.subtract).then_inc(s["vector_moved"], 1)
                    else:
                        dve.scalar_tensor_tensor(low(c), half(c), gain(c), high, ALU.mult, ALU.subtract).then_inc(s["vector_moved"], 1)
                elif c % 4 < 2:
                    dve.wait_ge(s["turned"], min(c // 2 * 2 + 2, n))
                    if gain is None:
                        dve.tensor_copy(dst(c), half(c)).then_inc(s["vector_moved"], 1)
                    else:
                        dve.tensor_scalar(dst(c), half(c), gain(c), None, ALU.mult).then_inc(s["vector_moved"], 1)

        @block.scalar
        def _(act):
            for c in [c for c in range(n) if low is not None or c % 4 >= 2]:
                act.wait_ge(s["turned"], min(c // 2 * 2 + 2, n))
                if gain is None:
                    act.copy(dst(c), half(c)).then_inc(s["scalar_moved"], 1)
                else:
                    act.activation(dst(c), half(c), ACT.Copy, scale=gain(c)).then_inc(s["scalar_moved"], 1)


def project(m, stream, n, lhs, z, early=None):
    def width(g, j):
        return min(BANK, n - (g * 2 + j) * BANK) if isinstance(g, int) else BANK

    def back(g, j):
        return (g, j - 1) if j else (g - 1, 1)

    with m.stage("project", "high_ready", "low_ready", "halves_used", "scalar_freed", "vector_freed") as (block, s):
        @block.sync
        def _(sp):
            if early:
                early(sp)
            stream.load_rest(sp)
            follow(m, stream, sp, s)

        @block.tensor
        def _(pe):
            def unit(g, j):
                pe.wait_ge(s["scalar_freed"], g * 2 + j + 1)
                pe.wait_ge(s["vector_freed"], g * 2 + j + 1)
                for k in range(2):
                    pe.wait_ge(s["low_ready"], (g * 2 + j) * 2 + k + 1)
                    for t in range(TT):
                        for c in range(DC // 2):
                            for i, (xp, wp) in enumerate(PASSES):
                                w = m.halves[:, k, wp, :].rearrange("p (c n) -> p c n", c=DC // 2)
                                last = pe.matmul(m.ps[:, 2 * j + t, 0:width(g, j)], lhs(xp, k * (DC // 2) + c, t),
                                                 w[:, c, 0:width(g, j)], start=(k == 0 and c == 0 and i == 0),
                                                 stop=(k == 1 and c == DC // 2 - 1 and i == 2))
                    last.then_inc(s["halves_used"], 1)

            stream.each(pe, unit)

        @block.scalar
        def _(act):
            act.sem_inc(s["scalar_freed"], 2)

            def move(g, j):
                act.wait_ge(s["halves_used"], (g * 2 + j) * 2 + 2)
                act.copy(z[:, 0, bass.ds((g * 2 + j) * BANK, width(g, j))],
                         m.ps[:, 2 * j, 0:width(g, j)]).then_inc(s["scalar_freed"], 1)

            def unit(g, j):
                for k in range(2):
                    high_part(m, stream, act, s, g, j, k)
                if not (isinstance(g, int) and g == 0 and j == 0):
                    move(*back(g, j))

            stream.each(act, unit, peel=True)
            move((stream.n - 1) // 2, (stream.n - 1) % 2)

        @block.vector
        def _(dve):
            dve.sem_inc(s["vector_freed"], 2)

            def move(g, j):
                dve.wait_ge(s["halves_used"], (g * 2 + j) * 2 + 2)
                dve.tensor_copy(z[:, 1, bass.ds((g * 2 + j) * BANK, width(g, j))],
                                m.ps[:, 2 * j + 1, 0:width(g, j)]).then_inc(s["vector_freed"], 1)

            def unit(g, j):
                for k in range(2):
                    low_part(m, stream, dve, s, g, j, k, last=False)
                if not (isinstance(g, int) and g == 0 and j == 0):
                    move(*back(g, j))

            stream.each(dve, unit, peel=True)
            move((stream.n - 1) // 2, (stream.n - 1) % 2)


def follow(m, stream, sp, s, halves=None):
    nxt = stream.next()
    if nxt:
        if nxt.depth > 2:
            sp.wait_ge(s["halves_used"], halves if halves else 2 * stream.n)
        nxt.prefetch(sp)


def project_out(m, stream, chunks, lhs, keep, add, norm=None):
    total = chunks // 2
    with m.stage("project_out", "high_ready", "low_ready", "halves_used", "residual", "done") as (block, s):
        @block.sync
        def _(sp):
            stream.load_rest(sp)
            m.load_norm(sp, norm)
            follow(m, stream, sp, s, total)

        @block.tensor
        def _(pe):
            for u in range(total):
                pe.wait_ge(s["low_ready"], u + 1)
                for c in range(2):
                    for t in range(TT):
                        for h in range(2):
                            for i, (xp, wp) in enumerate(PASSES):
                                w = m.halves[:, u % 2, wp, :].rearrange("p (c n) -> p c n", c=2)
                                last = pe.matmul(m.ps[:, 2 * t + h, :], lhs(xp, 2 * u + c, t),
                                                 w[:, c, h * BANK:(h + 1) * BANK], start=(u == 0 and c == 0 and i == 0),
                                                 stop=(u == total - 1 and c == 1 and i == 2))
                last.then_inc(s["halves_used"], 1)

        @block.scalar
        def _(act):
            for u in range(total):
                high_part(m, stream, act, s, u // 4, u // 2 % 2, u % 2)

        @block.vector
        def _(dve):
            acc = m.ps[:, 0:4, :].rearrange("p (t h) n -> p t (h n)", t=TT)
            link = chain(dve, s["residual"])
            if keep != 1.0:
                link(dve.tensor_scalar(m.x[:, :, :], m.x[:, :, :], keep, None, ALU.mult))
            for u in range(total):
                low_part(m, stream, dve, s, u // 4, u // 2 % 2, u % 2, last=(u == total - 1))
            dve.wait_ge(s["halves_used"], total)
            link(dve.scalar_tensor_tensor(m.x[:, :, :], acc, add, m.x[:, :, :], ALU.mult, ALU.add))


def layer_normed(m, eps=1e-5):
    gb = m.norm_rows
    stats = m.small[:, 0:24].rearrange("p (t h k) -> p t h k", t=TT, h=2)
    mv = m.small[:, 24:28].rearrange("p (t k) -> p t k", t=TT)
    rstd = m.small[:, 28:30]
    with m.stage("layer_normed", "var_ready", "std_ready", "steps") as (block, s):
        @block.vector
        def _(dve):
            link = chain(dve, s["steps"])
            for t in range(TT):
                for h in range(2):
                    dve.bn_stats(stats[:, t, h, :], m.x[:, t, h * BANK:(h + 1) * BANK]).then_inc(s["steps"], 1)
            dve.wait_ge(s["steps"], 4)
            link = chain(dve, s["steps"], 4)
            for t in range(TT):
                link(dve.bn_aggr(mv[:, t, :], stats[:, t, :, :]))
            dve.tensor_scalar(rstd, mv[:, :, 1], eps, None, ALU.add).then_inc(s["var_ready"], 1)
            dve.wait_ge(s["std_ready"], 1)
            link(dve.reciprocal(rstd, rstd))
            dve.wait_ge(m.norm_loaded, 32 * m.norms)
            for t in range(TT):
                x = m.x[:, t, :]
                link(dve.scalar_tensor_tensor(x, x, mv[:, t, 0:1], gb[:, 0, :], ALU.subtract, ALU.mult))
                link(dve.scalar_tensor_tensor(x, x, rstd[:, t:t + 1], gb[:, 1, :], ALU.mult, ALU.add))

        @block.scalar
        def _(act):
            act.wait_ge(s["var_ready"], 1)
            act.activation(rstd, rstd, ACT.Sqrt).then_inc(s["std_ready"], 1)


def turn_x(m, split=True):
    if split:
        transposed(m, DC, lambda c, t: m.x[:, t, c * P:(c + 1) * P], lambda c: m.xT_r[:, 0, c, :], None,
                   lambda c: m.xT_r[:, 1, c, :])
    else:
        transposed(m, DC, lambda c, t: m.x[:, t, c * P:(c + 1) * P], lambda c: m.xT[:, c, :])


def lhs_x(m):
    return lambda part, c, t: m.xT_r[:, part, c, t * P:(t + 1) * P]


def head_normed(dve, link, eps_added, std_ready, o, out, stats, mv, rstd, eps):
    for t in range(TT):
        link(dve.bn_stats(stats[:, 6 * t:6 * t + 6], o(t)))
    for t in range(TT):
        link(dve.bn_aggr(mv[:, 2 * t:2 * t + 2], stats[:, 6 * t:6 * t + 6]))
    dve.tensor_scalar(rstd, mv.rearrange("p (t k) -> p t k", t=TT)[:, :, 1], eps, None, ALU.add).then_inc(eps_added[0], 1)
    eps_added[1] += 1
    dve.wait_ge(std_ready, eps_added[1])
    link(dve.reciprocal(rstd, rstd))
    for t in range(TT):
        link(dve.tensor_scalar(out(t), o(t), mv[:, 2 * t:2 * t + 1], rstd[:, t:t + 1], ALU.subtract, ALU.mult))



def mlstm(m, in_stream, out_stream, gate_b, norm):
    NIN = 2 * ML_HEADS * ML_DK + 2 * D + 4 * ML_HEADS
    z = m.arena[:, 0:2 * NIN].rearrange("p (t n) -> p t n", t=TT)
    H = ML_HEADS
    project(m, in_stream, NIN, lhs_x(m), z)
    G = z[:, :, 3 * D:3 * D + 16]
    w = m.work
    gb = w[:, 0:16]
    tmp = w[:, 16:16 + 32].rearrange("p (k t n) -> p k t n", k=2, t=TT)
    rows = w[0:H, 128:128 + 4 * T].rearrange("p (d k t) -> p d k t", d=2, k=2)
    A = w[0:H, 1152:1152 + 2 * T].rearrange("p (d t) -> p d t", d=2)
    M = w[0:H, 1664:1664 + 2 * T].rearrange("p (d t) -> p d t", d=2)
    B = w[0:H, 2176:2176 + 2 * T].rearrange("p (d t) -> p d t", d=2)
    EM = w[0:H, 2688:2688 + 2 * T].rearrange("p (d t) -> p d t", d=2)
    cols = m.small[:, 0:32].rearrange("p (k d t h) -> p k d t h", k=2, d=2, t=TT)
    ident = m.const("ident")
    ones = m.const("ones")
    rps = m.ps[0:H, 0:2, :].rearrange("p b n -> p (b n)").rearrange("p (d k t) -> p d k t", d=2, k=2)
    with m.stage("mlstm_gates", "bias_loaded", "gates_ready", "exp_in", "exp_out", "steps", "turned", "rows_ready", "back_turned",
                 "m_ready", "em_ready") as (block, s):
        @block.sync
        def _(sp):
            sp.dma_start(gb, gate_b.rearrange("a b h -> (a b h)").partition_broadcast(P)).then_inc(s["bias_loaded"], 16)
            sp.wait_ge(m.columns_loaded, 16 * len(m.columns))

        @block.vector
        def _(dve):
            link = chain(dve, s["steps"])
            dve.wait_ge(s["bias_loaded"], 16)
            link(dve.tensor_tensor(G, G, bview(gb, 1, TT), ALU.add))
            Gf = G.rearrange("p t (d k h) -> p t d k h", d=2, k=2)[:, :, :, 1, :]
            lo, ab = (tmp[:, k].rearrange("p t (d h) -> p t d h", d=2) for k in range(2))
            for t in range(TT):
                link(dve.tensor_scalar(lo[:, t], Gf[:, t], 0.0, None, ALU.min))
                link(dve.scalar_tensor_tensor(ab[:, t], lo[:, t], 2.0, Gf[:, t], ALU.mult, ALU.subtract))
            dve.sem_inc(s["exp_in"], 1)
            dve.wait_ge(s["exp_out"], 2)
            for t in range(TT):
                link(dve.tensor_tensor(Gf[:, t], lo[:, t], ab[:, t], ALU.subtract))
            dve.sem_inc(s["gates_ready"], 1)
            dve.wait_ge(s["turned"], 1)
            link(dve.tensor_copy(rows, rps))
            for d in range(2):
                way = slice(None) if d == 0 else slice(None, None, -1)
                link(dve.tensor_tensor_scan(B[:, d, way], ones[0:H, 0:1].to_broadcast([H, T]), rows[:, d, 1, way], 0.0,
                                            ALU.mult, ALU.add))
                link(dve.tensor_tensor(A[:, d, :], rows[:, d, 0, :], B[:, d, :], ALU.subtract))
                link(dve.tensor_tensor_scan(M[:, d, way], ones[0:H, 0:1].to_broadcast([H, T]), A[:, d, way], 0.0,
                                            ALU.mult, ALU.max))
                link(dve.tensor_tensor(B[:, d, :], B[:, d, :], M[:, d, :], ALU.add))
            dve.sem_inc(s["m_ready"], 1)
            dve.wait_ge(s["back_turned"], 1)
            link(dve.tensor_copy(cols, m.ps[:, 2, 0:32].rearrange("p (k d t h) -> p k d t h", k=2, d=2, t=TT)))

        @block.scalar
        def _(act):
            act.wait_ge(s["exp_in"], 1)
            ab = tmp[:, 1]
            act.activation(ab, ab, ACT.Exp).then_inc(s["exp_out"], 1)
            act.wait_ge(s["exp_out"], 1)
            act.activation(ab, ab, ACT.Ln, bias=m.const("ones")[:, 0:1]).then_inc(s["exp_out"], 1)
            act.wait_ge(s["m_ready"], 1)
            act.activation(EM, B, ACT.Exp, scale=-1.0).then_inc(s["em_ready"], 1)

        @block.tensor
        def _(pe):
            pe.wait_ge(s["gates_ready"], 1)
            for d in range(2):
                for k in range(2):
                    for t in range(TT):
                        a = 8 * d + 4 * k
                        last = pe.transpose(rps[:, d, k, t * P:(t + 1) * P], G[:, t, a:a + H], ident)
            last.then_inc(s["turned"], 1)
            pe.wait_ge(s["em_ready"], 1)
            for k, src in enumerate((A, EM)):
                for d in range(2):
                    for t in range(TT):
                        a = ((k * 2 + d) * 2 + t) * H
                        last = pe.transpose(m.ps[:, 2, a:a + H], src[:, d, t * P:(t + 1) * P], ident[0:H, 0:H])
            last.then_inc(s["back_turned"], 1)

    spare = m.arena[:, 2 * NIN:]
    h_acc = [v.rearrange("p (t n) -> p t n", t=TT) for v in (w[:, 3200:3712], spare[:, 3072:3584])]
    qk = [v.rearrange("p (k t n) -> p k t n", k=2, t=TT) for v in (w[:, 128:640], spare[:, 0:512])]
    qkT = [v.rearrange("p (k t) -> p k t", k=2) for v in (w[:, 640:1152], spare[:, 512:1024])]
    Wt = [v.rearrange("p (d k t) -> p d k t", d=2, k=2) for v in (w[:, 3712:4736], spare[:, 1024:2048])]
    Wf = [v.rearrange("p (d n) -> p d n", d=2) for v in (w[:, 4736:5760], spare[:, 2048:3072])]
    hcol = [m.small[:, a:a + 32].rearrange("p (k d t o) -> p k d t o", k=2, d=2, t=TT)[:, :, :, :, 0:1] for a in (32, 128)]
    den = [m.small[:, a:a + 8] for a in (64, 160)]
    Mh = [A, EM]
    stats, mv, rstd = ([m.small[:, a + k:a + k + n] for a in (80, 168)] for k, n in ((0, 12), (12, 4), (16, 2)))
    with m.nc.Fori(0, H // 2) as pair:
        def column(b, first, width):
            return bass.ds(pair * (2 * width) + (first + b * width), width)

        with m.stage("mlstm_heads", "staged", "turned", "moved", "m_staged", "scores", "m_spread", "steps", "exp_in", "exp_out",
                     "weights_ready", "sums_ready", "eps_added", "std_ready") as (block, s):
            @block.vector
            def _(dve):
                link = chain(dve, s["steps"])
                for b in range(2):
                    dve.tensor_scalar(qk[b][:, 0], z[:, :, column(b, 0, ML_DK)], ML_DK ** -0.5, None, ALU.mult).then_inc(s["staged"], 1)
                    dve.tensor_copy(qk[b][:, 1], z[:, :, column(b, H * ML_DK, ML_DK)]).then_inc(s["staged"], 1)
                    for d in range(2):
                        dve.tensor_scalar(Mh[b][:, d, :], M[:, d, :], ident[0:H, column(b, 0, 1)], None, ALU.mult).then_inc(s["m_staged"], 1)
                for b in range(2):
                    for k in range(2):
                        for d in range(2):
                            link(dve.tensor_copy(hcol[b][:, k, d, :, 0], cols[:, k, d, :, column(b, 0, 1)].rearrange("p t o -> p (t o)")))
                for b in range(2):
                    dve.wait_ge(s["turned"], b + 1)
                    dve.tensor_copy(qkT[b], m.ps[:, 4 * b, :].rearrange("p (k t) -> p k t", k=2)).then_inc(s["moved"], 1)
                    dve.wait_ge(s["m_spread"], b + 1)
                    for d in range(2):
                        neg = m.const("neg_fwd" if d == 0 else "neg_bwd").rearrange("p (k t) -> p k t", k=2)
                        dve.scalar_tensor_tensor(Wt[b][:, d], bview(m.ps[:, 4 * b + 2 + d, 0:T], 1, 2), -1.0, neg,
                                                 ALU.mult, ALU.add).then_inc(s["exp_in"], 1)
                for b in range(2):
                    dve.wait_ge(s["exp_out"], 4 * b + 4)
                    dve.wait_ge(s["scores"], b + 1)
                    for d in range(2):
                        dve.tensor_tensor(Wf[b][:, d, :], Wt[b][:, d].rearrange("p k t -> p (k t)"),
                                          m.ps[:, 4 * b + 1, :], ALU.mult).then_inc(s["weights_ready"], 1)
                added = [s["eps_added"], 0]
                for b in range(2):
                    for d in range(2):
                        o = m.ps[:, 4 * b + 2 * d:4 * b + 2 * d + 2, :]
                        dc = den[b][:, 2 * d:2 * d + 2]
                        dve.wait_ge(s["sums_ready"], 4 * b + 2 * d + 2)
                        link(dve.tensor_scalar(dc, o[:, :, ML_DV], -1.0, None, ALU.mult))
                        link(dve.tensor_tensor(dc, dc, o[:, :, ML_DV], ALU.max))
                        link(dve.tensor_tensor(dc, dc, hcol[b][:, 1, d, :, 0], ALU.max))
                        link(dve.reciprocal(dc, dc))
                        for t in range(TT):
                            if d == 0:
                                link(dve.tensor_scalar(h_acc[b][:, t, :], o[:, t, 0:ML_DV], dc[:, t:t + 1], None, ALU.mult))
                            else:
                                link(dve.scalar_tensor_tensor(h_acc[b][:, t, :], o[:, t, 0:ML_DV], dc[:, t:t + 1], h_acc[b][:, t, :],
                                                              ALU.mult, ALU.add))
                    head_normed(dve, link, added, s["std_ready"], lambda t: h_acc[b][:, t, :],
                                lambda t: z[:, t, column(b, 2 * H * ML_DK, ML_DV)], stats[b], mv[b], rstd[b], 1e-5)

            @block.tensor
            def _(pe):
                for b in range(2):
                    pe.wait_ge(s["staged"], 2 * b + 2)
                    for k in range(2):
                        for t in range(TT):
                            last = pe.transpose(m.ps[:, 4 * b, k * T + t * P:k * T + (t + 1) * P], qk[b][:, k, t, :], ident)
                    last.then_inc(s["turned"], 1)
                    pe.wait_ge(s["m_staged"], 2 * b + 2)
                    for d in range(2):
                        last = pe.matmul(m.ps[:, 4 * b + 2 + d, 0:T], ones[0:H, :], Mh[b][:, d, :], start=True, stop=True)
                    last.then_inc(s["m_spread"], 1)
                for b in range(2):
                    pe.wait_ge(s["moved"], b + 1)
                    for k in range(2):
                        last = pe.matmul(m.ps[:, 4 * b + 1, k * T:(k + 1) * T], qkT[b][:, 1, k * P:(k + 1) * P], qkT[b][:, 0, :],
                                         start=True, stop=True)
                    last.then_inc(s["scores"], 1)
                for b in range(2):
                    pe.wait_ge(s["weights_ready"], 2 * b + 2)
                    for d in range(2):
                        for t in range(TT):
                            srcs = [k for k in range(2) if (k <= t if d == 0 else k >= t)]
                            o = m.ps[:, 4 * b + 2 * d + t, :]
                            for i, k in enumerate(srcs):
                                pe.matmul(o[:, 0:ML_DV], Wf[b][:, d, k * T + t * P:k * T + (t + 1) * P],
                                          z[:, k, column(b, 2 * H * ML_DK, ML_DV)], start=(i == 0), stop=(i == len(srcs) - 1))
                            for i, k in enumerate(srcs):
                                last = pe.matmul(o[:, ML_DV:ML_DV + 1], Wf[b][:, d, k * T + t * P:k * T + (t + 1) * P],
                                                 ones[:, 0:1], start=(i == 0), stop=(i == len(srcs) - 1))
                            last.then_inc(s["sums_ready"], 1)

            @block.scalar
            def _(act):
                act.wait_ge(s["steps"], 8)
                for b in range(2):
                    for d in range(2):
                        act.wait_ge(s["exp_in"], 2 * b + d + 1)
                        for k in range(2):
                            act.activation(Wt[b][:, d, k, :], Wt[b][:, d, k, :], ACT.Exp, bias=hcol[b][:, 0, d, k, :]).then_inc(s["exp_out"], 1)
                for b in range(2):
                    act.wait_ge(s["eps_added"], b + 1)
                    act.activation(rstd[b], rstd[b], ACT.Sqrt).then_inc(s["std_ready"], 1)
        with m.stage("even_number") as (block, s):
            pass
    v0 = 2 * H * ML_DK
    gated(m, z, [(v0, v0 + D, D)], ACT.Sigmoid)
    mixed_out(m, out_stream, z, [v0 + c * P for c in range(DC)], ALPHA, 1.0, "mlstm_norm_g", norm=norm)


def gated(m, z, parts, func):
    pieces = [(t, a + i, b + i, min(BANK, n - i)) for a, b, n in parts for i in range(0, n, BANK) for t in range(TT)]
    with m.stage("gated", "gate_ready", "steps") as (block, s):
        @block.scalar
        def _(act):
            for t, a, b, n in pieces:
                act.activation(z[:, t, b:b + n], z[:, t, b:b + n], func).then_inc(s["gate_ready"], 1)

        @block.vector
        def _(dve):
            for i, (t, a, b, n) in enumerate(pieces):
                dve.wait_ge(s["gate_ready"], i + 1)
                dve.tensor_tensor(z[:, t, a:a + n], z[:, t, a:a + n], z[:, t, b:b + n], ALU.mult).then_inc(s["steps"], 1)


def mixed_out(m, stream, z, chunks, keep, add, gains=None, norm=None, low=None):
    n = len(chunks)
    gain = None
    if gains is not None:
        gain = lambda c: m.columns[gains][:, c:c + 1]
    high = lambda c: m.work_r[:, c * T:(c + 1) * T]
    if low is None:
        low = lambda c: m.work_r[:, (n + c) * T:(n + c + 1) * T]
    transposed(m, n, lambda c, t: z[:, t, chunks[c]:chunks[c] + P], high, gain, low)
    project_out(m, stream, n, lambda part, c, t: (high, low)[part](c)[:, t * P:(t + 1) * P], keep, add, norm=norm)





def moe(m, stream, norm):
    ar = m.arena
    xin = ar[:, 0:4096].rearrange("p (c n) -> p c n", c=DC)
    outs = ar[:, 4096:8192].rearrange("p (q n) -> p q n", q=QUADS)
    scatter = ar[:, 8192:9216].rearrange("p (q t) -> p q t", q=QUADS)
    parts = m.arena_r[:, 4096:8192].rearrange("p (k t n) -> p k t n", k=2, t=TT)
    sel = m.arena_r[:, 9216:10240].rearrange("p (t e j) -> p t e j", t=TT, e=E)
    selg = ar[:, 10240:11264].rearrange("p (t e j) -> p t e j", t=TT, e=E)
    hid = ar[:, 11264:12288]
    w = m.work
    rt = m.router
    aff = w[:, 128:128 + 2 * E].rearrange("p (t e) -> p t e", t=TT)
    pos = w[:, 160:160 + 2 * E].rearrange("p (t e) -> p t e", t=TT)
    rmax, rsum = m.small[:, 0:2], m.small[:, 2:4]
    affT = w[0:E, 256:512]
    left = w[0:E, 512:768]
    took = w[0:E, 768:1024]
    count = w[0:E, 1024:1280]
    top = m.small[0:E, 16:24]
    ident, ones = m.const("ident"), m.const("ones")
    slot_no = m.const("slot_no")
    with m.stage("moe_routed", "high_ready", "logits", "max_ready", "exp_ready", "steps", "aff_ready", "aff_turned", "pos_ready",
                 "pos_turned", "sel_ready", "gathered", "scat_turned", "vector_moved", "scalar_moved") as (block, s):
        @block.tensor
        def _(pe):
            pe.wait_ge(m.router_loaded, 16 * m.routers)
            for t in range(TT):
                for c in range(DC):
                    last = pe.matmul(m.ps[:, 0, t * E:(t + 1) * E], m.xT[:, c, t * P:(t + 1) * P], rt[:, c, :],
                                     start=(c == 0), stop=(c == DC - 1))
            last.then_inc(s["logits"], 1)
            pe.wait_ge(s["aff_ready"], 1)
            for t in range(TT):
                last = pe.transpose(m.ps[0:E, 1, t * P:(t + 1) * P], aff[:, t, :], ident)
            last.then_inc(s["aff_turned"], 1)
            pe.wait_ge(s["pos_ready"], 1)
            for t in range(TT):
                last = pe.transpose(m.ps[:, 0, t * E:(t + 1) * E], took[:, t * P:(t + 1) * P], ident[0:E, 0:E])
            last.then_inc(s["pos_turned"], 1)
            pe.wait_ge(s["sel_ready"], 1)
            for c in range(DC):
                if c == DC // 2:
                    pe.wait_ge(s["sel_ready"], 2)
                    for q in range(QUADS):
                        for t in range(TT):
                            last = pe.transpose(m.ps[:, q // 2, (q % 2) * T + t * P:(q % 2) * T + (t + 1) * P],
                                                selg[:, t].rearrange("p e j -> p (e j)")[:, q * P:(q + 1) * P], ident)
                    last.then_inc(s["scat_turned"], 1)
                if c >= 6:
                    pe.wait_ge(s["vector_moved"] if c % 2 == 0 else s["scalar_moved"], (c - 6) // 2 + 1)
                for k in range(2):
                    for t in range(TT):
                        last = pe.matmul(m.ps[:, 2 + c % 6, :], parts[:, k, t, c * P:(c + 1) * P],
                                         sel[:, t].rearrange("p e j -> p (e j)"), start=(k == 0 and t == 0),
                                         stop=(k == 1 and t == TT - 1))
                last.then_inc(s["gathered"], 1)

        @block.vector
        def _(dve):
            link = chain(dve, s["steps"])
            dve.wait_ge(s["high_ready"], 1)
            link(dve.tensor_tensor(parts[:, 1], m.x[:, :, :], parts[:, 0].bitcast(F32), ALU.subtract))
            link(dve.tensor_scalar(m.x[:, :, :], m.x[:, :, :], ALPHA, None, ALU.mult))
            dve.wait_ge(s["logits"], 1)
            lg = m.ps[:, 0, 0:2 * E].rearrange("p (t e) -> p t e", t=TT)
            link(dve.tensor_reduce(rmax, lg, AX, ALU.max))
            dve.tensor_tensor(aff, lg, bview(rmax, 2, E), ALU.subtract).then_inc(s["max_ready"], 1)
            dve.wait_ge(s["exp_ready"], 1)
            link(dve.tensor_reduce(rsum, aff, AX, ALU.add))
            link(dve.reciprocal(rsum, rsum))
            dve.tensor_tensor(aff, aff, bview(rsum, 2, E), ALU.mult).then_inc(s["aff_ready"], 1)
            dve.wait_ge(s["aff_turned"], 1)
            link(dve.tensor_copy(left, m.ps[0:E, 1, 0:T]))
            for _ in range(CAP // 8):
                link(dve.max(top, left))
                link(dve.match_replace(left, top, left, -1.0))
            link(dve.tensor_scalar(took, left, -1.0, None, ALU.is_equal))
            link(dve.tensor_tensor_scan(count, ones[0:E, 0:1].to_broadcast([E, T]), took, 0.0, ALU.mult, ALU.add))
            dve.tensor_tensor(took, took, count, ALU.mult).then_inc(s["pos_ready"], 1)
            dve.wait_ge(s["pos_turned"], 1)
            link(dve.tensor_copy(pos, m.ps[:, 0, 0:2 * E].rearrange("p (t e) -> p t e", t=TT)))
            for t in range(TT):
                link(dve.tensor_tensor(sel[:, t], bview(slot_no, 1, E), bview(pos[:, t, :], 2, CAP), ALU.is_equal))
            dve.sem_inc(s["sel_ready"], 1)
            for t in range(TT):
                link(dve.tensor_tensor(selg[:, t], sel[:, t].bitcast(F32), bview(aff[:, t, :], 2, CAP), ALU.mult))
            dve.sem_inc(s["sel_ready"], 1)
            for c in range(0, DC, 2):
                if c == DC // 2:
                    dve.wait_ge(s["scat_turned"], 1)
                    dve.tensor_copy(scatter.rearrange("p q t -> p (q t)"),
                                    m.ps[:, 0:2, :].rearrange("p b n -> p (b n)")).then_inc(s["vector_moved"], 1)
                dve.wait_ge(s["gathered"], c + 1)
                dve.tensor_copy(xin[:, c, :], m.ps[:, 2 + c % 6, :]).then_inc(s["vector_moved"], 1)

        @block.scalar
        def _(act):
            act.copy(parts[:, 0], m.x[:, :, :]).then_inc(s["high_ready"], 1)
            act.wait_ge(s["max_ready"], 1)
            act.activation(aff, aff, ACT.Exp).then_inc(s["exp_ready"], 1)
            for c in range(1, DC, 2):
                act.wait_ge(s["gathered"], c + 1)
                act.copy(xin[:, c, :], m.ps[:, 2 + c % 6, :]).then_inc(s["scalar_moved"], 1)

    xq = w[:, 1280:1280 + D].rearrange("p (c n) -> p c n", c=DC)
    hT = w[:, 2304:2304 + D].rearrange("p (c n) -> p c n", c=DC)
    sg = ar[:, 12288:12288 + D]
    gate = m.ps[:, 0:2, :].rearrange("p b n -> p (b n)")
    up = m.ps[:, 2:4, :].rearrange("p b n -> p (b n)")
    down = m.ps[:, 4:6, :].rearrange("p b n -> p (b n)")
    turn = m.ps[:, 6:8, :].rearrange("p b n -> p (b n)")
    GATE, UP, DOWN = DC - 1, 2 * DC - 1, 3 * DC - 1
    with m.stage("moe_experts", "tokens_staged", "gate_done", "hidden_ready", "hidden_turned", "hT_ready", "answer_moved",
                 "steps") as (block, s):
        @block.sync
        def _(sp):
            stream.load_rest(sp)
            m.load_norm(sp, norm)
            if stream.next():
                stream.next().prefetch(sp)

        @block.tensor
        def _(pe):
            def unit(g, j):
                if j == 0:
                    pe.wait_ge(s["tokens_staged"], g + 1)
                if j == 2 * DC:
                    pe.wait_ge(s["hidden_ready"], g + 1)
                    for c in range(DC):
                        last = pe.transpose(turn[:, c * P:(c + 1) * P], hid[:, c * P:(c + 1) * P], ident)
                    last.then_inc(s["hidden_turned"], 1)
                    pe.wait_ge(s["hT_ready"], g + 1)
                stream.wait_loaded(pe, g, j)
                w4 = stream.slot(j).rearrange("p (e n) -> p e n", e=EQ)
                acc = (gate, up, down)[j // DC]
                lhs = xq if j < 2 * DC else hT
                c = j % DC
                for half in range(2):
                    for e in range(EQ):
                        last = pe.matmul(acc[e * CAP:(e + 1) * CAP, half * BANK:(half + 1) * BANK],
                                         lhs[:, c, e * CAP:(e + 1) * CAP], w4[:, e, half * BANK:(half + 1) * BANK],
                                         start=(c == 0), stop=(c == DC - 1), tile_position=(0, e * CAP))
                last.then_inc(m.unit_used, 1)

            stream.each(pe, unit)

        @block.scalar
        def _(act):
            with act.Fori(0, QUADS) as g:
                stream.wait_used(act, g, GATE)
                act.activation(sg, gate, ACT.Silu).then_inc(s["gate_done"], 1)
                stream.wait_used(act, g, DOWN)
                act.copy(outs[:, bass.ds(g, 1), :].rearrange("p o n -> p (o n)"), down).then_inc(s["answer_moved"], 1)

        @block.vector
        def _(dve):
            with dve.Fori(0, QUADS) as g:
                dve.tensor_copy(xq, xin[:, :, bass.ds(g * P, P)]).then_inc(s["tokens_staged"], 1)
                stream.wait_used(dve, g, UP)
                dve.wait_ge(s["gate_done"], g + 1)
                dve.tensor_tensor(hid, sg, up, ALU.mult).then_inc(s["hidden_ready"], 1)
                dve.wait_ge(s["hidden_turned"], g + 1)
                dve.tensor_copy(hT.rearrange("p c n -> p (c n)"), turn).then_inc(s["hT_ready"], 1)
                dve.wait_ge(s["answer_moved"], g + 1)

    with m.stage("moe_summed", "summed", "steps") as (block, s):
        @block.tensor
        def _(pe):
            for t in range(TT):
                for half in range(2):
                    for q in range(QUADS):
                        last = pe.matmul(m.ps[:, 2 * t + half, :], scatter[:, q, t * P:(t + 1) * P],
                                         outs[:, q, half * BANK:(half + 1) * BANK], start=(q == 0), stop=(q == QUADS - 1))
                last.then_inc(s["summed"], 1)

        @block.vector
        def _(dve):
            for t in range(TT):
                dve.wait_ge(s["summed"], t + 1)
                dve.tensor_tensor(m.x[:, t, :], m.ps[:, 2 * t:2 * t + 2, :].rearrange("p h n -> p (h n)"),
                                  m.x[:, t, :], ALU.add).then_inc(s["steps"], 1)



def gla(m, in_stream, out_stream, gate_w, norm):
    H, DK, DV = 4, P, 2 * P
    NIN = 2 * H * DK + 2 * D + 2 * GLA_RANK
    z = m.arena[:, 0:2 * NIN].rearrange("p (t n) -> p t n", t=TT)
    project(m, in_stream, NIN, lhs_x(m), z)
    w = m.work
    gbc = m.columns["gla_gate_b"]
    gw = w[0:GLA_RANK, 0:2 * H * DK].rearrange("p (d n) -> p d n", d=2)
    lowT = w[0:GLA_RANK, 1024:1024 + 2 * T].rearrange("p (d t) -> p d t", d=2)
    ident = m.const("ident")
    with m.stage("gla_gates", "turned", "steps", "gate_w_loaded") as (block, s):
        @block.sync
        def _(sp):
            sp.dma_start(gw, gate_w.rearrange("d r n -> r d n")).then_inc(s["gate_w_loaded"], 16)
            sp.wait_ge(s["gate_w_loaded"], 16)

        @block.tensor
        def _(pe):
            for d in range(2):
                for t in range(TT):
                    a = NIN - 2 * GLA_RANK + d * GLA_RANK
                    last = pe.transpose(m.ps[0:GLA_RANK, 0, d * T + t * P:d * T + (t + 1) * P], z[:, t, a:a + GLA_RANK], ident)
            last.then_inc(s["turned"], 1)

        @block.vector
        def _(dve):
            dve.wait_ge(s["turned"], 1)
            dve.tensor_copy(lowT, m.ps[0:GLA_RANK, 0, :].rearrange("p (d t) -> p d t", d=2)).then_inc(s["steps"], 1)

    places = (w[:, 1536:5888], m.arena[:, 2 * NIN:2 * NIN + 4352])
    qk = [v[:, 0:512].rearrange("p (k t n) -> p k t n", k=2, t=TT) for v in places]
    qkT = [v[:, 512:1024].rearrange("p (k t) -> p k t", k=2) for v in places]
    gwh = [v[0:GLA_RANK, 1024:1280].rearrange("p (d n) -> p d n", d=2) for v in places]
    lo = [v[:, 1280:1792].rearrange("p (d t) -> p d t", d=2) for v in places]
    ab = [v[:, 1792:2304].rearrange("p (d t) -> p d t", d=2) for v in places]
    B = [v[:, 2304:2816].rearrange("p (d t) -> p d t", d=2) for v in places]
    QE = [v[:, 2816:3584].rearrange("p (d i t) -> p d i t", d=2, i=3) for v in places]
    KE = [v[:, 3584:4352].rearrange("p (d i t) -> p d i t", d=2, i=3) for v in places]
    Wf = [v[:, 1280:2048].rearrange("p (d i t) -> p d i t", d=2, i=3) for v in places]
    bh, neg, stats, mv, rstd = ([m.small[:, a + k:a + k + n] for a in (10, 60)]
                                for k, n in ((0, 2), (2, 6), (8, 12), (20, 4), (24, 2)))
    neg = [v.rearrange("p (d i) -> p d i", d=2) for v in neg]
    ones = m.const("ones")
    v0 = 2 * H * DK
    centre = [[P // 2, P + P // 2, P - 1], [P // 2, P + P // 2, P]]
    q_tile = [[0, 1, 1], [0, 1, 0]]
    k_tile = [[0, 1, 0], [0, 1, 1]]
    with m.nc.Fori(0, H // 2) as pair:
        def column(b, first, width):
            return bass.ds(pair * (2 * width) + (first + b * width), width)

        with m.stage("gla_heads", "staged", "turned", "moved", "gates_staged", "gates_made", "steps", "exp_in", "exp_out", "ln_out",
                     "sums_ready", "decays_out", "products_ready", "scores", "weights_ready", "out_ready", "eps_added",
                     "std_ready") as (block, s):
            @block.vector
            def _(dve):
                link = chain(dve, s["steps"])
                for b in range(2):
                    dve.tensor_scalar(qk[b][:, 0], z[:, :, column(b, 0, DK)], DK ** -0.5, None, ALU.mult).then_inc(s["staged"], 1)
                    dve.tensor_copy(qk[b][:, 1], z[:, :, column(b, H * DK, DK)]).then_inc(s["staged"], 1)
                    dve.tensor_copy(gwh[b], gw[:, :, column(b, 0, DK)]).then_inc(s["gates_staged"], 1)
                    link(dve.tensor_copy(bh[b], gbc.rearrange("p (d h) -> p d h", d=2)[:, :, column(b, 0, 1)].rearrange("p d o -> p (d o)")))
                for b in range(2):
                    dve.wait_ge(s["turned"], b + 1)
                    dve.tensor_copy(qkT[b], m.ps[:, 4 * b, :].rearrange("p (k t) -> p k t", k=2)).then_inc(s["moved"], 1)
                    dve.wait_ge(s["gates_made"], b + 1)
                    for d in range(2):
                        y = m.ps[:, 4 * b + 1, d * T:(d + 1) * T]
                        link(dve.tensor_scalar(lo[b][:, d], y, bh[b][:, d:d + 1], 0.0, ALU.add, ALU.min))
                        link(dve.tensor_scalar(ab[b][:, d], y, bh[b][:, d:d + 1], None, ALU.add))
                    link(dve.scalar_tensor_tensor(ab[b], lo[b], 2.0, ab[b], ALU.mult, ALU.subtract))
                    dve.sem_inc(s["exp_in"], 1)
                for b in range(2):
                    dve.wait_ge(s["ln_out"], b + 1)
                    link(dve.tensor_tensor(lo[b], lo[b], ab[b], ALU.subtract))
                    link(dve.tensor_scalar(lo[b], lo[b], 1.0 / GLA_TAU, None, ALU.mult))
                    for d in range(2):
                        way = slice(None) if d == 0 else slice(None, None, -1)
                        link(dve.tensor_tensor_scan(B[b][:, d, way], ones[:, 0:1].to_broadcast([P, T]), lo[b][:, d, way], 0.0,
                                                    ALU.mult, ALU.add))
                    link(dve.tensor_scalar(neg[b][:, :, 0:2], B[b][:, :, P // 2:P // 2 + P + 1:P], -1.0, None, ALU.mult))
                    for d in range(2):
                        c = centre[d][2]
                        link(dve.tensor_scalar(neg[b][:, d, 2:3], B[b][:, d, c:c + 1], -1.0, None, ALU.mult))
                    dve.sem_inc(s["sums_ready"], 1)
                for b in range(2):
                    dve.wait_ge(s["decays_out"], 12 * b + 12)
                    dve.wait_ge(s["moved"], b + 1)
                    for d in range(2):
                        for X, k, tiles in ((QE[b], 0, q_tile[d]), (KE[b], 1, k_tile[d])):
                            dve.tensor_tensor(X[:, d, 0:2, :], X[:, d, 0:2, :], qkT[b][:, k, :].rearrange("p (i t) -> p i t", i=2),
                                              ALU.mult).then_inc(s["products_ready"], 1)
                            c = tiles[2]
                            dve.tensor_tensor(X[:, d, 2, :], X[:, d, 2, :], qkT[b][:, k, c * P:(c + 1) * P],
                                              ALU.mult).then_inc(s["products_ready"], 1)
                for b in range(2):
                    dve.wait_ge(s["scores"], b + 1)
                    for d in range(2):
                        keep = m.const("keep_fwd" if d == 0 else "keep_bwd")
                        sc = m.ps[:, 4 * b + 2 + d, 0:3 * P].rearrange("p (i t) -> p i t", i=3)
                        link(dve.tensor_tensor(Wf[b][:, d, 0:2, :], sc[:, 0:2, :], bview(keep, 1, 2), ALU.mult))
                        link(dve.tensor_copy(Wf[b][:, d, 2, :], sc[:, 2, :]))
                    dve.tensor_tensor(Wf[b][:, 0, 0:2, :], Wf[b][:, 0, 0:2, :], Wf[b][:, 1, 0:2, :], ALU.add).then_inc(s["weights_ready"], 1)
                added = [s["eps_added"], 0]
                for b in range(2):
                    dve.wait_ge(s["out_ready"], 2 * b + 2)
                    head_normed(dve, link, added, s["std_ready"], lambda t: m.ps[:, 4 * b + t, 0:DV],
                                lambda t: z[:, t, column(b, v0, DV)], stats[b], mv[b], rstd[b], 1e-5)

            @block.tensor
            def _(pe):
                for b in range(2):
                    pe.wait_ge(s["staged"], 2 * b + 2)
                    for k in range(2):
                        for t in range(TT):
                            last = pe.transpose(m.ps[:, 4 * b, k * T + t * P:k * T + (t + 1) * P], qk[b][:, k, t, :], ident)
                    last.then_inc(s["turned"], 1)
                    pe.wait_ge(s["gates_staged"], b + 1)
                    for d in range(2):
                        last = pe.matmul(m.ps[:, 4 * b + 1, d * T:(d + 1) * T], gwh[b][:, d, :], lowT[:, d, :], start=True, stop=True)
                    last.then_inc(s["gates_made"], 1)
                for b in range(2):
                    pe.wait_ge(s["products_ready"], 8 * b + 8)
                    for d in range(2):
                        for i in range(3):
                            last = pe.matmul(m.ps[:, 4 * b + 2 + d, i * P:(i + 1) * P], KE[b][:, d, i, :], QE[b][:, d, i, :],
                                             start=True, stop=True)
                    last.then_inc(s["scores"], 1)
                for b in range(2):
                    pe.wait_ge(s["weights_ready"], b + 1)
                    v = z[:, :, column(b, v0, DV)]
                    for t, d in ((0, 1), (1, 0)):
                        pe.matmul(m.ps[:, 4 * b + t, 0:DV], Wf[b][:, 0, t, :], v[:, t, :], start=True, stop=False)
                        pe.matmul(m.ps[:, 4 * b + t, 0:DV], Wf[b][:, d, 2, :], v[:, 1 - t, :], start=False,
                                  stop=True).then_inc(s["out_ready"], 1)

            @block.scalar
            def _(act):
                for b in range(2):
                    act.wait_ge(s["exp_in"], b + 1)
                    act.activation(ab[b], ab[b], ACT.Exp).then_inc(s["exp_out"], 1)
                for b in range(2):
                    act.wait_ge(s["exp_out"], b + 1)
                    act.activation(ab[b], ab[b], ACT.Ln, bias=ones[:, 0:1]).then_inc(s["ln_out"], 1)
                for b in range(2):
                    act.wait_ge(s["sums_ready"], b + 1)
                    for d in range(2):
                        for i in range(3):
                            c, qt, kt = centre[d][i], q_tile[d][i], k_tile[d][i]
                            act.activation(QE[b][:, d, i, :], B[b][:, d, qt * P:(qt + 1) * P], ACT.Exp,
                                           bias=neg[b][:, d, i:i + 1]).then_inc(s["decays_out"], 1)
                            act.activation(KE[b][:, d, i, :], B[b][:, d, kt * P:(kt + 1) * P], ACT.Exp, scale=-1.0,
                                           bias=B[b][:, d, c:c + 1]).then_inc(s["decays_out"], 1)
                for b in range(2):
                    act.wait_ge(s["eps_added"], b + 1)
                    act.activation(rstd[b], rstd[b], ACT.Sqrt).then_inc(s["std_ready"], 1)
        with m.stage("even_number") as (block, s):
            pass
    gated(m, z, [(v0, v0 + D, D)], ACT.Silu)
    mixed_out(m, out_stream, z, [v0 + c * P for c in range(DC)], ALPHA, 1.0, "gla_norm_g", norm=norm)



def rms_factors(dve, link, s, ss, eps):
    dve.wait_ge(s["squares"], TT)
    dve.tensor_scalar(ss, ss, 1.0 / D, eps, ALU.mult, ALU.add).then_inc(s["mean_ready"], 1)
    dve.wait_ge(s["std_ready"], 1)
    link(dve.reciprocal(ss, ss))


def rms_turned(m, src, gain, eps=1e-6):
    gcol = m.columns[gain]
    scaled = m.work[:, 0:2 * D].rearrange("p (t n) -> p t n", t=TT)
    squares = m.work[:, 2 * D:4 * D].rearrange("p (t n) -> p t n", t=TT)
    ss = m.small[:, 0:2]
    ident = m.const("ident")

    def half(c):
        return m.ps[:, c // 2, (c % 2) * T:(c % 2) * T + T]

    with m.stage("rms_turned", "squares", "mean_ready", "std_ready", "scaled", "steps", "turned", "vector_moved",
                 "scalar_moved") as (block, s):
        @block.scalar
        def _(act):
            for t in range(TT):
                act.activation(squares[:, t, :], src[:, t, :], ACT.Square, accum_out=ss[:, t:t + 1]).then_inc(s["squares"], 1)
            act.wait_ge(s["mean_ready"], 1)
            act.activation(ss, ss, ACT.Sqrt).then_inc(s["std_ready"], 1)
            act.wait_ge(s["steps"], 1)
            act.activation(scaled[:, 1, :], src[:, 1, :], ACT.Copy, scale=ss[:, 1:2]).then_inc(s["scaled"], 1)
            for c in range(DC):
                act.wait_ge(s["turned"], c // 2 * 2 + 2)
                act.activation(m.xT_r[:, 0, c, :], half(c), ACT.Copy, scale=gcol[:, c:c + 1]).then_inc(s["scalar_moved"], 1)

        @block.vector
        def _(dve):
            link = chain(dve, s["steps"])
            rms_factors(dve, link, s, ss, eps)
            dve.tensor_scalar(scaled[:, 0, :], src[:, 0, :], ss[:, 0:1], None, ALU.mult).then_inc(s["steps"], 1)
            for c in range(DC):
                dve.wait_ge(s["scalar_moved"], c // 2 * 2 + 2)
                dve.scalar_tensor_tensor(m.xT_r[:, 1, c, :], half(c), gcol[:, c:c + 1], m.xT_r[:, 0, c, :].bitcast(F32),
                                         ALU.mult, ALU.subtract).then_inc(s["vector_moved"], 1)

        @block.tensor
        def _(pe):
            pe.wait_ge(s["steps"], 2)
            pe.wait_ge(s["scaled"], 1)
            for c in range(DC):
                for t in range(TT):
                    last = pe.transpose(half(c)[:, t * P:(t + 1) * P], scaled[:, t, c * P:(c + 1) * P], ident)
                last.then_inc(s["turned"], 1)


def rms_normed(m, gain, eps=1e-6):
    g = m.work[:, 0:D]
    squares = m.work[:, 2 * D:4 * D].rearrange("p (t n) -> p t n", t=TT)
    ss = m.small[:, 0:2]
    with m.stage("rms_normed", "gain_loaded", "squares", "mean_ready", "std_ready", "steps") as (block, s):
        @block.sync
        def _(sp):
            sp.dma_start(g, gain.partition_broadcast(P)).then_inc(s["gain_loaded"], 16)

        @block.scalar
        def _(act):
            for t in range(TT):
                act.activation(squares[:, t, :], m.x[:, t, :], ACT.Square, accum_out=ss[:, t:t + 1]).then_inc(s["squares"], 1)
            act.wait_ge(s["mean_ready"], 1)
            act.activation(ss, ss, ACT.Sqrt).then_inc(s["std_ready"], 1)

        @block.vector
        def _(dve):
            link = chain(dve, s["steps"])
            rms_factors(dve, link, s, ss, eps)
            dve.wait_ge(s["gain_loaded"], 16)
            for t in range(TT):
                dve.scalar_tensor_tensor(m.x[:, t, :], m.x[:, t, :], ss[:, t:t + 1], g, ALU.mult, ALU.mult).then_inc(s["steps"], 1)


TURN = 6.28125
TURN_LOW = float(np.float32(2 * math.pi - TURN))
TURN_LAST = 2 * math.pi - TURN - TURN_LOW
ROUND = 1.5 * 2.0 ** 23
HALF_TURN = 3.1415925


def rotary_tables(m, positions, tables):
    pos_i = m.small_i[:, 0:2]
    pos = m.small[:, 0:2]
    with m.stage("rotary_tables", "positions_loaded", "angles_ready", "steps", "made") as (block, s):
        @block.sync
        def _(sp):
            with m.nc.allow_non_contiguous_dma("one position a partition"):
                sp.dma_start(pos_i, positions[0].rearrange("(t p) -> p t", p=P)).then_inc(s["positions_loaded"], 16)

        @block.vector
        def _(dve):
            link = chain(dve, s["steps"])
            dve.wait_ge(s["positions_loaded"], 16)
            link(dve.tensor_copy(pos, pos_i))
            for cos, sin, freq, n in tables:
                k = m.work[:, 0:2 * n].rearrange("p (t n) -> p t n", t=TT)
                for t in range(TT):
                    link(dve.tensor_scalar(sin[:, t], freq, pos[:, t:t + 1], None, ALU.mult))
                link(dve.tensor_scalar(k, sin, 1.0 / (2 * math.pi), None, ALU.mult))
                link(dve.tensor_scalar(k, k, ROUND, None, ALU.add))
                link(dve.tensor_scalar(k, k, -ROUND, None, ALU.add))
                for part in (TURN, TURN_LOW, TURN_LAST):
                    link(dve.scalar_tensor_tensor(sin, k, -part, sin, ALU.mult, ALU.add))
                link(dve.tensor_scalar(cos, sin, math.pi / 2, None, ALU.add))
                link(dve.tensor_scalar(k, cos, math.pi, -2 * math.pi, ALU.is_gt, ALU.mult))
                link(dve.tensor_tensor(cos, cos, k, ALU.add))
                for x in (cos, sin):
                    link(dve.tensor_scalar(x, x, -HALF_TURN, HALF_TURN, ALU.max, ALU.min))
            dve.sem_inc(s["angles_ready"], 1)

        @block.scalar
        def _(act):
            act.wait_ge(s["angles_ready"], 1)
            for cos, sin, freq, n in tables:
                act.activation(cos, cos, ACT.Sin).then_inc(s["made"], 1)
                act.activation(sin, sin, ACT.Sin).then_inc(s["made"], 1)


def rotated(m, z, regions, cos, sin, half, tmp):
    tmp = [tmp[:, 0:1024], tmp[:, 1024:2048]]
    with m.stage("rotated", "vector_steps", "pool_steps") as (block, s):
        def turn(eng, link, t, regions, i):
            for col, n in regions:
                zz = z[:, t, col:col + n * 2 * half].rearrange("p (h k j) -> p h k j", k=2, j=half)
                a, b = zz[:, :, 0, :], zz[:, :, 1, :]
                c, sn = bview(cos[:, t], 1, n), bview(sin[:, t], 1, n)
                ta, tb = (tmp[i][:, at:at + n * half].rearrange("p (h j) -> p h j", h=n) for at in (0, 512))
                link(eng.tensor_tensor(ta, a, sn, ALU.mult))
                link(eng.tensor_tensor(tb, b, sn, ALU.mult))
                link(eng.tensor_tensor(a, a, c, ALU.mult))
                link(eng.tensor_tensor(b, b, c, ALU.mult))
                link(eng.tensor_tensor(a, a, tb, ALU.subtract))
                link(eng.tensor_tensor(b, b, ta, ALU.add))

        @block.vector
        def _(dve):
            link = chain(dve, s["vector_steps"])
            turn(dve, link, 0, regions, 0)
            turn(dve, link, 1, regions[-1:], 0)

        @block.gpsimd
        def _(pool):
            turn(pool, chain(pool, s["pool_steps"]), 1, regions[:-1], 1)


def overlapped(eng, n, body):
    body(0, 0, True, False)
    if n > 2:
        with eng.Fori(0, (n - 2) // 2) as g:
            for r in range(2):
                body(g * 2 + (r + 1), (r + 1) % 2, True, True)
    body(n - 1, 1, True, True)
    body(n, 0, False, True)


def ahead(eng, n, body):
    body(0, 0)
    body(1, 1)
    if n > 2:
        with eng.Fori(1, n // 2) as g:
            for r in range(2):
                body(g * 2 + r, r)


def attention(m, n, z, kv, q_at, k_at, v_at, scale, staging, neg=None, bias=None, cmp=None):
    w = m.work
    qn = 1 if cmp else 2
    qs = [staging[:, 512 * p:512 * p + 256].rearrange("p (t n) -> p t n", t=TT) for p in range(2)]
    ks = [staging[:, 512 * p + 256:512 * p + 512].rearrange("p (b t n) -> p b t n", b=2, t=TT) for p in range(2)]
    qT = w[0:HD, 0:512].rearrange("p (b t) -> p b t", b=2)
    kT = w[0:HD, 512:1024].rearrange("p (b t) -> p b t", b=2)
    L = [w[:, 1024 + 1024 * p:2048 + 1024 * p].rearrange("p (b t s) -> p b t s", b=2, t=TT) for p in range(2)]
    PT = w[:, 3072:4096].rearrange("p (b s t) -> p b s t", b=2, s=2)
    mx, sm = ([m.small[:, 24 * p + k:24 * p + k + 6] for p in range(2)] for k in (0, 6))
    fac = [m.small[:, 24 * p + 12:24 * p + 18].rearrange("p (b t) -> p b t", b=3) for p in range(2)]
    ident = m.const("ident")
    K = 6 if cmp else 4
    with m.stage("attention", "staged", "q_turned", "k_turned", "q_moved", "k_moved", "scores", "cmp_scores", "bias0_loaded", "bias1_loaded",
                 "bias_ready", "masked", "first_steps", "max_ready", "exp_out", "p0_turned", "p1_turned", "pc_turned",
                 "p0_moved", "p1_moved", "pc_moved", "second_steps", "sums_ready", "out_done") as (block, s):
        @block.sync
        def _(sp):
            def load(i, p):
                if not (isinstance(i, int) and i < 2):
                    sp.wait_ge(s["masked"], i - 1)
                for b in range(2):
                    sp.dma_start(bias["tiles"][p][:, b], bias["source"](i, b)).then_inc(s["bias0_loaded"] if p == 0 else s["bias1_loaded"], 16)

            if bias:
                ahead(sp, n, load)

        @block.gpsimd
        def _(pool):
            def stage(i, p):
                if not (isinstance(i, int) and i < 2):
                    pool.wait_ge(s["k_turned"], i - 1)
                pool.tensor_copy(qs[p][:, :, 0:qn * HD], z[:, :, bass.ds(q_at(i), qn * HD)]).then_inc(s["staged"], 1)
                for b in range(2):
                    pool.tensor_copy(ks[p][:, b], kv[:, :, bass.ds(k_at(i, b), HD)]).then_inc(s["staged"], 1)
                if bias:
                    pool.wait_ge(s["bias0_loaded"] if p == 0 else s["bias1_loaded"], i * 16 + (32 - 16 * p))
                    pool.tensor_tensor(bias["tiles"][p], bias["tiles"][p], bview(neg, 1, 2), ALU.add).then_inc(s["bias_ready"], 1)

            ahead(pool, n, stage)

        @block.tensor
        def _(pe):
            def turn(i, p):
                for b in range(qn):
                    for t in range(TT):
                        last = pe.transpose(m.ps[0:HD, 0, b * T + t * P:b * T + (t + 1) * P], qs[p][:, t, b * HD:(b + 1) * HD], ident)
                last.then_inc(s["q_turned"], 1)
                for b in range(2):
                    for t in range(TT):
                        last = pe.transpose(m.ps[0:HD, 1, b * T + t * P:b * T + (t + 1) * P], ks[p][:, b, t, :], ident)
                last.then_inc(s["k_turned"], 1)

            def body(i, p, first, second):
                later = not (isinstance(i, int) and i == 0)
                more = not (isinstance(i, int) and i >= n - 1)
                if first:
                    pe.wait_ge(s["q_moved"], i + 1)
                    pe.wait_ge(s["k_moved"], i + 1)
                    if more:
                        pe.wait_ge(s["staged"], i * 3 + 6)
                    if later:
                        pe.wait_ge(s["masked"], i)
                    for b in range(2):
                        for t in range(TT):
                            last = pe.matmul(m.ps[:, 2 + b, t * T:(t + 1) * T], qT[:, b % qn, t * P:(t + 1) * P], kT[:, b, :],
                                             start=True, stop=True)
                    last.then_inc(s["scores"], 1)
                    if cmp:
                        if later:
                            pe.wait_ge(s["first_steps"], i * 3)
                        for t in range(TT):
                            last = pe.matmul(m.ps[:, 7, t * NCMP:(t + 1) * NCMP], qT[:, 0, t * P:(t + 1) * P],
                                             cmp["keys"], start=True, stop=True)
                        last.then_inc(s["cmp_scores"], 1)
                if second:
                    for b in range(2):
                        pe.wait_ge(s["exp_out"], i * K + (2 * b + 2 - K))
                        for k in range(2):
                            for t in range(TT):
                                last = pe.transpose(m.ps[:, 4 + b, k * T + t * P:k * T + (t + 1) * P],
                                                    L[1 - p][:, b, t, k * P:(k + 1) * P], ident)
                        last.then_inc(s["p0_turned"] if b == 0 else s["p1_turned"], 1)
                if more:
                    turn(i + 1, 1 - p)
                if second:
                    if cmp:
                        pe.wait_ge(s["exp_out"], i * K)
                        if first:
                            pe.wait_ge(s["first_steps"], i * 3 + 3)
                        for t in range(TT):
                            last = pe.transpose(m.ps[0:NCMP, 7, T + t * P:T + (t + 1) * P], cmp["scores"][1 - p][:, t, :], ident)
                        last.then_inc(s["pc_turned"], 1)
                    pe.wait_ge(s["p0_moved"], i)
                    pe.wait_ge(s["p1_moved"], i)
                    for b in range(2):
                        for t in range(TT):
                            parts = range(2) if neg is None or t else range(1)
                            for k in parts:
                                last = pe.matmul(m.ps[:, 6, (b * 2 + t) * HD:(b * 2 + t + 1) * HD], PT[:, b, k, t * P:(t + 1) * P],
                                                 kv[:, k, bass.ds(v_at(i - 1, b), HD)], start=(k == 0), stop=(k == parts[-1]))
                    if cmp:
                        pe.wait_ge(s["pc_moved"], i)
                        for t in range(TT):
                            last = pe.matmul(m.ps[:, 6, (4 + t) * HD:(5 + t) * HD], cmp["turned"][:, t * P:(t + 1) * P],
                                             cmp["values"], start=True, stop=True)
                    last.then_inc(s["sums_ready"], 1)

            pe.wait_ge(s["staged"], 3)
            turn(0, 0)
            overlapped(pe, n, body)

        @block.vector
        def _(dve):
            def move_q(i):
                dve.wait_ge(s["q_turned"], i + 1)
                dve.tensor_copy(qT[:, 0:qn], m.ps[0:HD, 0, 0:qn * T].rearrange("p (b t) -> p b t", b=qn)).then_inc(s["q_moved"], 1)

            def masked(i, p):
                dve.wait_ge(s["scores"], i + 1)
                flat = L[p].rearrange("p b t s -> p b (t s)")
                sc = m.ps[:, 2:4, :]
                if bias:
                    dve.wait_ge(s["bias_ready"], i + 1)
                    ins = dve.scalar_tensor_tensor(flat, sc, scale, bias["tiles"][p].rearrange("p b t s -> p b (t s)"), ALU.mult, ALU.add)
                elif neg is not None:
                    ins = dve.scalar_tensor_tensor(flat, sc, scale, bview(neg.rearrange("p t s -> p (t s)"), 1, 2), ALU.mult, ALU.add)
                else:
                    ins = dve.tensor_scalar(flat, sc, scale, None, ALU.mult)
                ins.then_inc(s["masked"], 1)
                dve.wait_ge(s["masked"], i + 1)
                link = chain(dve, s["first_steps"], i * (3 if cmp else 1))
                link(dve.tensor_reduce(mx[p][:, 0:4], L[p].rearrange("p b t s -> p (b t) s"), AX, ALU.max))
                if cmp:
                    dve.wait_ge(s["cmp_scores"], i + 1)
                    link(dve.scalar_tensor_tensor(cmp["scores"][p], m.ps[:, 7, 0:2 * NCMP].rearrange("p (t s) -> p t s", t=TT), scale,
                                                  m.const("neg_cmp").rearrange("p (t s) -> p t s", t=TT), ALU.mult, ALU.add))
                    link(dve.tensor_reduce(mx[p][:, 4:6], cmp["scores"][p], AX, ALU.max))
                dve.tensor_scalar(mx[p][:, 0:K], mx[p][:, 0:K], -1.0, None, ALU.mult).then_inc(s["max_ready"], 1)

            def answer(i, p):
                if cmp:
                    dve.wait_ge(s["pc_turned"], i + 1)
                    dve.tensor_copy(cmp["turned"], m.ps[0:NCMP, 7, T:2 * T]).then_inc(s["pc_moved"], 1)
                link = chain(dve, s["second_steps"], i * (10 if cmp else 1))
                dve.wait_ge(s["exp_out"], i * K + K)
                link(dve.reciprocal(sm[p][:, 0:K], sm[p][:, 0:K]))
                if cmp:
                    link(dve.tensor_tensor(sm[p][:, 4:6], sm[p][:, 4:6], m.const("row_cmp"), ALU.mult))
                    for b, branch in enumerate((1, 2, 0)):
                        link(dve.tensor_tensor(fac[p][:, b, :], sm[p][:, 2 * b:2 * b + 2], cmp["gate"](i, branch), ALU.mult))
                dve.wait_ge(s["sums_ready"], i + 1)
                for t in range(TT):
                    if cmp:
                        o = z[:, t, bass.ds(q_at(i), HD)]
                        for b in range(3):
                            part = m.ps[:, 6, (b * 2 + t) * HD:(b * 2 + t + 1) * HD]
                            if b == 0:
                                ins = dve.tensor_scalar(o, part, fac[p][:, b, t:t + 1], None, ALU.mult)
                            else:
                                ins = dve.scalar_tensor_tensor(o, part, fac[p][:, b, t:t + 1], o, ALU.mult, ALU.add)
                            if t == 0 or b < 2:
                                link(ins)
                    else:
                        for b in range(2):
                            ins = dve.tensor_scalar(z[:, t, bass.ds(q_at(i) + b * HD, HD)],
                                                    m.ps[:, 6, (b * 2 + t) * HD:(b * 2 + t + 1) * HD],
                                                    sm[p][:, 2 * b + t:2 * b + t + 1], None, ALU.mult)
                ins.then_inc(s["out_done"], 1)

            def body(i, p, first, second):
                if first:
                    masked(i, p)
                if second:
                    dve.wait_ge(s["p0_turned"], i)
                    dve.tensor_copy(PT[:, 0].rearrange("p s t -> p (s t)"), m.ps[:, 4, :]).then_inc(s["p0_moved"], 1)
                if not (isinstance(i, int) and i >= n - 1):
                    move_q(i + 1)
                if second:
                    answer(i - 1, 1 - p)

            move_q(0)
            overlapped(dve, n, body)

        @block.scalar
        def _(act):
            def move_k(i):
                act.wait_ge(s["k_turned"], i + 1)
                act.copy(kT, m.ps[0:HD, 1, :].rearrange("p (b t) -> p b t", b=2)).then_inc(s["k_moved"], 1)

            def exponentials(i, p):
                act.wait_ge(s["max_ready"], i + 1)
                for b in range(2):
                    for t in range(TT):
                        j = 2 * b + t
                        act.activation(L[p][:, b, t, :], L[p][:, b, t, :], ACT.Exp, bias=mx[p][:, j:j + 1],
                                       accum_out=sm[p][:, j:j + 1]).then_inc(s["exp_out"], 1)
                if cmp:
                    for t in range(TT):
                        act.activation(cmp["scores"][p][:, t, :], cmp["scores"][p][:, t, :], ACT.Exp, bias=mx[p][:, 4 + t:5 + t],
                                       accum_out=sm[p][:, 4 + t:5 + t]).then_inc(s["exp_out"], 1)

            def body(i, p, first, second):
                if second:
                    act.wait_ge(s["p1_turned"], i)
                    act.copy(PT[:, 1].rearrange("p s t -> p (s t)"), m.ps[:, 5, :]).then_inc(s["p1_moved"], 1)
                if first:
                    exponentials(i, p)
                if not (isinstance(i, int) and i >= n - 1):
                    move_k(i + 1)

            move_k(0)
            overlapped(act, n, body)



def memory_attention(m, z, q0, kvm, staging):
    attention(m, 2, z, kvm, lambda i: i * (2 * HD) + q0, lambda i, b: i * (2 * HD) + b * HD,
              lambda i, b: i * (2 * HD) + (b + 4) * HD, HD ** -0.5, staging)


def compressor_places(m):
    w = m.work
    return (w[0:HD, 0:4096].rearrange("p (k l e) -> p k l e", k=2, l=32), w[0:HD, 4224:4352].rearrange("p (k e) -> p k e", k=2),
            (w[0:32, 4352:4416], w[0:32, 4096:4160]), m.small[:, 50:74])


def load_compressor(m, a, sp):
    w1, w2, pe_rows, gate_bias = compressor_places(m)
    for k, kind in enumerate(("k", "v")):
        sp.dma_start(w1[:, k], a[f"l0_cmp_w1_{kind}_2"].rearrange("l d e -> d l e")).then_inc(m.compressor_loaded, 16)
        sp.dma_start(w2[:, k], a[f"l0_cmp_w2_{kind}_2"]).then_inc(m.compressor_loaded, 16)
        sp.dma_start(pe_rows[k], a[f"l0_cmp_pe_{kind}_2"]).then_inc(m.compressor_loaded, 16)
    sp.dma_start(gate_bias, a["l0_nsa_gate_b_2"].partition_broadcast(P)).then_inc(m.compressor_loaded, 16)


def compressed(m, z, keys, values, aT, blk):
    w = m.work
    w1, w2, pe_rows, _ = compressor_places(m)
    peT = w[0:HD, 4160:4224].rearrange("p (k l) -> p k l", k=2)
    hid = m.small[0:HD, 288:348].rearrange("p (k n) -> p k n", k=2)
    ident = m.const("ident")
    with m.stage("compressed", "turned", "moved", "blocks_ready", "hidden", "silu_out", "made", "steps") as (block, s):
        @block.tensor
        def _(pe):
            pe.wait_ge(m.compressor_loaded, 112)
            for k in range(2):
                for g in range(2):
                    for t in range(TT):
                        c = 512 + k * 128 + g * HD
                        last = pe.transpose(m.ps[0:HD, k, g * T + t * P:g * T + (t + 1) * P], z[:, t, c:c + HD], ident)
                last.then_inc(s["turned"], 1)
            for k, rows in enumerate(pe_rows):
                last = pe.transpose(m.ps[0:HD, 2, k * 32:(k + 1) * 32], rows, ident[0:32, 0:32])
            last.then_inc(s["turned"], 1)
            for k in range(2):
                for l in range(32):
                    if l % 8 == 0:
                        pe.wait_ge(s["blocks_ready"], k * 32 + l + 8)
                    last = pe.matmul(m.ps[0:HD, 3 + k, 0:2 * NCMP], w1[:, k, l, :], blk[:, k, l], start=(l == 0), stop=(l == 31))
                last.then_inc(s["hidden"], 1)
            pe.wait_ge(s["silu_out"], 2)
            pe.matmul(m.ps[0:HD, 5, 0:2 * NCMP], w2[:, 0, :], hid[:, 0, :], start=True, stop=True).then_inc(s["made"], 1)
            for g in range(2):
                last = pe.matmul(m.ps[0:NCMP, 6, g * HD:(g + 1) * HD], hid[:, 1, g * NCMP:(g + 1) * NCMP], w2[:, 1, :],
                                 start=True, stop=True)
            last.then_inc(s["made"], 1)

        @block.vector
        def _(dve):
            link = chain(dve, s["steps"])
            dve.wait_ge(s["turned"], 3)
            for k in range(2):
                link(dve.tensor_copy(aT[:, k], m.ps[0:HD, k, :].rearrange("p (g t) -> p g t", g=2)))
            link(dve.tensor_copy(peT, m.ps[0:HD, 2, 0:64].rearrange("p (k l) -> p k l", k=2)))
            for k in range(2):
                for l in range(32):
                    dve.tensor_scalar(blk[:, k, l].rearrange("p (g n) -> p g n", g=2), aT[:, k, :, l:l + 16 * NCMP - 15:16],
                                      peT[:, k, l:l + 1], None, ALU.add).then_inc(s["blocks_ready"], 1)
            dve.wait_ge(s["made"], 2)
            link(dve.tensor_copy(keys, m.ps[0:HD, 5, 0:2 * NCMP]))
            link(dve.tensor_copy(values, m.ps[0:NCMP, 6, 0:2 * HD]))

        @block.scalar
        def _(act):
            for k in range(2):
                act.wait_ge(s["hidden"], k + 1)
                act.activation(hid[:, k, :], m.ps[0:HD, 3 + k, 0:2 * NCMP], ACT.Silu).then_inc(s["silu_out"], 1)


def even_layer(m, in_stream, out_stream, a, kvm, cos, sin):
    NIN = 4376
    ar = m.arena
    z = ar[:, 0:2 * NIN].rearrange("p (t n) -> p t n", t=TT)
    project(m, in_stream, NIN, lhs_x(m), z, lambda sp: load_compressor(m, a, sp))
    rotated(m, z, [(0, 10), (768, 2), (1024, 2), (1816, 16)], cos, sin, HD // 2, ar[:, 8752:10800])
    keys = m.small[0:HD, 128:158]
    values = m.small[0:NCMP, 160:288]
    aT = ar[0:HD, 10672:11696].rearrange("p (k g t) -> p k g t", k=2, g=2)
    blk = ar[0:HD, 8752:10672].rearrange("p (k l n) -> p k l n", k=2, l=32)
    compressed(m, z, keys, values, aT, blk)
    gates = z[:, :, 1280:1304]
    gate_bias = compressor_places(m)[3]
    with m.stage("branch_gates", "added", "gates_ready") as (block, s):
        @block.vector
        def _(dve):
            dve.wait_ge(m.compressor_loaded, 112)
            dve.tensor_tensor(gates, gates, bview(gate_bias, 1, TT), ALU.add).then_inc(s["added"], 1)

        @block.scalar
        def _(act):
            act.wait_ge(s["added"], 1)
            act.activation(gates, gates, ACT.Sigmoid).then_inc(s["gates_ready"], 1)

    neg = m.const("neg_causal").rearrange("p (t s) -> p t s", t=TT)
    staging = ar[:, 8752:9776]
    for g in range(2):
        cmp = dict(
            keys=keys[:, g * NCMP:(g + 1) * NCMP],
            values=values[:, g * HD:(g + 1) * HD],
            scores=[ar[:, 9776 + 32 * p:9806 + 32 * p].rearrange("p (t s) -> p t s", t=TT) for p in range(2)],
            turned=ar[0:NCMP, 9840:9840 + T],
            gate=lambda i, branch: z[:, :, bass.ds(i + (1280 + branch * 8 + g * 4), 1)].rearrange("p t o -> p (t o)"))
        attention(m, 4, z, z, lambda i: i * HD + g * 4 * HD, lambda i, b: 768 + b * 256 + g * HD,
                  lambda i, b: 896 + b * 256 + g * HD, HD ** -0.5, staging, neg=neg, cmp=cmp)
    attention(m, 4, z, z, lambda i: i * (2 * HD) + 1816, lambda i, b: i * (2 * HD) + (2328 + b * HD),
              lambda i, b: i * (2 * HD) + (2840 + b * HD), HD ** -0.5, staging, neg=neg)
    memory_attention(m, z, 3864, kvm, staging)
    gated(m, z, [(0, 1304, 512), (1816, 3352, 512), (3864, 4120, 256)], ACT.Silu)
    mixed_out(m, out_stream, z, [c * P for c in range(4)] + [1816 + c * P for c in range(4)] + [3864, 3992], 1.0, 1.0,
              low=lambda c: m.arena_r[:, 8752 + c * T:8752 + (c + 1) * T])


def odd_layer(m, in_stream, out_stream, kvm, cos, sin):
    H, QK, V = RET_HEADS, RET_QK, RET_V
    NIN = 6656
    z = m.arena[:, 0:2 * NIN].rearrange("p (t n) -> p t n", t=TT)
    project(m, in_stream, NIN, lhs_x(m), z)
    rotated(m, z, [(0, 4), (1024, 4)], cos, sin, QK // 2, m.work[:, 0:2048])
    memory_attention(m, z, 6144, kvm, m.work[:, 4096:5120])
    w = m.work
    places = (w[:, 0:2816], w[:, 2816:5632])
    qk = [v[:, 0:1024].rearrange("p (k t n) -> p k t n", k=2, t=TT) for v in places]
    qkT = [v[:, 1024:2048].rearrange("p (k c t) -> p k c t", k=2, c=2) for v in places]
    W = [v[:, 2048:2560].rearrange("p (k t) -> p k t", k=2) for v in places]
    decay = [v[:, 2560:2816].rearrange("p (i t) -> p i t", i=2) for v in places]
    a0 = m.layout["decay"][0]
    decays = m.consts[:, a0:a0 + H * 2 * P].rearrange("p (h n) -> p h n", h=H)
    stats, mv, rstd = ([m.small[:, a + k:a + k + n] for a in (80, 100)] for k, n in ((0, 12), (12, 4), (16, 2)))
    ident = m.const("ident")
    v0 = 2 * H * QK
    with m.nc.Fori(0, H // 2) as pair:
        def column(b, first, width):
            return bass.ds(pair * (2 * width) + (first + b * width), width)

        with m.stage("retention_heads", "decay_loaded", "staged", "turned", "q_moved", "k_moved", "scores", "weights_ready", "out_ready", "steps",
                     "eps_added", "std_ready") as (block, s):
            @block.sync
            def _(sp):
                for b in range(2):
                    sp.dma_start(decay[b].rearrange("p i t -> p (i t)"),
                                 decays[:, bass.ds(pair * 2 + b, 1), :].rearrange("p o n -> p (o n)")).then_inc(s["decay_loaded"], 16)

            @block.vector
            def _(dve):
                link = chain(dve, s["steps"])
                for b in range(2):
                    dve.tensor_copy(qk[b][:, 0], z[:, :, column(b, 0, QK)]).then_inc(s["staged"], 1)
                    dve.tensor_scalar(qk[b][:, 1], z[:, :, column(b, H * QK, QK)], QK ** -0.5, None, ALU.mult).then_inc(s["staged"], 1)
                for b in range(2):
                    dve.wait_ge(s["turned"], 2 * b + 1)
                    dve.tensor_copy(qkT[b][:, 0].rearrange("p c t -> p (c t)"), m.ps[:, 4 * b, :]).then_inc(s["q_moved"], 1)
                dve.wait_ge(s["decay_loaded"], 32)
                for b in range(2):
                    dve.wait_ge(s["scores"], b + 1)
                    sc = m.ps[:, 4 * b + 2, :].rearrange("p (k t) -> p k t", k=2)
                    for k in range(2):
                        link(dve.tensor_tensor(W[b][:, k, k * P:(k + 1) * P], sc[:, k, k * P:(k + 1) * P], decay[b][:, 0, :], ALU.mult))
                    dve.tensor_tensor(W[b][:, 0, P:T], sc[:, 0, P:T], decay[b][:, 1, :], ALU.mult).then_inc(s["weights_ready"], 1)
                added = [s["eps_added"], 0]
                for b in range(2):
                    dve.wait_ge(s["out_ready"], 2 * b + 2)
                    head_normed(dve, link, added, s["std_ready"], lambda t: m.ps[:, 4 * b + t, :],
                                lambda t: z[:, t, column(b, v0, V)], stats[b], mv[b], rstd[b], 1e-6)

            @block.tensor
            def _(pe):
                for b in range(2):
                    pe.wait_ge(s["staged"], 2 * b + 2)
                    for k in range(2):
                        for c in range(2):
                            for t in range(TT):
                                last = pe.transpose(m.ps[:, 4 * b + k, c * T + t * P:c * T + (t + 1) * P],
                                                    qk[b][:, k, t, c * P:(c + 1) * P], ident)
                        last.then_inc(s["turned"], 1)
                for b in range(2):
                    pe.wait_ge(s["q_moved"], b + 1)
                    pe.wait_ge(s["k_moved"], b + 1)
                    for k in range(2):
                        for c in range(2):
                            last = pe.matmul(m.ps[:, 4 * b + 2, k * T:(k + 1) * T], qkT[b][:, 1, c, k * P:(k + 1) * P],
                                             qkT[b][:, 0, c, :], start=(c == 0), stop=(c == 1))
                    last.then_inc(s["scores"], 1)
                for b in range(2):
                    pe.wait_ge(s["weights_ready"], b + 1)
                    v = z[:, :, column(b, v0, V)]
                    for t in range(TT):
                        for k in range(t + 1):
                            last = pe.matmul(m.ps[:, 4 * b + t, :], W[b][:, k, t * P:(t + 1) * P], v[:, k, :], start=(k == 0), stop=(k == t))
                        last.then_inc(s["out_ready"], 1)

            @block.scalar
            def _(act):
                for b in range(2):
                    act.wait_ge(s["turned"], 2 * b + 2)
                    act.copy(qkT[b][:, 1].rearrange("p c t -> p (c t)"), m.ps[:, 4 * b + 1, :]).then_inc(s["k_moved"], 1)
                for b in range(2):
                    act.wait_ge(s["eps_added"], b + 1)
                    act.activation(rstd[b], rstd[b], ACT.Sqrt).then_inc(s["std_ready"], 1)
        with m.stage("even_number") as (block, s):
            pass
    gated(m, z, [(v0, 4096, 2048), (6144, 6400, 256)], ACT.Silu)

    def low(c):
        if c < 16:
            return m.arena_r[:, (c // 8) * NIN + (c % 8) * T:(c // 8) * NIN + (c % 8 + 1) * T]
        return m.work_r[:, (c + 2) * T:(c + 3) * T]

    mixed_out(m, out_stream, z, [v0 + c * P for c in range(16)] + [6144, 6272], 1.0, 1.0, low=low)


def second_block(m, q, a):
    kvm0 = m.arena[:, 12288:13312].rearrange("p (t n) -> p t n", t=TT)
    kvm1 = m.work[:, 5120:6144].rearrange("p (t n) -> p t n", t=TT)
    acos, asin = (m.arena[:, 12160 + 64 * i:12224 + 64 * i].rearrange("p (t n) -> p t n", t=TT) for i in range(2))
    rcos, rsin = (m.keep[:, 256 * i:256 * i + 256].rearrange("p (t n) -> p t n", t=TT) for i in range(2))
    rotary_tables(m, a["positions_2"], [(acos, asin, m.const("attn_inv"), HD // 2), (rcos, rsin, m.const("ret_inv"), P)])
    mem = m.arena[:, 0:2 * D].rearrange("p (t n) -> p t n", t=TT)
    with m.stage("memory_loaded", "memory_loaded") as (block, s):
        @block.sync
        def _(sp):
            sp.dma_start(mem, a["mem_2"][0].rearrange("(t p) n -> p t n", p=P)).then_inc(s["memory_loaded"], 16)
            sp.wait_ge(s["memory_loaded"], 16)
    rms_turned(m, mem, "mem_norm_g")
    project(m, next(q), 2 * 4 * HD, lhs_x(m), kvm0)
    project(m, next(q), 2 * 4 * HD, lhs_x(m), kvm1)
    rms_turned(m, m.x, "l0_norm_g")
    even_layer(m, next(q), next(q), a, kvm0, acos, asin)
    rms_turned(m, m.x, "l1_norm_g")
    odd_layer(m, next(q), next(q), kvm1, rcos, rsin)
    rms_normed(m, a["final_norm_g_2"])



def ffn(m, gu_stream, down_stream, norm):
    rms_turned(m, m.x, norm)
    hT = m.arena_r[:, 0:2 * FFC * T].rearrange("p (k c t) -> p k c t", k=2, c=FFC)
    sg = m.work[:, 0:2 * BANK].rearrange("p (j n) -> p j n", j=2)
    prod = m.work[:, 2 * BANK:3 * BANK].rearrange("p (f t) -> p f t", f=2)
    gs = gu_stream
    with m.stage("ffn", "high_ready", "low_ready", "halves_used", "gate_freed", "up_freed", "steps") as (block, s):
        @block.sync
        def _(sp):
            gs.load_rest(sp)
            follow(m, gs, sp, s)

        @block.tensor
        def _(pe):
            def unit(g, j):
                for k, freed in enumerate((s["gate_freed"], s["up_freed"])):
                    pe.wait_ge(freed, g * 2 + j + 1)
                    pe.wait_ge(s["low_ready"], (g * 2 + j) * 2 + k + 1)
                    for f in range(2):
                        for c in range(DC):
                            for i, (xp, wp) in enumerate(PASSES):
                                w = m.halves[:, k, wp, :].rearrange("p (c n) -> p c n", c=DC)
                                last = pe.matmul(m.ps[:, 2 * j + k, f * T:(f + 1) * T], w[:, c, f * P:(f + 1) * P],
                                                 m.xT_r[:, xp, c, :], start=(c == 0 and i == 0), stop=(c == DC - 1 and i == 2))
                    last.then_inc(s["halves_used"], 1)

            gs.each(pe, unit)

        def back(g, j):
            return (g, j - 1) if j else (g - 1, 1)

        @block.scalar
        def _(act):
            act.sem_inc(s["gate_freed"], 2)

            def silu(g, j):
                act.wait_ge(s["halves_used"], (g * 2 + j) * 2 + 1)
                act.wait_ge(s["up_freed"], g * 2 + j + 1)
                act.activation(sg[:, j, :], m.ps[:, 2 * j, :], ACT.Silu).then_inc(s["gate_freed"], 1)

            def unit(g, j):
                for k in range(2):
                    high_part(m, gs, act, s, g, j, k)
                if not (isinstance(g, int) and g == 0 and j == 0):
                    silu(*back(g, j))

            gs.each(act, unit, peel=True)
            silu((gs.n - 1) // 2, (gs.n - 1) % 2)

        @block.vector
        def _(dve):
            dve.sem_inc(s["up_freed"], 2)

            def hidden(g, j):
                u = g * 2 + j
                link = chain(dve, s["steps"], u * 3)
                dve.wait_ge(s["halves_used"], u * 2 + 2)
                dve.wait_ge(s["gate_freed"], u + 3)
                link(dve.tensor_tensor(prod, sg[:, j, :].rearrange("p (f t) -> p f t", f=2),
                                       m.ps[:, 2 * j + 1, :].rearrange("p (f t) -> p f t", f=2), ALU.mult))
                high = hT[:, 0, bass.ds(u * 2, 2), :]
                link(dve.tensor_copy(high, prod))
                link(dve.tensor_tensor(hT[:, 1, bass.ds(u * 2, 2), :], prod, high.bitcast(F32), ALU.subtract))
                dve.sem_inc(s["up_freed"], 1)

            def unit(g, j):
                for k in range(2):
                    low_part(m, gs, dve, s, g, j, k, last=False)
                if not (isinstance(g, int) and g == 0 and j == 0):
                    hidden(*back(g, j))

            gs.each(dve, unit, peel=True)
            hidden((gs.n - 1) // 2, (gs.n - 1) % 2)
    project_out(m, down_stream, FFC, lambda part, c, t: hT[:, part, c, t * P:(t + 1) * P], 1.0, 0.5)


def pool_conv(m, in_stream, out_stream, a):
    NIN = 3 * BANK
    C = 4
    ar, w = m.arena, m.work
    z = ar[:, 0:2 * NIN].rearrange("p (t n) -> p t n", t=TT)
    project(m, in_stream, NIN, lhs_x(m), z)
    uT = ar[:, 3072:6144].rearrange("p (c t) -> p c t", c=12)
    transposed(m, 12, lambda c, t: z[:, t, c * P:(c + 1) * P], lambda c: uT[:, c, :])
    yT = ar[:, 6144:8192].rearrange("p (c t) -> p c t", c=DC)
    dm = ar[:, 8192:9216].rearrange("p (c t) -> p c t", c=C)
    pw = ar[:, 9216:9728].rearrange("p (c d) -> p c d", c=C)
    PAD = CONV_K - 1
    zp = ar[:, 9728:9728 + C * (T + PAD)].rearrange("p (c t) -> p c t", c=C)
    acc = ar[:, 10880:11904].rearrange("p (c t) -> p c t", c=C)
    tn = ar[:, 0:1024].rearrange("p (t n) -> p t n", t=TT)
    cw_rows = ar[0:CONV_K, 1024:1536]
    cw = m.small[:, 100:100 + C * 32].rearrange("p (c k) -> p c k", c=C)
    scale, cb, lg, lb = (m.columns[k] for k in ("pool_scale", "conv_b", "conv_ln_g", "conv_ln_b"))
    OFF = 16
    lv = [w[:, k * C * (T + OFF):(k + 1) * C * (T + OFF)].rearrange("p (c t) -> p c t", c=C) for k in range(5)]
    stats, mv, rstd = m.small[:, 80:92], m.small[:, 92:96], m.small[:, 96:98]
    ident = m.const("ident")
    first = m.const("pool_count").rearrange("p (g t) -> p g t", g=C)
    VC, ND = 2, 8
    turns = [(c, k) for c in range(VC, C) for k in range(CONV_K)]
    diagonal = ar[:, 11904:11904 + ND * P].rearrange("p (i n) -> p i n", i=ND)
    with m.stage("pool_conv", "weights_loaded", "cw_turned", "means_ready", "pooled", "sig_out", "conv_done", "acc_turned", "eps_added",
                 "std_ready", "normed", "back_turned", "pool_out", "conv_out", "steps", "taps", "cw_ready", "gated", "diagonal_ready", "diagonal_used", "zeroed") as (block, s):
        @block.sync
        def _(sp):
            sp.dma_start(pw, a["pool_w_3"][0].rearrange("g c d -> c g d")).then_inc(s["weights_loaded"], 16)
            sp.dma_start(cw_rows, a["conv_w_3"][0]).then_inc(s["weights_loaded"], 16)

        @block.gpsimd
        def _(pool):
            pool.memset(zp[:, :, 0:PAD], 0.0).then_inc(s["zeroed"], 1)
            for k in range(5):
                pool.memset(lv[k][:, :, 0:OFF], 0.0).then_inc(s["zeroed"], 1)

        @block.vector
        def _(dve):
            link = chain(dve, s["steps"])
            dve.wait_ge(s["zeroed"], 6)
            dve.wait_ge(s["cw_turned"], 1)
            link(dve.tensor_copy(cw[:, :, 0:CONV_K], m.ps[:, 0, 0:C * 32].rearrange("p (c k) -> p c k", c=C)[:, :, 0:CONV_K]))
            dve.sem_inc(s["cw_ready"], 1)
            dve.wait_ge(s["sig_out"], 1)
            link(dve.tensor_tensor(zp[:, :, PAD:], uT[:, C:2 * C, :], uT[:, 2 * C:3 * C, :], ALU.mult))
            dve.sem_inc(s["gated"], 1)
            link(dve.tensor_copy(lv[0][:, :, OFF:], uT[:, 0:C, :]))
            for k in range(4):
                src, dst = lv[k][:, k if k else 0:, :], lv[k + 1][:, k if k else 0:, :]
                sh = 1 << k
                link(dve.tensor_tensor(dst[:, :, OFF:], src[:, :, OFF:], src[:, :, OFF - sh:OFF - sh + T], ALU.add))
            for g in range(C):
                sums = lv[g + 1][:, g, OFF:]
                link(dve.tensor_tensor(dm[:, g, 0:16], sums[:, 0:16], first[:, g, :], ALU.mult))
                link(dve.tensor_scalar(dm[:, g, 16:], sums[:, 16:], 1.0 / (2 << g), None, ALU.mult))
            dve.tensor_tensor(dm, dm, uT[:, 0:C, :], ALU.subtract).then_inc(s["means_ready"], 1)
            for k in range(CONV_K):
                for c in range(VC):
                    if k == 0:
                        dve.tensor_scalar(acc[:, c, :], zp[:, c, 0:T], cw[:, c, 0:1], cb[:, c:c + 1], ALU.mult,
                                          ALU.add).then_inc(s["taps"], 1)
                    else:
                        dve.wait_ge(s["taps"], (k - 1) * VC + c + 1)
                        dve.scalar_tensor_tensor(acc[:, c, :], zp[:, c, k:k + T], cw[:, c, k:k + 1], acc[:, c, :],
                                                 ALU.mult, ALU.add).then_inc(s["taps"], 1)
            for c in range(VC, C):
                dve.wait_ge(s["diagonal_used"], (c - VC + 1) * CONV_K)
                dve.tensor_scalar(acc[:, c, :], m.ps[:, c, 0:T], cb[:, c:c + 1], None, ALU.add).then_inc(s["taps"], 1)
            added = [s["eps_added"], 0]
            dve.wait_ge(s["acc_turned"], 1)
            head_normed(dve, link, added, s["std_ready"], lambda t: m.ps[:, 4 + t, :], lambda t: tn[:, t, :], stats, mv, rstd, 1e-6)
            dve.sem_inc(s["normed"], 1)
            dve.wait_ge(s["pooled"], 1)
            for g in range(C):
                dve.tensor_scalar(yT[:, g, :], m.ps[:, g // 2, (g % 2) * T:(g % 2 + 1) * T], scale[:, g:g + 1], None,
                                  ALU.mult).then_inc(s["pool_out"], 1)

        @block.tensor
        def _(pe):
            pe.wait_ge(s["weights_loaded"], 32)
            for c in range(C):
                last = pe.transpose(m.ps[:, 0, c * 32:c * 32 + CONV_K], cw_rows[:, c * P:(c + 1) * P], ident[0:CONV_K, 0:CONV_K])
            last.then_inc(s["cw_turned"], 1)
            pe.wait_ge(s["gated"], 1)
            for i, (c, k) in enumerate(turns):
                pe.wait_ge(s["diagonal_ready"], i + 1)
                pe.matmul(m.ps[:, c, 0:T], diagonal[:, i % ND, :], zp[:, c, k:k + T], start=(k == 0),
                          stop=(k == CONV_K - 1)).then_inc(s["diagonal_used"], 1)
            pe.wait_ge(s["means_ready"], 1)
            for g in range(C):
                last = pe.matmul(m.ps[:, g // 2, (g % 2) * T:(g % 2 + 1) * T], pw[:, g, :], dm[:, g, :], start=True, stop=True)
            last.then_inc(s["pooled"], 1)
            pe.wait_ge(s["taps"], CONV_K * VC + C - VC)
            for t in range(TT):
                for c in range(C):
                    last = pe.transpose(m.ps[:, 4 + t, c * P:(c + 1) * P], acc[:, c, t * P:(t + 1) * P], ident)
            last.then_inc(s["acc_turned"], 1)
            pe.wait_ge(s["normed"], 1)
            for c in range(C):
                for t in range(TT):
                    last = pe.transpose(m.ps[:, 6 + c // 2, (c % 2) * T + t * P:(c % 2) * T + (t + 1) * P],
                                        tn[:, t, c * P:(c + 1) * P], ident)
            last.then_inc(s["back_turned"], 1)

        @block.scalar
        def _(act):
            act.activation(uT[:, 2 * C:3 * C, :], uT[:, 2 * C:3 * C, :], ACT.Sigmoid).then_inc(s["sig_out"], 1)
            act.wait_ge(s["cw_ready"], 1)
            for i, (c, k) in enumerate(turns):
                if i >= ND:
                    act.wait_ge(s["diagonal_used"], i - ND + 1)
                act.activation(diagonal[:, i % ND, :], ident, ACT.Copy, scale=cw[:, c, k:k + 1]).then_inc(s["diagonal_ready"], 1)
            act.wait_ge(s["eps_added"], 1)
            act.activation(rstd, rstd, ACT.Sqrt).then_inc(s["std_ready"], 1)
            act.wait_ge(s["back_turned"], 1)
            for c in range(C):
                act.activation(yT[:, C + c, :], m.ps[:, 6 + c // 2, (c % 2) * T:(c % 2 + 1) * T], ACT.Silu,
                               bias=lb[:, c:c + 1], scale=lg[:, c:c + 1]).then_inc(s["conv_out"], 1)
    yT_r = m.arena_r[:, 0:4096].rearrange("p (k c t) -> p k c t", k=2, c=DC)
    with m.stage("pool_conv_parts", "high_ready", "low_ready") as (block, s):
        @block.scalar
        def _(act):
            for c in range(0, DC, 2):
                act.copy(yT_r[:, 0, c:c + 2, :], yT[:, c:c + 2, :]).then_inc(s["high_ready"], 1)

        @block.vector
        def _(dve):
            for c in range(0, DC, 2):
                dve.wait_ge(s["high_ready"], c // 2 + 1)
                dve.tensor_tensor(yT_r[:, 1, c:c + 2, :], yT[:, c:c + 2, :], yT_r[:, 0, c:c + 2, :].bitcast(F32),
                                  ALU.subtract).then_inc(s["low_ready"], 1)
    project_out(m, out_stream, DC, lambda part, c, t: yT_r[:, part, c, t * P:(t + 1) * P], 1.0, 1.0)


HEADS = 16
IDX_HEADS, IDX_DIM = 8, 64


def expand_bias(m, a, rows, tiles):
    rb = m.small[0:32, 0:HEADS]
    line = m.work[0:HEADS, 0:2 * T]
    bucket = m.work[0:32, 1024:1024 + T]
    with m.stage("expand_bias", "loaded", "spread", "ready", "stored", "zeroed") as (block, s):
        @block.sync
        def _(sp):
            a0 = m.layout["dist_bucket"][0]
            sp.dma_start(rb, a["rel_bias_3"]).then_inc(s["loaded"], 16)
            sp.dma_start(bucket, m.consts[0:32, a0:a0 + T]).then_inc(s["loaded"], 16)
            sp.wait_ge(s["ready"], 1)
            sp.dma_start(rows, line).then_inc(s["stored"], 16)
            sp.wait_ge(s["stored"], 16)
            for t in range(TT):
                src = bass.AP(rows.tensor, T - 1 - t * P, [[2 * T, HEADS], [-1, P], [1, T]])
                sp.dma_start(tiles[:, t], src).then_inc(m.bias_stored, 16)

        @block.tensor
        def _(pe):
            pe.wait_ge(s["loaded"], 32)
            pe.matmul(m.ps[0:HEADS, 0, 0:T], rb, bucket, start=True, stop=True).then_inc(s["spread"], 1)

        @block.vector
        def _(dve):
            dve.memset(line[:, T:], 0.0).then_inc(s["zeroed"], 1)
            dve.wait_ge(s["spread"], 1)
            dve.wait_ge(s["zeroed"], 1)
            dve.tensor_copy(line[:, 0:T], m.ps[0:HEADS, 0, 0:T]).then_inc(s["ready"], 1)


def selected_attention(m, in_stream, out_stream, tiles):
    NIN = 3 * D + IDX_HEADS * IDX_DIM + IDX_DIM + IDX_HEADS
    ar, w = m.arena, m.work
    z = ar[:, 0:2 * NIN].rearrange("p (t n) -> p t n", t=TT)
    project(m, in_stream, NIN, lhs_x(m), z)
    qi0, ki0, wi0 = 3 * D, 3 * D + IDX_HEADS * IDX_DIM, 3 * D + IDX_HEADS * IDX_DIM + IDX_DIM
    score = ar[:, 7312:7824].rearrange("p (t s) -> p t s", t=TT)
    neg = ar[:, 7824:8336].rearrange("p (t s) -> p t s", t=TT)
    kiT = ar[0:IDX_DIM, 8336:8592]
    causal = m.const("neg_causal").rearrange("p (t s) -> p t s", t=TT)
    ident = m.const("ident")
    with m.stage("indexer_keys", "turned", "steps") as (block, s):
        @block.tensor
        def _(pe):
            for t in range(TT):
                last = pe.transpose(m.ps[0:IDX_DIM, 0, t * P:(t + 1) * P], z[:, t, ki0:ki0 + IDX_DIM], ident)
            last.then_inc(s["turned"], 1)

        @block.vector
        def _(dve):
            dve.memset(score, 0.0).then_inc(s["steps"], 1)
            dve.wait_ge(s["turned"], 1)
            dve.tensor_copy(kiT, m.ps[0:IDX_DIM, 0, 0:T]).then_inc(s["steps"], 1)

    places = (w[:, 0:1792], w[:, 1792:3584])
    qs = [v[:, 0:256].rearrange("p (t n) -> p t n", t=TT) for v in places]
    qT = [v[0:IDX_DIM, 256:768].rearrange("p (b t) -> p b t", b=2) for v in places]
    R = [v[:, 768:1792].rearrange("p (b t s) -> p b t s", b=2, t=TT) for v in places]
    wi = [m.small[:, 4 * r:4 * r + 4].rearrange("p (t b) -> p t b", t=TT) for r in range(2)]
    with m.nc.Fori(0, IDX_HEADS // 4) as i:
        with m.stage("indexer_scores", "staged", "turned", "moved", "scores", "relu_out", "steps") as (block, s):
            @block.vector
            def _(dve):
                link = chain(dve, s["steps"])
                for r in range(2):
                    dve.tensor_copy(qs[r], z[:, :, bass.ds(i * (4 * IDX_DIM) + (qi0 + r * 2 * IDX_DIM), 2 * IDX_DIM)]).then_inc(s["staged"], 1)
                for r in range(2):
                    link(dve.tensor_copy(wi[r], z[:, :, bass.ds(i * 4 + (wi0 + 2 * r), 2)]))
                for r in range(2):
                    dve.wait_ge(s["turned"], r + 1)
                    dve.tensor_copy(qT[r], m.ps[0:IDX_DIM, 4 * r, :].rearrange("p (b t) -> p b t", b=2)).then_inc(s["moved"], 1)
                for r in range(2):
                    for b in range(2):
                        dve.wait_ge(s["relu_out"], 2 * r + b + 1)
                        for t in range(TT):
                            link(dve.scalar_tensor_tensor(score[:, t, :], R[r][:, b, t, :], wi[r][:, t, b:b + 1], score[:, t, :],
                                                          ALU.mult, ALU.add))

            @block.tensor
            def _(pe):
                for r in range(2):
                    pe.wait_ge(s["staged"], r + 1)
                    for b in range(2):
                        for t in range(TT):
                            last = pe.transpose(m.ps[0:IDX_DIM, 4 * r, b * T + t * P:b * T + (t + 1) * P],
                                                qs[r][:, t, b * IDX_DIM:(b + 1) * IDX_DIM], ident)
                    last.then_inc(s["turned"], 1)
                for r in range(2):
                    pe.wait_ge(s["moved"], r + 1)
                    for b in range(2):
                        for t in range(TT):
                            last = pe.matmul(m.ps[:, 4 * r + 1 + b, t * T:(t + 1) * T], qT[r][:, b, t * P:(t + 1) * P], kiT,
                                             start=True, stop=True)
                        last.then_inc(s["scores"], 1)

            @block.scalar
            def _(act):
                for r in range(2):
                    for b in range(2):
                        act.wait_ge(s["scores"], 2 * r + b + 1)
                        act.activation(R[r][:, b].rearrange("p t s -> p (t s)"), m.ps[:, 4 * r + 1 + b, :],
                                       ACT.Relu).then_inc(s["relu_out"], 1)
        with m.stage("even_number") as (block, s):
            pass

    top = m.small[:, 8:24].rearrange("p (t k) -> p t k", t=TT)
    STRUCK = -3e38
    with m.stage("keys_selected", "steps") as (block, s):
        @block.vector
        def _(dve):
            link = chain(dve, s["steps"])
            link(dve.tensor_scalar(score, score, (IDX_HEADS * IDX_DIM) ** -0.5, None, ALU.mult))
            link(dve.tensor_tensor(score, score, causal, ALU.add))
            done = 2
            for _ in range(TOPK // 8):
                for op in range(2):
                    for t in range(TT):
                        if done > 3:
                            dve.wait_ge(s["steps"], done - 1)
                        if op == 0:
                            ins = dve.max(top[:, t, :], score[:, t, :])
                        else:
                            ins = dve.match_replace(score[:, t, :], top[:, t, :], score[:, t, :], STRUCK)
                        ins.then_inc(s["steps"], 1)
                        done += 1
            dve.wait_ge(s["steps"], done)
            link = chain(dve, s["steps"], done)
            link(dve.tensor_scalar(neg, score, STRUCK / 2, NEG, ALU.is_gt, ALU.mult))
            link(dve.tensor_tensor(neg, neg, causal, ALU.add))

        @block.sync
        def _(sp):
            sp.wait_ge(m.bias_stored, 32)
    bias = dict(tiles=[ar[:, 8592 + 1024 * p:9616 + 1024 * p].rearrange("p (b t s) -> p b t s", b=2, t=TT) for p in range(2)],
                source=lambda i, b: tiles[bass.ds(i * 2 + b, 1)].rearrange("o t p s -> (o p) t s"))
    attention(m, HEADS // 2, z, z, lambda i: i * (2 * HD), lambda i, b: i * (2 * HD) + (D + b * HD),
              lambda i, b: i * (2 * HD) + (2 * D + b * HD), HD ** -0.5, w[:, 4096:5120], neg=neg, bias=bias)
    mixed_out(m, out_stream, z, [c * P for c in range(DC)], 1.0, 1.0)


def third_block(m, q, a, rows, tiles):
    expand_bias(m, a, rows, tiles)
    for layer in range(DEPTH):
        ffn(m, next(q), next(q), f"ffn1_norm_{layer}")
        rms_turned(m, m.x, f"mix_norm_{layer}")
        if layer == 0:
            pool_conv(m, next(q), next(q), a)
        else:
            selected_attention(m, next(q), next(q), tiles)
        ffn(m, next(q), next(q), f"ffn2_norm_{layer}")
    rms_normed(m, a["final_norm_3"])


USED = ["x", "mlstm_w_in", "mlstm_gate_b", "mlstm_norm_g", "mlstm_w_out", "gla_w_in", "gla_gate_w", "gla_gate_b",
        "gla_norm_g", "gla_w_out", "moe_router", "moe_w_gate", "moe_w_up", "moe_w_down", "ln_g", "ln_b",
        "mem_2", "positions_2", "l0_norm_g_2", "l0_w_in_2", "l0_nsa_gate_b_2", "l0_cmp_pe_k_2", "l0_cmp_w1_k_2",
        "l0_cmp_w2_k_2", "l0_cmp_pe_v_2", "l0_cmp_w1_v_2", "l0_cmp_w2_v_2", "l0_w_mem_kv_2", "l0_w_out_2", "l1_norm_g_2",
        "l1_w_in_2", "l1_w_mem_kv_2", "l1_w_out_2", "mem_norm_g_2", "final_norm_g_2",
        "ffn1_norm_3", "ffn1_w_gate_3", "ffn1_w_up_3", "ffn1_w_down_3", "mix_norm_3", "ffn2_norm_3", "ffn2_w_gate_3",
        "ffn2_w_up_3", "ffn2_w_down_3", "ab_w_in_3", "pool_w_3", "pool_scale_3", "conv_w_3", "conv_b_3", "conv_ln_g_3",
        "conv_ln_b_3", "ab_w_out_3", "c_w_in_3", "c_w_out_3", "rel_bias_3", "final_norm_3"]


def columns(a):
    out = [("mlstm_norm_g", a["mlstm_norm_g"][0]), ("gla_gate_b", a["gla_gate_b"][0].rearrange("d n -> (d n)")),
           ("gla_norm_g", a["gla_norm_g"][0]), ("mem_norm_g", a["mem_norm_g_2"]), ("l0_norm_g", a["l0_norm_g_2"]),
           ("l1_norm_g", a["l1_norm_g_2"])]
    out += [(f"{k}_{layer}", a[f"{k}_3"][layer]) for k in ("ffn1_norm", "mix_norm", "ffn2_norm") for layer in range(DEPTH)]
    return out + [(k, a[f"{k}_3"][0]) for k in ("pool_scale", "conv_b", "conv_ln_g", "conv_ln_b")]


def streams(m, a):
    columns_stream(m, a["mlstm_w_in"][0], 3088, 0)
    rows_stream(m, a["mlstm_w_out"][0], D, 2)
    expert_stream(m, a["moe_w_gate"][0], a["moe_w_up"][0], a["moe_w_down"][0], 0)
    columns_stream(m, a["gla_w_in"][0], 3104, 0)
    rows_stream(m, a["gla_w_out"][0], D, 2)
    expert_stream(m, a["moe_w_gate"][1], a["moe_w_up"][1], a["moe_w_down"][1], 0)
    columns_stream(m, a["l0_w_mem_kv_2"], 512, 0)
    columns_stream(m, a["l1_w_mem_kv_2"], 512, 2)
    columns_stream(m, a["l0_w_in_2"], 4376, 0)
    rows_stream(m, a["l0_w_out_2"], 1280, 2)
    columns_stream(m, a["l1_w_in_2"], 6656, 0)
    rows_stream(m, a["l1_w_out_2"], 2304, 2)
    for layer, (w_in, n, w_out) in enumerate((("ab_w_in_3", 1536, "ab_w_out_3"), ("c_w_in_3", 3656, "c_w_out_3"))):
        ffn_stream(m, a["ffn1_w_gate_3"][layer], a["ffn1_w_up_3"][layer], 0)
        rows_stream(m, a["ffn1_w_down_3"][layer], D_FF, 2)
        columns_stream(m, a[w_in][0], n, 0)
        rows_stream(m, a[w_out][0], D, 2)
        ffn_stream(m, a["ffn2_w_gate_3"][layer], a["ffn2_w_up_3"][layer], 0)
        rows_stream(m, a["ffn2_w_down_3"][layer], D_FF, 2)


def layers(m, a, rows, tiles):
    q = iter(m.queue)
    turn_x(m)
    mlstm(m, next(q), next(q), a["mlstm_gate_b"][0], (a["ln_g"][0, 0], a["ln_b"][0, 0], a["moe_router"][0]))
    layer_normed(m)
    turn_x(m, split=False)
    moe(m, next(q), (a["ln_g"][0, 1], a["ln_b"][0, 1]))
    layer_normed(m)
    turn_x(m)
    gla(m, next(q), next(q), a["gla_gate_w"][0], (a["ln_g"][1, 0], a["ln_b"][1, 0], a["moe_router"][1]))
    layer_normed(m)
    turn_x(m, split=False)
    moe(m, next(q), (a["ln_g"][1, 1], a["ln_b"][1, 1]))
    layer_normed(m)
    second_block(m, q, a)
    third_block(m, q, a, rows, tiles)


def program(nc, a, consts, out, rows, tiles):
    with ExitStack() as ctx:
        m = Machine(nc, ctx, consts)
        streams(m, a)
        with m.stage("inputs_loaded", "inputs_loaded") as (block, s):
            @block.scalar
            def _(act):
                for name, vec in columns(a):
                    m.load_columns(act, name, vec)

            @block.sync
            def _(sp):
                sp.dma_start(m.x[:, :, :], a["x"][0].rearrange("(t p) n -> p t n", p=P)).then_inc(s["inputs_loaded"], 16)
                sp.dma_start(m.cst[:, :], consts[:, 0:m.cst.shape[1]]).then_inc(s["inputs_loaded"], 16)
                m.queue[0].prefetch(sp)
                sp.wait_ge(s["inputs_loaded"], 32)
        layers(m, a, rows, tiles)
        with m.stage("answer_stored", "stored") as (block, s):
            @block.sync
            def _(sp):
                sp.dma_start(out[0].rearrange("(t p) n -> p t n", p=P), m.x[:, :, :]).then_inc(s["stored"], 16)
                sp.wait_ge(s["stored"], 16)



def kernel(**inputs):
    import numpy as _np
    import concourse.bacc as _bacc
    from concourse import mybir as _mybir
    from concourse.bass_utils import run_bass_kernel_spmd as _run

    nc = _bacc.Bacc("TRN2", target_bir_lowering=False, num_devices=1)
    arrays, aps = {}, {}
    for name in USED:
        a = _np.ascontiguousarray(inputs[name])
        arrays[f"in_{name}"] = a
        aps[name] = nc.dram_tensor(f"in_{name}", a.shape, _mybir.dt.from_np(a.dtype), kind="ExternalInput").ap()
    table = const_table()
    arrays["constants_dram"] = table
    consts = nc.dram_tensor("constants_dram", table.shape, F32, kind="ExternalInput").ap()
    out = nc.dram_tensor("out_dram", (1, T, D), F32, kind="ExternalOutput").ap()
    rows = nc.dram_tensor("bias_rows", (HEADS, 2 * T), F32, kind="Internal").ap()
    tiles = nc.dram_tensor("bias_tiles", (HEADS, TT, P, T), F32, kind="Internal").ap()
    program(nc, aps, consts, out, rows, tiles)
    r = _run(nc, [arrays], core_ids=[0])
    return r.results[0]["out_dram"]
```
